# Optimizing a Trainium2 kernel written in Bass

```python
import jax, jax.numpy as jnp
from jax import lax
import numpy as np
import math

D_MODEL = 1024
BATCH = 1
SEQ = 512
DEPTH = 2

N_MIXERS = 2
N_ATT_LAYERS = (DEPTH + 1) // 2
N_HGRN_LAYERS = DEPTH // 2
FOX_HEADS = 16
FOX_HEAD_DIM = D_MODEL // FOX_HEADS
FOX_Q_BLOCK = 128
HGRN_EXPAND = 128
HGRN_HEADS = D_MODEL // HGRN_EXPAND
HGRN_DK = HGRN_EXPAND
HGRN_DV = D_MODEL // HGRN_HEADS
HGRN_CHUNK = 64
FFN_DIM = 2816
CONV_WIDTH = 3
RMS_EPS = 1e-6


def rmsnorm(x, g):
    x32 = x.astype(jnp.float32)
    y = x32 * lax.rsqrt(jnp.mean(x32 * x32, axis=-1, keepdims=True) + RMS_EPS)
    return (y * g.astype(jnp.float32)).astype(x.dtype)

def fox_mixer(h, w_in, b_f, w_out):
    B, S, D = h.shape
    H, hd, QB = FOX_HEADS, FOX_HEAD_DIM, FOX_Q_BLOCK
    nqb = S // QB
    proj = h @ w_in
    q, k, v, fl = jnp.split(proj, [D, 2 * D, 3 * D], axis=-1)
    logf = jax.nn.log_sigmoid((fl + b_f).astype(jnp.float32))
    c = jnp.cumsum(logf, axis=1).transpose(0, 2, 1)
    qb = q.reshape(B, nqb, QB, H, hd).transpose(1, 0, 3, 2, 4)
    k = k.reshape(B, S, H, hd).transpose(0, 2, 1, 3)
    v = v.reshape(B, S, H, hd).transpose(0, 2, 1, 3)
    cqb = c.reshape(B, H, nqb, QB).transpose(2, 0, 1, 3)
    starts = jnp.arange(nqb, dtype=jnp.int32) * QB
    s_pos = jnp.arange(S, dtype=jnp.int32)
    scale = 1.0 / np.sqrt(hd)

    def block(args):
        qi, cqi, st = args
        logits = jnp.einsum('bhqd,bhkd->bhqk', qi, k).astype(jnp.float32) * scale
        logits = logits + (cqi[..., :, None] - c[:, :, None, :])
        t_pos = st + jnp.arange(QB, dtype=jnp.int32)
        logits = jnp.where(s_pos[None, :] <= t_pos[:, None], logits, -jnp.inf)
        p = jax.nn.softmax(logits, axis=-1)
        return jnp.einsum('bhqk,bhkd->bhqd', p.astype(v.dtype), v)

    o = lax.map(block, (qb, cqb, starts))
    o = o.transpose(1, 0, 3, 2, 4).reshape(B, S, D)
    return o @ w_out

def hgrn2_mixer(h, w_in, lb, onorm_g, w_out):
    B, S, D = h.shape
    H, Dk, Dv, C = HGRN_HEADS, HGRN_DK, HGRN_DV, HGRN_CHUNK
    nc = S // C
    proj = h @ w_in
    q, fl, i, g = jnp.split(proj, 4, axis=-1)
    q = jax.nn.silu(q).astype(jnp.float32)
    f = lb + (1.0 - lb) * jax.nn.sigmoid(fl.astype(jnp.float32))
    k = 1.0 - f
    logf = jnp.log(f)

    def to_chunks(t, d):
        return t.reshape(B, nc, C, H, d).transpose(0, 3, 1, 2, 4)

    q, k, logf = to_chunks(q, Dk), to_chunks(k, Dk), to_chunks(logf, Dk)
    iv = to_chunks(i.astype(jnp.float32), Dv)
    b = jnp.cumsum(logf, axis=3)
    b_last = b[..., -1:, :]
    q_dec = q * jnp.exp(b)
    k_inv = k * jnp.exp(-b)
    k_state = k * jnp.exp(b_last - b)
    A = jnp.einsum('bhncd,bhnsd->bhncs', q_dec, k_inv)
    causal = jnp.tril(jnp.ones((C, C), dtype=bool))
    A = jnp.where(causal, A, 0.0)
    o_intra = jnp.einsum('bhncs,bhnsv->bhncv', A, iv)
    U = jnp.einsum('bhnsd,bhnsv->bhndv', k_state, iv)
    decay = jnp.exp(b_last[..., 0, :])

    def step(state, xs):
        dec, u = xs
        return dec[..., None] * state + u, state

    s0 = jnp.zeros((B, H, Dk, Dv), jnp.float32)
    _, s_prev = lax.scan(step, s0, (jnp.moveaxis(decay, 2, 0), jnp.moveaxis(U, 2, 0)))
    s_prev = jnp.moveaxis(s_prev, 0, 2)
    o = o_intra + jnp.einsum('bhncd,bhndv->bhncv', q_dec, s_prev)
    o = o.transpose(0, 2, 3, 1, 4).reshape(B, S, H, Dv)
    o = o * lax.rsqrt(jnp.mean(o * o, axis=-1, keepdims=True) + RMS_EPS)
    o = o * onorm_g.astype(jnp.float32).reshape(H, Dv)
    o = o.reshape(B, S, D).astype(h.dtype) * jax.nn.silu(g)
    return o @ w_out

def conv_ffn(h, w_up, conv_w, conv_b, w_down):
    S = h.shape[1]
    u = h @ w_up
    up = jnp.pad(u, ((0, 0), (CONV_WIDTH - 1, 0), (0, 0)))
    y = conv_b
    for j in range(CONV_WIDTH):
        y = y + conv_w[j] * up[:, j:j + S]
    gate, val = jnp.split(y, 2, axis=-1)
    return (jax.nn.silu(gate) * val) @ w_down

def first_inputs(seed: int = 0) -> dict:
    key = jax.random.key(seed)
    ks = jax.random.split(key, 16)
    D, F = D_MODEL, FFN_DIM
    nrm = lambda k, shape, s: jax.random.normal(k, shape, jnp.float32) * s
    return {
        "x": nrm(ks[0], (BATCH, SEQ, D), 1.0),
        "att_norm_g": 1.0 + nrm(ks[1], (N_ATT_LAYERS, D), 0.02),
        "att_w_in": nrm(ks[2], (N_ATT_LAYERS, D, 3 * D + FOX_HEADS), D ** -0.5),
        "att_b_f": 3.0 + nrm(ks[3], (N_ATT_LAYERS, FOX_HEADS), 0.5),
        "att_w_out": nrm(ks[4], (N_ATT_LAYERS, D, D), D ** -0.5),
        "hgrn_norm_g": 1.0 + nrm(ks[5], (N_HGRN_LAYERS, D), 0.02),
        "hgrn_w_in": nrm(ks[6], (N_HGRN_LAYERS, D, 4 * D), D ** -0.5),
        "hgrn_lb_logits": nrm(ks[7], (DEPTH, D), 0.1),
        "hgrn_onorm_g": 1.0 + nrm(ks[8], (N_HGRN_LAYERS, D), 0.02),
        "hgrn_w_out": nrm(ks[9], (N_HGRN_LAYERS, D, D), D ** -0.5),
        "ffn_norm_g": 1.0 + nrm(ks[10], (DEPTH, D), 0.02),
        "ffn_w_up": nrm(ks[11], (DEPTH, D, 2 * F), D ** -0.5),
        "ffn_conv_w": nrm(ks[12], (DEPTH, CONV_WIDTH, 2 * F), CONV_WIDTH ** -0.5),
        "ffn_conv_b": nrm(ks[13], (DEPTH, 2 * F), 0.02),
        "ffn_w_down": nrm(ks[14], (DEPTH, F, D), F ** -0.5),
        "final_norm_g": 1.0 + nrm(ks[15], (D,), 0.02),
    }

def first_block(x, att_norm_g, att_w_in, att_b_f, att_w_out, hgrn_norm_g, hgrn_w_in,
              hgrn_lb_logits, hgrn_onorm_g, hgrn_w_out, ffn_norm_g, ffn_w_up,
              ffn_conv_w, ffn_conv_b, ffn_w_down, final_norm_g):
    sm = jax.nn.softmax(hgrn_lb_logits.astype(jnp.float32), axis=0)
    lower_bounds = jnp.cumsum(sm, axis=0) - sm[0:1]
    for layer in range(DEPTH):
        j = layer // N_MIXERS
        if layer % N_MIXERS == 0:
            x = x + fox_mixer(rmsnorm(x, att_norm_g[j]), att_w_in[j], att_b_f[j], att_w_out[j])
        else:
            x = x + hgrn2_mixer(rmsnorm(x, hgrn_norm_g[j]), hgrn_w_in[j],
                                lower_bounds[layer], hgrn_onorm_g[j], hgrn_w_out[j])
        x = x + conv_ffn(rmsnorm(x, ffn_norm_g[layer]), ffn_w_up[layer], ffn_conv_w[layer],
                         ffn_conv_b[layer], ffn_w_down[layer])
    return rmsnorm(x, final_norm_g)


_first_inputs = first_inputs


def first_inputs(seed=0):
    import zlib

    import numpy as np

    out = dict(_first_inputs(seed))
    spreads = {}
    factors = {}
    for name, (base, spread) in spreads.items():
        noise = np.random.default_rng([zlib.crc32(name.encode()), seed]).standard_normal(out[name].shape)
        drawn = base * np.exp(spread * noise) if base else spread * noise
        out[name] = __import__('jax').numpy.asarray(drawn.astype(out[name].dtype))
    for name, factor in factors.items():
        out[name] = (out[name] * factor).astype(out[name].dtype)
    return out


_narrow_inputs = first_inputs


def first_inputs(seed=0):

    out = dict(_narrow_inputs(seed))
    wider = {'att_norm_g': 4.7,
     'hgrn_norm_g': 4.32,
     'hgrn_lb_logits': 9.69,
     'hgrn_onorm_g': 7.0,
     'ffn_norm_g': 3.04,
     'final_norm_g': 3.22}
    for name, times in wider.items():
        mean = out[name].mean()
        out[name] = (mean + times * (out[name] - mean)).astype(out[name].dtype)
    return out


MIX_WIDTH = D_MODEL
DIFF_HEADS = 4
DIFF_QK_DIM = 64
DIFF_V_DIM = 2 * DIFF_QK_DIM
A_QK = DIFF_HEADS * 2 * DIFF_QK_DIM
A_WIDTH = DIFF_HEADS * DIFF_V_DIM
Q_BLOCK = 128
B_WIDTH = MIX_WIDTH - A_WIDTH
CONV_GROUPS = 8
EVEN_IN = 2 * A_QK + A_WIDTH + 3 * B_WIDTH
EVEN_SPLITS = (A_QK, 2 * A_QK, 2 * A_QK + A_WIDTH,
               2 * A_QK + A_WIDTH + B_WIDTH, 2 * A_QK + A_WIDTH + 2 * B_WIDTH)
CHUNK = 128
SGU_WIDTH = MIX_WIDTH
SGU_GROUPS = 8
SGU_GROUP_DIM = SGU_WIDTH // SGU_GROUPS
ODD_IN = 2 * SGU_WIDTH
REL_BUCKETS = 32
REL_MAX_DIST = 128
FFN_HIDDEN = -(-8 * D_MODEL // (3 * 256)) * 256

N_EVEN = (DEPTH + 1) // 2
N_ODD = DEPTH // 2


def rms_norm(x, g, eps=RMS_EPS):
    xf = x.astype(jnp.float32)
    y = xf * lax.rsqrt(jnp.mean(xf * xf, axis=-1, keepdims=True) + eps)
    return (y * g.astype(jnp.float32)).astype(x.dtype)

def layer_norm(x, g, b, eps=1e-5):
    xf = x.astype(jnp.float32)
    mu = jnp.mean(xf, axis=-1, keepdims=True)
    xc = xf - mu
    y = xc * lax.rsqrt(jnp.mean(xc * xc, axis=-1, keepdims=True) + eps)
    return (y * g.astype(jnp.float32) + b.astype(jnp.float32)).astype(x.dtype)

def t5_bucket(q_pos, k_pos):
    n = jnp.maximum(q_pos[:, None] - k_pos[None, :], 0)
    max_exact = REL_BUCKETS // 2
    nf = jnp.maximum(n, 1).astype(jnp.float32)
    large = max_exact + (jnp.log(nf / max_exact) / math.log(REL_MAX_DIST / max_exact)
                         * (REL_BUCKETS - max_exact)).astype(jnp.int32)
    large = jnp.minimum(large, REL_BUCKETS - 1)
    return jnp.where(n < max_exact, n, large)

def diff_attention(q, k, v, rel_bias, lam, subln_g, lambda_init):
    bsz, s = q.shape[0], q.shape[1]
    nblk = s // Q_BLOCK
    lam = lam.astype(jnp.float32)
    lam_full = (jnp.exp(jnp.sum(lam[0] * lam[1])) - jnp.exp(jnp.sum(lam[2] * lam[3]))
                + lambda_init)
    scale = DIFF_QK_DIM ** -0.5
    k_pos = jnp.arange(s, dtype=jnp.int32)
    table = rel_bias.astype(jnp.float32)
    qb = q.reshape(bsz, nblk, Q_BLOCK, DIFF_HEADS, 2, DIFF_QK_DIM)
    qb = jnp.moveaxis(qb, 1, 0)
    starts = jnp.arange(nblk, dtype=jnp.int32) * Q_BLOCK

    def block(args):
        q_blk, start = args
        q_pos = start + jnp.arange(Q_BLOCK, dtype=jnp.int32)
        logits = jnp.einsum('bqhmd,bkhmd->bhmqk', q_blk, k).astype(jnp.float32) * scale
        bias = jnp.transpose(table[t5_bucket(q_pos, k_pos)], (2, 0, 1))
        logits = logits + bias[:, None]
        causal = q_pos[:, None] >= k_pos[None, :]
        logits = jnp.where(causal, logits, -jnp.inf)
        p = jax.nn.softmax(logits, axis=-1)
        attn = p[:, :, 0] - lam_full * p[:, :, 1]
        return jnp.einsum('bhqk,bkhe->bqhe', attn.astype(v.dtype), v)

    o = lax.map(block, (qb, starts))
    o = jnp.moveaxis(o, 0, 1).reshape(bsz, s, DIFF_HEADS, DIFF_V_DIM)
    o = rms_norm(o, subln_g, eps=1e-5) * (1.0 - lambda_init)
    return o.reshape(bsz, s, A_WIDTH)

def short_gated_conv(b_gate, c_gate, h, conv_w):
    z = c_gate * h
    y = lax.conv_general_dilated(
        z, conv_w[:, None, :].astype(z.dtype), window_strides=(1,),
        padding=((CONV_WIDTH - 1, 0),), dimension_numbers=('NWC', 'WIO', 'NWC'),
        feature_group_count=z.shape[-1])
    return b_gate * y

def spatial_gating(xn, w_in, ln_g, ln_b, sgu_w, sgu_b, w_out):
    z = jax.nn.gelu(xn @ w_in, approximate=False)
    u, v = jnp.split(z, 2, axis=-1)
    v = layer_norm(v, ln_g, ln_b)
    bsz, s = v.shape[0], v.shape[1]
    vc = v.reshape(bsz, s // CHUNK, CHUNK, SGU_GROUPS, SGU_GROUP_DIM)
    mask = jnp.tril(jnp.ones((CHUNK, CHUNK), dtype=bool))
    ws = jnp.where(mask[None], sgu_w, jnp.zeros_like(sgu_w))
    mixed = jnp.einsum('gts,bnsgc->bntgc', ws.astype(v.dtype), vc)
    mixed = mixed + jnp.transpose(sgu_b)[:, :, None].astype(v.dtype)
    mixed = mixed.reshape(bsz, s, SGU_WIDTH)
    return (u * mixed) @ w_out

def second_inputs(seed: int = 0) -> dict:
    key = jax.random.key(seed)
    ks = jax.random.split(key, 20)
    n = jax.random.normal
    f32 = jnp.float32
    return {
        "x": n(ks[0], (BATCH, SEQ, D_MODEL), f32),
        "rel_bias": 0.5 * n(ks[1], (REL_BUCKETS, DIFF_HEADS), f32),
        "w_in_even": n(ks[2], (N_EVEN, D_MODEL, EVEN_IN), f32) * D_MODEL ** -0.5,
        "diff_lambda": 0.1 * n(ks[3], (N_EVEN, 4, DIFF_QK_DIM), f32),
        "diff_subln_g": 1.0 + 0.02 * n(ks[4], (N_EVEN, DIFF_V_DIM), f32),
        "conv_w": n(ks[5], (N_EVEN, CONV_WIDTH, B_WIDTH), f32) * CONV_WIDTH ** -0.5,
        "w_out_even": n(ks[6], (N_EVEN, MIX_WIDTH, D_MODEL), f32) * MIX_WIDTH ** -0.5,
        "w_in_odd": n(ks[7], (N_ODD, D_MODEL, ODD_IN), f32) * D_MODEL ** -0.5,
        "sgu_ln_g": 1.0 + 0.02 * n(ks[8], (N_ODD, SGU_WIDTH), f32),
        "sgu_ln_b": 0.02 * n(ks[9], (N_ODD, SGU_WIDTH), f32),
        "sgu_w": n(ks[10], (N_ODD, SGU_GROUPS, CHUNK, CHUNK), f32) * CHUNK ** -0.5,
        "sgu_b": 1.0 + 0.02 * n(ks[11], (N_ODD, SGU_GROUPS, CHUNK), f32),
        "w_out_odd": n(ks[12], (N_ODD, SGU_WIDTH, D_MODEL), f32) * SGU_WIDTH ** -0.5,
        "norm_g": 1.0 + 0.02 * n(ks[13], (DEPTH, 4, D_MODEL), f32),
        "w_gate": n(ks[14], (DEPTH, D_MODEL, FFN_HIDDEN), f32) * D_MODEL ** -0.5,
        "w_up": n(ks[15], (DEPTH, D_MODEL, FFN_HIDDEN), f32) * D_MODEL ** -0.5,
        "w_down": n(ks[16], (DEPTH, FFN_HIDDEN, D_MODEL), f32) * FFN_HIDDEN ** -0.5,
    }

def second_block(x, rel_bias, w_in_even, diff_lambda, diff_subln_g, conv_w, w_out_even,
              w_in_odd, sgu_ln_g, sgu_ln_b, sgu_w, sgu_b, w_out_odd, norm_g,
              w_gate, w_up, w_down):
    bsz, s = x.shape[0], x.shape[1]
    for i in range(DEPTH):
        j = i // 2
        h = rms_norm(x, norm_g[i, 0])
        if i % 2 == 0:
            lambda_init = 0.8 - 0.6 * math.exp(-0.3 * i)
            p = h @ w_in_even[j]
            q, k, v, b_gate, c_gate, hc = jnp.split(p, EVEN_SPLITS, axis=-1)
            q = q.reshape(bsz, s, DIFF_HEADS, 2, DIFF_QK_DIM)
            k = k.reshape(bsz, s, DIFF_HEADS, 2, DIFF_QK_DIM)
            v = v.reshape(bsz, s, DIFF_HEADS, DIFF_V_DIM)
            a_out = diff_attention(q, k, v, rel_bias, diff_lambda[j], diff_subln_g[j],
                                   lambda_init)
            b_out = short_gated_conv(b_gate, c_gate, hc, conv_w[j])
            mix = jnp.concatenate([a_out, b_out], axis=-1) @ w_out_even[j]
        else:
            mix = spatial_gating(h, w_in_odd[j], sgu_ln_g[j], sgu_ln_b[j], sgu_w[j],
                                 sgu_b[j], w_out_odd[j])
        x = x + rms_norm(mix, norm_g[i, 1])
        h = rms_norm(x, norm_g[i, 2])
        f = (jax.nn.silu(h @ w_gate[i]) * (h @ w_up[i])) @ w_down[i]
        x = x + rms_norm(f, norm_g[i, 3])
    return x


_first_inputs_2 = second_inputs


def second_inputs(seed=0):
    import zlib

    import numpy as np

    out = dict(_first_inputs_2(seed))
    spreads = {}
    factors = {'diff_lambda': 8.0,
     'diff_subln_g': 4.456,
     'sgu_ln_g': 8.0,
     'sgu_ln_b': 8.0,
     'sgu_b': 6.545}
    for name, (base, spread) in spreads.items():
        noise = np.random.default_rng([zlib.crc32(name.encode()), seed]).standard_normal(out[name].shape)
        drawn = base * np.exp(spread * noise) if base else spread * noise
        out[name] = __import__('jax').numpy.asarray(drawn.astype(out[name].dtype))
    for name, factor in factors.items():
        out[name] = (out[name] * factor).astype(out[name].dtype)
    return out


_narrow_inputs_2 = second_inputs


def second_inputs(seed=0):

    out = dict(_narrow_inputs_2(seed))
    wider = {'diff_subln_g': 3.23, 'sgu_ln_g': 9.99, 'sgu_ln_b': 9.46, 'sgu_b': 7.83}
    for name, times in wider.items():
        mean = out[name].mean()
        out[name] = (mean + times * (out[name] - mean)).astype(out[name].dtype)
    return out


DEPTH_3 = 1

N_META = 16
GRID_W = 64
HEAD_DIM = 64
N_DIR = 2
RWKV_HEADS = 8
RWKV_WIDTH = RWKV_HEADS * HEAD_DIM
DECAY_LORA = 64
ICL_LORA = 64
GATE_LORA = 160
LNX_EPS = 64e-5
ATTN_Q_HEADS = 8
ATTN_KV_HEADS = 2
ATTN_GROUP = ATTN_Q_HEADS // ATTN_KV_HEADS
ATTN_Q_WIDTH = ATTN_Q_HEADS * HEAD_DIM
ATTN_KV_WIDTH = ATTN_KV_HEADS * HEAD_DIM
ROPE_THETA = 10000.0
AXIS_DIM = HEAD_DIM // 2
AXIS_FREQS = AXIS_DIM // 2
D_FF = 4 * D_MODEL
NORM_EPS = 1e-6
RWKV_IN_WIDTH = 3 * RWKV_WIDTH + N_DIR * DECAY_LORA + N_DIR * ICL_LORA + GATE_LORA
IN_WIDTH = RWKV_IN_WIDTH + ATTN_Q_WIDTH + 2 * ATTN_KV_WIDTH + 2 * D_MODEL
IN_SPLITS = [RWKV_IN_WIDTH,
             RWKV_IN_WIDTH + ATTN_Q_WIDTH,
             RWKV_IN_WIDTH + ATTN_Q_WIDTH + ATTN_KV_WIDTH,
             RWKV_IN_WIDTH + ATTN_Q_WIDTH + 2 * ATTN_KV_WIDTH,
             RWKV_IN_WIDTH + ATTN_Q_WIDTH + 2 * ATTN_KV_WIDTH + D_MODEL]
RWKV_SPLITS = [RWKV_WIDTH, 2 * RWKV_WIDTH, 3 * RWKV_WIDTH,
               3 * RWKV_WIDTH + N_DIR * DECAY_LORA,
               3 * RWKV_WIDTH + N_DIR * DECAY_LORA + N_DIR * ICL_LORA]


def rms_norm_3(x, g, eps=NORM_EPS):
    xf = x.astype(jnp.float32)
    y = xf * lax.rsqrt(jnp.mean(xf * xf, axis=-1, keepdims=True) + eps)
    return (y * g.astype(jnp.float32)).astype(x.dtype)

def centred_shift(p, mu):
    prev = jnp.pad(p[:, :-1], ((0, 0), (1, 0), (0, 0)))
    nxt = jnp.pad(p[:, 1:], ((0, 0), (0, 1), (0, 0)))
    return p + mu[0] * (prev - p) + mu[1] * (nxt - p)

def to_dirs(fwd, bwd):
    B, L, _ = fwd.shape
    t = jnp.stack([fwd, jnp.flip(bwd, axis=1)], axis=0).astype(jnp.float32)
    return t.reshape(N_DIR, B, L, RWKV_HEADS, HEAD_DIM).transpose(2, 0, 1, 3, 4)

def rwkv7_step(S, inp):
    r, w, k, v, kk, kka = inp
    sa = jnp.einsum('dbhij,dbhj->dbhi', S, -kk)
    S = S * w[..., None, :] + sa[..., :, None] * kka[..., None, :] + v[..., :, None] * k[..., None, :]
    y = jnp.einsum('dbhij,dbhj->dbhi', S, r)
    return S, y

def rwkv7_mixer(p, shift_mu, w0, w2, a0, a2, g2, k_k, k_a, r_k, lnx_g, lnx_b):
    B, L, _ = p.shape
    z = centred_shift(p, shift_mu)
    r, k, v, wd, ad, gd = jnp.split(z, RWKV_SPLITS, axis=-1)
    wd = wd.reshape(B, L, N_DIR, DECAY_LORA)
    ad = ad.reshape(B, L, N_DIR, ICL_LORA)
    w_log = -jax.nn.softplus(-(w0 + jnp.einsum('bldr,drc->bldc', jnp.tanh(wd), w2))) - 0.5
    decay = jnp.exp(-jnp.exp(w_log.astype(jnp.float32)))
    a = jax.nn.sigmoid(a0 + jnp.einsum('bldr,drc->bldc', ad, a2))
    g = jax.nn.sigmoid(gd) @ g2
    kk = (k * k_k).reshape(B, L, RWKV_HEADS, HEAD_DIM).astype(jnp.float32)
    kk = kk / jnp.maximum(jnp.linalg.norm(kk, axis=-1, keepdims=True), 1e-12)
    kk = kk.reshape(B, L, RWKV_WIDTH)
    k_dir = k[:, :, None, :] * (1.0 + (a - 1.0) * k_a)
    kka = kk[:, :, None, :] * a
    xs = (to_dirs(r, r), to_dirs(decay[:, :, 0], decay[:, :, 1]),
          to_dirs(k_dir[:, :, 0], k_dir[:, :, 1]), to_dirs(v, v), to_dirs(kk, kk),
          to_dirs(kka[:, :, 0], kka[:, :, 1]))
    S0 = jnp.zeros((N_DIR, B, RWKV_HEADS, HEAD_DIM, HEAD_DIM), jnp.float32)
    _, ys = lax.scan(rwkv7_step, S0, xs)
    ys = ys.transpose(1, 2, 0, 3, 4)
    y = ys[0] + jnp.flip(ys[1], axis=1)
    mu = jnp.mean(y, axis=-1, keepdims=True)
    var = jnp.mean(jnp.square(y - mu), axis=-1, keepdims=True)
    y = (y - mu) * lax.rsqrt(var + LNX_EPS)
    y = y * lnx_g.reshape(RWKV_HEADS, HEAD_DIM) + lnx_b.reshape(RWKV_HEADS, HEAD_DIM)
    rh = r.reshape(B, L, RWKV_HEADS, HEAD_DIM).astype(jnp.float32)
    kh = jnp.mean(k_dir, axis=2).reshape(B, L, RWKV_HEADS, HEAD_DIM).astype(jnp.float32)
    vh = v.reshape(B, L, RWKV_HEADS, HEAD_DIM).astype(jnp.float32)
    bonus = jnp.sum(rh * kh * r_k, axis=-1, keepdims=True) * vh
    out = (y + bonus).reshape(B, L, RWKV_WIDTH).astype(p.dtype)
    return out * g

def axial_rope_tables(n_tokens):
    rows = n_tokens // GRID_W
    inv_freq = ROPE_THETA ** (-jnp.arange(AXIS_FREQS, dtype=jnp.float32) * 2.0 / AXIS_DIM)
    row_ang = jnp.arange(rows, dtype=jnp.float32)[:, None] * inv_freq
    col_ang = jnp.arange(GRID_W, dtype=jnp.float32)[:, None] * inv_freq
    grid = jnp.stack([jnp.broadcast_to(row_ang[:, None, :], (rows, GRID_W, AXIS_FREQS)),
                      jnp.broadcast_to(col_ang[None, :, :], (rows, GRID_W, AXIS_FREQS))], axis=2)
    grid = grid.reshape(rows * GRID_W, 2, AXIS_FREQS)
    ang = jnp.concatenate([jnp.zeros((N_META, 2, AXIS_FREQS), jnp.float32), grid], axis=0)
    return jnp.cos(ang), jnp.sin(ang)

def apply_axial_rope(x, cos, sin):
    B, L, H, _ = x.shape
    xf = x.astype(jnp.float32).reshape(B, L, H, 2, 2, AXIS_FREQS)
    x1, x2 = xf[..., 0, :], xf[..., 1, :]
    c, s = cos[None, :, None], sin[None, :, None]
    out = jnp.stack([x1 * c - x2 * s, x2 * c + x1 * s], axis=-2)
    return out.reshape(B, L, H, HEAD_DIM).astype(x.dtype)

def gqa_axial_attention(q, k, v, q_norm_g, k_norm_g, cos, sin):
    B, L, _ = q.shape
    q = rms_norm_3(q.reshape(B, L, ATTN_Q_HEADS, HEAD_DIM), q_norm_g)
    k = rms_norm_3(k.reshape(B, L, ATTN_KV_HEADS, HEAD_DIM), k_norm_g)
    q = apply_axial_rope(q, cos, sin)
    k = apply_axial_rope(k, cos, sin)
    v = v.reshape(B, L, ATTN_KV_HEADS, HEAD_DIM)
    q = q.reshape(B, L, ATTN_KV_HEADS, ATTN_GROUP, HEAD_DIM) * (HEAD_DIM ** -0.5)

    def block_attn(qb):
        s = jnp.einsum('bqhgn,bkhn->bhgqk', qb, k).astype(jnp.float32)
        pr = jax.nn.softmax(s, axis=-1).astype(v.dtype)
        return jnp.einsum('bhgqk,bkhn->bqhgn', pr, v)

    meta_out = block_attn(q[:, :N_META])
    n_blk = (L - N_META) // Q_BLOCK
    qr = q[:, N_META:].reshape(B, n_blk, Q_BLOCK, ATTN_KV_HEADS, ATTN_GROUP, HEAD_DIM)
    real_out = lax.map(block_attn, qr.transpose(1, 0, 2, 3, 4, 5))
    real_out = real_out.transpose(1, 0, 2, 3, 4, 5).reshape(B, L - N_META, ATTN_Q_WIDTH)
    return jnp.concatenate([meta_out.reshape(B, N_META, ATTN_Q_WIDTH), real_out], axis=1)

def third_inputs(seed: int = 0) -> dict:
    key = jax.random.key(seed)
    ks = jax.random.split(key, 26)
    f32 = jnp.float32

    def nrm(k, shape, scale):
        return jax.random.normal(k, shape, f32) * scale

    ramp = jnp.linspace(-6.5, -1.5, RWKV_WIDTH, dtype=f32)
    return {
        "x": nrm(ks[0], (BATCH, SEQ, D_MODEL), 1.0),
        "meta_tokens": nrm(ks[1], (N_META, D_MODEL), 1.0),
        "mix_norm_g": 1.0 + nrm(ks[2], (DEPTH_3, D_MODEL), 0.02),
        "w_in": nrm(ks[3], (DEPTH_3, D_MODEL, IN_WIDTH), D_MODEL ** -0.5),
        "rwkv_shift": jax.random.uniform(ks[4], (DEPTH_3, 2, RWKV_IN_WIDTH), f32, 0.0, 0.5),
        "decay_w0": ramp + nrm(ks[5], (DEPTH_3, N_DIR, RWKV_WIDTH), 0.1),
        "decay_w2": nrm(ks[6], (DEPTH_3, N_DIR, DECAY_LORA, RWKV_WIDTH), 0.5 * DECAY_LORA ** -0.5),
        "icl_a0": nrm(ks[7], (DEPTH_3, N_DIR, RWKV_WIDTH), 0.1),
        "icl_a2": nrm(ks[8], (DEPTH_3, N_DIR, ICL_LORA, RWKV_WIDTH), 0.5 * ICL_LORA ** -0.5),
        "gate_w2": nrm(ks[9], (DEPTH_3, GATE_LORA, RWKV_WIDTH), GATE_LORA ** -0.5),
        "k_k": 0.85 + nrm(ks[10], (DEPTH_3, RWKV_WIDTH), 0.02),
        "k_a": 1.0 + nrm(ks[11], (DEPTH_3, RWKV_WIDTH), 0.02),
        "r_k": nrm(ks[12], (DEPTH_3, RWKV_HEADS, HEAD_DIM), 0.1),
        "lnx_g": 1.0 + nrm(ks[13], (DEPTH_3, RWKV_WIDTH), 0.02),
        "lnx_b": nrm(ks[14], (DEPTH_3, RWKV_WIDTH), 0.02),
        "q_norm_g": 1.0 + nrm(ks[15], (DEPTH_3, HEAD_DIM), 0.02),
        "k_norm_g": 1.0 + nrm(ks[16], (DEPTH_3, HEAD_DIM), 0.02),
        "w_branch_rwkv": nrm(ks[17], (DEPTH_3, RWKV_WIDTH, D_MODEL), RWKV_WIDTH ** -0.5),
        "w_branch_attn": nrm(ks[18], (DEPTH_3, ATTN_Q_WIDTH, D_MODEL), ATTN_Q_WIDTH ** -0.5),
        "w_out": nrm(ks[19], (DEPTH_3, D_MODEL, D_MODEL), D_MODEL ** -0.5),
        "ffn_norm_g": 1.0 + nrm(ks[20], (DEPTH_3, D_MODEL), 0.02),
        "w_ff1": nrm(ks[21], (DEPTH_3, D_MODEL, D_FF), D_MODEL ** -0.5),
        "w_ff2": nrm(ks[22], (DEPTH_3, D_FF, D_MODEL), D_FF ** -0.5),
        "final_norm_g": 1.0 + nrm(ks[23], (D_MODEL,), 0.02),
    }

def third_block(x, meta_tokens, mix_norm_g, w_in, rwkv_shift, decay_w0, decay_w2, icl_a0, icl_a2,
              gate_w2, k_k, k_a, r_k, lnx_g, lnx_b, q_norm_g, k_norm_g, w_branch_rwkv,
              w_branch_attn, w_out, ffn_norm_g, w_ff1, w_ff2, final_norm_g):
    B, n_tok, D = x.shape
    meta = jnp.broadcast_to(meta_tokens[None].astype(x.dtype), (B, N_META, D))
    h = jnp.concatenate([meta, x], axis=1)
    cos, sin = axial_rope_tables(n_tok)
    for i in range(DEPTH_3):
        u = rms_norm_3(h, mix_norm_g[i])
        proj = u @ w_in[i]
        p_rwkv, p_q, p_k, p_v, p_gate_a, p_gate_b = jnp.split(proj, IN_SPLITS, axis=-1)
        y_a = rwkv7_mixer(p_rwkv, rwkv_shift[i], decay_w0[i], decay_w2[i], icl_a0[i], icl_a2[i],
                          gate_w2[i], k_k[i], k_a[i], r_k[i], lnx_g[i], lnx_b[i])
        y_b = gqa_axial_attention(p_q, p_k, p_v, q_norm_g[i], k_norm_g[i], cos, sin)
        merged = (jax.nn.sigmoid(p_gate_a) * (y_a @ w_branch_rwkv[i])
                  + jax.nn.sigmoid(p_gate_b) * (y_b @ w_branch_attn[i]))
        h = h + merged @ w_out[i]
        f = rms_norm_3(h, ffn_norm_g[i]) @ w_ff1[i]
        h = h + jnp.square(jax.nn.relu(f)) @ w_ff2[i]
    return rms_norm_3(h, final_norm_g)[:, N_META:]


_first_inputs_3 = third_inputs


def third_inputs(seed=0):
    import zlib

    import numpy as np

    out = dict(_first_inputs_3(seed))
    spreads = {}
    factors = {'mix_norm_g': 4.69,
     'decay_w2': 6.252,
     'icl_a0': 4.411,
     'k_k': 64.0,
     'k_a': 7.569,
     'lnx_g': 64.0,
     'lnx_b': 64.0,
     'q_norm_g': 30.998,
     'k_norm_g': 24.391,
     'ffn_norm_g': 19.872,
     'final_norm_g': 8.432}
    for name, (base, spread) in spreads.items():
        noise = np.random.default_rng([zlib.crc32(name.encode()), seed]).standard_normal(out[name].shape)
        drawn = base * np.exp(spread * noise) if base else spread * noise
        out[name] = __import__('jax').numpy.asarray(drawn.astype(out[name].dtype))
    for name, factor in factors.items():
        out[name] = (out[name] * factor).astype(out[name].dtype)
    return out


_narrow_inputs_3 = third_inputs


def third_inputs(seed=0):

    out = dict(_narrow_inputs_3(seed))
    wider = {'k_k': 7.22, 'lnx_g': 4.07, 'lnx_b': 4.22, 'q_norm_g': 3.58, 'final_norm_g': 3.27}
    for name, times in wider.items():
        mean = out[name].mean()
        out[name] = (mean + times * (out[name] - mean)).astype(out[name].dtype)
    return out


def setup_inputs(seed=0):
    out = dict(first_inputs(seed))
    for name, value in second_inputs(seed + 1).items():
        if name != "x":
            out[name + "_2"] = value
    for name, value in third_inputs(seed + 2).items():
        if name != "x":
            out[name + "_3"] = value
    return out


def reference(
    x, att_norm_g, att_w_in, att_b_f, att_w_out, hgrn_norm_g, hgrn_w_in, hgrn_lb_logits,
    hgrn_onorm_g, hgrn_w_out, ffn_norm_g, ffn_w_up, ffn_conv_w, ffn_conv_b, ffn_w_down,
    final_norm_g, rel_bias_2, w_in_even_2, diff_lambda_2, diff_subln_g_2, conv_w_2,
    w_out_even_2, w_in_odd_2, sgu_ln_g_2, sgu_ln_b_2, sgu_w_2, sgu_b_2, w_out_odd_2, norm_g_2,
    w_gate_2, w_up_2, w_down_2, meta_tokens_3, mix_norm_g_3, w_in_3, rwkv_shift_3, decay_w0_3,
    decay_w2_3, icl_a0_3, icl_a2_3, gate_w2_3, k_k_3, k_a_3, r_k_3, lnx_g_3, lnx_b_3,
    q_norm_g_3, k_norm_g_3, w_branch_rwkv_3, w_branch_attn_3, w_out_3, ffn_norm_g_3, w_ff1_3,
    w_ff2_3, final_norm_g_3,
):
    x = first_block(
        x, att_norm_g, att_w_in, att_b_f, att_w_out, hgrn_norm_g, hgrn_w_in, hgrn_lb_logits,
        hgrn_onorm_g, hgrn_w_out, ffn_norm_g, ffn_w_up, ffn_conv_w, ffn_conv_b, ffn_w_down,
        final_norm_g,
    )
    x = second_block(
        x, rel_bias_2, w_in_even_2, diff_lambda_2, diff_subln_g_2, conv_w_2, w_out_even_2,
        w_in_odd_2, sgu_ln_g_2, sgu_ln_b_2, sgu_w_2, sgu_b_2, w_out_odd_2, norm_g_2, w_gate_2,
        w_up_2, w_down_2,
    )
    return third_block(
        x, meta_tokens_3, mix_norm_g_3, w_in_3, rwkv_shift_3, decay_w0_3, decay_w2_3, icl_a0_3,
        icl_a2_3, gate_w2_3, k_k_3, k_a_3, r_k_3, lnx_g_3, lnx_b_3, q_norm_g_3, k_norm_g_3,
        w_branch_rwkv_3, w_branch_attn_3, w_out_3, ffn_norm_g_3, w_ff1_3, w_ff2_3,
        final_norm_g_3,
    )


_drawn_inputs = setup_inputs


def setup_inputs(seed=0):
    import zlib

    import numpy as np

    out = dict(_drawn_inputs(seed))
    spreads = {}
    factors = {}
    for name, (base, spread) in spreads.items():
        noise = np.random.default_rng([zlib.crc32(name.encode()), seed]).standard_normal(out[name].shape)
        drawn = base * np.exp(spread * noise) if base else spread * noise
        out[name] = __import__('jax').numpy.asarray(drawn.astype(out[name].dtype))
    for name, factor in factors.items():
        out[name] = (out[name] * factor).astype(out[name].dtype)
    return out
```

```python
from contextlib import ExitStack

import numpy as np

import concourse.bass as bass
from concourse import mybir

F32 = mybir.dt.float32
F32R = mybir.dt.float32r
I32 = mybir.dt.int32
ALU = mybir.AluOpType
ACT = mybir.ActivationFunctionType
AX = mybir.AxisListType

BLOCKS = (1, 2, 3)
D = 1024
S = 512
KT = D // 128
PANEL = 2048
META = 16
TM = S + META
FFN = 2816
FT = FFN // 128
FFN_CHUNKS = ((0, 12), (12, 10))
FF3_CHUNKS = ((0, 12), (12, 12), (24, 8))
EPS = 1e-6
NEG = -1e30


class Engine:

    def __init__(self, ctx, nc, sems, e, tag):
        self.ctx, self.nc, self.sems, self.e, self.tag = ctx, nc, sems, e, tag
        self.n, self.off = {}, {}
        self.parity = 0

    def sem(self, name):
        if name not in self.sems:
            self.sems[name] = self.ctx.enter_context(self.nc.semaphore(name))
        return self.sems[name]

    def count(self, name, k):
        self.n[name] = self.n.get(name, 0) + k

    def adds(self, name, by=1):
        self.count(name, by)
        return by

    def due(self, name, k=1, less=0):
        self.count(name, k)
        return self.off.get(name, 0) + (self.n[name] - less)

    def settle(self):
        self.e.sem_inc(self.sem(self.tag + "_passed_waits"), 1)

    def loop(self, times, body, **per):
        if times <= 0:
            return
        if times == 1:
            body(0)
            return
        start = dict(self.n)
        with self.e.Fori(0, times) as i:
            for name, k in per.items():
                self.off[name] = i * k
            body(i)
            self.off = {}
        got = {k: v - start.get(k, 0) for k, v in self.n.items() if v != start.get(k, 0)}
        assert got == {k: v for k, v in per.items() if v}, f"{self.tag} loop counts {got}"
        for name, k in per.items():
            self.n[name] = start.get(name, 0) + times * k

    def stage_end(self):
        self.e.drain().then_inc(self.sem("stage_done"), 1)
        self.e.wait_ge(self.sem("stage_done"), self.due("stage_done", 4))


class Mem:

    def __init__(self, nc):
        self.nc, self.at = nc, (nc.sbuf_base + 31) // 32 * 32
        self.end = nc.sbuf_usable_end

    def new(self, name, shape, dt=F32):
        words = int(np.prod(shape[1:]))
        t = self.nc.alloc_sbuf_tensor_at(name, shape, dt, offset=self.at)
        t_at = self.at
        self.at += (4 * words + 31) // 32 * 32
        assert self.at <= self.end, (name, self.at, self.end)
        return t, t_at


def sl(i, k=1):
    return slice(i, i + k) if isinstance(i, int) else bass.ds(i, k)


class Bufs:
    pass


def split_act(K, P):
    if P.split_left <= 0:
        return
    s = P.split_par
    P.e.wait_ge(P.sem(f"weights_loaded{s}"), P.due(f"weights_loaded{s}", 16))
    P.e.activation(K.WH[:, s, :], K.W[:, s, :], ACT.Copy).then_inc(P.sem("hi_ready"), P.adds("hi_ready"))
    P.split_par ^= 1


def split_dve(K, P):
    if P.split_left <= 0:
        return
    s = P.split_par
    P.e.wait_ge(P.sem("hi_ready"), P.due("hi_ready"))
    P.e.tensor_tensor(K.WL[:, s, :], K.W[:, s, :], K.WH[:, s, :].bitcast(F32), ALU.subtract).then_inc(P.sem("weights_split"), P.adds("weights_split"))
    P.split_par ^= 1


def stream_sync(K, P, n_panels):
    for s in range(2):
        P.e.dma_start(K.W[:, s, :], K.weights[s]).then_inc(P.sem(f"weights_loaded{s}"), P.adds(f"weights_loaded{s}", 16))

    def body(i):
        for s in range(2):
            P.e.wait_ge(P.sem("weights_split"), P.due("weights_split"))
            src = K.weights[sl(2 * i + 2 + s)].rearrange("a p n -> (a p) n")
            P.e.dma_start(K.W[:, s, :], src).then_inc(P.sem(f"weights_loaded{s}"), P.adds(f"weights_loaded{s}", 16))

    pairs = (n_panels - 2) // 2
    P.loop(pairs, body, weights_split=2, weights_loaded0=16, weights_loaded1=16)
    for s in range((n_panels - 2) % 2):
        P.e.wait_ge(P.sem("weights_split"), P.due("weights_split"))
        P.e.dma_start(K.W[:, s, :], K.weights[2 * pairs + 2 + s]).then_inc(P.sem(f"weights_loaded{s}"), P.adds(f"weights_loaded{s}", 16))


def wide_pe(K, P, n, xh, xl, toks):
    def panel(_):
        s = P.parity
        P.e.wait_ge(P.sem("weights_split"), P.due("weights_split"))
        wh = K.WH[:, s, :].rearrange("p (k n) -> p k n", k=KT)
        wl = K.WL[:, s, :].rearrange("p (k n) -> p k n", k=KT)
        for t in range(2):
            P.e.wait_ge(P.sem(f"tile_evacuated{t}"), P.due(f"tile_evacuated{t}"))
            bank = 2 * (2 * s + t)
            c = slice(128 * t, 128 * t + 128)
            for part, (t0, tn) in enumerate(toks):
                out = K.PS[:, bank + part, 0:tn]
                for k in range(KT):
                    r = slice(t0, t0 + tn)
                    P.e.matmul(out, wh[:, k, c], xh[:, k, r], start=(k == 0), stop=False)
                    P.e.matmul(out, wh[:, k, c], xl[:, k, r], start=False, stop=False)
                    last = P.e.matmul(out, wl[:, k, c], xh[:, k, r], start=False, stop=(k == KT - 1))
            last.then_inc(P.sem("tile_done"), P.adds("tile_done"))
        P.parity ^= 1

    def body(i):
        panel(i)
        panel(i)

    P.loop(n // 2, body, weights_split=2, tile_evacuated0=2, tile_evacuated1=2, tile_done=4)
    if n % 2:
        panel(0)


def wide_evac(K, P, n, evac, split, per):
    def panel(p, s):
        evac(P, p, s, "first")
        split(K, P)
        evac(P, p, s, "rest")
        P.count("tile_evacuated0", 1)
        P.count("tile_evacuated1", 1)

    def body(i):
        panel(2 * i, P.parity)
        panel(2 * i + 1, P.parity ^ 1)

    counts = {k: 2 * v for k, v in dict(per, tile_evacuated0=1, tile_evacuated1=1).items()}
    if split is split_act:
        counts.update(hi_ready=2, weights_loaded0=16, weights_loaded1=16)
    else:
        counts.update(hi_ready=2, weights_split=2)
    left = P.split_left
    whole = min(n, left) if min(n, left) % 2 == 0 else min(n, left) - 1
    P.loop(whole // 2, body, **counts)
    P.split_left = left - whole
    for p in range(whole, n):
        panel(p, P.parity)
        P.parity ^= 1
        P.split_left -= 1


def narrow_pe(K, P, nk, xh, xl):
    def panel(k0, first, last_panel):
        s = P.parity
        P.e.wait_ge(P.sem("weights_split"), P.due("weights_split"))
        for kk in range(2):
            for t in range(8):
                c = slice(kk * D + 128 * t, kk * D + 128 * t + 128)
                out = K.PS[:, t, 0:S]
                k = sl(k0 + kk)
                h = xh[:, k, 0:S].rearrange("p a n -> p (a n)")
                l = xl[:, k, 0:S].rearrange("p a n -> p (a n)")
                P.e.matmul(out, K.WH[:, s, c], h, start=(first and kk == 0), stop=False)
                P.e.matmul(out, K.WH[:, s, c], l, start=False, stop=False)
                last = P.e.matmul(out, K.WL[:, s, c], h, start=False, stop=(last_panel and kk == 1))
            last.then_inc(P.sem("tile_done"), P.adds("tile_done"))
        P.parity ^= 1

    n = nk // 2
    panel(0, True, n == 1)
    pairs = max(0, (n - 2) // 2)

    def body(i):
        panel(4 * i + 2, False, False)
        panel(4 * i + 4, False, False)

    P.loop(pairs, body, weights_split=2, tile_done=4)
    for p in range(1 + 2 * pairs, n):
        panel(2 * p, False, p == n - 1)


def narrow_split(K, P, nk, split):
    def panel():
        if split is split_act:
            P.e.wait_ge(P.sem("tile_done"), P.due("tile_done", 2))
        split(K, P)
        P.parity ^= 1

    def body(i):
        panel()
        panel()

    left = P.split_left
    n = nk // 2
    whole = min(n, left) // 2 * 2
    if split is split_act:
        P.loop(whole // 2, body, tile_done=4, hi_ready=2, weights_loaded0=16, weights_loaded1=16)
    else:
        P.loop(whole // 2, body, hi_ready=2, weights_split=2)
    P.split_left = left - whole
    for p in range(whole, n):
        panel()
        P.split_left -= 1
    if split is split_dve:
        P.e.wait_ge(P.sem("tile_done"), P.due("tile_done", nk))


class Stage:

    def pe(self, K, P):
        pass

    def act(self, K, P):
        pass

    def dve(self, K, P):
        pass

    def pool(self, K, P):
        pass


class Wide(Stage):

    def __init__(self, n, xh, xl, toks=((0, S),)):
        self.n, self.xh, self.xl, self.toks = n, xh, xl, toks

    per_act = {}
    per_dve = {}

    def pe(self, K, P):
        wide_pe(K, P, self.n, self.xh, self.xl, self.toks)

    def act(self, K, P):
        wide_evac(K, P, self.n, lambda P, p, s, when: self.evac_act(K, P, p, s, when), split_act,
                  dict(self.per_act, tile_done=2))

    def dve(self, K, P):
        wide_evac(K, P, self.n, lambda P, p, s, when: self.evac_dve(K, P, p, s, when), split_dve,
                  dict(self.per_dve, tile_done=2))

    def evac_act(self, K, P, p, s, when):
        if when == "first":
            P.e.wait_ge(P.sem("tile_done"), P.due("tile_done", 2))

    def evac_dve(self, K, P, p, s, when):
        if when == "first":
            P.e.wait_ge(P.sem("tile_done"), P.due("tile_done", 2))


class Store(Wide):

    def __init__(self, n, xh, xl, dst, first=0, func=None, toks=((0, S),), off=0):
        super().__init__(n, xh, xl, toks)
        self.off = off
        self.dst, self.first, self.func = dst, first, func

    def both(self):
        return self.func is not None

    def evac_act(self, K, P, p, s, when):
        if when != "first":
            return
        for t in range(2):
            P.e.wait_ge(P.sem("tile_done"), P.due("tile_done"))
            if t and not self.both():
                continue
            for part, (t0, tn) in enumerate(self.toks):
                last = P.e.activation(self.dst[:, sl(2 * p + t + self.first), t0 - self.off:t0 - self.off + tn].rearrange("p a n -> p (a n)"),
                                      K.PS[:, 2 * (2 * s + t) + part, 0:tn], self.func or ACT.Copy)
            last.then_inc(P.sem(f"tile_evacuated{t}"), 1)

    def evac_dve(self, K, P, p, s, when):
        if when != "first":
            return
        P.e.wait_ge(P.sem("tile_done"), P.due("tile_done", 2))
        if self.both():
            return
        for part, (t0, tn) in enumerate(self.toks):
            last = P.e.tensor_copy(self.dst[:, sl(2 * p + 1 + self.first), t0 - self.off:t0 - self.off + tn].rearrange("p a n -> p (a n)"),
                                   K.PS[:, 2 * (2 * s + 1) + part, 0:tn])
        last.then_inc(P.sem("tile_evacuated1"), 1)


class Narrow(Stage):

    def __init__(self, nk, xh, xl, dst, add=True, off=0):
        self.nk, self.xh, self.xl, self.dst, self.add, self.off = nk, xh, xl, dst, add, off

    def pe(self, K, P):
        narrow_pe(K, P, self.nk, self.xh, self.xl)

    def act(self, K, P):
        narrow_split(K, P, self.nk, split_act)
        if not self.add:
            for t in range(0, 8, 2):
                P.e.activation(self.dst[:, t, 0:S], K.PS[:, t, 0:S], ACT.Copy)

    def dve(self, K, P):
        narrow_split(K, P, self.nk, split_dve)
        for t in range(8):
            d = self.dst[:, t, self.off:self.off + S]
            if self.add:
                P.e.tensor_tensor(d, d, K.PS[:, t, 0:S], ALU.add)
            elif t % 2:
                P.e.tensor_copy(d, K.PS[:, t, 0:S])


class Small(Stage):

    def __init__(self, w, m, bank=0, toks=((0, S),)):
        self.w, self.m, self.bank, self.toks = w, m, bank, toks

    def pe(self, K, P):
        for part, (t0, tn) in enumerate(self.toks):
            for k in range(KT):
                P.e.matmul(K.PS[0:self.m, self.bank + part, 0:tn], self.w[:, k, :], K.Y[:, k, t0:t0 + tn],
                           start=(k == 0), stop=(k == KT - 1))


class RmsNorm(Stage):

    def __init__(self, src, gain, toks=((0, S),), out=None, add=False, out_off=0, eps=EPS):
        self.src, self.gain, self.toks, self.out, self.add, self.eps = src, gain, toks, out, add, eps
        self.t0, self.t1 = toks[0][0], toks[-1][0] + toks[-1][1]
        self.out_off = out_off

    def act(self, K, P):
        for k in range(KT):
            P.e.activation(K.Y[:, k, self.t0:self.t1], self.src[:, k, self.t0:self.t1], ACT.Square).then_inc(P.sem("norm_squared"), P.adds("norm_squared"))
        P.e.wait_ge(P.sem("norm_inverse"), P.due("norm_inverse"))
        P.e.activation(K.R[:, self.t0:self.t1], K.R[:, self.t0:self.t1], ACT.Sqrt).then_inc(P.sem("norm_root"), P.adds("norm_root"))
        if self.out is None:
            for k in range(KT):
                P.e.wait_ge(P.sem("norm_scaled"), P.due("norm_scaled"))
                P.e.activation(K.XH[:, k, self.t0:self.t1], K.Y[:, k, self.t0:self.t1], ACT.Copy).then_inc(P.sem("norm_hi"), P.adds("norm_hi"))

    def pe(self, K, P):
        for k in range(KT):
            P.e.wait_ge(P.sem("norm_squared"), P.due("norm_squared"))
            for part, (t0, tn) in enumerate(self.toks):
                last = P.e.matmul(K.PS[:, part, 0:tn], K.inv_d[:, :], K.Y[:, k, t0:t0 + tn],
                                  start=(k == 0), stop=(k == KT - 1))
        last.then_inc(P.sem("norm_mean"), P.adds("norm_mean"))

    def dve(self, K, P):
        P.e.wait_ge(P.sem("norm_mean"), P.due("norm_mean"))
        for part, (t0, tn) in enumerate(self.toks):
            last = P.e.tensor_scalar(K.R[:, t0:t0 + tn], K.PS[:, part, 0:tn], self.eps, None, ALU.add)
        last.then_inc(P.sem("dve_order"), P.adds("dve_order"))
        P.e.wait_ge(P.sem("dve_order"), P.due("dve_order", 0))
        r = K.R[:, self.t0:self.t1]
        P.e.reciprocal(r, r).then_inc(P.sem("norm_inverse"), P.adds("norm_inverse"))
        P.e.wait_ge(P.sem("norm_root"), P.due("norm_root"))
        lag = 2
        for k in range(KT + lag):
            if k < KT:
                src = self.src[:, k, self.t0:self.t1]
                g = self.gain[:, k:k + 1]
                if self.out is None or self.add:
                    last = P.e.scalar_tensor_tensor(K.Y[:, k, self.t0:self.t1], src, g, r, ALU.mult, ALU.mult)
                    last.then_inc(P.sem("norm_scaled" if self.out is None else "norm_term"), P.adds("norm_scaled" if self.out is None else "norm_term"))
                else:
                    P.e.scalar_tensor_tensor(self.out[:, k, 0:self.t1 - self.t0], src, g, r, ALU.mult, ALU.mult)
            if k >= lag:
                y = K.Y[:, k - lag, self.t0:self.t1]
                if self.out is None:
                    P.e.wait_ge(P.sem("norm_hi"), P.due("norm_hi"))
                    P.e.tensor_tensor(K.XL[:, k - lag, self.t0:self.t1], y,
                                      K.XH[:, k - lag, self.t0:self.t1].bitcast(F32), ALU.subtract)
                elif self.add:
                    P.e.wait_ge(P.sem("norm_term"), P.due("norm_term", 0, less=min(lag, KT - 1 - (k - lag))))
                    o = self.out[:, k - lag, self.out_off + self.t0:self.out_off + self.t1]
                    P.e.tensor_tensor(o, o, y, ALU.add)


class GatedUp(Wide):

    def __init__(self, n, first, conv=None):
        super().__init__(n, None, None)
        self.c0, self.conv = first, conv
        if conv is None:
            self.per_act = self.per_dve = {"hidden_hi": 1}
        else:
            self.per_act = {"conv_seeded": 2, "gate_activated": 1, "hidden_ready": 1, "hidden_hi": 1}
            self.per_dve = dict(self.per_act, dve_order=2)

    def evac_act(self, K, P, p, s, when):
        ps = [K.PS[:, 2 * (2 * s + t), 0:S] for t in range(2)]
        if when == "first":
            if self.conv is None:
                P.e.wait_ge(P.sem("tile_done"), P.due("tile_done"))
                P.e.activation(K.SG[:, s, :], ps[0], ACT.Silu).then_inc(P.sem("tile_evacuated0"), 1)
                P.e.wait_ge(P.sem("tile_done"), P.due("tile_done"))
                return
            w, b = self.conv
            for t in range(2):
                c = sl(t * FT + self.c0 + p)
                P.e.wait_ge(P.sem("tile_done"), P.due("tile_done"))
                P.e.activation(K.CV[:, s, t, :], ps[t], ACT.Identity, bias=b[:, c], scale=w[2][:, c]).then_inc(P.sem("conv_seeded"), P.adds("conv_seeded"))
            P.e.wait_ge(P.sem("tile_evacuated0"), P.due("tile_evacuated0", 0, less=-3))
            P.e.activation(K.SG[:, s, :], K.CV[:, s, 0, :], ACT.Silu).then_inc(P.sem("gate_activated"), P.adds("gate_activated"))
        else:
            if self.conv is None:
                P.e.wait_ge(P.sem("tile_evacuated1"), P.due("tile_evacuated1", 0, less=-3))
            else:
                P.e.wait_ge(P.sem("hidden_ready"), P.due("hidden_ready"))
            P.e.activation(K.HH[:, sl(p), :].rearrange("p a n -> p (a n)"), K.HF[:, s, :], ACT.Copy).then_inc(P.sem("hidden_hi"), P.adds("hidden_hi"))

    def evac_dve(self, K, P, p, s, when):
        ps = [K.PS[:, 2 * (2 * s + t), 0:S] for t in range(2)]
        if when == "first":
            P.e.wait_ge(P.sem("tile_done"), P.due("tile_done", 2))
            if self.conv is None:
                P.e.wait_ge(P.sem("tile_evacuated0"), P.due("tile_evacuated0", 0, less=-3))
                last = P.e.tensor_tensor(K.HF[:, s, :], K.SG[:, s, :], ps[1], ALU.mult)
                last.then_inc(P.sem("tile_evacuated1"), 1)
            else:
                w, b = self.conv
                for t in range(2):
                    c = sl(t * FT + self.c0 + p)
                    y = K.CV[:, s, t, :]
                    P.e.wait_ge(P.sem("conv_seeded"), P.due("conv_seeded"))
                    P.e.scalar_tensor_tensor(y[:, 1:S], ps[t][:, 0:S - 1], w[1][:, c], y[:, 1:S], ALU.mult, ALU.add).then_inc(P.sem("dve_order"), P.adds("dve_order"))
                    P.e.wait_ge(P.sem("dve_order"), P.due("dve_order", 0))
                    last = P.e.scalar_tensor_tensor(y[:, 2:S], ps[t][:, 0:S - 2], w[0][:, c], y[:, 2:S], ALU.mult, ALU.add)
                    last.then_inc(P.sem(f"tile_evacuated{t}"), 1)
                P.e.wait_ge(P.sem("tile_evacuated1"), P.due("tile_evacuated1", 0, less=-3))
                P.e.wait_ge(P.sem("gate_activated"), P.due("gate_activated"))
                P.e.tensor_tensor(K.HF[:, s, :], K.SG[:, s, :], K.CV[:, s, 1, :], ALU.mult).then_inc(P.sem("hidden_ready"), P.adds("hidden_ready"))
        else:
            P.e.wait_ge(P.sem("hidden_hi"), P.due("hidden_hi"))
            h = sl(p)
            P.e.tensor_tensor(K.HL[:, h, :].rearrange("p a n -> p (a n)"), K.HF[:, s, :],
                              K.HH[:, h, :].rearrange("p a n -> p (a n)").bitcast(F32), ALU.subtract)


class SquaredReluUp(Wide):

    per_act = per_dve = {"hidden_ready": 2, "hidden_hi": 2}

    def evac_act(self, K, P, p, s, when):
        if when == "first":
            for t in range(2):
                P.e.wait_ge(P.sem("tile_done"), P.due("tile_done"))
                P.e.activation(K.CV[:, s, t, :], K.PS[:, 2 * (2 * s + t), 0:S], ACT.Relu)\
                   .then_inc(P.sem(f"tile_evacuated{t}"), 1)
        else:
            for t in range(2):
                P.e.wait_ge(P.sem("hidden_ready"), P.due("hidden_ready"))
                P.e.activation(K.HH[:, sl(2 * p + t), :].rearrange("p a n -> p (a n)"), K.CF[:, s, t, :], ACT.Copy).then_inc(P.sem("hidden_hi"), P.adds("hidden_hi"))

    def evac_dve(self, K, P, p, s, when):
        if when == "first":
            for t in range(2):
                P.e.wait_ge(P.sem("tile_done"), P.due("tile_done"))
                P.e.wait_ge(P.sem(f"tile_evacuated{t}"), P.due(f"tile_evacuated{t}", 0, less=-3))
                P.e.tensor_tensor(K.CF[:, s, t, :], K.CV[:, s, t, :], K.CV[:, s, t, :], ALU.mult).then_inc(P.sem("hidden_ready"), P.adds("hidden_ready"))
        else:
            for t in range(2):
                P.e.wait_ge(P.sem("hidden_hi"), P.due("hidden_hi"))
                h = sl(2 * p + t)
                P.e.tensor_tensor(K.HL[:, h, :].rearrange("p a n -> p (a n)"), K.CF[:, s, t, :],
                                  K.HH[:, h, :].rearrange("p a n -> p (a n)").bitcast(F32), ALU.subtract)


class ForgetGates(Small):

    def pe(self, K, P):
        super().pe(K, P)
        P.e.matmul(K.PS[0:16, 7, 0:2], K.ident[:, 0:16], K.ident[:, 0:2], start=True, stop=True).then_inc(P.sem("gates_projected"), P.adds("gates_projected"))

    def act(self, K, P):
        g = K.gate_rows
        P.e.wait_ge(P.sem("gates_projected"), P.due("gates_projected"))
        P.e.activation(g[0:16, 0, :], K.PS[0:16, 0, 0:S], ACT.Abs, bias=K.att_b_f[0:16, 0:1]).then_inc(P.sem("act_order"), P.adds("act_order"))
        P.e.wait_ge(P.sem("act_order"), P.due("act_order", 0))
        P.e.activation(g[0:16, 0, :], g[0:16, 0, :], ACT.Exp, scale=-1.0).then_inc(P.sem("act_order"), P.adds("act_order"))
        P.e.wait_ge(P.sem("act_order"), P.due("act_order", 0))
        P.e.activation(g[0:16, 0, :], g[0:16, 0, :], ACT.Ln, bias=K.one_col[0:16, 0:1]).then_inc(P.sem("log_term"), P.adds("log_term"))

    def dve(self, K, P):
        g = K.gate_rows
        P.e.wait_ge(P.sem("gates_projected"), P.due("gates_projected"))
        P.e.wait_ge(P.sem("log_term"), P.due("log_term"))
        P.e.tensor_scalar(g[0:16, 1, :], K.PS[0:16, 0, 0:S], K.att_b_f[0:16, 0:1], 0.0, ALU.add, ALU.min).then_inc(P.sem("dve_order"), P.adds("dve_order"))
        P.e.wait_ge(P.sem("dve_order"), P.due("dve_order", 0))
        P.e.tensor_tensor(g[0:16, 1, :], g[0:16, 1, :], g[0:16, 0, :], ALU.subtract).then_inc(P.sem("dve_order"), P.adds("dve_order"))
        P.e.wait_ge(P.sem("dve_order"), P.due("dve_order", 0))
        P.e.tensor_tensor_scan(K.c_rows[0:16, :], K.ones_row[0:16, :], g[0:16, 1, :], 0.0, ALU.mult, ALU.add)


class ForgettingAttention(Stage):

    UNITS = [(u, b) for u in range(2) for b in range(S // 128)]

    def dve(self, K, P):
        P.e.tensor_copy(K.one_row16[0:16, :], K.ones_row[0:16, :]).then_inc(P.sem("att_staged"), P.adds("att_staged"))

        def body(i):
            t = sl(i)
            for u in range(2):
                h = sl(2 * i + u)
                if True:
                    P.e.tensor_scalar(K.cm[0:16, u, :], K.c_rows[0:16, :], K.ident[0:16, h], None, ALU.mult).then_inc(P.sem("dve_order"), P.adds("dve_order"))
                    P.e.wait_ge(P.sem("dve_order"), P.due("dve_order", 0))
                    P.e.tensor_scalar(K.ncm[0:16, u, :], K.cm[0:16, u, :], -1.0, None, ALU.mult).then_inc(P.sem("att_staged"), P.adds("att_staged"))
            for n, (u, b) in enumerate(self.UNITS):
                s, nk = n % 2, 128 * (b + 1)
                P.e.wait_ge(P.sem("logits_done"), P.due("logits_done"))
                P.e.reduce_max(K.st[:, s, 0:1], K.PS[:, s, 0:nk], AX.X).then_inc(P.sem("dve_order"), P.adds("dve_order"))
                P.e.wait_ge(P.sem("dve_order"), P.due("dve_order", 0))
                P.e.tensor_scalar(K.st[:, s, 1:2], K.st[:, s, 0:1], -1.0, None, ALU.mult).then_inc(P.sem("max_negated"), P.adds("max_negated"))
                P.e.wait_ge(P.sem("exp_done"), P.due("exp_done"))
                P.e.reciprocal(K.st[:, s, 3:4], K.st[:, s, 2:3]).then_inc(P.sem("dve_order"), P.adds("dve_order"))
                P.e.wait_ge(P.sem("dve_order"), P.due("dve_order", 0))
                P.e.tensor_scalar(K.pr[:, s, 0:nk], K.pr[:, s, 0:nk], K.st[:, s, 3:4], None, ALU.mult).then_inc(P.sem("probs_ready"), P.adds("probs_ready"))
                P.e.wait_ge(P.sem("probs_transposed"), P.due("probs_transposed"))
                P.e.tensor_copy(K.pT[:, s, 0:nk], K.PS[:, 2 + s, 0:nk]).then_inc(P.sem("probsT_ready"), P.adds("probsT_ready"))
            P.e.wait_ge(P.sem("att_out_done"), P.due("att_out_done"))
            P.e.wait_ge(P.sem("att_out_hi"), P.due("att_out_hi"))
            P.e.tensor_tensor(K.XL[:, t, 0:S].rearrange("p a n -> p (a n)"), K.PS[:, 4, 0:S],
                                    K.XH[:, t, 0:S].rearrange("p a n -> p (a n)").bitcast(F32), ALU.subtract).then_inc(P.sem("att_out_lo"), P.adds("att_out_lo"))

        P.loop(8, body, dve_order=18, att_staged=2, logits_done=8, max_negated=8, exp_done=8, probs_ready=8,
               probs_transposed=8, probsT_ready=8, att_out_done=1, att_out_hi=1, att_out_lo=1)

    def act(self, K, P):
        def body(i):
            t = sl(i)
            for u in range(2):
                half = slice(64 * u, 64 * u + 64)
                P.e.activation(K.qs[0:64, u, :], K.q1[half, t, :].rearrange("p a n -> p (a n)"), ACT.Copy, scale=0.125).then_inc(P.sem("qk_staged"), P.adds("qk_staged"))
                P.e.activation(K.ks[0:64, u, :], K.k1[half, t, :].rearrange("p a n -> p (a n)"), ACT.Copy).then_inc(P.sem("qk_staged"), P.adds("qk_staged"))
            P.e.activation(K.vs[:, :], K.v1[:, t, :].rearrange("p a n -> p (a n)"), ACT.Copy).then_inc(P.sem("v_staged"), P.adds("v_staged"))
            P.e.wait_ge(P.sem("v_transposed"), P.due("v_transposed"))
            P.e.activation(K.vT[:, :], K.PS[:, 5, :], ACT.Copy).then_inc(P.sem("vT_ready"), P.adds("vT_ready"))
            for n, (u, b) in enumerate(self.UNITS):
                s, nk = n % 2, 128 * (b + 1)
                P.e.wait_ge(P.sem("logits_done"), P.due("logits_done"))
                P.e.wait_ge(P.sem("max_negated"), P.due("max_negated"))
                P.e.activation(K.pr[:, s, 0:nk], K.PS[:, s, 0:nk], ACT.Exp, bias=K.st[:, s, 1:2],
                                     accum_out=K.st[:, s, 2:3]).then_inc(P.sem("exp_done"), P.adds("exp_done"))
            P.e.wait_ge(P.sem("att_out_done"), P.due("att_out_done"))
            P.e.activation(K.XH[:, t, 0:S].rearrange("p a n -> p (a n)"), K.PS[:, 4, 0:S], ACT.Copy).then_inc(P.sem("att_out_hi"), P.adds("att_out_hi"))

        P.loop(8, body, qk_staged=4, v_staged=1, v_transposed=1, vT_ready=1, logits_done=8, max_negated=8, exp_done=8,
               att_out_done=1, att_out_hi=1)

    def pe(self, K, P):
        P.e.wait_ge(P.sem("att_staged"), P.due("att_staged"))

        def logits(n):
            u, b = self.UNITS[n]
            s, nk, q = n % 2, 128 * (b + 1), slice(128 * b, 128 * b + 128)
            out = K.PS[:, s, 0:nk]
            P.e.matmul(out, K.qs[0:64, u, q], K.ks[0:64, u, 0:nk], start=True, stop=False)
            P.e.matmul(out, K.cm[0:16, u, q], K.one_row16[0:16, 0:nk], start=False, stop=False)
            P.e.matmul(out, K.one_row16[0:16, 0:128], K.ncm[0:16, u, 0:nk], start=False, stop=False)
            P.e.matmul(K.PS[:, s, nk - 128:nk], K.ident[:, :], K.causal[:, :], start=False, stop=True).then_inc(P.sem("logits_done"), P.adds("logits_done"))

        def body(i):
            P.e.wait_ge(P.sem("v_staged"), P.due("v_staged"))
            for b in range(4):
                last = P.e.transpose(K.PS[:, 5, 128 * b:128 * b + 128], K.vs[:, 128 * b:128 * b + 128], K.ident[:, :])
            last.then_inc(P.sem("v_transposed"), P.adds("v_transposed"))
            P.e.wait_ge(P.sem("qk_staged"), P.due("qk_staged", 4))
            P.e.wait_ge(P.sem("att_staged"), P.due("att_staged", 2))
            logits(0)
            for n, (u, b) in enumerate(self.UNITS):
                if n + 1 < len(self.UNITS):
                    if n >= 1:
                        P.e.wait_ge(P.sem("exp_done"), P.due("exp_done", 0))
                    logits(n + 1)
                s = n % 2
                P.e.wait_ge(P.sem("probs_ready"), P.due("probs_ready"))
                P.e.wait_ge(P.sem("exp_done"), P.due("exp_done"))
                for kb in range(b + 1):
                    c = slice(128 * kb, 128 * kb + 128)
                    last = P.e.transpose(K.PS[:, 2 + s, c], K.pr[:, s, c], K.ident[:, :])
                last.then_inc(P.sem("probs_transposed"), P.adds("probs_transposed"))
                P.e.wait_ge(P.sem("probsT_ready"), P.due("probsT_ready"))
                if n == 0:
                    P.e.wait_ge(P.sem("vT_ready"), P.due("vT_ready"))
                for kb in range(b + 1):
                    last = P.e.matmul(K.PS[64 * u:64 * u + 64, 4, 128 * b:128 * b + 128],
                                      K.vT[:, 128 * kb + 64 * u:128 * kb + 64 * u + 64],
                                      K.pT[:, s, 128 * kb:128 * kb + 128], start=(kb == 0), stop=(kb == b))
            last.then_inc(P.sem("att_out_done"), P.adds("att_out_done"))
            P.e.wait_ge(P.sem("att_out_lo"), P.due("att_out_lo"))

        P.loop(8, body, v_staged=1, v_transposed=1, qk_staged=4, att_staged=2, logits_done=8, exp_done=8,
               probs_ready=8, probs_transposed=8, probsT_ready=8, vT_ready=1, att_out_done=1, att_out_lo=1)


class LowerBounds(Stage):

    def dve(self, K, P):
        a, b, m, t = K.lb_logits[:, 0:8], K.lb_logits[:, 8:16], K.lbt[:, 0:8], K.lbt
        P.e.tensor_tensor(m, a, b, ALU.max).then_inc(P.sem("dve_order"), P.adds("dve_order"))
        P.e.wait_ge(P.sem("dve_order"), P.due("dve_order", 0))
        P.e.tensor_tensor(t[:, 8:16], a, m, ALU.subtract)
        P.e.tensor_tensor(t[:, 16:24], b, m, ALU.subtract).then_inc(P.sem("lb_shifted"), P.adds("lb_shifted"))
        P.e.wait_ge(P.sem("lb_exp"), P.due("lb_exp"))
        P.e.tensor_tensor(t[:, 0:8], t[:, 8:16], t[:, 16:24], ALU.add).then_inc(P.sem("dve_order"), P.adds("dve_order"))
        P.e.wait_ge(P.sem("dve_order"), P.due("dve_order", 0))
        P.e.reciprocal(t[:, 0:8], t[:, 0:8]).then_inc(P.sem("dve_order"), P.adds("dve_order"))
        P.e.wait_ge(P.sem("dve_order"), P.due("dve_order", 0))
        P.e.tensor_tensor(K.lb[:, 0:8], t[:, 16:24], t[:, 0:8], ALU.mult)
        P.e.tensor_tensor(K.lb[:, 8:16], t[:, 8:16], t[:, 0:8], ALU.mult)

    def act(self, K, P):
        P.e.wait_ge(P.sem("lb_shifted"), P.due("lb_shifted"))
        P.e.activation(K.lbt[:, 8:24], K.lbt[:, 8:24], ACT.Exp).then_inc(P.sem("lb_exp"), P.adds("lb_exp"))


class Hgrn(Stage):

    def dve(self, K, P):
        P.e.memset(K.sp[:, 0, :], 0.0)

        def body(i):
            t = sl(i)
            f = K.f1[:, t, :].rearrange("p a n -> p (a n)")
            q = K.q1h[:, t, :].rearrange("p a n -> p (a n)")
            P.e.tensor_scalar(K.h_f[:, :], f, K.lb[:, sl(i + 8)], K.lb[:, t], ALU.mult, ALU.add).then_inc(P.sem("dve_order"), P.adds("dve_order"))
            P.e.wait_ge(P.sem("dve_order"), P.due("dve_order", 0))
            P.e.tensor_scalar(K.h_k[:, :], K.h_f[:, :], -1.0, 1.0, ALU.mult, ALU.add).then_inc(P.sem("f_ready"), P.adds("f_ready"))
            P.e.wait_ge(P.sem("logf_ready"), P.due("logf_ready"))
            P.e.tensor_tensor_scan(K.h_b[:, :], K.reset64[:, :], K.h_lf[:, :], 0.0, ALU.mult, ALU.add).then_inc(P.sem("dve_order"), P.adds("dve_order"))
            P.e.wait_ge(P.sem("dve_order"), P.due("dve_order", 0))
            b3 = K.h_b[:, :].rearrange("p (n c) -> p n c", c=64)
            P.e.tensor_tensor(K.h_lf[:, :].rearrange("p (n c) -> p n c", c=64),
                                    b3[:, :, 63:64].broadcast_to([128, 8, 64]), b3, ALU.subtract).then_inc(P.sem("b_ready"), P.adds("b_ready"))
            P.e.wait_ge(P.sem("exps_ready"), P.due("exps_ready"))
            P.e.tensor_tensor(K.h_ks[:, :], K.h_k[:, :], K.h_lf[:, :], ALU.mult)
            P.e.tensor_tensor(K.h_qd[:, :], q, K.h_eb[:, :], ALU.mult)
            P.e.tensor_tensor(K.h_ki[:, :], K.h_k[:, :], K.h_en[:, :], ALU.mult).then_inc(P.sem("keys_ready"), P.adds("keys_ready"))
            P.e.wait_ge(P.sem("ksT_done"), P.due("ksT_done"))
            P.e.tensor_copy(K.ksT[:, :, :].rearrange("p n c -> p (n c)"), K.PS[:, 2, :]).then_inc(P.sem("ksT_ready"), P.adds("ksT_ready"))
            P.e.wait_ge(P.sem("A_done"), P.due("A_done"))
            P.e.tensor_tensor(K.aT[:, :], K.PS[:, 4, 0:256], K.causal64[:, 0:256], ALU.mult).then_inc(P.sem("A_ready"), P.adds("A_ready"))
            P.e.wait_ge(P.sem("U_done"), P.due("U_done"))
            for n in range(7):
                ins = P.e.scalar_tensor_tensor(K.sp[:, n + 1, :], K.sp[:, n, :], K.h_eb[:, 64 * n + 63:64 * n + 64],
                                               K.PS[:, 5 + n % 2, 128 * (n // 2):128 * (n // 2) + 128], ALU.mult, ALU.add)
                if n < 6:
                    ins.then_inc(P.sem("dve_order"), P.adds("dve_order"))
                    P.e.wait_ge(P.sem("dve_order"), P.due("dve_order", 0))
                else:
                    ins.then_inc(P.sem("states_ready"), P.adds("states_ready"))
            P.e.wait_ge(P.sem("o_mean"), P.due("o_mean"))
            P.e.tensor_scalar(K.R[:, 0:S], K.PS[:, 0, :], EPS, None, ALU.add).then_inc(P.sem("dve_order"), P.adds("dve_order"))
            P.e.wait_ge(P.sem("dve_order"), P.due("dve_order", 0))
            P.e.reciprocal(K.R[:, 0:S], K.R[:, 0:S]).then_inc(P.sem("o_inverse"), P.adds("o_inverse"))
            P.e.wait_ge(P.sem("o_root"), P.due("o_root"))
            for u in range(2):
                last = P.e.scalar_tensor_tensor(K.halves(K.h_b, u), K.halves_ps(u), K.p["hgrn_onorm_g"][:, t],
                                                K.halves(K.R, u), ALU.mult, ALU.mult)
            last.then_inc(P.sem("dve_order"), P.adds("dve_order"))
            P.e.wait_ge(P.sem("dve_order"), P.due("dve_order", 0))
            P.e.tensor_tensor(K.h_b[:, :], K.h_b[:, :], K.g1[:, t, :].rearrange("p a n -> p (a n)"), ALU.mult).then_inc(P.sem("o_gated"), P.adds("o_gated"))
            P.e.wait_ge(P.sem("o_hi"), P.due("o_hi"))
            P.e.tensor_tensor(K.XL[:, t, 0:S].rearrange("p a n -> p (a n)"), K.h_b[:, :],
                                    K.XH[:, t, 0:S].rearrange("p a n -> p (a n)").bitcast(F32), ALU.subtract).then_inc(P.sem("o_lo"), P.adds("o_lo"))

        P.loop(8, body, dve_order=10, f_ready=1, logf_ready=1, b_ready=1, exps_ready=1, keys_ready=1, ksT_done=1,
               ksT_ready=1, A_done=1, A_ready=1, U_done=1, states_ready=1, o_mean=1, o_inverse=1, o_root=1, o_gated=1,
               o_hi=1, o_lo=1)

    def act(self, K, P):
        def body(i):
            t = sl(i)
            P.e.activation(K.h_i[:, :], K.i1[:, t, :].rearrange("p a n -> p (a n)"), ACT.Copy).then_inc(P.sem("i_staged"), P.adds("i_staged"))
            P.e.wait_ge(P.sem("f_ready"), P.due("f_ready"))
            P.e.activation(K.h_lf[:, :], K.h_f[:, :], ACT.Ln).then_inc(P.sem("logf_ready"), P.adds("logf_ready"))
            P.e.wait_ge(P.sem("b_ready"), P.due("b_ready"))
            P.e.activation(K.h_eb[:, :], K.h_b[:, :], ACT.Exp)
            P.e.activation(K.h_en[:, :], K.h_b[:, :], ACT.Exp, scale=-1.0)
            P.e.activation(K.h_lf[:, :], K.h_lf[:, :], ACT.Exp).then_inc(P.sem("exps_ready"), P.adds("exps_ready"))
            P.e.wait_ge(P.sem("iT_done"), P.due("iT_done"))
            P.e.activation(K.iT[:, :, :].rearrange("p n c -> p (n c)"), K.PS[:, 0, :], ACT.Copy).then_inc(P.sem("iT_ready"), P.adds("iT_ready"))
            P.e.wait_ge(P.sem("o_done"), P.due("o_done"))
            for u in range(2):
                last = P.e.activation(K.halves(K.h_en, u), K.halves_ps(u), ACT.Square)
            last.then_inc(P.sem("o_squared"), P.adds("o_squared"))
            P.e.wait_ge(P.sem("o_inverse"), P.due("o_inverse"))
            P.e.activation(K.R[:, 0:S], K.R[:, 0:S], ACT.Sqrt).then_inc(P.sem("o_root"), P.adds("o_root"))
            P.e.wait_ge(P.sem("o_gated"), P.due("o_gated"))
            P.e.activation(K.XH[:, t, 0:S].rearrange("p a n -> p (a n)"), K.h_b[:, :], ACT.Copy).then_inc(P.sem("o_hi"), P.adds("o_hi"))
            P.e.wait_ge(P.sem("o_lo"), P.due("o_lo"))

        P.loop(8, body, i_staged=1, f_ready=1, logf_ready=1, b_ready=1, exps_ready=1, iT_done=1, iT_ready=1, o_done=1,
               o_squared=1, o_inverse=1, o_root=1, o_gated=1, o_hi=1, o_lo=1)

    def pe(self, K, P):
        def body(i):
            P.e.wait_ge(P.sem("i_staged"), P.due("i_staged"))
            for j in range(4):
                c = slice(128 * j, 128 * j + 128)
                last = P.e.transpose(K.PS[:, 0, c], K.h_i[:, c], K.ident[:, :])
            last.then_inc(P.sem("iT_done"), P.adds("iT_done"))
            P.e.wait_ge(P.sem("keys_ready"), P.due("keys_ready"))
            for j in range(4):
                c = slice(128 * j, 128 * j + 128)
                last = P.e.transpose(K.PS[:, 2, c], K.h_ks[:, c], K.ident[:, :])
            last.then_inc(P.sem("ksT_done"), P.adds("ksT_done"))
            chunks = [(n, slice(64 * (n % 2), 64 * (n % 2) + 64), n // 2, slice(64 * n, 64 * n + 64)) for n in range(8)]
            for n, half, j, c in chunks:
                last = P.e.matmul(K.PS[half, 4, 64 * j:64 * j + 64], K.h_ki[:, c], K.h_qd[:, c], start=True, stop=True)
            last.then_inc(P.sem("A_done"), P.adds("A_done"))
            P.e.wait_ge(P.sem("iT_ready"), P.due("iT_ready"))
            P.e.wait_ge(P.sem("ksT_ready"), P.due("ksT_ready"))
            for n, half, j, c in chunks[:7]:
                last = P.e.matmul(K.PS[:, 5 + n % 2, 128 * j:128 * j + 128], K.ksT[half, j, :], K.iT[half, j, :],
                                  start=True, stop=True)
            last.then_inc(P.sem("U_done"), P.adds("U_done"))
            P.e.wait_ge(P.sem("A_ready"), P.due("A_ready"))
            P.e.wait_ge(P.sem("states_ready"), P.due("states_ready"))
            for n, half, j, c in chunks:
                out = K.PS[:, (7, 3)[n % 2], 64 * j:64 * j + 64]
                P.e.matmul(out, K.iT[half, j, :], K.aT[half, 64 * j:64 * j + 64], start=True, stop=False)
                last = P.e.matmul(out, K.sp[:, n, :], K.h_qd[:, c], start=False, stop=True)
            last.then_inc(P.sem("o_done"), P.adds("o_done"))
            P.e.wait_ge(P.sem("o_squared"), P.due("o_squared"))
            P.e.matmul(K.PS[:, 0, :], K.inv_dv[:, :], K.h_en[:, :], start=True, stop=True).then_inc(P.sem("o_mean"), P.adds("o_mean"))
            P.e.wait_ge(P.sem("o_gated"), P.due("o_gated"))

        P.loop(8, body, i_staged=1, iT_done=1, keys_ready=1, ksT_done=1, A_done=1, iT_ready=1, ksT_ready=1, U_done=1,
               A_ready=1, states_ready=1, o_done=1, o_squared=1, o_mean=1, o_gated=1)


BIAS_W = 640


class Load(Stage):

    def __init__(self, loads):
        self.loads = loads

    def act(self, K, P):
        for dst, src in self.loads:
            P.e.dma_start(dst, src).then_inc(P.sem("inputs_loaded"), P.adds("inputs_loaded", 16))
        P.e.wait_ge(P.sem("inputs_loaded"), P.due("inputs_loaded", 0))


class BiasTable(Stage):

    def dve(self, K, P):
        P.e.memset(K.bias_t[32:33, :], NEG).then_inc(P.sem("bias_staged"), P.adds("bias_staged"))
        P.e.wait_ge(P.sem("bias_rows_done"), P.due("bias_rows_done"))
        P.e.tensor_copy(K.bias_rows[0:4, 0:512], K.PS[0:4, 0, :])
        P.e.tensor_copy(K.bias_rows[0:4, 512:BIAS_W], K.PS[0:4, 1, 0:BIAS_W - 512]).then_inc(P.sem("bias_rows_ready"), P.adds("bias_rows_ready"))
        lam = K.lam[:, :].rearrange("p (a b c) -> p a b c", a=2, b=2)
        P.e.tensor_tensor(K.lam_prod[:, :].rearrange("p (a c) -> p a c", a=2), lam[:, :, 0, :], lam[:, :, 1, :], ALU.mult).then_inc(P.sem("dve_order"), P.adds("dve_order"))
        P.e.wait_ge(P.sem("dve_order"), P.due("dve_order", 0))
        P.e.reduce_sum(K.lamt[:, 0:2], K.lam_prod[:, :].rearrange("p (a c) -> p a c", a=2), AX.X).then_inc(P.sem("lambda_dots"), P.adds("lambda_dots"))
        P.e.wait_ge(P.sem("lambda_exps"), P.due("lambda_exps"))
        P.e.tensor_tensor(K.lamt[:, 4:5], K.lamt[:, 3:4], K.lamt[:, 2:3], ALU.subtract).then_inc(P.sem("dve_order"), P.adds("dve_order"))
        P.e.wait_ge(P.sem("dve_order"), P.due("dve_order", 0))
        P.e.tensor_scalar(K.lamt[:, 5:6], K.lamt[:, 4:5], -0.2, None, ALU.add)

    def act(self, K, P):
        P.e.wait_ge(P.sem("lambda_dots"), P.due("lambda_dots"))
        P.e.activation(K.lamt[:, 2:4], K.lamt[:, 0:2], ACT.Exp).then_inc(P.sem("lambda_exps"), P.adds("lambda_exps"))
        P.e.wait_ge(P.sem("bias_rows_ready"), P.due("bias_rows_ready"))
        P.e.dma_start(K.bias_dram, K.bias_rows[0:4, :]).then_inc(P.sem("bias_moved"), P.adds("bias_moved", 16))
        P.e.wait_ge(P.sem("bias_moved"), P.due("bias_moved", 0))
        for h in range(4):
            src = bass.AP(tensor=K.bias_dram.tensor, offset=h * BIAS_W, ap=[[1, 128], [1, 512]])
            P.e.dma_start(K.bias[:, h, :], src).then_inc(P.sem("bias_moved"), P.adds("bias_moved", 16))
        P.e.wait_ge(P.sem("bias_moved"), P.due("bias_moved", 0))

    def pe(self, K, P):
        P.e.wait_ge(P.sem("bias_staged"), P.due("bias_staged"))
        P.e.matmul(K.PS[0:4, 0, :], K.bias_t[0:33, :], K.onehot[0:33, 0:512], start=True, stop=True)
        P.e.matmul(K.PS[0:4, 1, 0:BIAS_W - 512], K.bias_t[0:33, :], K.onehot[0:33, 512:BIAS_W], start=True, stop=True).then_inc(P.sem("bias_rows_done"), P.adds("bias_rows_done"))


class DiffAttention(Stage):

    def act(self, K, P):
        def body(i):
            t = sl(i)
            flat = lambda ap: ap.rearrange("p a n -> p (a n)")
            for m in range(2):
                half = slice(64 * m, 64 * m + 64)
                P.e.activation(K.d_q[0:64, m, :], flat(K.in2[half, sl(i), :]), ACT.Copy, scale=0.125).then_inc(P.sem("qk_staged"), P.adds("qk_staged"))
                P.e.activation(K.d_k[0:64, m, :], flat(K.in2[half, sl(i + 4), :]), ACT.Copy).then_inc(P.sem("qk_staged"), P.adds("qk_staged"))
            P.e.activation(K.d_vs[:, :], flat(K.in2[:, sl(i + 8), :]), ACT.Copy).then_inc(P.sem("v_staged"), P.adds("v_staged"))
            P.e.wait_ge(P.sem("v_transposed"), P.due("v_transposed"))
            P.e.activation(K.d_vT[:, :], K.PS[:, 5, :], ACT.Copy).then_inc(P.sem("vT_ready"), P.adds("vT_ready"))
            for b in range(4):
                nk = 128 * (b + 1)
                for m in range(2):
                    P.e.wait_ge(P.sem("logits_done"), P.due("logits_done"))
                    P.e.wait_ge(P.sem("max_negated"), P.due("max_negated"))
                    P.e.activation(K.d_p[:, m, 0:nk], K.PS[:, m, 0:nk], ACT.Exp, bias=K.d_st[:, m, 1:2],
                                         accum_out=K.d_st[:, m, 2:3]).then_inc(P.sem("exp_done"), P.adds("exp_done"))
            P.e.wait_ge(P.sem("att_out_done"), P.due("att_out_done"))
            P.e.activation(K.d_sq[:, :], K.PS[:, 4, :], ACT.Square).then_inc(P.sem("o_squared"), P.adds("o_squared"))
            P.e.wait_ge(P.sem("o_inverse"), P.due("o_inverse"))
            P.e.activation(K.R[:, 0:S], K.R[:, 0:S], ACT.Sqrt).then_inc(P.sem("o_root"), P.adds("o_root"))
            P.e.wait_ge(P.sem("o_gated"), P.due("o_gated"))
            P.e.activation(flat(K.XH[:, t, 0:S]), K.d_sq[:, :], ACT.Copy).then_inc(P.sem("o_hi"), P.adds("o_hi"))
            P.e.wait_ge(P.sem("o_lo"), P.due("o_lo"))

        P.loop(4, body, qk_staged=4, v_staged=1, v_transposed=1, vT_ready=1, logits_done=8, max_negated=8, exp_done=8,
               att_out_done=1, o_squared=1, o_inverse=1, o_root=1, o_gated=1, o_hi=1, o_lo=1)

        def conv(i):
            P.e.wait_ge(P.sem("conv_z"), P.due("conv_z"))
            P.e.activation(K.d_cy[:, :], K.d_cz[:, :], ACT.Copy, scale=K.p["conv2_w2"][:, sl(i)]).then_inc(P.sem("conv_seeded"), P.adds("conv_seeded"))
            P.e.wait_ge(P.sem("conv_gated"), P.due("conv_gated"))
            P.e.activation(K.XH[:, sl(i + 4), 0:S].rearrange("p a n -> p (a n)"), K.d_cz[:, :], ACT.Copy).then_inc(P.sem("conv_hi"), P.adds("conv_hi"))
            P.e.wait_ge(P.sem("conv_lo"), P.due("conv_lo"))

        P.loop(4, conv, conv_z=1, conv_seeded=1, conv_gated=1, conv_hi=1, conv_lo=1)

    def dve(self, K, P):
        flat = lambda ap: ap.rearrange("p a n -> p (a n)")

        def body(i):
            t = sl(i)
            for b in range(4):
                nk = 128 * (b + 1)
                for m in range(2):
                    st = K.d_st
                    P.e.wait_ge(P.sem("logits_done"), P.due("logits_done"))
                    P.e.reduce_max(st[:, m, 0:1], K.PS[:, m, 0:nk], AX.X).then_inc(P.sem("dve_order"), P.adds("dve_order"))
                    P.e.wait_ge(P.sem("dve_order"), P.due("dve_order", 0))
                    P.e.tensor_scalar(st[:, m, 1:2], st[:, m, 0:1], -1.0, None, ALU.mult).then_inc(P.sem("max_negated"), P.adds("max_negated"))
                for m in range(2):
                    P.e.wait_ge(P.sem("exp_done"), P.due("exp_done"))
                    P.e.reciprocal(st[:, m, 3:4], st[:, m, 2:3]).then_inc(P.sem("dve_order"), P.adds("dve_order"))
                    P.e.wait_ge(P.sem("dve_order"), P.due("dve_order", 0))
                P.e.tensor_scalar(st[:, 1, 3:4], st[:, 1, 3:4], K.lamt[:, 5:6], None, ALU.mult).then_inc(P.sem("dve_order"), P.adds("dve_order"))
                P.e.wait_ge(P.sem("dve_order"), P.due("dve_order", 0))
                P.e.tensor_scalar(K.d_p[:, 0, 0:nk], K.d_p[:, 0, 0:nk], st[:, 0, 3:4], None, ALU.mult).then_inc(P.sem("dve_order"), P.adds("dve_order"))
                P.e.wait_ge(P.sem("dve_order"), P.due("dve_order", 0))
                P.e.scalar_tensor_tensor(K.d_p[:, 0, 0:nk], K.d_p[:, 1, 0:nk], st[:, 1, 3:4], K.d_p[:, 0, 0:nk],
                                               ALU.mult, ALU.add).then_inc(P.sem("probs_ready"), P.adds("probs_ready"))
                P.e.wait_ge(P.sem("probs_transposed"), P.due("probs_transposed"))
                P.e.tensor_copy(K.d_pT[:, b % 2, 0:nk], K.PS[:, 2 + b % 2, 0:nk]).then_inc(P.sem("probsT_ready"), P.adds("probsT_ready"))
            P.e.wait_ge(P.sem("o_mean"), P.due("o_mean"))
            P.e.tensor_scalar(K.R[:, 0:S], K.PS[:, 6, :], 1e-5, None, ALU.add).then_inc(P.sem("dve_order"), P.adds("dve_order"))
            P.e.wait_ge(P.sem("dve_order"), P.due("dve_order", 0))
            P.e.reciprocal(K.R[:, 0:S], K.R[:, 0:S]).then_inc(P.sem("o_inverse"), P.adds("o_inverse"))
            P.e.wait_ge(P.sem("o_root"), P.due("o_root"))
            P.e.scalar_tensor_tensor(K.d_sq[:, :], K.PS[:, 4, :], K.p["subln_g"][:, 0:1], K.R[:, 0:S], ALU.mult, ALU.mult).then_inc(P.sem("dve_order"), P.adds("dve_order"))
            P.e.wait_ge(P.sem("dve_order"), P.due("dve_order", 0))
            P.e.tensor_scalar(K.d_sq[:, :], K.d_sq[:, :], 0.8, None, ALU.mult).then_inc(P.sem("o_gated"), P.adds("o_gated"))
            P.e.wait_ge(P.sem("o_hi"), P.due("o_hi"))
            P.e.tensor_tensor(flat(K.XL[:, t, 0:S]), K.d_sq[:, :], flat(K.XH[:, t, 0:S]).bitcast(F32), ALU.subtract).then_inc(P.sem("o_lo"), P.adds("o_lo"))

        P.loop(4, body, dve_order=8 + 4 * 4 + 2, logits_done=8, max_negated=8, exp_done=8, probs_ready=4, probs_transposed=4,
               probsT_ready=4, o_mean=1, o_inverse=1, o_root=1, o_gated=1, o_hi=1, o_lo=1)

        def conv(i):
            z, y = K.d_cz, K.d_cy
            P.e.tensor_tensor(z[:, :], flat(K.in2[:, sl(i + 16), :]), flat(K.in2[:, sl(i + 20), :]), ALU.mult).then_inc(P.sem("conv_z"), P.adds("conv_z"))
            P.e.wait_ge(P.sem("conv_seeded"), P.due("conv_seeded"))
            P.e.scalar_tensor_tensor(y[:, 1:S], z[:, 0:S - 1], K.p["conv2_w1"][:, sl(i)], y[:, 1:S], ALU.mult, ALU.add).then_inc(P.sem("dve_order"), P.adds("dve_order"))
            P.e.wait_ge(P.sem("dve_order"), P.due("dve_order", 0))
            P.e.scalar_tensor_tensor(y[:, 2:S], z[:, 0:S - 2], K.p["conv2_w0"][:, sl(i)], y[:, 2:S], ALU.mult, ALU.add).then_inc(P.sem("dve_order"), P.adds("dve_order"))
            P.e.wait_ge(P.sem("dve_order"), P.due("dve_order", 0))
            P.e.tensor_tensor(z[:, :], y[:, :], flat(K.in2[:, sl(i + 12), :]), ALU.mult).then_inc(P.sem("conv_gated"), P.adds("conv_gated"))
            P.e.wait_ge(P.sem("conv_hi"), P.due("conv_hi"))
            P.e.tensor_tensor(flat(K.XL[:, sl(i + 4), 0:S]), z[:, :], flat(K.XH[:, sl(i + 4), 0:S]).bitcast(F32), ALU.subtract).then_inc(P.sem("conv_lo"), P.adds("conv_lo"))
            P.e.wait_ge(P.sem("conv_lo"), P.due("conv_lo", 0))

        P.loop(4, conv, dve_order=2, conv_z=1, conv_seeded=1, conv_gated=1, conv_hi=1, conv_lo=1)

    def pe(self, K, P):
        def body(i):
            P.e.wait_ge(P.sem("v_staged"), P.due("v_staged"))
            for b in range(4):
                last = P.e.transpose(K.PS[:, 5, 128 * b:128 * b + 128], K.d_vs[:, 128 * b:128 * b + 128], K.ident[:, :])
            last.then_inc(P.sem("v_transposed"), P.adds("v_transposed"))
            P.e.wait_ge(P.sem("qk_staged"), P.due("qk_staged", 4))
            for b in range(4):
                nk = 128 * (b + 1)
                if b:
                    P.e.wait_ge(P.sem("exp_done"), P.due("exp_done", 0))
                for m in range(2):
                    P.e.matmul(K.PS[:, m, 0:nk], K.d_q[0:64, m, 128 * b:128 * b + 128], K.d_k[0:64, m, 0:nk], start=True, stop=False)
                    last = P.e.matmul(K.PS[:, m, 0:nk], K.flip[:, :], K.bias[:, sl(i), 512 - nk:512].rearrange("p a n -> p (a n)"),
                                      start=False, stop=True)
                    last.then_inc(P.sem("logits_done"), P.adds("logits_done"))
                P.e.wait_ge(P.sem("exp_done"), P.due("exp_done", 2))
                P.e.wait_ge(P.sem("probs_ready"), P.due("probs_ready"))
                for kb in range(b + 1):
                    c = slice(128 * kb, 128 * kb + 128)
                    last = P.e.transpose(K.PS[:, 2 + b % 2, c], K.d_p[:, 0, c], K.ident[:, :])
                last.then_inc(P.sem("probs_transposed"), P.adds("probs_transposed"))
                P.e.wait_ge(P.sem("probsT_ready"), P.due("probsT_ready"))
                if b == 0:
                    P.e.wait_ge(P.sem("vT_ready"), P.due("vT_ready"))
                for kb in range(b + 1):
                    c = slice(128 * kb, 128 * kb + 128)
                    last = P.e.matmul(K.PS[:, 4, 128 * b:128 * b + 128], K.d_vT[:, c], K.d_pT[:, b % 2, c], start=(kb == 0), stop=(kb == b))
            last.then_inc(P.sem("att_out_done"), P.adds("att_out_done"))
            P.e.wait_ge(P.sem("o_squared"), P.due("o_squared"))
            P.e.matmul(K.PS[:, 6, :], K.inv_dv[:, :], K.d_sq[:, :], start=True, stop=True).then_inc(P.sem("o_mean"), P.adds("o_mean"))
            P.e.wait_ge(P.sem("o_gated"), P.due("o_gated"))

        P.loop(4, body, v_staged=1, v_transposed=1, qk_staged=4, exp_done=8, logits_done=8, probs_ready=4, probs_transposed=4,
               probsT_ready=4, vT_ready=1, att_out_done=1, o_squared=1, o_mean=1, o_gated=1)


class CentreV(Stage):

    def pe(self, K, P):
        for k in range(KT):
            last = P.e.matmul(K.PS[:, 0, :], K.inv_d[:, :], K.v2[:, k, :], start=(k == 0), stop=(k == KT - 1))
        last.then_inc(P.sem("v_mean"), P.adds("v_mean"))
        for k in range(KT):
            P.e.wait_ge(P.sem("norm_squared"), P.due("norm_squared"))
            last = P.e.matmul(K.PS[:, 1, :], K.inv_d[:, :], K.Y[:, k, 0:S], start=(k == 0), stop=(k == KT - 1))
        last.then_inc(P.sem("norm_mean"), P.adds("norm_mean"))

    def act(self, K, P):
        for k in range(KT):
            P.e.wait_ge(P.sem("v_centred"), P.due("v_centred"))
            P.e.activation(K.Y[:, k, 0:S], K.v2[:, k, :], ACT.Square).then_inc(P.sem("norm_squared"), P.adds("norm_squared"))
        P.e.wait_ge(P.sem("norm_inverse"), P.due("norm_inverse"))
        P.e.activation(K.R[:, 0:S], K.R[:, 0:S], ACT.Sqrt).then_inc(P.sem("norm_root"), P.adds("norm_root"))

    def dve(self, K, P):
        P.e.wait_ge(P.sem("v_mean"), P.due("v_mean"))
        for k in range(KT):
            P.e.tensor_tensor(K.v2[:, k, :], K.v2[:, k, :], K.PS[:, 0, :], ALU.subtract).then_inc(P.sem("v_centred"), P.adds("v_centred"))
        P.e.tensor_tensor(K.ws[:, :, :], K.ws[:, :, :],
                          K.keep_upper[:, :].rearrange("p (a n) -> p a n", a=1).broadcast_to([128, 8, 128]), ALU.mult)
        P.e.wait_ge(P.sem("norm_mean"), P.due("norm_mean"))
        P.e.tensor_scalar(K.R[:, 0:S], K.PS[:, 1, :], 1e-5, None, ALU.add).then_inc(P.sem("dve_order"), P.adds("dve_order"))
        P.e.wait_ge(P.sem("dve_order"), P.due("dve_order", 0))
        P.e.reciprocal(K.R[:, 0:S], K.R[:, 0:S]).then_inc(P.sem("norm_inverse"), P.adds("norm_inverse"))
        P.e.wait_ge(P.sem("norm_root"), P.due("norm_root"))


class SpatialGate(Stage):

    def dve(self, K, P):
        flat = lambda ap: ap.rearrange("p a n -> p (a n)")

        def body(i):
            t = sl(i)
            P.e.scalar_tensor_tensor(K.s_a[:, :], flat(K.v2[:, t, :]), K.p["sgu_ln_g"][:, t], K.R[:, 0:S], ALU.mult, ALU.mult).then_inc(P.sem("sgu_scaled"), P.adds("sgu_scaled"))
            P.e.wait_ge(P.sem("sgu_transposed"), P.due("sgu_transposed"))
            P.e.tensor_copy(K.s_vT[:, :], K.PS[:, 0, :]).then_inc(P.sem("sgu_vT"), P.adds("sgu_vT"))
            P.e.wait_ge(P.sem("sgu_mixed"), P.due("sgu_mixed"))
            P.e.tensor_tensor(K.s_o[:, :], K.PS[:, 1, :], flat(K.u2[:, t, :]), ALU.mult).then_inc(P.sem("sgu_gated"), P.adds("sgu_gated"))
            P.e.wait_ge(P.sem("sgu_hi"), P.due("sgu_hi"))
            P.e.tensor_tensor(flat(K.XL[:, t, 0:S]), K.s_o[:, :], flat(K.XH[:, t, 0:S]).bitcast(F32), ALU.subtract).then_inc(P.sem("sgu_lo"), P.adds("sgu_lo"))

        P.loop(8, body, sgu_scaled=1, sgu_transposed=1, sgu_vT=1, sgu_mixed=1, sgu_gated=1, sgu_hi=1, sgu_lo=1)

    def act(self, K, P):
        def body(i):
            t = sl(i)
            P.e.wait_ge(P.sem("sgu_scaled"), P.due("sgu_scaled"))
            P.e.activation(K.s_b[:, :], K.s_a[:, :], ACT.Identity, bias=K.p["sgu_ln_b"][:, t]).then_inc(P.sem("sgu_normed"), P.adds("sgu_normed"))
            P.e.wait_ge(P.sem("sgu_gated"), P.due("sgu_gated"))
            P.e.activation(K.XH[:, t, 0:S].rearrange("p a n -> p (a n)"), K.s_o[:, :], ACT.Copy).then_inc(P.sem("sgu_hi"), P.adds("sgu_hi"))
            P.e.wait_ge(P.sem("sgu_lo"), P.due("sgu_lo"))

        P.loop(8, body, sgu_scaled=1, sgu_normed=1, sgu_gated=1, sgu_hi=1, sgu_lo=1)

    def pe(self, K, P):
        def body(i):
            P.e.wait_ge(P.sem("sgu_normed"), P.due("sgu_normed"))
            for n in range(4):
                c = slice(128 * n, 128 * n + 128)
                last = P.e.transpose(K.PS[:, 0, c], K.s_b[:, c], K.ident[:, :])
            last.then_inc(P.sem("sgu_transposed"), P.adds("sgu_transposed"))
            P.e.wait_ge(P.sem("sgu_vT"), P.due("sgu_vT"))
            for n in range(4):
                c = slice(128 * n, 128 * n + 128)
                P.e.matmul(K.PS[:, 1, c], K.s_vT[:, c], K.ws[:, sl(i), :].rearrange("p a n -> p (a n)"), start=True, stop=False)
                last = P.e.matmul(K.PS[:, 1, c], K.one_row2[0:1, 0:128], K.sgu_b[0:1, sl(i), :].rearrange("p a n -> p (a n)"),
                                  start=False, stop=True)
            last.then_inc(P.sem("sgu_mixed"), P.adds("sgu_mixed"))
            P.e.wait_ge(P.sem("sgu_gated"), P.due("sgu_gated"))

        P.loop(8, body, sgu_normed=1, sgu_transposed=1, sgu_vT=1, sgu_mixed=1, sgu_gated=1)


def ffn2(K, layer):
    g = [K.p[f"norm2_g{layer}{j}"] for j in range(4)]
    st = [RmsNorm(K.X, g[2])]
    for c0, n in FFN_CHUNKS:
        up = GatedUp(n, c0)
        up.xh, up.xl = K.XH, K.XL
        st += [up, Narrow(n, K.HH, K.HL, K.F, add=c0 > 0)]
    return st + [RmsNorm(K.F, g[3], out=K.X, add=True)]


def block2(K):
    g = [[K.p[f"norm2_g{i}{j}"] for j in range(4)] for i in range(2)]
    st = [Load(K.loads2), RmsNorm(K.X, g[0][0]), Store(12, K.XH, K.XL, K.in2), BiasTable(), DiffAttention(),
          Narrow(8, K.XH, K.XL, K.F, add=False), RmsNorm(K.F, g[0][1], out=K.X, add=True)] + ffn2(K, 0)
    st += [Load(K.loads2b), RmsNorm(K.X, g[1][0]), Store(8, K.XH, K.XL, K.uv2, func=ACT.Gelu), CentreV(), SpatialGate(),
           Narrow(8, K.XH, K.XL, K.F, add=False), RmsNorm(K.F, g[1][1], out=K.X, add=True)] + ffn2(K, 1)
    return st


def specs2():
    v = [("subln_g", "diff_subln_g_2", 0), ("sgu_ln_g", "sgu_ln_g_2", 0), ("sgu_ln_b", "sgu_ln_b_2", 0)]
    v += [(f"norm2_g{i}{j}", "norm_g_2", (i, j)) for i in range(2) for j in range(4)]
    return v + [(f"conv2_w{j}", "conv_w_2", (0, j)) for j in range(3)]


def weights2(a):
    out = [wide_panels(a["w_in_even_2"][0]), narrow_panels(a["w_out_even_2"][0])]
    out += ffn_panels(a["w_gate_2"][0], a["w_up_2"][0], a["w_down_2"][0], FFN_CHUNKS)
    out += [wide_panels(a["w_in_odd_2"][0]), narrow_panels(a["w_out_odd_2"][0])]
    return out + ffn_panels(a["w_gate_2"][1], a["w_up_2"][1], a["w_down_2"][1], FFN_CHUNKS)


def bucket_onehot():
    n = 511 - np.arange(BIAS_W)
    nf = np.maximum(n, 1).astype(np.float32)
    large = 16 + (np.log(nf / np.float32(16)) / np.float32(np.log(8.0)) * np.float32(16)).astype(np.int32)
    b = np.where(n < 0, 32, np.where(n < 16, n, np.minimum(large, 31)))
    return (b[None, :] == np.arange(33)[:, None]).astype(np.float32)


T3 = ((0, TM // 2), (TM // 2, TM // 2))
HALF_T = TM // 2
N_CHUNK = TM // 16
DECAY = float(np.exp(-0.5))


def flat(ap):
    return ap.rearrange("p a n -> p (a n)")


def both_parts(K, bank, lo=0, hi=128):
    return K.PS[lo:hi, bank:bank + 2, 0:HALF_T]


def parts(ap):
    return ap.rearrange("p (a n) -> p a n", a=2)


class GateRows(Stage):

    def pe(self, K, P):
        for m, (c0, cn) in enumerate(((0, 128), (128, 32))):
            for part, (t0, tn) in enumerate(T3):
                for k in range(KT):
                    last = P.e.matmul(K.PS[0:cn, 2 * m + part, 0:tn], K.w_gd[:, k, c0:c0 + cn], K.Y[:, k, t0:t0 + tn],
                                      start=(k == 0), stop=(k == KT - 1))
        last.then_inc(P.sem("gate_rows_done"), P.adds("gate_rows_done"))

    def dve(self, K, P):
        P.e.wait_ge(P.sem("gate_rows_done"), P.due("gate_rows_done"))
        P.e.tensor_copy(parts(K.rp[:, 14, :]), both_parts(K, 0))
        P.e.tensor_copy(parts(K.rp[0:32, 15, :]), both_parts(K, 2, 0, 32))


class CentredShift(Stage):

    def dve(self, K, P):
        mu0, mu1, c = K.mu[:, :, 0], K.mu[:, :, 1], K.mu_rest
        areas = ((slice(0, 128), slice(0, 15)), (slice(0, 32), slice(15, 16)))
        for r, q in areas:
            P.e.tensor_tensor(c[r, q], mu0[r, q], mu1[r, q], ALU.add).then_inc(P.sem("dve_order"), P.adds("dve_order"))
            P.e.wait_ge(P.sem("dve_order"), P.due("dve_order", 0))
        for r, q in areas:
            P.e.tensor_scalar(c[r, q], c[r, q], -1.0, 1.0, ALU.mult, ALU.add).then_inc(P.sem("shift_weights"), P.adds("shift_weights"))
        for q in range(16):
            r = slice(0, 128 if q < 15 else 32)
            P.e.wait_ge(P.sem("shift_seeded"), P.due("shift_seeded"))
            z, p = K.rz[r, q, :], K.rp[r, q, :]
            P.e.scalar_tensor_tensor(z[:, 1:TM], p[:, 0:TM - 1], mu0[r, q:q + 1], z[:, 1:TM], ALU.mult, ALU.add).then_inc(P.sem("dve_order"), P.adds("dve_order"))
            P.e.wait_ge(P.sem("dve_order"), P.due("dve_order", 0))
            P.e.scalar_tensor_tensor(z[:, 0:TM - 1], p[:, 1:TM], mu1[r, q:q + 1], z[:, 0:TM - 1], ALU.mult, ALU.add)

    def act(self, K, P):
        P.e.wait_ge(P.sem("shift_weights"), P.due("shift_weights", 2))
        for q in range(16):
            r = slice(0, 128 if q < 15 else 32)
            P.e.activation(K.rz[r, q, :], K.rp[r, q, :], ACT.Copy, scale=K.mu_rest[r, q:q + 1]).then_inc(P.sem("shift_seeded"), P.adds("shift_seeded"))


class RwkvPrepare(Stage):

    def act(self, K, P):
        P.e.activation(K.rz[:, 12, :], K.rz[:, 12, :], ACT.Tanh).then_inc(P.sem("wd_tanh"), P.adds("wd_tanh"))
        for q in range(4):
            for d in range(2):
                P.e.wait_ge(P.sem("lora_done"), P.due("lora_done", 2))
                P.e.activation(parts(K.t_s[:, d, :]), both_parts(K, 2 * d), ACT.Sigmoid, bias=K.p[f"decay_w0{d}"][:, q:q + 1])
                P.e.activation(parts(K.t_a[:, d, :]), both_parts(K, 4 + 2 * d), ACT.Sigmoid,
                                     bias=K.p[f"icl_a0{d}"][:, q:q + 1]).then_inc(P.sem("gates_open"), P.adds("gates_open"))
            P.e.wait_ge(P.sem("kk_scaled"), P.due("kk_scaled"))
            P.e.activation(K.t_n[:, :], K.t_kk[:, :], ACT.Square).then_inc(P.sem("kk_squared"), P.adds("kk_squared"))
            P.e.wait_ge(P.sem("kk_sumsq"), P.due("kk_sumsq"))
            P.e.activation(K.t_n[:, :], K.t_n[:, :], ACT.Sqrt).then_inc(P.sem("kk_norm"), P.adds("kk_norm"))
            for d in range(2):
                P.e.wait_ge(P.sem("decay_cumulated"), P.due("decay_cumulated"))
                P.e.activation(K.t_s[:, d, :], K.t_bi[:, :], ACT.Exp)
                P.e.activation(K.wc[:, d, q, :], K.t_bc[:, :], ACT.Exp)
                P.e.activation(K.t_en[:, :], K.t_bi[:, :], ACT.Exp, scale=-1.0)
                P.e.activation(K.t_bx[:, :], K.t_bx[:, :], ACT.Exp).then_inc(P.sem("decay_exps"), P.adds("decay_exps"))
                P.e.wait_ge(P.sem("direction_done"), P.due("direction_done"))

    def pe(self, K, P):
        P.e.wait_ge(P.sem("wd_tanh"), P.due("wd_tanh"))
        for q in range(4):
            if q:
                P.e.wait_ge(P.sem("direction_done"), P.due("direction_done", 2))
                P.e.wait_ge(P.sem("bonus_done"), P.due("bonus_done"))
            c = slice(128 * q, 128 * q + 128)
            for d in range(2):
                rows = slice(64 * d, 64 * d + 64)
                for w, tile, bank in ((K.w2, 12, 2 * d), (K.a2, 13, 4 + 2 * d)):
                    for part, (t0, tn) in enumerate(T3):
                        last = P.e.matmul(K.PS[:, bank + part, 0:tn], w[rows, c], K.rz[rows, tile, t0:t0 + tn], start=True, stop=True)
                    last.then_inc(P.sem("lora_done"), P.adds("lora_done"))
            P.e.wait_ge(P.sem("kk_squared"), P.due("kk_squared"))
            for part, (t0, tn) in enumerate(T3):
                last = P.e.matmul(K.PS[:, part, 0:tn], K.head_ones[:, :], K.t_n[:, t0:t0 + tn], start=True, stop=True)
            last.then_inc(P.sem("kk_summed"), P.adds("kk_summed"))
            P.e.wait_ge(P.sem("bonus_product"), P.due("bonus_product"))
            for part, (t0, tn) in enumerate(T3):
                last = P.e.matmul(K.PS[:, 2 + part, 0:tn], K.head_ones[:, :], K.t_u[:, t0:t0 + tn], start=True, stop=True)
            last.then_inc(P.sem("bonus_summed"), P.adds("bonus_summed"))

    def dve(self, K, P):
        e = P.e
        for q in range(4):
            vec = lambda n: K.p[n][:, q:q + 1]
            r, k, v = K.rz[:, q, :], K.rz[:, 4 + q, :], K.rz[:, 8 + q, :]
            e.tensor_scalar(K.t_c[:, 0:1], vec("k_a"), -1.0, 1.0, ALU.mult, ALU.add).then_inc(P.sem("dve_order"), P.adds("dve_order"))
            P.e.wait_ge(P.sem("dve_order"), P.due("dve_order", 0))
            e.tensor_scalar(K.t_kk[:, :], k, vec("k_k"), None, ALU.mult).then_inc(P.sem("kk_scaled"), P.adds("kk_scaled"))
            P.e.wait_ge(P.sem("gates_open"), P.due("gates_open", 2))
            P.e.wait_ge(P.sem("kk_summed"), P.due("kk_summed"))
            e.tensor_scalar(parts(K.t_n[:, :]), both_parts(K, 0), 1e-24, None, ALU.max).then_inc(P.sem("kk_sumsq"), P.adds("kk_sumsq"))
            P.e.wait_ge(P.sem("kk_norm"), P.due("kk_norm"))
            e.reciprocal(K.t_n[:, :], K.t_n[:, :]).then_inc(P.sem("dve_order"), P.adds("dve_order"))
            P.e.wait_ge(P.sem("dve_order"), P.due("dve_order", 0))
            e.tensor_tensor(K.t_kk[:, :], K.t_kk[:, :], K.t_n[:, :], ALU.mult).then_inc(P.sem("dve_order"), P.adds("dve_order"))
            P.e.wait_ge(P.sem("dve_order"), P.due("dve_order", 0))
            for d in range(2):
                lw, al = K.t_s[:, d, :], K.t_a[:, d, :]
                e.tensor_scalar(lw, lw, -DECAY, None, ALU.mult).then_inc(P.sem("dve_order"), P.adds("dve_order"))
                P.e.wait_ge(P.sem("dve_order"), P.due("dve_order", 0))
                e.tensor_tensor_scan(K.t_bi[:, :], K.reset16[:, :], lw, 0.0, ALU.mult, ALU.add).then_inc(P.sem("dve_order"), P.adds("dve_order"))
                P.e.wait_ge(P.sem("dve_order"), P.due("dve_order", 0))
                b3 = K.t_bi[:, :].rearrange("p (n c) -> p n c", c=16)
                e.tensor_copy(K.t_bc[:, :], b3[:, :, 15]).then_inc(P.sem("dve_order"), P.adds("dve_order"))
                P.e.wait_ge(P.sem("dve_order"), P.due("dve_order", 0))
                if d == 0:
                    e.tensor_tensor(K.t_bx[:, :], K.t_bi[:, :], lw, ALU.subtract).then_inc(P.sem("decay_cumulated"), P.adds("decay_cumulated"))
                else:
                    total = K.t_bc[:, :].rearrange("p (n c) -> p n c", c=1).broadcast_to([128, N_CHUNK, 16])
                    e.tensor_tensor(K.t_bx[:, :].rearrange("p (n c) -> p n c", c=16), total, b3, ALU.subtract).then_inc(P.sem("dve_order"), P.adds("dve_order"))
                    P.e.wait_ge(P.sem("dve_order"), P.due("dve_order", 0))
                    e.tensor_tensor(K.t_bi[:, :], K.t_bx[:, :], lw, ALU.add).then_inc(P.sem("decay_cumulated"), P.adds("decay_cumulated"))
                e.tensor_scalar(K.t_k[:, d, :], al, vec("k_a"), K.t_c[:, 0:1], ALU.mult, ALU.add).then_inc(P.sem("dve_order"), P.adds("dve_order"))
                P.e.wait_ge(P.sem("dve_order"), P.due("dve_order", 0))
                e.tensor_tensor(K.t_k[:, d, :], K.t_k[:, d, :], k, ALU.mult).then_inc(P.sem("dve_order"), P.adds("dve_order"))
                P.e.wait_ge(P.sem("dve_order"), P.due("dve_order", 0))
                e.tensor_tensor(al, al, K.t_kk[:, :], ALU.mult).then_inc(P.sem("dve_order"), P.adds("dve_order"))
                P.e.wait_ge(P.sem("dve_order"), P.due("dve_order", 0))
                P.e.wait_ge(P.sem("decay_exps"), P.due("decay_exps"))
                ar = K.ar[d]
                e.scalar_tensor_tensor(ar[:, 0, q, :], K.t_kk[:, :], -1.0, K.t_bx[:, :], ALU.mult, ALU.mult)
                e.tensor_tensor(ar[:, 1, q, :], r, lw, ALU.mult)
                e.tensor_tensor(ar[:, 2, q, :], al, K.t_en[:, :], ALU.mult)
                e.tensor_tensor(ar[:, 3, q, :], K.t_k[:, d, :], K.t_en[:, :], ALU.mult).then_inc(P.sem("direction_done"), P.adds("direction_done"))
                P.e.wait_ge(P.sem("direction_done"), P.due("direction_done", 0))
            e.tensor_tensor(K.t_u[:, :], K.t_k[:, 0, :], K.t_k[:, 1, :], ALU.add).then_inc(P.sem("dve_order"), P.adds("dve_order"))
            P.e.wait_ge(P.sem("dve_order"), P.due("dve_order", 0))
            e.scalar_tensor_tensor(K.t_u[:, :], K.t_u[:, :], vec("r_k"), r, ALU.mult, ALU.mult).then_inc(P.sem("bonus_product"), P.adds("bonus_product"))
            P.e.wait_ge(P.sem("bonus_summed"), P.due("bonus_summed"))
            e.scalar_tensor_tensor(parts(K.rz[:, q, :]), both_parts(K, 2), 0.5, parts(v), ALU.mult, ALU.mult).then_inc(P.sem("bonus_done"), P.adds("bonus_done"))
            P.e.wait_ge(P.sem("bonus_done"), P.due("bonus_done", 0))


class RwkvScan(Stage):

    HALVES = [slice(0, 64), slice(64, 128)]

    def act(self, K, P):
        def body(i):
            for d in range(2):
                t = sl_t(16 * i if d == 0 else (N_CHUNK - 1) * 16 - 16 * i, 16)
                P.e.activation(K.c_st[:, d, 0:4, :].rearrange("p a (q t) -> p a q t", q=4), K.ar[d][:, :, :, t], ACT.Copy)
                last = P.e.activation(K.c_st[:, d, 4, :].rearrange("p (q t) -> p q t", q=4), K.rz[:, 8:12, t], ACT.Copy)
            last.then_inc(P.sem("chunk_staged"), P.adds("chunk_staged"))
            P.e.wait_ge(P.sem("betas_transposed"), P.due("betas_transposed"))
            for par, half in enumerate(self.HALVES):
                last = P.e.activation(K.c_bt[half, :, :], K.PS[0:64, 5, :].rearrange("p (a q n) -> p a q n", q=2, n=64)[:, :, par, :], ACT.Copy)
            last.then_inc(P.sem("betas_ready"), P.adds("betas_ready"))
            P.e.wait_ge(P.sem("u_done"), P.due("u_done"))
            P.e.activation(K.c_u[:, :], K.PS[:, 2, :], ACT.Copy).then_inc(P.sem("u_ready"), P.adds("u_ready"))
            P.e.wait_ge(P.sem("chunk_finished"), P.due("chunk_finished"))

        P.loop(N_CHUNK, body, chunk_staged=1, betas_transposed=1, betas_ready=1, u_done=1, u_ready=1, chunk_finished=1)

    def pe(self, K, P):
        mm = P.e.matmul

        def body(i):
            P.e.wait_ge(P.sem("chunk_staged"), P.due("chunk_staged"))
            P.settle()
            st, g = K.c_st, K.c_g
            both = [(d, half) for d in range(2) for half in self.HALVES]
            for d, h in both:
                mm(K.PS[h, d, 0:128], st[h, d, 2, :], st[h, d, 0:2, :].rearrange("p a n -> p (a n)"), start=True, stop=True)
                mm(K.PS[h, d, 128:256], st[h, d, 3, :], st[h, d, 0:2, :].rearrange("p a n -> p (a n)"), start=True, stop=True)
                last = mm(K.PS[h, d, 256:320], st[h, d, 0, :], st[h, d, 2, :], start=True, stop=True)
            last.then_inc(P.sem("grams_done"), P.adds("grams_done"))
            for d in range(2):
                for j in range(2):
                    last = P.e.transpose(K.PS[0:64, 5, 256 * d + 128 * j:256 * d + 128 * j + 128], st[:, d, 2 + j, :], K.ident[:, :])
            last.then_inc(P.sem("betas_transposed"), P.adds("betas_transposed"))
            for d in range(2):
                last = P.e.transpose(K.PS[0:64, 6, 128 * d:128 * d + 128], st[:, d, 4, :], K.ident[:, :])
            last.then_inc(P.sem("v_rows_done"), P.adds("v_rows_done"))
            P.e.wait_ge(P.sem("grams_masked"), P.due("grams_masked"))
            P.settle()
            for d, h in both:
                c = 128 * d
                mm(K.PS[h, 2, c:c + 64], g[h, d, 256:320], g[h, d, 0:64], start=True, stop=True)
                last = mm(K.PS[h, 2, c + 64:c + 128], g[h, d, 0:64], g[h, d, 256:320], start=True, stop=True)
            last.then_inc(P.sem("squares_done"), P.adds("squares_done"))
            P.e.wait_ge(P.sem("squares_ready"), P.due("squares_ready"))
            P.settle()
            for d, h in both:
                n2, n2t = K.c_n2[h, d, 0:64], K.c_n2[h, d, 64:128]
                mm(K.PS[h, 3, 128 * d:128 * d + 64], n2t, n2, start=True, stop=True)
                mm(K.PS[h, 3, 128 * d + 64:128 * d + 128], n2, n2t, start=True, stop=True)
                last = mm(K.PS[h, 3, 256 + 64 * d:320 + 64 * d], n2t, K.c_p[h, 0, d, :], start=True, stop=True)
            last.then_inc(P.sem("squares_done"), P.adds("squares_done"))
            P.e.wait_ge(P.sem("squares_ready"), P.due("squares_ready"))
            P.settle()
            for d, h in both:
                n4, n4t = K.c_n4[h, d, 0:64], K.c_n4[h, d, 64:128]
                mm(K.PS[h, 4, 64 * d:64 * d + 64], n4, n4t, start=True, stop=True)
                last = mm(K.PS[h, 4, 128 + 64 * d:192 + 64 * d], n4t, K.c_p[h, 1, d, :], start=True, stop=True)
            last.then_inc(P.sem("squares_done"), P.adds("squares_done"))
            P.e.wait_ge(P.sem("squares_ready"), P.due("squares_ready"))
            P.settle()
            for d, h in both:
                last = mm(K.PS[h, 2, 64 * d:64 * d + 64], K.c_n8[h, d, :], K.c_p[h, 0, d, :], start=True, stop=True)
            last.then_inc(P.sem("squares_done"), P.adds("squares_done"))
            P.e.wait_ge(P.sem("v_rows_ready"), P.due("v_rows_ready"))
            P.settle()
            for d, h in both:
                c = slice(256 * d, 256 * d + 256)
                mm(K.PS[h, 7, c], g[h, d, 128:192], K.c_v[h, c], start=True, stop=False)
                last = mm(K.PS[h, 7, c], st[h, d, 0, :], K.c_s[h, c], start=False, stop=True)
            last.then_inc(P.sem("rhs_done"), P.adds("rhs_done"))
            P.e.wait_ge(P.sem("squares_ready"), P.due("squares_ready"))
            P.e.wait_ge(P.sem("rhs_ready"), P.due("rhs_ready"))
            P.settle()
            for d, h in both:
                c = slice(256 * d, 256 * d + 256)
                last = mm(K.PS[h, 2, c], K.c_p[h, 1, d, :], K.c_r[h, c], start=True, stop=True)
            last.then_inc(P.sem("u_done"), P.adds("u_done"))
            P.e.wait_ge(P.sem("u_ready"), P.due("u_ready"))
            P.e.wait_ge(P.sem("betas_ready"), P.due("betas_ready"))
            P.settle()
            for d, h in both:
                c = slice(256 * d, 256 * d + 256)
                mm(K.PS[h, 3, c], K.c_bt[h, 2 * d, :], K.c_u[h, c], start=True, stop=False)
                last = mm(K.PS[h, 3, c], K.c_bt[h, 2 * d + 1, :], K.c_v[h, c], start=False, stop=True)
            last.then_inc(P.sem("state_done"), P.adds("state_done"))
            for d, h in both:
                c = slice(256 * d, 256 * d + 256)
                mm(K.PS[h, 4, c], st[h, d, 1, :], K.c_s[h, c], start=True, stop=False)
                mm(K.PS[h, 4, c], g[h, d, 192:256], K.c_v[h, c], start=False, stop=False)
                last = mm(K.PS[h, 4, c], g[h, d, 64:128], K.c_u[h, c], start=False, stop=True)
            last.then_inc(P.sem("y_done"), P.adds("y_done"))
            P.e.wait_ge(P.sem("chunk_finished"), P.due("chunk_finished"))
            P.settle()

        P.e.wait_ge(P.sem("state_cleared"), P.due("state_cleared"))
        P.loop(N_CHUNK, body, chunk_staged=1, grams_done=1, betas_transposed=1, v_rows_done=1, grams_masked=1, squares_done=4,
               squares_ready=4, v_rows_ready=1, rhs_done=1, rhs_ready=1, u_done=1, u_ready=1, betas_ready=1, state_done=1,
               y_done=1, chunk_finished=1)

    def dve(self, K, P):
        e = P.e
        e.memset(K.yt[:, :, :], 0.0)
        e.memset(K.c_s[:, :], 0.0).then_inc(P.sem("state_cleared"), P.adds("state_cleared"))
        P.e.wait_ge(P.sem("state_cleared"), P.due("state_cleared", 0))

        def body(i):
            P.e.wait_ge(P.sem("grams_done"), P.due("grams_done"))
            e.tensor_tensor(K.c_g[:, :, :], K.PS[:, 0:2, 0:320], K.gram_mask[:, :, :], ALU.mult).then_inc(P.sem("grams_masked"), P.adds("grams_masked"))
            P.e.wait_ge(P.sem("grams_masked"), P.due("grams_masked", 0))
            e.tensor_tensor(K.c_p[:, 0, :, :], K.c_g[:, :, 0:64], K.eye64[:, :, :], ALU.add)
            P.e.wait_ge(P.sem("squares_done"), P.due("squares_done"))
            e.tensor_copy(K.c_n2[:, :, :].rearrange("p d n -> p (d n)"), K.PS[:, 2, 0:256]).then_inc(P.sem("squares_ready"), P.adds("squares_ready"))
            P.e.wait_ge(P.sem("v_rows_done"), P.due("v_rows_done"))
            for par, half in enumerate(self.HALVES):
                v = K.PS[0:64, 6, 0:256].rearrange("p (d a q n) -> p d a q n", d=2, a=1, q=2)[:, :, :, par, :]
                m = K.block_mask[0:64, :].rearrange("p (q n) -> p q n", q=4)
                for d in range(2):
                    last = e.tensor_tensor(K.c_v[half, 256 * d:256 * d + 256].rearrange("p (q n) -> p q n", q=4),
                                           v[:, d].broadcast_to([64, 4, 64]), m, ALU.mult)
            last.then_inc(P.sem("v_rows_ready"), P.adds("v_rows_ready"))
            P.e.wait_ge(P.sem("squares_done"), P.due("squares_done"))
            e.tensor_copy(K.c_n4[:, :, :].rearrange("p d n -> p (d n)"), K.PS[:, 3, 0:256])
            e.tensor_tensor(K.c_p[:, 1, :, :], K.PS[:, 3, 256:384].rearrange("p (d n) -> p d n", d=2), K.c_p[:, 0, :, :], ALU.add).then_inc(P.sem("squares_ready"), P.adds("squares_ready"))
            P.e.wait_ge(P.sem("squares_done"), P.due("squares_done"))
            P.e.wait_ge(P.sem("squares_ready"), P.due("squares_ready", 0))
            e.tensor_copy(K.c_n8[:, :, :].rearrange("p d n -> p (d n)"), K.PS[:, 4, 0:128])
            e.tensor_tensor(K.c_p[:, 0, :, :], K.PS[:, 4, 128:256].rearrange("p (d n) -> p d n", d=2), K.c_p[:, 1, :, :], ALU.add).then_inc(P.sem("squares_ready"), P.adds("squares_ready"))
            P.e.wait_ge(P.sem("squares_done"), P.due("squares_done"))
            P.e.wait_ge(P.sem("squares_ready"), P.due("squares_ready", 0))
            e.tensor_tensor(K.c_p[:, 1, :, :], K.PS[:, 2, 0:128].rearrange("p (d n) -> p d n", d=2), K.c_p[:, 0, :, :], ALU.add).then_inc(P.sem("squares_ready"), P.adds("squares_ready"))
            P.e.wait_ge(P.sem("rhs_done"), P.due("rhs_done"))
            mask = K.block_mask[:, :].rearrange("p (a n) -> p a n", a=1).broadcast_to([128, 2, 256])
            halves = lambda ap: ap.rearrange("p (d n) -> p d n", d=2)
            e.tensor_tensor(halves(K.c_r[:, :]), halves(K.PS[:, 7, :]), mask, ALU.mult).then_inc(P.sem("rhs_ready"), P.adds("rhs_ready"))
            P.e.wait_ge(P.sem("y_done"), P.due("y_done"))
            P.e.wait_ge(P.sem("state_done"), P.due("state_done"))
            e.tensor_tensor(K.c_s[:, :], K.c_s[:, :], K.PS[:, 3, :], ALU.add).then_inc(P.sem("dve_order"), P.adds("dve_order"))
            P.e.wait_ge(P.sem("dve_order"), P.due("dve_order", 0))
            for d in range(2):
                s4 = K.c_s[:, 256 * d:256 * d + 256].rearrange("p (q n) -> p q n", q=4)
                decay = K.wc[:, d, :, sl_t(i if d == 0 else N_CHUNK - 1 - i, 1)].broadcast_to([128, 4, 64])
                e.tensor_tensor(s4, s4, decay, ALU.mult)
            e.tensor_tensor(halves(K.c_y[:, :]), halves(K.PS[:, 4, :]), mask, ALU.mult).then_inc(P.sem("dve_order"), P.adds("dve_order"))
            P.e.wait_ge(P.sem("dve_order"), P.due("dve_order", 0))
            e.reduce_sum(K.c_yr[:, :, :], K.c_y[:, :].rearrange("p (d q n) -> p d n q", d=2, q=4), AX.X).then_inc(P.sem("dve_order"), P.adds("dve_order"))
            P.e.wait_ge(P.sem("dve_order"), P.due("dve_order", 0))
            y0 = flat(K.yt[:, sl(i), :])
            y1 = flat(K.yt[:, sl_(N_CHUNK - 1 - i), :])
            e.tensor_tensor(y0, y0, K.c_yr[:, 0, :], ALU.add).then_inc(P.sem("dve_order"), P.adds("dve_order"))
            P.e.wait_ge(P.sem("dve_order"), P.due("dve_order", 0))
            e.tensor_tensor(y1, y1, K.c_yr[:, 1, :], ALU.add).then_inc(P.sem("chunk_finished"), P.adds("chunk_finished"))
            P.e.wait_ge(P.sem("chunk_finished"), P.due("chunk_finished", 0))

        P.loop(N_CHUNK, body, grams_done=1, grams_masked=1, squares_done=4, squares_ready=4, v_rows_done=1, v_rows_ready=1,
               rhs_done=1, rhs_ready=1, y_done=1, state_done=1, dve_order=4, chunk_finished=1)


def sl_t(start, n):
    return slice(start, start + n) if isinstance(start, int) else bass.ds(start, n)


def sl_(i):
    return sl_t(i, 1)


class RwkvOutput(Stage):

    def dve(self, K, P):
        e = P.e
        col = lambda j: K.g_c[:, j, :]
        wide = lambda j: K.g_c[:, j, :].rearrange("p (n c) -> p n c", c=1).broadcast_to([128, N_CHUNK, 64])
        e.reduce_sum(col(0), K.yt[:, :, :], AX.X).then_inc(P.sem("dve_order"), P.adds("dve_order"))
        P.e.wait_ge(P.sem("dve_order"), P.due("dve_order", 0))
        e.tensor_scalar(col(0), col(0), 1.0 / 64, None, ALU.mult).then_inc(P.sem("dve_order"), P.adds("dve_order"))
        P.e.wait_ge(P.sem("dve_order"), P.due("dve_order", 0))
        e.tensor_tensor(K.yt[:, :, :], K.yt[:, :, :], wide(0), ALU.subtract).then_inc(P.sem("y_centred"), P.adds("y_centred"))
        P.e.wait_ge(P.sem("y_squared"), P.due("y_squared"))
        e.reduce_sum(col(1), K.y2[:, :, :], AX.X).then_inc(P.sem("dve_order"), P.adds("dve_order"))
        P.e.wait_ge(P.sem("dve_order"), P.due("dve_order", 0))
        e.tensor_scalar(col(1), col(1), 1.0 / 64, 64e-5, ALU.mult, ALU.add).then_inc(P.sem("dve_order"), P.adds("dve_order"))
        P.e.wait_ge(P.sem("dve_order"), P.due("dve_order", 0))
        e.reciprocal(col(1), col(1)).then_inc(P.sem("y_inverse"), P.adds("y_inverse"))
        P.e.wait_ge(P.sem("y_root"), P.due("y_root"))
        e.tensor_tensor(K.yt[:, :, :], K.yt[:, :, :], wide(1), ALU.mult).then_inc(P.sem("y_normed"), P.adds("y_normed"))
        P.e.wait_ge(P.sem("y_transposed"), P.due("y_transposed"))
        for b in range(8):
            for par in range(2):
                src = K.PS[0:64, b, :].rearrange("p (c a q t) -> p c a q t", c=4, a=2, q=4)[:, :, par]
                dst = K.yf[64 * par:64 * par + 64, :, 64 * b:64 * b + 64].rearrange("p q (c t) -> p c q t", c=4)
                last = e.tensor_copy(dst, src)
        last.then_inc(P.sem("y_rows"), P.adds("y_rows"))
        P.e.wait_ge(P.sem("y_rows"), P.due("y_rows", 0))
        for q in range(4):
            e.scalar_tensor_tensor(K.yf[:, q, :], K.yf[:, q, :], K.p["lnx_g"][:, q:q + 1], K.rz[:, q, META:TM], ALU.mult, ALU.add).then_inc(P.sem("y_bonus"), P.adds("y_bonus"))
        for q in range(4):
            P.e.wait_ge(P.sem("y_shifted"), P.due("y_shifted"))
            P.e.wait_ge(P.sem("gate_done"), P.due("gate_done"))
            e.tensor_tensor(K.ya[:, q, :], K.yf[:, q, :], K.PS[:, q, :], ALU.mult).then_inc(P.sem("y_gated"), P.adds("y_gated"))

    def act(self, K, P):
        P.e.activation(K.rz[:, 14, :], K.rz[:, 14, :], ACT.Sigmoid)
        P.e.activation(K.rz[0:32, 15, :], K.rz[0:32, 15, :], ACT.Sigmoid).then_inc(P.sem("gate_open"), P.adds("gate_open"))
        P.e.wait_ge(P.sem("y_centred"), P.due("y_centred"))
        P.e.activation(K.y2[:, :, :], K.yt[:, :, :], ACT.Square).then_inc(P.sem("y_squared"), P.adds("y_squared"))
        P.e.wait_ge(P.sem("y_inverse"), P.due("y_inverse"))
        P.e.activation(K.g_c[:, 1, :], K.g_c[:, 1, :], ACT.Sqrt).then_inc(P.sem("y_root"), P.adds("y_root"))
        for q in range(4):
            P.e.wait_ge(P.sem("y_bonus"), P.due("y_bonus"))
            P.e.activation(K.yf[:, q, :], K.yf[:, q, :], ACT.Identity, bias=K.p["lnx_b"][:, q:q + 1]).then_inc(P.sem("y_shifted"), P.adds("y_shifted"))

    def pe(self, K, P):
        P.e.wait_ge(P.sem("y_normed"), P.due("y_normed"))
        for b in range(8):
            for c in range(4):
                last = P.e.transpose(K.PS[0:64, b, 128 * c:128 * c + 128], K.yt[:, 1 + 4 * b + c, :], K.ident[:, :])
        last.then_inc(P.sem("y_transposed"), P.adds("y_transposed"))
        P.e.wait_ge(P.sem("y_rows"), P.due("y_rows"))
        P.e.wait_ge(P.sem("gate_open"), P.due("gate_open"))
        for q in range(4):
            c = slice(128 * q, 128 * q + 128)
            P.e.matmul(K.PS[:, q, :], K.g2a[:, c], K.rz[:, 14, META:TM], start=True, stop=False)
            P.e.matmul(K.PS[:, q, :], K.g2b[0:32, c], K.rz[0:32, 15, META:TM], start=False, stop=True).then_inc(P.sem("gate_done"), P.adds("gate_done"))


class QkNormRope(Stage):

    def tiles(self, K):
        out = [(K.a_q[:, q, :], K.p["q_norm_g"], META, ((0, S),)) for q in range(4)]
        return out + [(K.a_kv[:, 0, :], K.p["k_norm_g"], 0, T3)]

    def act(self, K, P):
        for x, g, off, toks in self.tiles(K):
            n = toks[-1][0] + toks[-1][1]
            P.e.activation(K.a_t[:, 0, 0:n], x, ACT.Square).then_inc(P.sem("qk_squared"), P.adds("qk_squared"))
            P.e.wait_ge(P.sem("qk_inverse"), P.due("qk_inverse"))
            P.e.activation(K.a_t[:, 1, 0:n], K.a_t[:, 1, 0:n], ACT.Sqrt).then_inc(P.sem("qk_root"), P.adds("qk_root"))
            P.e.wait_ge(P.sem("qk_rotated"), P.due("qk_rotated"))

    def pe(self, K, P):
        for x, g, off, toks in self.tiles(K):
            P.e.wait_ge(P.sem("qk_squared"), P.due("qk_squared"))
            for part, (t0, tn) in enumerate(toks):
                last = P.e.matmul(K.PS[:, part, 0:tn], K.head_ones2[:, :], K.a_t[:, 0, t0:t0 + tn], start=True, stop=True)
            last.then_inc(P.sem("qk_sumsq"), P.adds("qk_sumsq"))
            P.e.wait_ge(P.sem("qk_normed"), P.due("qk_normed"))
            for part, (t0, tn) in enumerate(toks):
                last = P.e.matmul(K.PS[:, 2 + part, 0:tn], K.rot[:, :], x[:, t0:t0 + tn], start=True, stop=True)
            last.then_inc(P.sem("qk_partner"), P.adds("qk_partner"))
            P.e.wait_ge(P.sem("qk_rotated"), P.due("qk_rotated"))

    def dve(self, K, P):
        e = P.e
        for x, g, off, toks in self.tiles(K):
            n = toks[-1][0] + toks[-1][1]
            P.e.wait_ge(P.sem("qk_sumsq"), P.due("qk_sumsq"))
            for part, (t0, tn) in enumerate(toks):
                last = e.tensor_scalar(K.a_t[:, 1, t0:t0 + tn], K.PS[:, part, 0:tn], 1.0 / 64, EPS, ALU.mult, ALU.add)
            last.then_inc(P.sem("dve_order"), P.adds("dve_order"))
            P.e.wait_ge(P.sem("dve_order"), P.due("dve_order", 0))
            e.reciprocal(K.a_t[:, 1, 0:n], K.a_t[:, 1, 0:n]).then_inc(P.sem("qk_inverse"), P.adds("qk_inverse"))
            P.e.wait_ge(P.sem("qk_root"), P.due("qk_root"))
            e.scalar_tensor_tensor(x, x, g[:, 0:1], K.a_t[:, 1, 0:n], ALU.mult, ALU.mult).then_inc(P.sem("qk_normed"), P.adds("qk_normed"))
            P.e.wait_ge(P.sem("qk_partner"), P.due("qk_partner"))
            for part, (t0, tn) in enumerate(toks):
                last = e.tensor_tensor(K.a_t[:, 0, t0:t0 + tn], K.PS[:, 2 + part, 0:tn], K.rope[:, 1, off + t0:off + t0 + tn], ALU.mult)
            e.tensor_tensor(x, x, K.rope[:, 0, off:off + n], ALU.mult).then_inc(P.sem("dve_order"), P.adds("dve_order"))
            P.e.wait_ge(P.sem("dve_order"), P.due("dve_order", 0))
            e.tensor_tensor(x, x, K.a_t[:, 0, 0:n], ALU.add).then_inc(P.sem("qk_rotated"), P.adds("qk_rotated"))


class GroupedAttention(Stage):

    UNITS = [(u, b) for u in range(2) for b in range(4)]
    KEYS = [(128 * j, min(128, TM - 128 * j)) for j in range(5)]

    def act(self, K, P):
        P.e.activation(K.a_ks[0:64, 0, :], K.a_kv[0:64, 0, :], ACT.Copy).then_inc(P.sem("k_staged"), P.adds("k_staged"))
        P.e.activation(K.a_ks[0:64, 1, :], K.a_kv[64:128, 0, :], ACT.Copy).then_inc(P.sem("k_staged"), P.adds("k_staged"))
        P.e.wait_ge(P.sem("v_transposed"), P.due("v_transposed"))
        P.e.activation(K.a_vT[:, 0:4, :].rearrange("p a n -> p (a n)"), K.PS[:, 7, :], ACT.Copy)
        P.e.activation(K.a_vT[0:16, 4, :], K.PS[0:16, 5, 0:128], ACT.Copy).then_inc(P.sem("vT_ready"), P.adds("vT_ready"))
        for kv in range(2):
            def body(i):
                for u in range(2):
                    P.e.activation(K.a_qs[0:64, u, :], flat(K.a_q[64 * u:64 * u + 64, sl(i + 2 * kv), :]), ACT.Copy, scale=0.125).then_inc(P.sem("qk_staged"), P.adds("qk_staged"))
                for n, (u, b) in enumerate(self.UNITS):
                    s = n % 2
                    P.e.wait_ge(P.sem("logits_done"), P.due("logits_done"))
                    P.e.wait_ge(P.sem("max_negated"), P.due("max_negated"))
                    P.e.activation(parts(K.a_p[:, s, :]), K.PS[:, 2 * s:2 * s + 2, 0:HALF_T], ACT.Exp,
                                         bias=K.a_st[:, s, 1:2], accum_out=K.a_st[:, s, 2:3]).then_inc(P.sem("exp_done"), P.adds("exp_done"))
                P.e.wait_ge(P.sem("att_out_done"), P.due("att_out_done"))
                P.e.activation(flat(K.HH[:, sl(i + 4 + 2 * kv), :]), K.PS[:, 6, :], ACT.Copy).then_inc(P.sem("att_out_hi"), P.adds("att_out_hi"))

            P.loop(2, body, qk_staged=2, logits_done=8, max_negated=8, exp_done=8, att_out_done=1, att_out_hi=1)

    def dve(self, K, P):
        e = P.e
        for kv in range(2):
            def body(i):
                for n, (u, b) in enumerate(self.UNITS):
                    s = n % 2
                    P.e.wait_ge(P.sem("logits_done"), P.due("logits_done"))
                    e.tensor_reduce(K.a_st[:, s, 0:1], K.PS[:, 2 * s:2 * s + 2, 0:HALF_T], AX.XY, ALU.max).then_inc(P.sem("dve_order"), P.adds("dve_order"))
                    P.e.wait_ge(P.sem("dve_order"), P.due("dve_order", 0))
                    e.tensor_scalar(K.a_st[:, s, 1:2], K.a_st[:, s, 0:1], -1.0, None, ALU.mult).then_inc(P.sem("max_negated"), P.adds("max_negated"))
                    P.e.wait_ge(P.sem("exp_done"), P.due("exp_done"))
                    e.reciprocal(K.a_st[:, s, 3:4], K.a_st[:, s, 2:3]).then_inc(P.sem("dve_order"), P.adds("dve_order"))
                    P.e.wait_ge(P.sem("dve_order"), P.due("dve_order", 0))
                    e.tensor_scalar(K.a_p[:, s, :], K.a_p[:, s, :], K.a_st[:, s, 3:4], None, ALU.mult).then_inc(P.sem("probs_ready"), P.adds("probs_ready"))
                    P.e.wait_ge(P.sem("probs_transposed"), P.due("probs_transposed"))
                    e.tensor_copy(K.a_pT[:, s, 0:4, :].rearrange("p a n -> p (a n)"), K.PS[:, 4, :])
                    e.tensor_copy(K.a_pT[0:16, s, 4, :], K.PS[0:16, 5, 0:128]).then_inc(P.sem("probsT_ready"), P.adds("probsT_ready"))
                P.e.wait_ge(P.sem("att_out_done"), P.due("att_out_done"))
                P.e.wait_ge(P.sem("att_out_hi"), P.due("att_out_hi"))
                h = sl(i + 4 + 2 * kv)
                e.tensor_tensor(flat(K.HL[:, h, :]), K.PS[:, 6, :], flat(K.HH[:, h, :]).bitcast(F32), ALU.subtract).then_inc(P.sem("att_out_lo"), P.adds("att_out_lo"))

            P.loop(2, body, dve_order=16, logits_done=8, max_negated=8, exp_done=8, probs_ready=8, probs_transposed=8,
                   probsT_ready=8, att_out_done=1, att_out_hi=1, att_out_lo=1)

    def pe(self, K, P):
        for j, (k0, kn) in enumerate(self.KEYS):
            out = K.PS[0:kn, 7, k0:k0 + 128] if j < 4 else K.PS[0:kn, 5, 0:128]
            last = P.e.transpose(out, K.a_kv[:, 1, k0:k0 + kn], K.ident[:, :])
        last.then_inc(P.sem("v_transposed"), P.adds("v_transposed"))
        P.e.wait_ge(P.sem("k_staged"), P.due("k_staged", 2))
        for kv in range(2):
            def logits(n):
                u, b = self.UNITS[n]
                for part, (t0, tn) in enumerate(T3):
                    last = P.e.matmul(K.PS[:, 2 * (n % 2) + part, 0:tn], K.a_qs[0:64, u, 128 * b:128 * b + 128],
                                      K.a_ks[0:64, kv, t0:t0 + tn], start=True, stop=True)
                last.then_inc(P.sem("logits_done"), P.adds("logits_done"))

            def body(i):
                P.e.wait_ge(P.sem("qk_staged"), P.due("qk_staged", 2))
                logits(0)
                for n, (u, b) in enumerate(self.UNITS):
                    if n + 1 < len(self.UNITS):
                        if n >= 1:
                            P.e.wait_ge(P.sem("exp_done"), P.due("exp_done", 0))
                        logits(n + 1)
                    s = n % 2
                    P.e.wait_ge(P.sem("probs_ready"), P.due("probs_ready"))
                    P.e.wait_ge(P.sem("exp_done"), P.due("exp_done"))
                    if n:
                        P.e.wait_ge(P.sem("probsT_ready"), P.due("probsT_ready", 0))
                    for j, (k0, kn) in enumerate(self.KEYS):
                        out = K.PS[0:kn, 4, k0:k0 + 128] if j < 4 else K.PS[0:kn, 5, 0:128]
                        last = P.e.transpose(out, K.a_p[:, s, k0:k0 + kn], K.ident[:, :])
                    last.then_inc(P.sem("probs_transposed"), P.adds("probs_transposed"))
                    P.e.wait_ge(P.sem("probsT_ready"), P.due("probsT_ready"))
                    if n == 0 and kv == 0 and isinstance(i, int):
                        pass
                    for j, (k0, kn) in enumerate(self.KEYS):
                        last = P.e.matmul(K.PS[64 * u:64 * u + 64, 6, 128 * b:128 * b + 128],
                                          K.a_vT[0:kn, j, 64 * kv:64 * kv + 64], K.a_pT[0:kn, s, j, :],
                                          start=(j == 0), stop=(j == 4))
                last.then_inc(P.sem("att_out_done"), P.adds("att_out_done"))
                P.e.wait_ge(P.sem("att_out_lo"), P.due("att_out_lo"))

            if kv == 0:
                P.e.wait_ge(P.sem("vT_ready"), P.due("vT_ready"))
            P.loop(2, body, qk_staged=2, logits_done=8, exp_done=8, probs_ready=8, probs_transposed=8, probsT_ready=8,
                   att_out_done=1, att_out_lo=1)


class SplitYa(Stage):

    def act(self, K, P):
        P.e.activation(K.HH[:, 0:4, :], K.ya[:, :, :], ACT.Copy).then_inc(P.sem("ya_hi"), P.adds("ya_hi"))

    def dve(self, K, P):
        P.e.wait_ge(P.sem("ya_hi"), P.due("ya_hi"))
        P.e.tensor_tensor(K.HL[:, 0:4, :], K.ya[:, :, :], K.HH[:, 0:4, :].bitcast(F32), ALU.subtract)


class GatedNarrow(Narrow):

    def __init__(self, nk, xh, xl, gate):
        super().__init__(nk, xh, xl, gate)

    def act(self, K, P):
        narrow_split(K, P, self.nk, split_act)

    def dve(self, K, P):
        narrow_split(K, P, self.nk, split_dve)
        for t in range(8):
            P.e.tensor_tensor(self.dst[:, t, :], self.dst[:, t, :], K.PS[:, t, 0:S], ALU.mult)


class Merge(Stage):

    def dve(self, K, P):
        for t in range(8):
            P.e.tensor_tensor(K.gates[:, t, :], K.gates[:, t, :], K.gates[:, 8 + t, :], ALU.add).then_inc(P.sem("merged"), P.adds("merged"))
        for t in range(8):
            P.e.wait_ge(P.sem("merged_hi"), P.due("merged_hi"))
            P.e.wait_ge(P.sem("merged"), P.due("merged", 0))
            P.e.tensor_tensor(K.XL[:, t, 0:S], K.gates[:, t, :], K.XH[:, t, 0:S].bitcast(F32), ALU.subtract)

    def act(self, K, P):
        for t in range(8):
            P.e.wait_ge(P.sem("merged"), P.due("merged"))
            P.e.activation(K.XH[:, t, 0:S], K.gates[:, t, :], ACT.Copy).then_inc(P.sem("merged_hi"), P.adds("merged_hi"))


def block3(K):
    real = ((META, S),)
    st = [Load(K.loads3), RmsNorm(K.XM, K.p["mix_norm_g"], T3), GateRows(), Store(7, K.XH, K.XL, K.rp, toks=T3),
          CentredShift(), Load(K.loads3b), RwkvPrepare(), Load(K.loads3c), RwkvScan(), Load(K.loads3d), RwkvOutput(),
          RmsNorm(K.XM, K.p["mix_norm_g"], T3), Load(K.loads3e), Store(2, K.XH, K.XL, K.a_q, toks=real, off=META),
          Store(1, K.XH, K.XL, K.a_kv, toks=T3), QkNormRope(), GroupedAttention(), SplitYa(),
          Store(8, K.XH, K.XL, K.gates, toks=real, off=META, func=ACT.Sigmoid),
          GatedNarrow(4, K.HH, K.HL, K.gates[:, 0:8, :]), GatedNarrow(4, K.HH[:, 4:8, :], K.HL[:, 4:8, :], K.gates[:, 8:16, :]),
          Merge(), Narrow(8, K.XH, K.XL, K.X), RmsNorm(K.X, K.p["ffn3_norm_g"])]
    for c0, n in FF3_CHUNKS:
        st += [SquaredReluUp(n // 2, K.XH, K.XL), Narrow(n, K.HH, K.HL, K.X)]
    return st + [RmsNorm(K.X, K.p["final3_norm_g"], out=K.X)]


def specs3():
    v = [("mix_norm_g", "mix_norm_g_3", 0), ("ffn3_norm_g", "ffn_norm_g_3", 0), ("final3_norm_g", "final_norm_g_3", None),
         ("k_k", "k_k_3", 0), ("k_a", "k_a_3", 0), ("r_k", "r_k_3", 0), ("lnx_g", "lnx_g_3", 0), ("lnx_b", "lnx_b_3", 0)]
    v += [(f"decay_w0{d}", "decay_w0_3", (0, d)) for d in range(2)] + [(f"icl_a0{d}", "icl_a0_3", (0, d)) for d in range(2)]
    v += [("q_norm_g", "q_norm_g_3", 0), ("k_norm_g", "k_norm_g_3", 0)]
    return v


def weights3(a):
    w = a["w_in_3"][0]
    rk = 1952
    out = [wide_panels(w[:, 0:1792]), wide_panels(w[:, rk:rk + 512]), wide_panels(w[:, rk + 512:rk + 768]),
           wide_panels(w[:, rk + 768:]), narrow_panels(a["w_branch_rwkv_3"][0]), narrow_panels(a["w_branch_attn_3"][0]),
           narrow_panels(a["w_out_3"][0])]
    for c0, n in FF3_CHUNKS:
        c = slice(128 * c0, 128 * (c0 + n))
        out += [wide_panels(a["w_ff1_3"][0][:, c]), narrow_panels(a["w_ff2_3"][0][c])]
    return out


def consts3():
    r = np.arange(128)
    tile, tok = (r % 64) // 16, r % 16
    ct, ck = np.arange(64) // 16, np.arange(64) % 16
    same = tile[:, None] == ct[None, :]
    gram = []
    for d in range(2):
        before = (tok[:, None] < ck[None, :]) if d == 0 else (tok[:, None] > ck[None, :])
        after = (tok[:, None] > ck[None, :]) if d == 0 else (tok[:, None] < ck[None, :])
        here = before | (tok[:, None] == ck[None, :])
        gram += [same & before, same & here, same & before, same & here, same & after]
    block = np.repeat(tile[:, None] == np.arange(4)[None, :], 64, axis=1)
    eye = np.tile(np.eye(64), (2, 2))
    head = (r[:, None] // 64) == (r[None, :] // 64)
    rot = np.zeros((128, 128))
    for d in range(128):
        if (d % 32) < 16:
            rot[d + 16, d] = -1.0
        else:
            rot[d - 16, d] = 1.0
    inv = np.float32(10000.0) ** (-np.arange(16, dtype=np.float32) * np.float32(2.0) / np.float32(32))
    t = np.arange(S)
    row, colu = (t // 64).astype(np.float32), (t % 64).astype(np.float32)
    ang = np.zeros((128, TM), np.float32)
    for d in range(128):
        pos = row if (d % 64) < 32 else colu
        ang[d, META:] = pos * inv[d % 16]
    reset = np.broadcast_to((np.arange(TM) % 16 != 0), (128, TM))
    f = lambda x: np.ascontiguousarray(x.astype(np.float32))
    return {"gram_mask": f(np.concatenate(gram, axis=1).reshape(128, 2, 320)), "block_mask": f(block), "eye64": f(eye.reshape(128, 2, 64)),
            "head_ones": f(head), "rot": f(rot), "rope": f(np.stack([np.cos(ang), np.sin(ang)], axis=1)), "reset16": f(reset)}


class Prologue(Stage):

    def act(self, K, P):
        for dst, src in K.loads:
            P.e.dma_start(dst, src).then_inc(P.sem("inputs_loaded"), P.adds("inputs_loaded", 16))
        P.e.wait_ge(P.sem("inputs_loaded"), P.due("inputs_loaded", 0))
        for _ in range(2):
            split_act(K, P)

    def dve(self, K, P):
        for t in range(2):
            P.e.memset(K.zero_credit[:, t:t + 1], 0.0).then_inc(P.sem(f"tile_evacuated{t}"), 2)
        for _ in range(2):
            split_dve(K, P)
        


class Epilogue(Stage):

    def __init__(self, src):
        self.src = src

    def act(self, K, P):
        P.e.dma_start(K.out, self.src).then_inc(P.sem("output_stored"), P.adds("output_stored", 16))
        P.e.wait_ge(P.sem("output_stored"), P.due("output_stored", 0))


def block1(K):
    g1, hh, hl = K.p, K.HH, K.HL
    st = [RmsNorm(K.X, g1["att_norm_g"]), ForgetGates(K.w_fl, 16),
          Store(4, K.XH, K.XL, K.q1), Store(4, K.XH, K.XL, K.k1), Store(4, K.XH, K.XL, K.v1),
          ForgettingAttention(), Narrow(8, K.XH, K.XL, K.X)]
    st += ffn1(K, 0)
    st += [RmsNorm(K.X, g1["hgrn_norm_g"]), LowerBounds(),
           Store(4, K.XH, K.XL, K.q1h, func=ACT.Silu), Store(4, K.XH, K.XL, K.g1, func=ACT.Silu),
           Store(4, K.XH, K.XL, K.f1, func=ACT.Sigmoid), Store(4, K.XH, K.XL, K.i1),
           Hgrn(), Narrow(8, K.XH, K.XL, K.X)]
    st += ffn1(K, 1)
    st += [RmsNorm(K.X, g1["final_norm_g"], out=K.X)]
    return st


def ffn1(K, layer):
    conv = ([K.p[f"ffn_conv_w{layer}{j}"] for j in range(3)], K.p[f"ffn_conv_b{layer}"])
    st = [RmsNorm(K.X, K.p[f"ffn_norm_g{layer}"])]
    for c0, n in FFN_CHUNKS:
        up = GatedUp(n, c0, conv)
        up.xh, up.xl = K.XH, K.XL
        st += [up, Narrow(n, K.HH, K.HL, K.X)]
    return st


def vec_specs():
    v = [("att_norm_g", "att_norm_g", 0), ("hgrn_norm_g", "hgrn_norm_g", 0), ("hgrn_onorm_g", "hgrn_onorm_g", 0),
         ("final_norm_g", "final_norm_g", None)]
    for l in range(2):
        v += [(f"ffn_norm_g{l}", "ffn_norm_g", l), (f"ffn_conv_b{l}", "ffn_conv_b", l)]
        v += [(f"ffn_conv_w{l}{j}", "ffn_conv_w", (l, j)) for j in range(3)]
    return v


CONSTS = [("ident", 128), ("inv_d", 128), ("inv_dv", 128), ("causal", 128), ("ones_row", 512), ("reset64", 512),
          ("causal64", 256), ("one_col", 2), ("flip", 128), ("keep_upper", 128)]


def program(nc, args, out):
    n_panels = args["weights"].shape[0]
    with ExitStack() as ctx:
        K, M = Bufs(), Mem(nc)
        K.XM, _ = M.new("X", [128, KT, TM])
        K.X = K.XM[:, :, META:TM]
        K.XH, xa = M.new("XH", [128, KT, TM], F32R)
        K.XL, xb = M.new("XL", [128, KT, TM], F32R)
        K.W, _ = M.new("W", [128, 2, PANEL])
        K.WH, _ = M.new("WH", [128, 2, PANEL], F32R)
        K.WL, _ = M.new("WL", [128, 2, PANEL], F32R)
        K.HH, ha = M.new("HH", [128, 12, S], F32R)
        K.HL, _ = M.new("HL", [128, 12, S], F32R)
        consts, _ = M.new("consts", [128, sum(n for _, n in CONSTS)])
        params, _ = M.new("params", [128, args["params"].shape[1]])
        K.R, _ = M.new("R", [128, TM])
        K.zero_credit, _ = M.new("zero_credit", [128, 8])
        K.att_b_f, _ = M.new("att_b_f", [16, 1])
        K.lb_logits, _ = M.new("lb_logits", [128, 16])
        K.lbt, _ = M.new("lbt", [128, 24])
        K.lb, _ = M.new("lb", [128, 16])
        K.PS = ctx.enter_context(nc.psum_tensor("PS", [128, 8, 512], F32))
        at = 0
        cols = {}
        for name, n in CONSTS:
            cols[name] = consts[:, at:at + n]
            at += n
        K.ident, K.inv_d, K.inv_dv, K.causal = cols["ident"], cols["inv_d"], cols["inv_dv"], cols["causal"]
        K.ones_row, K.reset64, K.causal64, K.one_col = cols["ones_row"], cols["reset64"], cols["causal64"], cols["one_col"]
        K.flip, K.keep_upper = cols["flip"], cols["keep_upper"]
        K.p, at = {}, 0
        for name, n in args["param_tiles"]:
            K.p[name] = params[:, at:at + n]
            at += n
        scr = M.at
        room = (M.end - scr) // 32 * 8

        def v(name, shape, words, base=None, dt=F32):
            assert words + int(np.prod(shape[1:])) <= (room if base is None else 24 * S), (name, room)
            return nc.alloc_sbuf_tensor_at(name, shape, dt, offset=(scr if base is None else base) + 4 * words)

        K.Y = v("Y", [128, KT, TM], 0)
        K.w_fl = v("w_fl", [128, KT, 16], 4224)
        K.q1, K.k1 = v("q1", [128, 8, S], 0, ha), v("k1", [128, 8, S], 4096, ha)
        K.qs, K.ks = v("qs", [128, 2, S], 8192, ha), v("ks", [128, 2, S], 9216, ha)
        K.vs, K.vT = v("vs", [128, S], 10240, ha), v("vT", [128, S], 10752, ha)
        K.v1 = v("v1", [128, 8, S], 0)
        K.c_rows, K.gate_rows = v("c_rows", [16, S], 4608), v("gate_rows", [16, 2, S], 5120)
        K.cm, K.ncm = v("cm", [16, 2, S], 6144), v("ncm", [16, 2, S], 7168)
        K.pr, K.pT, K.st = v("pr", [128, 2, S], 8192), v("pT", [128, 2, S], 9216), v("st", [128, 2, 4], 10240)
        K.one_row16 = v("one_row16", [16, S], 10256)

        K.q1h, K.f1 = v("q1h", [128, 8, S], 0), v("f1", [128, 8, S], 4096)
        K.i1, K.g1 = v("i1", [128, 8, S], 0, ha), v("g1", [128, 8, S], 4096, ha)
        (K.h_f, K.h_k, K.h_lf, K.h_b, K.h_eb, K.h_en, K.h_qd, K.h_ki) = (v(f"head{j}", [128, S], 8192 + 512 * j) for j in range(8))
        K.aT = v("aT", [128, 256], 12288)
        K.h_ks, K.h_i = v("h_ks", [128, S], 8192, ha), v("h_i", [128, S], 8704, ha)
        K.iT, K.ksT = v("iT", [128, 4, 128], 9216, ha), v("ksT", [128, 4, 128], 10240, ha)
        K.sp = v("sp", [128, 8, 128], 11264, ha)

        K.CV, K.CF = v("CV", [128, 2, 2, S], 4224), v("CF", [128, 2, 2, S], 6272)
        K.SG, K.HF = v("SG", [128, 2, S], 6272), v("HF", [128, 2, S], 7296)

        K.F = v("F", [128, KT, S], 8320)
        K.in2 = v("in2", [128, 24, S], 0, ha)
        K.d_q, K.d_k = v("d_q", [128, 2, S], 0), v("d_k", [128, 2, S], 1024)
        K.d_vs, K.d_vT = v("d_vs", [128, S], 2048), v("d_vT", [128, S], 2560)
        K.d_p, K.d_pT = v("d_p", [128, 2, S], 3072), v("d_pT", [128, 2, S], 4096)
        K.bias, K.d_st, K.lam = v("bias", [128, 4, 512], 5120), v("d_st", [128, 2, 4], 7168), v("lam", [128, 256], 7184)
        K.lamt, K.bias_t, K.onehot = v("lamt", [128, 8], 7440), v("bias_t", [33, 4], 7448), v("onehot", [33, BIAS_W], 7456)
        K.d_cz, K.d_cy, K.d_sq = v("d_cz", [128, S], 8104), v("d_cy", [128, S], 8616), v("d_sq", [128, S], 9128)
        K.bias_rows, K.lam_prod = v("bias_rows", [4, BIAS_W], 9640), v("lam_prod", [128, 128], 10280)
        K.bias_dram = nc.dram_tensor("bias_spread", (4, BIAS_W), F32, kind="Internal").ap()
        K.uv2 = v("uv2", [128, 16, S], 0, ha)
        K.u2, K.v2 = K.uv2[:, 0:8, :], K.uv2[:, 8:16, :]
        K.ws, K.sgu_b, K.one_row2 = v("ws", [128, 8, 128], 4224), v("sgu_b", [1, 8, 128], 5248), K.ones_row
        K.s_a, K.s_b, K.s_vT, K.s_o = (v("s_" + n, [128, S], 6272 + 512 * j) for j, n in enumerate(("a", "b", "vT", "o")))

        if 3 in BLOCKS:
            rest = 4 * 4 * TM
            K.w_gd = v("w_gd", [128, KT, 160], 4224)
            K.mu, K.mu_rest = v("mu", [128, 16, 2], 5504), v("mu_rest", [128, 16], 5536)
            K.rp = v("rp", [128, 16, TM], 0, ha)
            rz = nc.alloc_sbuf_tensor_at("rz", [128, 16 * TM], F32, offset=xa)
            K.rz = rz[:, :].rearrange("p (q t) -> p q t", q=16)
            K.yt = rz[:, 4 * TM:8 * TM].rearrange("p (n c) -> p n c", c=64)
            K.ar = [v("ar0", [128, 4, 4, TM], 0, ha), v("ar1", [128, 4, 4, TM], 0)]
            K.t_s, K.t_a = v("t_s", [128, 2, TM], rest, ha), v("t_a", [128, 2, TM], rest + 2 * TM, ha)
            K.t_k, K.t_n = v("t_k", [128, 2, TM], rest + 4 * TM, ha), v("t_n", [128, TM], rest + 6 * TM, ha)
            K.head_ones = v("head_ones", [128, 128], rest + 7 * TM, ha)
            K.wc = v("wc", [128, 2, 4, N_CHUNK], rest)
            K.reset16, K.t_kk, K.t_bi, K.t_bx, K.t_en = (v(f"prepare{j}", [128, TM], rest + 264 + TM * j) for j in range(5))
            K.t_u = K.t_en
            at = rest + 264 + 5 * TM
            K.w2, K.a2 = v("w2", [128, 512], at), v("a2", [128, 512], at + 512)
            K.t_bc, K.t_c = v("t_bc", [128, N_CHUNK], at + 1024), v("t_c", [128, 2], at + 1064)

            def row(base, at, *named):
                out = []
                for name, shape in named:
                    out.append(v(name, shape, at, base))
                    at += int(np.prod(shape[1:]))
                return out

            (K.c_st, K.c_g, K.c_n2, K.c_n4, K.c_n8, K.c_p, K.c_bt, K.c_v, K.c_r) = row(ha, rest, ("c_st", [128, 2, 5, 64]), ("c_g", [128, 2, 320]), ("c_n2", [128, 2, 128]), ("c_n4", [128, 2, 128]),
                                ("c_n8", [128, 2, 64]), ("c_p", [128, 2, 2, 64]), ("c_bt", [128, 4, 64]), ("c_v", [128, 512]),
                                ("c_r", [128, 512]))
            (K.c_u, K.c_s, K.c_y, K.c_yr, K.gram_mask, K.block_mask, K.eye64) = row(None, rest + 264, ("c_u", [128, 512]), ("c_s", [128, 512]), ("c_y", [128, 512]), ("c_yr", [128, 2, 64]),
                                ("gram_mask", [128, 2, 320]), ("block_mask", [128, 256]), ("eye64", [128, 2, 64]))
            K.ya = v("ya", [128, 4, S], room - 2048 - 8)
            K.y2, K.yf = v("y2", [128, N_CHUNK, 64], 0, ha), v("yf", [128, 4, S], 2112, ha)
            K.g_c = v("g_c", [128, 2, N_CHUNK], 4160, ha)
            K.g2a, K.g2b = v("g2a", [128, 512], 0), v("g2b", [32, 512], 512)
            (K.a_q, K.a_kv, K.a_t, K.rope, K.rot, K.a_ks, K.a_vT, K.a_qs, K.a_p, K.a_st, K.a_pT, K.head_ones2) = row(None, 0, ("a_q", [128, 4, S]), ("a_kv", [128, 2, TM]), ("a_t", [128, 2, TM]), ("rope", [128, 2, TM]),
                                ("rot", [128, 128]), ("a_ks", [64, 2, TM]), ("a_vT", [128, 5, 128]), ("a_qs", [64, 2, S]),
                                ("a_p", [128, 2, TM]), ("a_st", [128, 2, 4]), ("a_pT", [128, 2, 5, 128]), ("head_ones2", [128, 128]))
            K.gates = v("gates", [128, 16, S], 0)
            A = args
            K.loads3 = [(K.w_gd[:, :, :], A["w_gd"]), (K.mu[:, 0:15, :], A["mu"]), (K.mu[0:32, 15:16, :], A["mu_tail"]),
                        (K.XM[:, :, 0:META], A["meta"])]
            K.loads3b = [(K.w2[:, :], A["w2"]), (K.a2[:, :], A["a2"]), (K.reset16[:, :], A["c3_reset16"]), (K.head_ones[:, :], A["c3_head_ones"])]
            K.loads3c = [(K.gram_mask[:, :, :], A["c3_gram_mask"]), (K.block_mask[:, :], A["c3_block_mask"]), (K.eye64[:, :, :], A["c3_eye64"])]
            K.loads3d = [(K.g2a[:, :], A["g2"][0:128, :]), (K.g2b[:, :], A["g2"][128:160, :])]
            K.loads3e = [(K.rope[:, :, :], A["c3_rope"]), (K.rot[:, :], A["c3_rot"]), (K.head_ones2[:, :], A["c3_head_ones"])]

        K.halves = lambda t, u: t[:, 0:S].rearrange("p (j u c) -> p u j c", u=2, c=64)[:, u]
        K.halves_ps = lambda u: K.PS[:, (7, 3)[u], 0:256].rearrange("p (j c) -> p j c", c=64)
        K.weights = args["weights"]
        K.out = out
        K.loads = [(consts[:, :], args["consts"]), (params[:, :], args["params"]), (K.X[:, :, 0:S], args["x"])]
        if 1 in BLOCKS:
            K.loads += [(K.att_b_f[:, :], args["att_b_f"]), (K.lb_logits[:, :], args["lb_logits"]),
                        (K.w_fl[:, :, :], args["w_fl"])]
        if 2 in BLOCKS:
            K.loads2 = [(K.lam[:, :], args["lam"].partition_broadcast(128)), (K.bias_t[0:32, :], args["rel_bias"]),
                        (K.onehot[:, :], args["onehot"])]
            K.loads2b = [(K.ws[:, :, :], args["ws"]), (K.sgu_b[0:1, :, :], args["sgu_b"])]
        stages = [Prologue()]
        if 1 in BLOCKS:
            stages += block1(K)
        if 2 in BLOCKS:
            stages += block2(K)
        if 3 in BLOCKS:
            stages += block3(K)
        stages += [Epilogue(K.X[:, :, 0:S])]

        sems = {}
        block = ctx.enter_context(nc.Block())

        def engine(e, tag):
            P = Engine(ctx, nc, sems, e, tag)
            P.split_left, P.split_par = n_panels, 0
            return P

        def left_after_prologue(P, stage):
            if isinstance(stage, Prologue):
                P.split_left = n_panels - 2

        @block.sync
        def _(e):
            stream_sync(K, engine(e, "sync"), n_panels)

        @block.tensor
        def _(e):
            P = engine(e, "pe")
            for st in stages:
                st.pe(K, P)
                P.stage_end()

        @block.scalar
        def _(e):
            P = engine(e, "act")
            for st in stages:
                st.act(K, P)
                left_after_prologue(P, st)
                P.stage_end()

        @block.vector
        def _(e):
            P = engine(e, "dve")
            for st in stages:
                st.dve(K, P)
                left_after_prologue(P, st)
                P.stage_end()

        @block.gpsimd
        def _(e):
            P = engine(e, "pool")
            for st in stages:
                st.pool(K, P)
                P.stage_end()


def wide_panels(w):
    return w.reshape(KT, 128, -1, 256).transpose(2, 1, 0, 3).reshape(-1, 128, PANEL)


def narrow_panels(w):
    return w.reshape(-1, 2, 128, D).transpose(0, 2, 1, 3).reshape(-1, 128, PANEL)


def paired_panels(gate, value):
    g = gate.reshape(KT, 128, -1, 1, 128)
    v = value.reshape(KT, 128, -1, 1, 128)
    return np.concatenate([g, v], axis=3).transpose(2, 1, 0, 3, 4).reshape(-1, 128, PANEL)


def ffn_panels(gate, value, down, chunks):
    out = []
    for c0, n in chunks:
        c = slice(128 * c0, 128 * (c0 + n))
        out += [paired_panels(gate[:, c], value[:, c]), narrow_panels(down[c])]
    return out


def weights1(a):
    w = a["att_w_in"][0]
    out = [wide_panels(w[:, 0:3 * D]), narrow_panels(a["att_w_out"][0])]
    up, down = a["ffn_w_up"], a["ffn_w_down"]
    out += ffn_panels(up[0][:, :FFN], up[0][:, FFN:], down[0], FFN_CHUNKS)
    w = a["hgrn_w_in"][0]
    out += [wide_panels(w[:, c * D:(c + 1) * D]) for c in (0, 3, 1, 2)] + [narrow_panels(a["hgrn_w_out"][0])]
    out += ffn_panels(up[1][:, :FFN], up[1][:, FFN:], down[1], FFN_CHUNKS)
    return out


def make_consts():
    r = np.arange(128)
    c = {
        "ident": np.eye(128),
        "inv_d": np.full((128, 128), 1.0 / D),
        "inv_dv": np.full((128, 128), 1.0 / 128),
        "causal": np.where(r[None, :] <= r[:, None], 0.0, NEG),
        "ones_row": np.ones((128, 512)),
        "reset64": np.broadcast_to((np.arange(512) % 64 != 0).astype(np.float32), (128, 512)),
        "causal64": (np.arange(256)[None, :] % 64 >= (r % 64)[:, None]).astype(np.float32),
        "one_col": np.ones((128, 2)),
        "flip": np.eye(128)[::-1],
        "keep_upper": (r[:, None] <= r[None, :]).astype(np.float32),
    }
    return np.ascontiguousarray(np.concatenate([c[n].astype(np.float32) for n, _ in CONSTS], axis=1))


def kernel(**inputs):
    import concourse.bacc as bacc
    from concourse.bass_utils import run_bass_kernel_spmd

    a = {k: np.asarray(v) for k, v in inputs.items()}
    cols, tiles = [], []
    for name, key, idx in (vec_specs() if 1 in BLOCKS else []) + (specs2() if 2 in BLOCKS else []) + (specs3() if 3 in BLOCKS else []):
        x = a[key] if idx is None else a[key][idx]
        if x.size == 64:
            x = np.concatenate([x, x])
        cols.append(x.reshape(-1, 128).T)
        tiles.append((name, cols[-1].shape[1]))
    weights = []
    if 1 in BLOCKS:
        weights += weights1(a)
    if 2 in BLOCKS:
        weights += weights2(a)
    if 3 in BLOCKS:
        weights += weights3(a)
    arrays = {
        "weights": np.concatenate(weights, axis=0),
        "x": a["x"][0].T.reshape(KT, 128, S).transpose(1, 0, 2),
        "params": np.concatenate(cols, axis=1),
        "consts": make_consts(),
    }
    if 1 in BLOCKS:
        arrays["att_b_f"] = a["att_b_f"].reshape(16, 1)
        arrays["lb_logits"] = a["hgrn_lb_logits"].reshape(2, KT, 128).transpose(2, 0, 1).reshape(128, 16)
        arrays["w_fl"] = a["att_w_in"][0][:, 3 * D:].reshape(KT, 128, 16).transpose(1, 0, 2)
    if 2 in BLOCKS:
        arrays["lam"] = a["diff_lambda_2"].reshape(256)
        arrays["rel_bias"] = a["rel_bias_2"]
        arrays["onehot"] = bucket_onehot()
        arrays["ws"] = a["sgu_w_2"][0].transpose(2, 0, 1)
        arrays["sgu_b"] = a["sgu_b_2"]
    if 3 in BLOCKS:
        w, mu = a["w_in_3"][0], a["rwkv_shift_3"][0]
        arrays["w_gd"] = w[:, 1792:1952].reshape(KT, 128, 160).transpose(1, 0, 2)
        arrays["mu"] = mu[:, 0:1920].reshape(2, 15, 128).transpose(2, 1, 0)
        arrays["mu_tail"] = mu[:, 1920:].T.reshape(32, 1, 2)
        arrays["meta"] = a["meta_tokens_3"].T.reshape(KT, 128, META).transpose(1, 0, 2)
        arrays["w2"] = a["decay_w2_3"].reshape(128, 512)
        arrays["a2"] = a["icl_a2_3"].reshape(128, 512)
        arrays["g2"] = a["gate_w2_3"].reshape(160, 512)
        for name, x in consts3().items():
            arrays["c3_" + name] = x
    nc = bacc.Bacc("TRN2", target_bir_lowering=False, num_devices=1)
    sent, args = {}, {}
    for name, x in arrays.items():
        sent["in_" + name] = np.ascontiguousarray(x)
        args[name] = nc.dram_tensor("in_" + name, x.shape, mybir.dt.from_np(x.dtype), kind="ExternalInput").ap()
    args["param_tiles"] = tiles
    out = nc.dram_tensor("out_0", (128, KT, S), F32, kind="ExternalOutput").ap()
    program(nc, args, out)
    r = run_bass_kernel_spmd(nc, [sent], core_ids=[0])
    y = r.results[0]["out_0"]
    return y.transpose(1, 0, 2).reshape(D, S).T.reshape(1, S, D)
```

```python
from contextlib import ExitStack

import numpy as np

import concourse.bass as bass
from concourse import mybir

F32 = mybir.dt.float32
F32R = mybir.dt.float32r
I32 = mybir.dt.int32
ALU = mybir.AluOpType
ACT = mybir.ActivationFunctionType
AX = mybir.AxisListType

BLOCKS = (1, 2, 3)
D = 1024
S = 512
KT = D // 128
PANEL = 2048
META = 16
TM = S + META
FFN = 2816
FT = FFN // 128
FFN_CHUNKS = ((0, 12), (12, 10))
FF3_CHUNKS = ((0, 12), (12, 12), (24, 8))
EPS = 1e-6
NEG = -1e30


class Engine:

    def __init__(self, ctx, nc, sems, e, tag):
        self.ctx, self.nc, self.sems, self.e, self.tag = ctx, nc, sems, e, tag
        self.n, self.off = {}, {}
        self.parity = 0
        self.split_later = False

    def sem(self, name):
        if name not in self.sems:
            self.sems[name] = self.ctx.enter_context(self.nc.semaphore(name))
        return self.sems[name]

    def count(self, name, k):
        self.n[name] = self.n.get(name, 0) + k

    def adds(self, name, by=1):
        self.count(name, by)
        return by

    def due(self, name, k=1, less=0):
        self.count(name, k)
        return self.off.get(name, 0) + (self.n[name] - less)

    def settle(self):
        self.e.sem_inc(self.sem(self.tag + "_passed_waits"), 1)

    def loop(self, times, body, **per):
        if times <= 0:
            return
        if times == 1:
            body(0)
            return
        start = dict(self.n)
        with self.e.Fori(0, times) as i:
            for name, k in per.items():
                self.off[name] = i * k
            body(i)
            self.off = {}
        got = {k: v - start.get(k, 0) for k, v in self.n.items() if v != start.get(k, 0)}
        assert got == {k: v for k, v in per.items() if v}, f"{self.tag} loop counts {got}"
        for name, k in per.items():
            self.n[name] = start.get(name, 0) + times * k

    def stage_end(self):
        self.e.drain().then_inc(self.sem("stage_done"), 1)
        self.e.wait_ge(self.sem("stage_done"), self.due("stage_done", 3))

    def stage_end_open(self):
        self.e.drain().then_inc(self.sem("stage_done"), 1)
        self.count("stage_done", 3)


class Mem:

    def __init__(self, nc):
        self.nc, self.at = nc, (nc.sbuf_base + 31) // 32 * 32
        self.end = nc.sbuf_usable_end

    def new(self, name, shape, dt=F32):
        words = int(np.prod(shape[1:]))
        t = self.nc.alloc_sbuf_tensor_at(name, shape, dt, offset=self.at)
        t_at = self.at
        self.at += (4 * words + 31) // 32 * 32
        assert self.at <= self.end, (name, self.at, self.end)
        return t, t_at


def sl(i, k=1):
    return slice(i, i + k) if isinstance(i, int) else bass.ds(i, k)


class Bufs:
    pass


def split_act(K, P):
    if P.split_left <= 0:
        return
    s = P.split_par
    P.e.wait_ge(P.sem(f"weights_loaded{s}"), P.due(f"weights_loaded{s}", 16))
    P.e.activation(K.WH[:, s, :], K.W[:, s, :], ACT.Copy).then_inc(P.sem("hi_ready"), P.adds("hi_ready"))
    P.split_par ^= 1


def split_dve(K, P):
    if P.split_left <= 0:
        return
    s = P.split_par
    P.e.wait_ge(P.sem("hi_ready"), P.due("hi_ready"))
    P.e.tensor_tensor(K.WL[:, s, :], K.W[:, s, :], K.WH[:, s, :].bitcast(F32), ALU.subtract).then_inc(P.sem("weights_split"), P.adds("weights_split"))
    P.split_par ^= 1


def stream_sync(K, P, n_panels):
    for s in range(2):
        P.e.dma_start(K.W[:, s, :], K.weights[s]).then_inc(P.sem(f"weights_loaded{s}"), P.adds(f"weights_loaded{s}", 16))

    def body(i):
        for s in range(2):
            P.e.wait_ge(P.sem("weights_split"), P.due("weights_split"))
            src = K.weights[sl(2 * i + 2 + s)].rearrange("a p n -> (a p) n")
            P.e.dma_start(K.W[:, s, :], src).then_inc(P.sem(f"weights_loaded{s}"), P.adds(f"weights_loaded{s}", 16))

    pairs = (n_panels - 2) // 2
    P.loop(pairs, body, weights_split=2, weights_loaded0=16, weights_loaded1=16)
    for s in range((n_panels - 2) % 2):
        P.e.wait_ge(P.sem("weights_split"), P.due("weights_split"))
        P.e.dma_start(K.W[:, s, :], K.weights[2 * pairs + 2 + s]).then_inc(P.sem(f"weights_loaded{s}"), P.adds(f"weights_loaded{s}", 16))


def wide_pe(K, P, n, xh, xl, toks, after_norm, after_narrow):
    def panel(i, first=False, sums=0):
        s = P.parity
        P.e.wait_ge(P.sem("weights_split"), P.due("weights_split"))
        wh = K.WH[:, s, :].rearrange("p (k n) -> p k n", k=KT)
        wl = K.WL[:, s, :].rearrange("p (k n) -> p k n", k=KT)
        for t in range(2):
            P.e.wait_ge(P.sem(f"tile_evacuated{t}"), P.due(f"tile_evacuated{t}"))
            bank = 2 * (2 * s + t)
            if sums:
                P.e.wait_ge(P.sem("sum_stored"), P.due("sum_stored", 0, less=7 - bank))
            c = slice(128 * t, 128 * t + 128)
            for part, (t0, tn) in enumerate(toks):
                out = K.PS[:, bank + part, 0:tn]
                for k in range(KT):
                    r = slice(t0, t0 + tn)
                    if first and t == 0 and part == 0:
                        P.e.wait_ge(P.sem("norm_lo"), P.due("norm_lo"))
                    P.e.matmul(out, wh[:, k, c], xh[:, k, r], start=(k == 0), stop=False)
                    P.e.matmul(out, wh[:, k, c], xl[:, k, r], start=False, stop=False)
                    last = P.e.matmul(out, wl[:, k, c], xh[:, k, r], start=False, stop=(k == KT - 1))
            last.then_inc(P.sem("tile_done"), P.adds("tile_done"))
        P.parity ^= 1

    def body(i):
        panel(i)
        panel(i)

    peeled = 2 if after_narrow else (2 if n % 2 == 0 else 1) if after_norm else 0
    for p in range(peeled):
        panel(0, after_norm and p == 0, after_narrow)
    P.loop((n - peeled) // 2, body, weights_split=2, tile_evacuated0=2, tile_evacuated1=2, tile_done=4)
    if (n - peeled) % 2:
        panel(0)


def wide_evac(K, P, n, evac, split, per):
    def panel(p, s):
        evac(P, p, s, "first")
        split(K, P)
        evac(P, p, s, "rest")
        P.count("tile_evacuated0", 1)
        P.count("tile_evacuated1", 1)

    def body(i):
        panel(2 * i, P.parity)
        panel(2 * i + 1, P.parity ^ 1)

    counts = {k: 2 * v for k, v in dict(per, tile_evacuated0=1, tile_evacuated1=1).items()}
    if split is split_act:
        counts.update(hi_ready=2, weights_loaded0=16, weights_loaded1=16)
    else:
        counts.update(hi_ready=2, weights_split=2)
    left = P.split_left
    whole = min(n, left) if min(n, left) % 2 == 0 else min(n, left) - 1
    P.loop(whole // 2, body, **counts)
    P.split_left = left - whole
    for p in range(whole, n):
        panel(p, P.parity)
        P.parity ^= 1
        P.split_left -= 1


def narrow_pe(K, P, nk, xh, xl, after_wide):
    def panel(k0, first, last_panel):
        s = P.parity
        P.e.wait_ge(P.sem("weights_split"), P.due("weights_split"))
        order = [(kk, t) for kk in range(2) for t in range(8)]
        if first and after_wide:
            order = [(kk, t) for t0 in (1, 0) for kk in range(2) for t in range(t0, 8, 2)]
        if last_panel and after_wide:
            P.e.wait_ge(P.sem("stage_done"), P.due("stage_done", 0))
        for kk, t in order:
            if first and after_wide and kk == 0 and t == 0:
                for j in range(2):
                    P.e.wait_ge(P.sem(f"tile_evacuated{j}"), P.due(f"tile_evacuated{j}", 0, less=-2))
            c = slice(kk * D + 128 * t, kk * D + 128 * t + 128)
            out = K.PS[:, t, 0:S]
            k = sl(k0 + kk)
            h = xh[:, k, 0:S].rearrange("p a n -> p (a n)")
            l = xl[:, k, 0:S].rearrange("p a n -> p (a n)")
            P.e.matmul(out, K.WH[:, s, c], h, start=(first and kk == 0), stop=False)
            P.e.matmul(out, K.WH[:, s, c], l, start=False, stop=False)
            last = P.e.matmul(out, K.WL[:, s, c], h, start=False, stop=(last_panel and kk == 1))
            if last_panel and kk == 1 and t < 7:
                last.then_inc(P.sem("sum_done"), P.adds("sum_done"))
            elif (kk, t) == order[len(order) // 2 - 1] or (kk, t) == order[-1]:
                last.then_inc(P.sem("tile_done"), P.adds("tile_done"))
        P.parity ^= 1

    n = nk // 2
    panel(0, True, n == 1)
    pairs = max(0, (n - 2) // 2)

    def body(i):
        panel(4 * i + 2, False, False)
        panel(4 * i + 4, False, False)

    P.loop(pairs, body, weights_split=2, tile_done=4)
    for p in range(1 + 2 * pairs, n):
        panel(2 * p, False, p == n - 1)


def narrow_split(K, P, nk, split):
    def panel():
        if split is split_act:
            P.e.wait_ge(P.sem("tile_done"), P.due("tile_done", 2))
        split(K, P)
        P.parity ^= 1

    def body(i):
        panel()
        panel()

    left = P.split_left
    n = nk // 2
    P.split_later = min(n, left) == n
    whole = (min(n, left) - P.split_later) // 2 * 2
    if split is split_act:
        P.loop(whole // 2, body, tile_done=4, hi_ready=2, weights_loaded0=16, weights_loaded1=16)
    else:
        P.loop(whole // 2, body, hi_ready=2, weights_split=2)
    P.split_left = left - whole
    for p in range(whole, n - P.split_later):
        panel()
        P.split_left -= 1
    if split is split_dve:
        P.count("tile_done", nk)


def split_last(K, P, split):
    if P.split_later:
        if split is split_act:
            P.e.wait_ge(P.sem("tile_done"), P.due("tile_done", 2))
        split(K, P)
        P.parity ^= 1
        P.split_left -= 1
        P.split_later = False


def sum_wait(P, t):
    if t < 7:
        P.e.wait_ge(P.sem("sum_done"), P.due("sum_done"))
    else:
        P.e.wait_ge(P.sem("tile_done"), P.due("tile_done", 0))


class Stage:

    gives_normed = gives_sums = gives_banks = False

    def pe(self, K, P):
        pass

    def act(self, K, P):
        pass

    def dve(self, K, P):
        pass


class Wide(Stage):

    def __init__(self, n, xh, xl, toks=((0, S),)):
        self.n, self.xh, self.xl, self.toks = n, xh, xl, toks

    gives_banks = True
    after_norm = after_narrow = False
    per_act = {}
    per_dve = {}

    def pe(self, K, P):
        wide_pe(K, P, self.n, self.xh, self.xl, self.toks, self.after_norm, self.after_narrow)

    def act(self, K, P):
        wide_evac(K, P, self.n, lambda P, p, s, when: self.evac_act(K, P, p, s, when), split_act,
                  dict(self.per_act, tile_done=2))

    def dve(self, K, P):
        wide_evac(K, P, self.n, lambda P, p, s, when: self.evac_dve(K, P, p, s, when), split_dve,
                  dict(self.per_dve, tile_done=2))

    def evac_act(self, K, P, p, s, when):
        if when == "first":
            P.e.wait_ge(P.sem("tile_done"), P.due("tile_done", 2))

    def evac_dve(self, K, P, p, s, when):
        if when == "first":
            P.e.wait_ge(P.sem("tile_done"), P.due("tile_done", 2))


class Store(Wide):

    def __init__(self, n, xh, xl, dst, first=0, func=None, toks=((0, S),), off=0):
        super().__init__(n, xh, xl, toks)
        self.off = off
        self.dst, self.first, self.func = dst, first, func

    def both(self):
        return self.func is not None

    def evac_act(self, K, P, p, s, when):
        if when != "first":
            return
        for t in range(2):
            P.e.wait_ge(P.sem("tile_done"), P.due("tile_done"))
            if t and not self.both():
                continue
            for part, (t0, tn) in enumerate(self.toks):
                last = P.e.activation(self.dst[:, sl(2 * p + t + self.first), t0 - self.off:t0 - self.off + tn].rearrange("p a n -> p (a n)"),
                                      K.PS[:, 2 * (2 * s + t) + part, 0:tn], self.func or ACT.Copy)
            last.then_inc(P.sem(f"tile_evacuated{t}"), 1)

    def evac_dve(self, K, P, p, s, when):
        if when != "first":
            return
        P.e.wait_ge(P.sem("tile_done"), P.due("tile_done", 2))
        if self.both():
            return
        for part, (t0, tn) in enumerate(self.toks):
            last = P.e.tensor_copy(self.dst[:, sl(2 * p + 1 + self.first), t0 - self.off:t0 - self.off + tn].rearrange("p a n -> p (a n)"),
                                   K.PS[:, 2 * (2 * s + 1) + part, 0:tn])
        last.then_inc(P.sem("tile_evacuated1"), 1)


class Narrow(Stage):

    gives_sums = True
    before_norm = after_wide = False

    def __init__(self, nk, xh, xl, dst, add=True, off=0):
        self.nk, self.xh, self.xl, self.dst, self.add, self.off = nk, xh, xl, dst, add, off

    def pe(self, K, P):
        narrow_pe(K, P, self.nk, self.xh, self.xl, self.after_wide)
        P.count("sum_stored", 8)

    def act(self, K, P):
        narrow_split(K, P, self.nk, split_act)
        if not self.before_norm:
            split_last(K, P, split_act)

    def dve(self, K, P):
        narrow_split(K, P, self.nk, split_dve)
        for t in range(8):
            d = self.dst[:, t, self.off:self.off + S]
            sum_wait(P, t)
            if self.add:
                last = P.e.tensor_tensor(d, d, K.PS[:, t, 0:S], ALU.add)
            else:
                last = P.e.tensor_copy(d, K.PS[:, t, 0:S])
            last.then_inc(P.sem("sum_stored"), P.adds("sum_stored"))
        if not self.before_norm:
            split_last(K, P, split_dve)


class Small(Stage):

    def __init__(self, w, m, bank=0, toks=((0, S),)):
        self.w, self.m, self.bank, self.toks = w, m, bank, toks

    def pe(self, K, P):
        for part, (t0, tn) in enumerate(self.toks):
            for k in range(KT):
                P.e.matmul(K.PS[0:self.m, self.bank + part, 0:tn], self.w[:, k, :], K.Y[:, k, t0:t0 + tn],
                           start=(k == 0), stop=(k == KT - 1))


class RmsNorm(Stage):

    def __init__(self, src, gain, toks=((0, S),), out=None, add=False, out_off=0, eps=EPS):
        self.src, self.gain, self.toks, self.out, self.add, self.eps = src, gain, toks, out, add, eps
        self.t0, self.t1 = toks[0][0], toks[-1][0] + toks[-1][1]
        self.out_off = out_off

    gives_normed = property(lambda self: self.out is None)
    after_sums = before_panels = False

    def blocks(self):
        out = [(part, c, min(128, tn - c)) for part, (t0, tn) in enumerate(self.toks) for c in range(0, tn, 128)]
        return sorted(out, key=lambda b: -b[2])

    def columns(self, K):
        n, rows = len(self.blocks()), self.blocks()[-1][2]
        return [K.R[:, 0:4]] + ([K.R[0:rows, 4:n]] if n > 4 else [])

    def act(self, K, P):
        for k in range(KT):
            if self.after_sums:
                P.e.wait_ge(P.sem("sum_stored"), P.due("sum_stored"))
            P.e.activation(K.Y[:, k, self.t0:self.t1], self.src[:, k, self.t0:self.t1], ACT.Square).then_inc(P.sem("norm_squared"), P.adds("norm_squared"))
        split_last(K, P, split_act)
        P.e.wait_ge(P.sem("norm_inverse"), P.due("norm_inverse"))
        for r in self.columns(K):
            last = P.e.activation(r, r, ACT.Sqrt)
        last.then_inc(P.sem("norm_root"), P.adds("norm_root"))
        if self.out is None:
            for k in range(KT):
                P.e.wait_ge(P.sem("norm_scaled"), P.due("norm_scaled"))
                P.e.activation(K.XH[:, k, self.t0:self.t1], K.Y[:, k, self.t0:self.t1], ACT.Copy).then_inc(P.sem("norm_hi"), P.adds("norm_hi"))

    def pe(self, K, P):
        P.e.wait_ge(P.sem("norm_summed"), P.due("norm_summed"))
        for j, (part, c, n) in enumerate(self.blocks()):
            t = self.toks[part][0] + c
            for half in range(2):
                last = P.e.matmul(K.PS[0:n, 0, 2 * j:2 * j + 2], K.Y[:, half, t:t + n], K.inv_d[:, 0:2], start=(half == 0), stop=(half == 1))
        last.then_inc(P.sem("norm_mean"), P.adds("norm_mean"))
        for j, (part, c, n) in enumerate(self.blocks()):
            P.e.wait_ge(P.sem("norm_diagonal"), P.due("norm_diagonal"))
            last = P.e.matmul(K.PS[:, 6 + part, c:c + n], K.ones_row[0:n, 0:128], K.R[0:n, 16 + 128 * (j % 4):16 + 128 * (j % 4) + n], start=True, stop=True)
            last.then_inc(P.sem("norm_spread"), P.adds("norm_spread"))
        if self.out is None and not self.before_panels:
            P.count("norm_lo", KT)

    def dve(self, K, P):
        for k in range(2, KT):
            P.e.wait_ge(P.sem("norm_squared"), P.due("norm_squared", 3 if k == 2 else 1))
            if k >= 4:
                P.e.wait_ge(P.sem("norm_partial"), P.due("norm_partial", 0, less=1))
            y = K.Y[:, k % 2, self.t0:self.t1]
            last = P.e.tensor_tensor(y, y, K.Y[:, k, self.t0:self.t1], ALU.add)
            last.then_inc(P.sem("norm_summed" if k == KT - 1 else "norm_partial"), P.adds("norm_summed" if k == KT - 1 else "norm_partial"))
        split_last(K, P, split_dve)
        blocks = self.blocks()
        P.e.wait_ge(P.sem("norm_mean"), P.due("norm_mean"))
        for j, (part, c, n) in enumerate(blocks):
            last = P.e.tensor_scalar(K.R[0:n, j:j + 1], K.PS[0:n, 0, 2 * j:2 * j + 1], self.eps, None, ALU.add)
        last.then_inc(P.sem("dve_order"), P.adds("dve_order"))
        P.e.wait_ge(P.sem("dve_order"), P.due("dve_order", 0))
        for r in self.columns(K):
            last = P.e.reciprocal(r, r)
        last.then_inc(P.sem("norm_inverse"), P.adds("norm_inverse"))
        P.e.wait_ge(P.sem("norm_root"), P.due("norm_root"))
        for j, (part, c, n) in enumerate(blocks):
            if j >= 4:
                P.e.wait_ge(P.sem("norm_spread"), P.due("norm_spread"))
            at = 16 + 128 * (j % 4)
            P.e.tensor_scalar(K.R[0:n, at:at + n], K.ident[0:n, 0:n], K.R[0:n, j:j + 1], None, ALU.mult).then_inc(P.sem("norm_diagonal"), P.adds("norm_diagonal"))
        P.e.wait_ge(P.sem("norm_spread"), P.due("norm_spread", min(4, len(blocks))))
        two = len(self.toks) == 2
        r = K.PS[:, 6:8, 0:self.toks[0][1]] if two else K.PS[:, 6, 0:self.toks[0][1]]
        view = (lambda ap: ap.rearrange("p (a n) -> p a n", a=2)) if two else (lambda ap: ap)
        lag = 2
        for k in range(KT + lag):
            if k < KT:
                src = view(self.src[:, k, self.t0:self.t1])
                g = self.gain[:, k:k + 1]
                y = view(K.Y[:, k, self.t0:self.t1])
                if self.out is None:
                    P.e.scalar_tensor_tensor(y, src, g, r, ALU.mult, ALU.mult).then_inc(P.sem("norm_scaled"), P.adds("norm_scaled"))
                elif self.add:
                    P.e.scalar_tensor_tensor(y, src, g, r, ALU.mult, ALU.mult).then_inc(P.sem("norm_term"), P.adds("norm_term"))
                else:
                    P.e.scalar_tensor_tensor(view(self.out[:, k, 0:self.t1 - self.t0]), src, g, r, ALU.mult, ALU.mult)
            if k >= lag:
                y = K.Y[:, k - lag, self.t0:self.t1]
                if self.out is None:
                    P.e.wait_ge(P.sem("norm_hi"), P.due("norm_hi"))
                    P.e.tensor_tensor(K.XL[:, k - lag, self.t0:self.t1], y,
                                      K.XH[:, k - lag, self.t0:self.t1].bitcast(F32), ALU.subtract).then_inc(P.sem("norm_lo"), P.adds("norm_lo"))
                elif self.add:
                    P.e.wait_ge(P.sem("norm_term"), P.due("norm_term", 0, less=min(lag, KT - 1 - (k - lag))))
                    o = self.out[:, k - lag, self.out_off + self.t0:self.out_off + self.t1]
                    P.e.tensor_tensor(o, o, y, ALU.add)


class GatedUp(Wide):

    def __init__(self, n, first, conv=None):
        super().__init__(n, None, None)
        self.c0, self.conv = first, conv
        if conv is None:
            self.per_act = self.per_dve = {"hidden_hi": 1}
        else:
            self.per_act = {"conv_seeded": 2, "gate_activated": 1, "hidden_ready": 1, "hidden_hi": 1}
            self.per_dve = dict(self.per_act, dve_order=2)

    def evac_act(self, K, P, p, s, when):
        ps = [K.PS[:, 2 * (2 * s + t), 0:S] for t in range(2)]
        if when == "first":
            if self.conv is None:
                P.e.wait_ge(P.sem("tile_done"), P.due("tile_done"))
                P.e.activation(K.SG[:, s, :], ps[0], ACT.Silu).then_inc(P.sem("tile_evacuated0"), 1)
                P.e.wait_ge(P.sem("tile_done"), P.due("tile_done"))
                return
            w, b = self.conv
            for t in range(2):
                c = sl(t * FT + self.c0 + p)
                P.e.wait_ge(P.sem("tile_done"), P.due("tile_done"))
                P.e.activation(K.CV[:, s, t, :], ps[t], ACT.Identity, bias=b[:, c], scale=w[2][:, c]).then_inc(P.sem("conv_seeded"), P.adds("conv_seeded"))
            P.e.wait_ge(P.sem("tile_evacuated0"), P.due("tile_evacuated0", 0, less=-3))
            P.e.activation(K.SG[:, s, :], K.CV[:, s, 0, :], ACT.Silu).then_inc(P.sem("gate_activated"), P.adds("gate_activated"))
        else:
            if self.conv is None:
                P.e.wait_ge(P.sem("tile_evacuated1"), P.due("tile_evacuated1", 0, less=-3))
            else:
                P.e.wait_ge(P.sem("hidden_ready"), P.due("hidden_ready"))
            P.e.activation(K.HH[:, sl(p), :].rearrange("p a n -> p (a n)"), K.HF[:, s, :], ACT.Copy).then_inc(P.sem("hidden_hi"), P.adds("hidden_hi"))

    def evac_dve(self, K, P, p, s, when):
        ps = [K.PS[:, 2 * (2 * s + t), 0:S] for t in range(2)]
        if when == "first":
            P.e.wait_ge(P.sem("tile_done"), P.due("tile_done", 2))
            if self.conv is None:
                P.e.wait_ge(P.sem("tile_evacuated0"), P.due("tile_evacuated0", 0, less=-3))
                last = P.e.tensor_tensor(K.HF[:, s, :], K.SG[:, s, :], ps[1], ALU.mult)
                last.then_inc(P.sem("tile_evacuated1"), 1)
            else:
                w, b = self.conv
                for t in range(2):
                    c = sl(t * FT + self.c0 + p)
                    y = K.CV[:, s, t, :]
                    P.e.wait_ge(P.sem("conv_seeded"), P.due("conv_seeded"))
                    P.e.scalar_tensor_tensor(y[:, 1:S], ps[t][:, 0:S - 1], w[1][:, c], y[:, 1:S], ALU.mult, ALU.add).then_inc(P.sem("dve_order"), P.adds("dve_order"))
                    P.e.wait_ge(P.sem("dve_order"), P.due("dve_order", 0))
                    last = P.e.scalar_tensor_tensor(y[:, 2:S], ps[t][:, 0:S - 2], w[0][:, c], y[:, 2:S], ALU.mult, ALU.add)
                    last.then_inc(P.sem(f"tile_evacuated{t}"), 1)
                P.e.wait_ge(P.sem("tile_evacuated1"), P.due("tile_evacuated1", 0, less=-3))
                P.e.wait_ge(P.sem("gate_activated"), P.due("gate_activated"))
                P.e.tensor_tensor(K.HF[:, s, :], K.SG[:, s, :], K.CV[:, s, 1, :], ALU.mult).then_inc(P.sem("hidden_ready"), P.adds("hidden_ready"))
        else:
            P.e.wait_ge(P.sem("hidden_hi"), P.due("hidden_hi"))
            h = sl(p)
            P.e.tensor_tensor(K.HL[:, h, :].rearrange("p a n -> p (a n)"), K.HF[:, s, :],
                              K.HH[:, h, :].rearrange("p a n -> p (a n)").bitcast(F32), ALU.subtract)


class SquaredReluUp(Wide):

    per_act = per_dve = {"hidden_ready": 2, "hidden_hi": 2}

    def evac_act(self, K, P, p, s, when):
        if when == "first":
            for t in range(2):
                P.e.wait_ge(P.sem("tile_done"), P.due("tile_done"))
                P.e.activation(K.CV[:, s, t, :], K.PS[:, 2 * (2 * s + t), 0:S], ACT.Relu)\
                   .then_inc(P.sem(f"tile_evacuated{t}"), 1)
        else:
            for t in range(2):
                P.e.wait_ge(P.sem("hidden_ready"), P.due("hidden_ready"))
                P.e.activation(K.HH[:, sl(2 * p + t), :].rearrange("p a n -> p (a n)"), K.CF[:, s, t, :], ACT.Copy).then_inc(P.sem("hidden_hi"), P.adds("hidden_hi"))

    def evac_dve(self, K, P, p, s, when):
        if when == "first":
            for t in range(2):
                P.e.wait_ge(P.sem("tile_done"), P.due("tile_done"))
                P.e.wait_ge(P.sem(f"tile_evacuated{t}"), P.due(f"tile_evacuated{t}", 0, less=-3))
                P.e.tensor_tensor(K.CF[:, s, t, :], K.CV[:, s, t, :], K.CV[:, s, t, :], ALU.mult).then_inc(P.sem("hidden_ready"), P.adds("hidden_ready"))
        else:
            for t in range(2):
                P.e.wait_ge(P.sem("hidden_hi"), P.due("hidden_hi"))
                h = sl(2 * p + t)
                P.e.tensor_tensor(K.HL[:, h, :].rearrange("p a n -> p (a n)"), K.CF[:, s, t, :],
                                  K.HH[:, h, :].rearrange("p a n -> p (a n)").bitcast(F32), ALU.subtract)


class ForgetGates(Small):

    def pe(self, K, P):
        super().pe(K, P)
        P.e.matmul(K.PS[0:16, 7, 0:2], K.ident[:, 0:16], K.ident[:, 0:2], start=True, stop=True).then_inc(P.sem("gates_projected"), P.adds("gates_projected"))

    def act(self, K, P):
        g = K.gate_rows
        P.e.wait_ge(P.sem("gates_projected"), P.due("gates_projected"))
        P.e.activation(g[0:16, 0, :], K.PS[0:16, 0, 0:S], ACT.Abs, bias=K.att_b_f[0:16, 0:1]).then_inc(P.sem("act_order"), P.adds("act_order"))
        P.e.wait_ge(P.sem("act_order"), P.due("act_order", 0))
        P.e.activation(g[0:16, 0, :], g[0:16, 0, :], ACT.Exp, scale=-1.0).then_inc(P.sem("act_order"), P.adds("act_order"))
        P.e.wait_ge(P.sem("act_order"), P.due("act_order", 0))
        P.e.activation(g[0:16, 0, :], g[0:16, 0, :], ACT.Ln, bias=K.one_col[0:16, 0:1]).then_inc(P.sem("log_term"), P.adds("log_term"))

    def dve(self, K, P):
        g = K.gate_rows
        P.e.wait_ge(P.sem("gates_projected"), P.due("gates_projected"))
        P.e.wait_ge(P.sem("log_term"), P.due("log_term"))
        P.e.tensor_scalar(g[0:16, 1, :], K.PS[0:16, 0, 0:S], K.att_b_f[0:16, 0:1], 0.0, ALU.add, ALU.min).then_inc(P.sem("dve_order"), P.adds("dve_order"))
        P.e.wait_ge(P.sem("dve_order"), P.due("dve_order", 0))
        P.e.tensor_tensor(g[0:16, 1, :], g[0:16, 1, :], g[0:16, 0, :], ALU.subtract).then_inc(P.sem("dve_order"), P.adds("dve_order"))
        P.e.wait_ge(P.sem("dve_order"), P.due("dve_order", 0))
        P.e.tensor_tensor_scan(K.c_rows[0:16, :], K.ones_row[0:16, :], g[0:16, 1, :], 0.0, ALU.mult, ALU.add)


class ForgettingAttention(Stage):

    UNITS = [(u, b) for u in range(2) for b in range(S // 128)]

    def dve(self, K, P):
        P.e.tensor_copy(K.one_row16[0:16, :], K.ones_row[0:16, :]).then_inc(P.sem("att_staged"), P.adds("att_staged"))

        def body(i):
            t = sl(i)
            for u in range(2):
                h = sl(2 * i + u)
                if True:
                    P.e.tensor_scalar(K.cm[0:16, u, :], K.c_rows[0:16, :], K.ident[0:16, h], None, ALU.mult).then_inc(P.sem("dve_order"), P.adds("dve_order"))
                    P.e.wait_ge(P.sem("dve_order"), P.due("dve_order", 0))
                    P.e.tensor_scalar(K.ncm[0:16, u, :], K.cm[0:16, u, :], -1.0, None, ALU.mult).then_inc(P.sem("att_staged"), P.adds("att_staged"))
            for n, (u, b) in enumerate(self.UNITS):
                s, nk = n % 2, 128 * (b + 1)
                P.e.wait_ge(P.sem("logits_done"), P.due("logits_done"))
                P.e.reduce_max(K.st[:, s, 0:1], K.PS[:, s, 0:nk], AX.X).then_inc(P.sem("dve_order"), P.adds("dve_order"))
                P.e.wait_ge(P.sem("dve_order"), P.due("dve_order", 0))
                P.e.tensor_scalar(K.st[:, s, 1:2], K.st[:, s, 0:1], -1.0, None, ALU.mult).then_inc(P.sem("max_negated"), P.adds("max_negated"))
                P.e.wait_ge(P.sem("exp_done"), P.due("exp_done"))
                P.e.reciprocal(K.st[:, s, 3:4], K.st[:, s, 2:3]).then_inc(P.sem("dve_order"), P.adds("dve_order"))
                P.e.wait_ge(P.sem("dve_order"), P.due("dve_order", 0))
                P.e.tensor_scalar(K.pr[:, s, 0:nk], K.pr[:, s, 0:nk], K.st[:, s, 3:4], None, ALU.mult).then_inc(P.sem("probs_ready"), P.adds("probs_ready"))
                P.e.wait_ge(P.sem("probs_transposed"), P.due("probs_transposed"))
                P.e.tensor_copy(K.pT[:, s, 0:nk], K.PS[:, 2 + s, 0:nk]).then_inc(P.sem("probsT_ready"), P.adds("probsT_ready"))
            P.e.wait_ge(P.sem("att_out_done"), P.due("att_out_done"))
            P.e.wait_ge(P.sem("att_out_hi"), P.due("att_out_hi"))
            P.e.tensor_tensor(K.XL[:, t, 0:S].rearrange("p a n -> p (a n)"), K.PS[:, 4, 0:S],
                                    K.XH[:, t, 0:S].rearrange("p a n -> p (a n)").bitcast(F32), ALU.subtract).then_inc(P.sem("att_out_lo"), P.adds("att_out_lo"))

        P.loop(8, body, dve_order=18, att_staged=2, logits_done=8, max_negated=8, exp_done=8, probs_ready=8,
               probs_transposed=8, probsT_ready=8, att_out_done=1, att_out_hi=1, att_out_lo=1)

    def act(self, K, P):
        def body(i):
            t = sl(i)
            for u in range(2):
                half = slice(64 * u, 64 * u + 64)
                P.e.activation(K.qs[0:64, u, :], K.q1[half, t, :].rearrange("p a n -> p (a n)"), ACT.Copy, scale=0.125).then_inc(P.sem("qk_staged"), P.adds("qk_staged"))
                P.e.activation(K.ks[0:64, u, :], K.k1[half, t, :].rearrange("p a n -> p (a n)"), ACT.Copy).then_inc(P.sem("qk_staged"), P.adds("qk_staged"))
            P.e.activation(K.vs[:, :], K.v1[:, t, :].rearrange("p a n -> p (a n)"), ACT.Copy).then_inc(P.sem("v_staged"), P.adds("v_staged"))
            P.e.wait_ge(P.sem("v_transposed"), P.due("v_transposed"))
            P.e.activation(K.vT[:, :], K.PS[:, 5, :], ACT.Copy).then_inc(P.sem("vT_ready"), P.adds("vT_ready"))
            for n, (u, b) in enumerate(self.UNITS):
                s, nk = n % 2, 128 * (b + 1)
                P.e.wait_ge(P.sem("logits_done"), P.due("logits_done"))
                P.e.wait_ge(P.sem("max_negated"), P.due("max_negated"))
                P.e.activation(K.pr[:, s, 0:nk], K.PS[:, s, 0:nk], ACT.Exp, bias=K.st[:, s, 1:2],
                                     accum_out=K.st[:, s, 2:3]).then_inc(P.sem("exp_done"), P.adds("exp_done"))
            P.e.wait_ge(P.sem("att_out_done"), P.due("att_out_done"))
            P.e.activation(K.XH[:, t, 0:S].rearrange("p a n -> p (a n)"), K.PS[:, 4, 0:S], ACT.Copy).then_inc(P.sem("att_out_hi"), P.adds("att_out_hi"))

        P.loop(8, body, qk_staged=4, v_staged=1, v_transposed=1, vT_ready=1, logits_done=8, max_negated=8, exp_done=8,
               att_out_done=1, att_out_hi=1)

    def pe(self, K, P):
        P.e.wait_ge(P.sem("att_staged"), P.due("att_staged"))

        def logits(n):
            u, b = self.UNITS[n]
            s, nk, q = n % 2, 128 * (b + 1), slice(128 * b, 128 * b + 128)
            out = K.PS[:, s, 0:nk]
            P.e.matmul(out, K.qs[0:64, u, q], K.ks[0:64, u, 0:nk], start=True, stop=False)
            P.e.matmul(out, K.cm[0:16, u, q], K.one_row16[0:16, 0:nk], start=False, stop=False)
            P.e.matmul(out, K.one_row16[0:16, 0:128], K.ncm[0:16, u, 0:nk], start=False, stop=False)
            P.e.matmul(K.PS[:, s, nk - 128:nk], K.ident[:, :], K.causal[:, :], start=False, stop=True).then_inc(P.sem("logits_done"), P.adds("logits_done"))

        def body(i):
            P.e.wait_ge(P.sem("v_staged"), P.due("v_staged"))
            for b in range(4):
                last = P.e.transpose(K.PS[:, 5, 128 * b:128 * b + 128], K.vs[:, 128 * b:128 * b + 128], K.ident[:, :])
            last.then_inc(P.sem("v_transposed"), P.adds("v_transposed"))
            P.e.wait_ge(P.sem("qk_staged"), P.due("qk_staged", 4))
            P.e.wait_ge(P.sem("att_staged"), P.due("att_staged", 2))
            logits(0)
            for n, (u, b) in enumerate(self.UNITS):
                if n + 1 < len(self.UNITS):
                    if n >= 1:
                        P.e.wait_ge(P.sem("exp_done"), P.due("exp_done", 0))
                    logits(n + 1)
                s = n % 2
                P.e.wait_ge(P.sem("probs_ready"), P.due("probs_ready"))
                P.e.wait_ge(P.sem("exp_done"), P.due("exp_done"))
                for kb in range(b + 1):
                    c = slice(128 * kb, 128 * kb + 128)
                    last = P.e.transpose(K.PS[:, 2 + s, c], K.pr[:, s, c], K.ident[:, :])
                last.then_inc(P.sem("probs_transposed"), P.adds("probs_transposed"))
                P.e.wait_ge(P.sem("probsT_ready"), P.due("probsT_ready"))
                if n == 0:
                    P.e.wait_ge(P.sem("vT_ready"), P.due("vT_ready"))
                for kb in range(b + 1):
                    last = P.e.matmul(K.PS[64 * u:64 * u + 64, 4, 128 * b:128 * b + 128],
                                      K.vT[:, 128 * kb + 64 * u:128 * kb + 64 * u + 64],
                                      K.pT[:, s, 128 * kb:128 * kb + 128], start=(kb == 0), stop=(kb == b))
            last.then_inc(P.sem("att_out_done"), P.adds("att_out_done"))
            P.e.wait_ge(P.sem("att_out_lo"), P.due("att_out_lo"))

        P.loop(8, body, v_staged=1, v_transposed=1, qk_staged=4, att_staged=2, logits_done=8, exp_done=8,
               probs_ready=8, probs_transposed=8, probsT_ready=8, vT_ready=1, att_out_done=1, att_out_lo=1)


class LowerBounds(Stage):

    def dve(self, K, P):
        a, b, m, t = K.lb_logits[:, 0:8], K.lb_logits[:, 8:16], K.lbt[:, 0:8], K.lbt
        P.e.tensor_tensor(m, a, b, ALU.max).then_inc(P.sem("dve_order"), P.adds("dve_order"))
        P.e.wait_ge(P.sem("dve_order"), P.due("dve_order", 0))
        P.e.tensor_tensor(t[:, 8:16], a, m, ALU.subtract)
        P.e.tensor_tensor(t[:, 16:24], b, m, ALU.subtract).then_inc(P.sem("lb_shifted"), P.adds("lb_shifted"))
        P.e.wait_ge(P.sem("lb_exp"), P.due("lb_exp"))
        P.e.tensor_tensor(t[:, 0:8], t[:, 8:16], t[:, 16:24], ALU.add).then_inc(P.sem("dve_order"), P.adds("dve_order"))
        P.e.wait_ge(P.sem("dve_order"), P.due("dve_order", 0))
        P.e.reciprocal(t[:, 0:8], t[:, 0:8]).then_inc(P.sem("dve_order"), P.adds("dve_order"))
        P.e.wait_ge(P.sem("dve_order"), P.due("dve_order", 0))
        P.e.tensor_tensor(K.lb[:, 0:8], t[:, 16:24], t[:, 0:8], ALU.mult)
        P.e.tensor_tensor(K.lb[:, 8:16], t[:, 8:16], t[:, 0:8], ALU.mult)

    def act(self, K, P):
        P.e.wait_ge(P.sem("lb_shifted"), P.due("lb_shifted"))
        P.e.activation(K.lbt[:, 8:24], K.lbt[:, 8:24], ACT.Exp).then_inc(P.sem("lb_exp"), P.adds("lb_exp"))


class Hgrn(Stage):

    def dve(self, K, P):
        P.e.memset(K.sp[:, 0, :], 0.0)

        def body(i):
            t = sl(i)
            f = K.f1[:, t, :].rearrange("p a n -> p (a n)")
            q = K.q1h[:, t, :].rearrange("p a n -> p (a n)")
            P.e.tensor_scalar(K.h_f[:, :], f, K.lb[:, sl(i + 8)], K.lb[:, t], ALU.mult, ALU.add).then_inc(P.sem("dve_order"), P.adds("dve_order"))
            P.e.wait_ge(P.sem("dve_order"), P.due("dve_order", 0))
            P.e.tensor_scalar(K.h_k[:, :], K.h_f[:, :], -1.0, 1.0, ALU.mult, ALU.add).then_inc(P.sem("f_ready"), P.adds("f_ready"))
            P.e.wait_ge(P.sem("logf_ready"), P.due("logf_ready"))
            P.e.tensor_tensor_scan(K.h_b[:, :], K.reset64[:, :], K.h_lf[:, :], 0.0, ALU.mult, ALU.add).then_inc(P.sem("dve_order"), P.adds("dve_order"))
            P.e.wait_ge(P.sem("dve_order"), P.due("dve_order", 0))
            b3 = K.h_b[:, :].rearrange("p (n c) -> p n c", c=64)
            P.e.tensor_tensor(K.h_lf[:, :].rearrange("p (n c) -> p n c", c=64),
                                    b3[:, :, 63:64].broadcast_to([128, 8, 64]), b3, ALU.subtract).then_inc(P.sem("b_ready"), P.adds("b_ready"))
            P.e.wait_ge(P.sem("exps_ready"), P.due("exps_ready"))
            P.e.tensor_tensor(K.h_ks[:, :], K.h_k[:, :], K.h_lf[:, :], ALU.mult)
            P.e.tensor_tensor(K.h_qd[:, :], q, K.h_eb[:, :], ALU.mult)
            P.e.tensor_tensor(K.h_ki[:, :], K.h_k[:, :], K.h_en[:, :], ALU.mult).then_inc(P.sem("keys_ready"), P.adds("keys_ready"))
            P.e.wait_ge(P.sem("ksT_done"), P.due("ksT_done"))
            P.e.tensor_copy(K.ksT[:, :, :].rearrange("p n c -> p (n c)"), K.PS[:, 2, :]).then_inc(P.sem("ksT_ready"), P.adds("ksT_ready"))
            P.e.wait_ge(P.sem("A_done"), P.due("A_done"))
            P.e.tensor_tensor(K.aT[:, :], K.PS[:, 4, 0:256], K.causal64[:, 0:256], ALU.mult).then_inc(P.sem("A_ready"), P.adds("A_ready"))
            P.e.wait_ge(P.sem("U_done"), P.due("U_done"))
            for n in range(7):
                ins = P.e.scalar_tensor_tensor(K.sp[:, n + 1, :], K.sp[:, n, :], K.h_eb[:, 64 * n + 63:64 * n + 64],
                                               K.PS[:, 5 + n % 2, 128 * (n // 2):128 * (n // 2) + 128], ALU.mult, ALU.add)
                if n < 6:
                    ins.then_inc(P.sem("dve_order"), P.adds("dve_order"))
                    P.e.wait_ge(P.sem("dve_order"), P.due("dve_order", 0))
                else:
                    ins.then_inc(P.sem("states_ready"), P.adds("states_ready"))
            P.e.wait_ge(P.sem("o_mean"), P.due("o_mean"))
            P.e.tensor_scalar(K.R[:, 0:S], K.PS[:, 0, :], EPS, None, ALU.add).then_inc(P.sem("dve_order"), P.adds("dve_order"))
            P.e.wait_ge(P.sem("dve_order"), P.due("dve_order", 0))
            P.e.reciprocal(K.R[:, 0:S], K.R[:, 0:S]).then_inc(P.sem("o_inverse"), P.adds("o_inverse"))
            P.e.wait_ge(P.sem("o_root"), P.due("o_root"))
            for u in range(2):
                last = P.e.scalar_tensor_tensor(K.halves(K.h_b, u), K.halves_ps(u), K.p["hgrn_onorm_g"][:, t],
                                                K.halves(K.R, u), ALU.mult, ALU.mult)
            last.then_inc(P.sem("dve_order"), P.adds("dve_order"))
            P.e.wait_ge(P.sem("dve_order"), P.due("dve_order", 0))
            P.e.tensor_tensor(K.h_b[:, :], K.h_b[:, :], K.g1[:, t, :].rearrange("p a n -> p (a n)"), ALU.mult).then_inc(P.sem("o_gated"), P.adds("o_gated"))
            P.e.wait_ge(P.sem("o_hi"), P.due("o_hi"))
            P.e.tensor_tensor(K.XL[:, t, 0:S].rearrange("p a n -> p (a n)"), K.h_b[:, :],
                                    K.XH[:, t, 0:S].rearrange("p a n -> p (a n)").bitcast(F32), ALU.subtract).then_inc(P.sem("o_lo"), P.adds("o_lo"))

        P.loop(8, body, dve_order=10, f_ready=1, logf_ready=1, b_ready=1, exps_ready=1, keys_ready=1, ksT_done=1,
               ksT_ready=1, A_done=1, A_ready=1, U_done=1, states_ready=1, o_mean=1, o_inverse=1, o_root=1, o_gated=1,
               o_hi=1, o_lo=1)

    def act(self, K, P):
        def body(i):
            t = sl(i)
            P.e.activation(K.h_i[:, :], K.i1[:, t, :].rearrange("p a n -> p (a n)"), ACT.Copy).then_inc(P.sem("i_staged"), P.adds("i_staged"))
            P.e.wait_ge(P.sem("f_ready"), P.due("f_ready"))
            P.e.activation(K.h_lf[:, :], K.h_f[:, :], ACT.Ln).then_inc(P.sem("logf_ready"), P.adds("logf_ready"))
            P.e.wait_ge(P.sem("b_ready"), P.due("b_ready"))
            P.e.activation(K.h_eb[:, :], K.h_b[:, :], ACT.Exp)
            P.e.activation(K.h_en[:, :], K.h_b[:, :], ACT.Exp, scale=-1.0)
            P.e.activation(K.h_lf[:, :], K.h_lf[:, :], ACT.Exp).then_inc(P.sem("exps_ready"), P.adds("exps_ready"))
            P.e.wait_ge(P.sem("iT_done"), P.due("iT_done"))
            P.e.activation(K.iT[:, :, :].rearrange("p n c -> p (n c)"), K.PS[:, 0, :], ACT.Copy).then_inc(P.sem("iT_ready"), P.adds("iT_ready"))
            P.e.wait_ge(P.sem("o_done"), P.due("o_done"))
            for u in range(2):
                last = P.e.activation(K.halves(K.h_en, u), K.halves_ps(u), ACT.Square)
            last.then_inc(P.sem("o_squared"), P.adds("o_squared"))
            P.e.wait_ge(P.sem("o_inverse"), P.due("o_inverse"))
            P.e.activation(K.R[:, 0:S], K.R[:, 0:S], ACT.Sqrt).then_inc(P.sem("o_root"), P.adds("o_root"))
            P.e.wait_ge(P.sem("o_gated"), P.due("o_gated"))
            P.e.activation(K.XH[:, t, 0:S].rearrange("p a n -> p (a n)"), K.h_b[:, :], ACT.Copy).then_inc(P.sem("o_hi"), P.adds("o_hi"))
            P.e.wait_ge(P.sem("o_lo"), P.due("o_lo"))

        P.loop(8, body, i_staged=1, f_ready=1, logf_ready=1, b_ready=1, exps_ready=1, iT_done=1, iT_ready=1, o_done=1,
               o_squared=1, o_inverse=1, o_root=1, o_gated=1, o_hi=1, o_lo=1)

    def pe(self, K, P):
        def body(i):
            P.e.wait_ge(P.sem("i_staged"), P.due("i_staged"))
            for j in range(4):
                c = slice(128 * j, 128 * j + 128)
                last = P.e.transpose(K.PS[:, 0, c], K.h_i[:, c], K.ident[:, :])
            last.then_inc(P.sem("iT_done"), P.adds("iT_done"))
            P.e.wait_ge(P.sem("keys_ready"), P.due("keys_ready"))
            for j in range(4):
                c = slice(128 * j, 128 * j + 128)
                last = P.e.transpose(K.PS[:, 2, c], K.h_ks[:, c], K.ident[:, :])
            last.then_inc(P.sem("ksT_done"), P.adds("ksT_done"))
            chunks = [(n, slice(64 * (n % 2), 64 * (n % 2) + 64), n // 2, slice(64 * n, 64 * n + 64)) for n in range(8)]
            for n, half, j, c in chunks:
                last = P.e.matmul(K.PS[half, 4, 64 * j:64 * j + 64], K.h_ki[:, c], K.h_qd[:, c], start=True, stop=True)
            last.then_inc(P.sem("A_done"), P.adds("A_done"))
            P.e.wait_ge(P.sem("iT_ready"), P.due("iT_ready"))
            P.e.wait_ge(P.sem("ksT_ready"), P.due("ksT_ready"))
            for n, half, j, c in chunks[:7]:
                last = P.e.matmul(K.PS[:, 5 + n % 2, 128 * j:128 * j + 128], K.ksT[half, j, :], K.iT[half, j, :],
                                  start=True, stop=True)
            last.then_inc(P.sem("U_done"), P.adds("U_done"))
            P.e.wait_ge(P.sem("A_ready"), P.due("A_ready"))
            P.e.wait_ge(P.sem("states_ready"), P.due("states_ready"))
            for n, half, j, c in chunks:
                out = K.PS[:, (7, 3)[n % 2], 64 * j:64 * j + 64]
                P.e.matmul(out, K.iT[half, j, :], K.aT[half, 64 * j:64 * j + 64], start=True, stop=False)
                last = P.e.matmul(out, K.sp[:, n, :], K.h_qd[:, c], start=False, stop=True)
            last.then_inc(P.sem("o_done"), P.adds("o_done"))
            P.e.wait_ge(P.sem("o_squared"), P.due("o_squared"))
            P.e.matmul(K.PS[:, 0, :], K.inv_dv[:, :], K.h_en[:, :], start=True, stop=True).then_inc(P.sem("o_mean"), P.adds("o_mean"))
            P.e.wait_ge(P.sem("o_gated"), P.due("o_gated"))

        P.loop(8, body, i_staged=1, iT_done=1, keys_ready=1, ksT_done=1, A_done=1, iT_ready=1, ksT_ready=1, U_done=1,
               A_ready=1, states_ready=1, o_done=1, o_squared=1, o_mean=1, o_gated=1)


BIAS_W = 640


class Load(Stage):

    def __init__(self, loads):
        self.loads = loads

    def act(self, K, P):
        for dst, src in self.loads:
            P.e.dma_start(dst, src).then_inc(P.sem("inputs_loaded"), P.adds("inputs_loaded", 16))
        P.e.wait_ge(P.sem("inputs_loaded"), P.due("inputs_loaded", 0))


class BiasTable(Stage):

    def dve(self, K, P):
        P.e.memset(K.bias_t[32:33, :], NEG).then_inc(P.sem("bias_staged"), P.adds("bias_staged"))
        P.e.wait_ge(P.sem("bias_rows_done"), P.due("bias_rows_done"))
        P.e.tensor_copy(K.bias_rows[0:4, 0:512], K.PS[0:4, 0, :])
        P.e.tensor_copy(K.bias_rows[0:4, 512:BIAS_W], K.PS[0:4, 1, 0:BIAS_W - 512]).then_inc(P.sem("bias_rows_ready"), P.adds("bias_rows_ready"))
        lam = K.lam[:, :].rearrange("p (a b c) -> p a b c", a=2, b=2)
        P.e.tensor_tensor(K.lam_prod[:, :].rearrange("p (a c) -> p a c", a=2), lam[:, :, 0, :], lam[:, :, 1, :], ALU.mult).then_inc(P.sem("dve_order"), P.adds("dve_order"))
        P.e.wait_ge(P.sem("dve_order"), P.due("dve_order", 0))
        P.e.reduce_sum(K.lamt[:, 0:2], K.lam_prod[:, :].rearrange("p (a c) -> p a c", a=2), AX.X).then_inc(P.sem("lambda_dots"), P.adds("lambda_dots"))
        P.e.wait_ge(P.sem("lambda_exps"), P.due("lambda_exps"))
        P.e.tensor_tensor(K.lamt[:, 4:5], K.lamt[:, 3:4], K.lamt[:, 2:3], ALU.subtract).then_inc(P.sem("dve_order"), P.adds("dve_order"))
        P.e.wait_ge(P.sem("dve_order"), P.due("dve_order", 0))
        P.e.tensor_scalar(K.lamt[:, 5:6], K.lamt[:, 4:5], -0.2, None, ALU.add)

    def act(self, K, P):
        P.e.wait_ge(P.sem("lambda_dots"), P.due("lambda_dots"))
        P.e.activation(K.lamt[:, 2:4], K.lamt[:, 0:2], ACT.Exp).then_inc(P.sem("lambda_exps"), P.adds("lambda_exps"))
        P.e.wait_ge(P.sem("bias_rows_ready"), P.due("bias_rows_ready"))
        P.e.dma_start(K.bias_dram, K.bias_rows[0:4, :]).then_inc(P.sem("bias_moved"), P.adds("bias_moved", 16))
        P.e.wait_ge(P.sem("bias_moved"), P.due("bias_moved", 0))
        for h in range(4):
            src = bass.AP(tensor=K.bias_dram.tensor, offset=h * BIAS_W, ap=[[1, 128], [1, 512]])
            P.e.dma_start(K.bias[:, h, :], src).then_inc(P.sem("bias_moved"), P.adds("bias_moved", 16))
        P.e.wait_ge(P.sem("bias_moved"), P.due("bias_moved", 0))

    def pe(self, K, P):
        P.e.wait_ge(P.sem("bias_staged"), P.due("bias_staged"))
        P.e.matmul(K.PS[0:4, 0, :], K.bias_t[0:33, :], K.onehot[0:33, 0:512], start=True, stop=True)
        P.e.matmul(K.PS[0:4, 1, 0:BIAS_W - 512], K.bias_t[0:33, :], K.onehot[0:33, 512:BIAS_W], start=True, stop=True).then_inc(P.sem("bias_rows_done"), P.adds("bias_rows_done"))


class DiffAttention(Stage):

    def act(self, K, P):
        def body(i):
            t = sl(i)
            flat = lambda ap: ap.rearrange("p a n -> p (a n)")
            for m in range(2):
                half = slice(64 * m, 64 * m + 64)
                P.e.activation(K.d_q[0:64, m, :], flat(K.in2[half, sl(i), :]), ACT.Copy, scale=0.125).then_inc(P.sem("qk_staged"), P.adds("qk_staged"))
                P.e.activation(K.d_k[0:64, m, :], flat(K.in2[half, sl(i + 4), :]), ACT.Copy).then_inc(P.sem("qk_staged"), P.adds("qk_staged"))
            P.e.activation(K.d_vs[:, :], flat(K.in2[:, sl(i + 8), :]), ACT.Copy).then_inc(P.sem("v_staged"), P.adds("v_staged"))
            P.e.wait_ge(P.sem("v_transposed"), P.due("v_transposed"))
            P.e.activation(K.d_vT[:, :], K.PS[:, 5, :], ACT.Copy).then_inc(P.sem("vT_ready"), P.adds("vT_ready"))
            for b in range(4):
                nk = 128 * (b + 1)
                for m in range(2):
                    P.e.wait_ge(P.sem("logits_done"), P.due("logits_done"))
                    P.e.wait_ge(P.sem("max_negated"), P.due("max_negated"))
                    P.e.activation(K.d_p[:, m, 0:nk], K.PS[:, m, 0:nk], ACT.Exp, bias=K.d_st[:, m, 1:2],
                                         accum_out=K.d_st[:, m, 2:3]).then_inc(P.sem("exp_done"), P.adds("exp_done"))
            P.e.wait_ge(P.sem("att_out_done"), P.due("att_out_done"))
            P.e.activation(K.d_sq[:, :], K.PS[:, 4, :], ACT.Square).then_inc(P.sem("o_squared"), P.adds("o_squared"))
            P.e.wait_ge(P.sem("o_inverse"), P.due("o_inverse"))
            P.e.activation(K.R[:, 0:S], K.R[:, 0:S], ACT.Sqrt).then_inc(P.sem("o_root"), P.adds("o_root"))
            P.e.wait_ge(P.sem("o_gated"), P.due("o_gated"))
            P.e.activation(flat(K.XH[:, t, 0:S]), K.d_sq[:, :], ACT.Copy).then_inc(P.sem("o_hi"), P.adds("o_hi"))
            P.e.wait_ge(P.sem("o_lo"), P.due("o_lo"))

        P.loop(4, body, qk_staged=4, v_staged=1, v_transposed=1, vT_ready=1, logits_done=8, max_negated=8, exp_done=8,
               att_out_done=1, o_squared=1, o_inverse=1, o_root=1, o_gated=1, o_hi=1, o_lo=1)

        def conv(i):
            P.e.wait_ge(P.sem("conv_z"), P.due("conv_z"))
            P.e.activation(K.d_cy[:, :], K.d_cz[:, :], ACT.Copy, scale=K.p["conv2_w2"][:, sl(i)]).then_inc(P.sem("conv_seeded"), P.adds("conv_seeded"))
            P.e.wait_ge(P.sem("conv_gated"), P.due("conv_gated"))
            P.e.activation(K.XH[:, sl(i + 4), 0:S].rearrange("p a n -> p (a n)"), K.d_cz[:, :], ACT.Copy).then_inc(P.sem("conv_hi"), P.adds("conv_hi"))
            P.e.wait_ge(P.sem("conv_lo"), P.due("conv_lo"))

        P.loop(4, conv, conv_z=1, conv_seeded=1, conv_gated=1, conv_hi=1, conv_lo=1)

    def dve(self, K, P):
        flat = lambda ap: ap.rearrange("p a n -> p (a n)")

        def body(i):
            t = sl(i)
            for b in range(4):
                nk = 128 * (b + 1)
                for m in range(2):
                    st = K.d_st
                    P.e.wait_ge(P.sem("logits_done"), P.due("logits_done"))
                    P.e.reduce_max(st[:, m, 0:1], K.PS[:, m, 0:nk], AX.X).then_inc(P.sem("dve_order"), P.adds("dve_order"))
                    P.e.wait_ge(P.sem("dve_order"), P.due("dve_order", 0))
                    P.e.tensor_scalar(st[:, m, 1:2], st[:, m, 0:1], -1.0, None, ALU.mult).then_inc(P.sem("max_negated"), P.adds("max_negated"))
                for m in range(2):
                    P.e.wait_ge(P.sem("exp_done"), P.due("exp_done"))
                    P.e.reciprocal(st[:, m, 3:4], st[:, m, 2:3]).then_inc(P.sem("dve_order"), P.adds("dve_order"))
                    P.e.wait_ge(P.sem("dve_order"), P.due("dve_order", 0))
                P.e.tensor_scalar(st[:, 1, 3:4], st[:, 1, 3:4], K.lamt[:, 5:6], None, ALU.mult).then_inc(P.sem("dve_order"), P.adds("dve_order"))
                P.e.wait_ge(P.sem("dve_order"), P.due("dve_order", 0))
                P.e.tensor_scalar(K.d_p[:, 0, 0:nk], K.d_p[:, 0, 0:nk], st[:, 0, 3:4], None, ALU.mult).then_inc(P.sem("dve_order"), P.adds("dve_order"))
                P.e.wait_ge(P.sem("dve_order"), P.due("dve_order", 0))
                P.e.scalar_tensor_tensor(K.d_p[:, 0, 0:nk], K.d_p[:, 1, 0:nk], st[:, 1, 3:4], K.d_p[:, 0, 0:nk],
                                               ALU.mult, ALU.add).then_inc(P.sem("probs_ready"), P.adds("probs_ready"))
                P.e.wait_ge(P.sem("probs_transposed"), P.due("probs_transposed"))
                P.e.tensor_copy(K.d_pT[:, b % 2, 0:nk], K.PS[:, 2 + b % 2, 0:nk]).then_inc(P.sem("probsT_ready"), P.adds("probsT_ready"))
            P.e.wait_ge(P.sem("o_mean"), P.due("o_mean"))
            P.e.tensor_scalar(K.R[:, 0:S], K.PS[:, 6, :], 1e-5, None, ALU.add).then_inc(P.sem("dve_order"), P.adds("dve_order"))
            P.e.wait_ge(P.sem("dve_order"), P.due("dve_order", 0))
            P.e.reciprocal(K.R[:, 0:S], K.R[:, 0:S]).then_inc(P.sem("o_inverse"), P.adds("o_inverse"))
            P.e.wait_ge(P.sem("o_root"), P.due("o_root"))
            P.e.scalar_tensor_tensor(K.d_sq[:, :], K.PS[:, 4, :], K.p["subln_g"][:, 0:1], K.R[:, 0:S], ALU.mult, ALU.mult).then_inc(P.sem("dve_order"), P.adds("dve_order"))
            P.e.wait_ge(P.sem("dve_order"), P.due("dve_order", 0))
            P.e.tensor_scalar(K.d_sq[:, :], K.d_sq[:, :], 0.8, None, ALU.mult).then_inc(P.sem("o_gated"), P.adds("o_gated"))
            P.e.wait_ge(P.sem("o_hi"), P.due("o_hi"))
            P.e.tensor_tensor(flat(K.XL[:, t, 0:S]), K.d_sq[:, :], flat(K.XH[:, t, 0:S]).bitcast(F32), ALU.subtract).then_inc(P.sem("o_lo"), P.adds("o_lo"))

        P.loop(4, body, dve_order=8 + 4 * 4 + 2, logits_done=8, max_negated=8, exp_done=8, probs_ready=4, probs_transposed=4,
               probsT_ready=4, o_mean=1, o_inverse=1, o_root=1, o_gated=1, o_hi=1, o_lo=1)

        def conv(i):
            z, y = K.d_cz, K.d_cy
            P.e.tensor_tensor(z[:, :], flat(K.in2[:, sl(i + 16), :]), flat(K.in2[:, sl(i + 20), :]), ALU.mult).then_inc(P.sem("conv_z"), P.adds("conv_z"))
            P.e.wait_ge(P.sem("conv_seeded"), P.due("conv_seeded"))
            P.e.scalar_tensor_tensor(y[:, 1:S], z[:, 0:S - 1], K.p["conv2_w1"][:, sl(i)], y[:, 1:S], ALU.mult, ALU.add).then_inc(P.sem("dve_order"), P.adds("dve_order"))
            P.e.wait_ge(P.sem("dve_order"), P.due("dve_order", 0))
            P.e.scalar_tensor_tensor(y[:, 2:S], z[:, 0:S - 2], K.p["conv2_w0"][:, sl(i)], y[:, 2:S], ALU.mult, ALU.add).then_inc(P.sem("dve_order"), P.adds("dve_order"))
            P.e.wait_ge(P.sem("dve_order"), P.due("dve_order", 0))
            P.e.tensor_tensor(z[:, :], y[:, :], flat(K.in2[:, sl(i + 12), :]), ALU.mult).then_inc(P.sem("conv_gated"), P.adds("conv_gated"))
            P.e.wait_ge(P.sem("conv_hi"), P.due("conv_hi"))
            P.e.tensor_tensor(flat(K.XL[:, sl(i + 4), 0:S]), z[:, :], flat(K.XH[:, sl(i + 4), 0:S]).bitcast(F32), ALU.subtract).then_inc(P.sem("conv_lo"), P.adds("conv_lo"))
            P.e.wait_ge(P.sem("conv_lo"), P.due("conv_lo", 0))

        P.loop(4, conv, dve_order=2, conv_z=1, conv_seeded=1, conv_gated=1, conv_hi=1, conv_lo=1)

    def pe(self, K, P):
        def body(i):
            P.e.wait_ge(P.sem("v_staged"), P.due("v_staged"))
            for b in range(4):
                last = P.e.transpose(K.PS[:, 5, 128 * b:128 * b + 128], K.d_vs[:, 128 * b:128 * b + 128], K.ident[:, :])
            last.then_inc(P.sem("v_transposed"), P.adds("v_transposed"))
            P.e.wait_ge(P.sem("qk_staged"), P.due("qk_staged", 4))
            for b in range(4):
                nk = 128 * (b + 1)
                if b:
                    P.e.wait_ge(P.sem("exp_done"), P.due("exp_done", 0))
                for m in range(2):
                    P.e.matmul(K.PS[:, m, 0:nk], K.d_q[0:64, m, 128 * b:128 * b + 128], K.d_k[0:64, m, 0:nk], start=True, stop=False)
                    last = P.e.matmul(K.PS[:, m, 0:nk], K.flip[:, :], K.bias[:, sl(i), 512 - nk:512].rearrange("p a n -> p (a n)"),
                                      start=False, stop=True)
                    last.then_inc(P.sem("logits_done"), P.adds("logits_done"))
                P.e.wait_ge(P.sem("exp_done"), P.due("exp_done", 2))
                P.e.wait_ge(P.sem("probs_ready"), P.due("probs_ready"))
                for kb in range(b + 1):
                    c = slice(128 * kb, 128 * kb + 128)
                    last = P.e.transpose(K.PS[:, 2 + b % 2, c], K.d_p[:, 0, c], K.ident[:, :])
                last.then_inc(P.sem("probs_transposed"), P.adds("probs_transposed"))
                P.e.wait_ge(P.sem("probsT_ready"), P.due("probsT_ready"))
                if b == 0:
                    P.e.wait_ge(P.sem("vT_ready"), P.due("vT_ready"))
                for kb in range(b + 1):
                    c = slice(128 * kb, 128 * kb + 128)
                    last = P.e.matmul(K.PS[:, 4, 128 * b:128 * b + 128], K.d_vT[:, c], K.d_pT[:, b % 2, c], start=(kb == 0), stop=(kb == b))
            last.then_inc(P.sem("att_out_done"), P.adds("att_out_done"))
            P.e.wait_ge(P.sem("o_squared"), P.due("o_squared"))
            P.e.matmul(K.PS[:, 6, :], K.inv_dv[:, :], K.d_sq[:, :], start=True, stop=True).then_inc(P.sem("o_mean"), P.adds("o_mean"))
            P.e.wait_ge(P.sem("o_gated"), P.due("o_gated"))

        P.loop(4, body, v_staged=1, v_transposed=1, qk_staged=4, exp_done=8, logits_done=8, probs_ready=4, probs_transposed=4,
               probsT_ready=4, vT_ready=1, att_out_done=1, o_squared=1, o_mean=1, o_gated=1)


class CentreV(Stage):

    def pe(self, K, P):
        for k in range(KT):
            last = P.e.matmul(K.PS[:, 0, :], K.inv_d[:, :], K.v2[:, k, :], start=(k == 0), stop=(k == KT - 1))
        last.then_inc(P.sem("v_mean"), P.adds("v_mean"))
        for k in range(KT):
            P.e.wait_ge(P.sem("v_squared"), P.due("v_squared"))
            last = P.e.matmul(K.PS[:, 1, :], K.inv_d[:, :], K.Y[:, k, 0:S], start=(k == 0), stop=(k == KT - 1))
        last.then_inc(P.sem("norm_mean"), P.adds("norm_mean"))

    def act(self, K, P):
        for k in range(KT):
            P.e.wait_ge(P.sem("v_centred"), P.due("v_centred"))
            P.e.activation(K.Y[:, k, 0:S], K.v2[:, k, :], ACT.Square).then_inc(P.sem("v_squared"), P.adds("v_squared"))
        P.e.wait_ge(P.sem("norm_inverse"), P.due("norm_inverse"))
        P.e.activation(K.R[:, 0:S], K.R[:, 0:S], ACT.Sqrt).then_inc(P.sem("norm_root"), P.adds("norm_root"))

    def dve(self, K, P):
        P.e.wait_ge(P.sem("v_mean"), P.due("v_mean"))
        for k in range(KT):
            P.e.tensor_tensor(K.v2[:, k, :], K.v2[:, k, :], K.PS[:, 0, :], ALU.subtract).then_inc(P.sem("v_centred"), P.adds("v_centred"))
        P.e.tensor_tensor(K.ws[:, :, :], K.ws[:, :, :],
                          K.keep_upper[:, :].rearrange("p (a n) -> p a n", a=1).broadcast_to([128, 8, 128]), ALU.mult)
        P.e.wait_ge(P.sem("norm_mean"), P.due("norm_mean"))
        P.e.tensor_scalar(K.R[:, 0:S], K.PS[:, 1, :], 1e-5, None, ALU.add).then_inc(P.sem("dve_order"), P.adds("dve_order"))
        P.e.wait_ge(P.sem("dve_order"), P.due("dve_order", 0))
        P.e.reciprocal(K.R[:, 0:S], K.R[:, 0:S]).then_inc(P.sem("norm_inverse"), P.adds("norm_inverse"))
        P.e.wait_ge(P.sem("norm_root"), P.due("norm_root"))


class SpatialGate(Stage):

    def dve(self, K, P):
        flat = lambda ap: ap.rearrange("p a n -> p (a n)")

        def body(i):
            t = sl(i)
            P.e.scalar_tensor_tensor(K.s_a[:, :], flat(K.v2[:, t, :]), K.p["sgu_ln_g"][:, t], K.R[:, 0:S], ALU.mult, ALU.mult).then_inc(P.sem("sgu_scaled"), P.adds("sgu_scaled"))
            P.e.wait_ge(P.sem("sgu_transposed"), P.due("sgu_transposed"))
            P.e.tensor_copy(K.s_vT[:, :], K.PS[:, 0, :]).then_inc(P.sem("sgu_vT"), P.adds("sgu_vT"))
            P.e.wait_ge(P.sem("sgu_mixed"), P.due("sgu_mixed"))
            P.e.tensor_tensor(K.s_o[:, :], K.PS[:, 1, :], flat(K.u2[:, t, :]), ALU.mult).then_inc(P.sem("sgu_gated"), P.adds("sgu_gated"))
            P.e.wait_ge(P.sem("sgu_hi"), P.due("sgu_hi"))
            P.e.tensor_tensor(flat(K.XL[:, t, 0:S]), K.s_o[:, :], flat(K.XH[:, t, 0:S]).bitcast(F32), ALU.subtract).then_inc(P.sem("sgu_lo"), P.adds("sgu_lo"))

        P.loop(8, body, sgu_scaled=1, sgu_transposed=1, sgu_vT=1, sgu_mixed=1, sgu_gated=1, sgu_hi=1, sgu_lo=1)

    def act(self, K, P):
        def body(i):
            t = sl(i)
            P.e.wait_ge(P.sem("sgu_scaled"), P.due("sgu_scaled"))
            P.e.activation(K.s_b[:, :], K.s_a[:, :], ACT.Identity, bias=K.p["sgu_ln_b"][:, t]).then_inc(P.sem("sgu_normed"), P.adds("sgu_normed"))
            P.e.wait_ge(P.sem("sgu_gated"), P.due("sgu_gated"))
            P.e.activation(K.XH[:, t, 0:S].rearrange("p a n -> p (a n)"), K.s_o[:, :], ACT.Copy).then_inc(P.sem("sgu_hi"), P.adds("sgu_hi"))
            P.e.wait_ge(P.sem("sgu_lo"), P.due("sgu_lo"))

        P.loop(8, body, sgu_scaled=1, sgu_normed=1, sgu_gated=1, sgu_hi=1, sgu_lo=1)

    def pe(self, K, P):
        def body(i):
            P.e.wait_ge(P.sem("sgu_normed"), P.due("sgu_normed"))
            for n in range(4):
                c = slice(128 * n, 128 * n + 128)
                last = P.e.transpose(K.PS[:, 0, c], K.s_b[:, c], K.ident[:, :])
            last.then_inc(P.sem("sgu_transposed"), P.adds("sgu_transposed"))
            P.e.wait_ge(P.sem("sgu_vT"), P.due("sgu_vT"))
            for n in range(4):
                c = slice(128 * n, 128 * n + 128)
                P.e.matmul(K.PS[:, 1, c], K.s_vT[:, c], K.ws[:, sl(i), :].rearrange("p a n -> p (a n)"), start=True, stop=False)
                last = P.e.matmul(K.PS[:, 1, c], K.one_row2[0:1, 0:128], K.sgu_b[0:1, sl(i), :].rearrange("p a n -> p (a n)"),
                                  start=False, stop=True)
            last.then_inc(P.sem("sgu_mixed"), P.adds("sgu_mixed"))
            P.e.wait_ge(P.sem("sgu_gated"), P.due("sgu_gated"))

        P.loop(8, body, sgu_normed=1, sgu_transposed=1, sgu_vT=1, sgu_mixed=1, sgu_gated=1)


def ffn2(K, layer):
    g = [K.p[f"norm2_g{layer}{j}"] for j in range(4)]
    st = [RmsNorm(K.X, g[2])]
    for c0, n in FFN_CHUNKS:
        up = GatedUp(n, c0)
        up.xh, up.xl = K.XH, K.XL
        st += [up, Narrow(n, K.HH, K.HL, K.F, add=c0 > 0)]
    return st + [RmsNorm(K.F, g[3], out=K.X, add=True)]


def block2(K):
    g = [[K.p[f"norm2_g{i}{j}"] for j in range(4)] for i in range(2)]
    st = [Load(K.loads2), RmsNorm(K.X, g[0][0]), Store(12, K.XH, K.XL, K.in2), BiasTable(), DiffAttention(),
          Narrow(8, K.XH, K.XL, K.F, add=False), RmsNorm(K.F, g[0][1], out=K.X, add=True)] + ffn2(K, 0)
    st += [Load(K.loads2b), RmsNorm(K.X, g[1][0]), Store(8, K.XH, K.XL, K.uv2, func=ACT.Gelu), CentreV(), SpatialGate(),
           Narrow(8, K.XH, K.XL, K.F, add=False), RmsNorm(K.F, g[1][1], out=K.X, add=True)] + ffn2(K, 1)
    return st


def specs2():
    v = [("subln_g", "diff_subln_g_2", 0), ("sgu_ln_g", "sgu_ln_g_2", 0), ("sgu_ln_b", "sgu_ln_b_2", 0)]
    v += [(f"norm2_g{i}{j}", "norm_g_2", (i, j)) for i in range(2) for j in range(4)]
    return v + [(f"conv2_w{j}", "conv_w_2", (0, j)) for j in range(3)]


def weights2(a):
    out = [wide_panels(a["w_in_even_2"][0]), narrow_panels(a["w_out_even_2"][0])]
    out += ffn_panels(a["w_gate_2"][0], a["w_up_2"][0], a["w_down_2"][0], FFN_CHUNKS)
    out += [wide_panels(a["w_in_odd_2"][0]), narrow_panels(a["w_out_odd_2"][0])]
    return out + ffn_panels(a["w_gate_2"][1], a["w_up_2"][1], a["w_down_2"][1], FFN_CHUNKS)


def bucket_onehot():
    n = 511 - np.arange(BIAS_W)
    nf = np.maximum(n, 1).astype(np.float32)
    large = 16 + (np.log(nf / np.float32(16)) / np.float32(np.log(8.0)) * np.float32(16)).astype(np.int32)
    b = np.where(n < 0, 32, np.where(n < 16, n, np.minimum(large, 31)))
    return (b[None, :] == np.arange(33)[:, None]).astype(np.float32)


T3 = ((0, TM // 2), (TM // 2, TM // 2))
HALF_T = TM // 2
N_CHUNK = TM // 16
DECAY = float(np.exp(-0.5))


def flat(ap):
    return ap.rearrange("p a n -> p (a n)")


def both_parts(K, bank, lo=0, hi=128):
    return K.PS[lo:hi, bank:bank + 2, 0:HALF_T]


def parts(ap):
    return ap.rearrange("p (a n) -> p a n", a=2)


class GateRows(Stage):

    def pe(self, K, P):
        for m, (c0, cn) in enumerate(((0, 128), (128, 32))):
            for part, (t0, tn) in enumerate(T3):
                for k in range(KT):
                    last = P.e.matmul(K.PS[0:cn, 2 * m + part, 0:tn], K.w_gd[:, k, c0:c0 + cn], K.Y[:, k, t0:t0 + tn],
                                      start=(k == 0), stop=(k == KT - 1))
        last.then_inc(P.sem("gate_rows_done"), P.adds("gate_rows_done"))

    def dve(self, K, P):
        P.e.wait_ge(P.sem("gate_rows_done"), P.due("gate_rows_done"))
        P.e.tensor_copy(parts(K.rp[:, 14, :]), both_parts(K, 0))
        P.e.tensor_copy(parts(K.rp[0:32, 15, :]), both_parts(K, 2, 0, 32))


class CentredShift(Stage):

    def dve(self, K, P):
        mu0, mu1, c = K.mu[:, :, 0], K.mu[:, :, 1], K.mu_rest
        areas = ((slice(0, 128), slice(0, 15)), (slice(0, 32), slice(15, 16)))
        for r, q in areas:
            P.e.tensor_tensor(c[r, q], mu0[r, q], mu1[r, q], ALU.add).then_inc(P.sem("dve_order"), P.adds("dve_order"))
            P.e.wait_ge(P.sem("dve_order"), P.due("dve_order", 0))
        for r, q in areas:
            P.e.tensor_scalar(c[r, q], c[r, q], -1.0, 1.0, ALU.mult, ALU.add).then_inc(P.sem("shift_weights"), P.adds("shift_weights"))
        for q in range(16):
            r = slice(0, 128 if q < 15 else 32)
            P.e.wait_ge(P.sem("shift_seeded"), P.due("shift_seeded"))
            z, p = K.rz[r, q, :], K.rp[r, q, :]
            P.e.scalar_tensor_tensor(z[:, 1:TM], p[:, 0:TM - 1], mu0[r, q:q + 1], z[:, 1:TM], ALU.mult, ALU.add).then_inc(P.sem("dve_order"), P.adds("dve_order"))
            P.e.wait_ge(P.sem("dve_order"), P.due("dve_order", 0))
            P.e.scalar_tensor_tensor(z[:, 0:TM - 1], p[:, 1:TM], mu1[r, q:q + 1], z[:, 0:TM - 1], ALU.mult, ALU.add)

    def act(self, K, P):
        P.e.wait_ge(P.sem("shift_weights"), P.due("shift_weights", 2))
        for q in range(16):
            r = slice(0, 128 if q < 15 else 32)
            P.e.activation(K.rz[r, q, :], K.rp[r, q, :], ACT.Copy, scale=K.mu_rest[r, q:q + 1]).then_inc(P.sem("shift_seeded"), P.adds("shift_seeded"))


class RwkvPrepare(Stage):

    def act(self, K, P):
        P.e.activation(K.rz[:, 12, :], K.rz[:, 12, :], ACT.Tanh).then_inc(P.sem("wd_tanh"), P.adds("wd_tanh"))
        for q in range(4):
            for d in range(2):
                P.e.wait_ge(P.sem("lora_done"), P.due("lora_done", 2))
                P.e.activation(parts(K.t_s[:, d, :]), both_parts(K, 2 * d), ACT.Sigmoid, bias=K.p[f"decay_w0{d}"][:, q:q + 1])
                P.e.activation(parts(K.t_a[:, d, :]), both_parts(K, 4 + 2 * d), ACT.Sigmoid,
                                     bias=K.p[f"icl_a0{d}"][:, q:q + 1]).then_inc(P.sem("gates_open"), P.adds("gates_open"))
            P.e.wait_ge(P.sem("kk_scaled"), P.due("kk_scaled"))
            P.e.activation(K.t_n[:, :], K.t_kk[:, :], ACT.Square).then_inc(P.sem("kk_squared"), P.adds("kk_squared"))
            P.e.wait_ge(P.sem("kk_sumsq"), P.due("kk_sumsq"))
            P.e.activation(K.t_n[:, :], K.t_n[:, :], ACT.Sqrt).then_inc(P.sem("kk_norm"), P.adds("kk_norm"))
            for d in range(2):
                P.e.wait_ge(P.sem("decay_cumulated"), P.due("decay_cumulated"))
                P.e.activation(K.t_s[:, d, :], K.t_bi[:, :], ACT.Exp)
                P.e.activation(K.wc[:, d, q, :], K.t_bc[:, :], ACT.Exp)
                P.e.activation(K.t_en[:, :], K.t_bi[:, :], ACT.Exp, scale=-1.0)
                P.e.activation(K.t_bx[:, :], K.t_bx[:, :], ACT.Exp).then_inc(P.sem("decay_exps"), P.adds("decay_exps"))
                P.e.wait_ge(P.sem("direction_done"), P.due("direction_done"))

    def pe(self, K, P):
        P.e.wait_ge(P.sem("wd_tanh"), P.due("wd_tanh"))
        for q in range(4):
            if q:
                P.e.wait_ge(P.sem("direction_done"), P.due("direction_done", 2))
                P.e.wait_ge(P.sem("bonus_done"), P.due("bonus_done"))
            c = slice(128 * q, 128 * q + 128)
            for d in range(2):
                rows = slice(64 * d, 64 * d + 64)
                for w, tile, bank in ((K.w2, 12, 2 * d), (K.a2, 13, 4 + 2 * d)):
                    for part, (t0, tn) in enumerate(T3):
                        last = P.e.matmul(K.PS[:, bank + part, 0:tn], w[rows, c], K.rz[rows, tile, t0:t0 + tn], start=True, stop=True)
                    last.then_inc(P.sem("lora_done"), P.adds("lora_done"))
            P.e.wait_ge(P.sem("kk_squared"), P.due("kk_squared"))
            for part, (t0, tn) in enumerate(T3):
                last = P.e.matmul(K.PS[:, part, 0:tn], K.head_ones[:, :], K.t_n[:, t0:t0 + tn], start=True, stop=True)
            last.then_inc(P.sem("kk_summed"), P.adds("kk_summed"))
            P.e.wait_ge(P.sem("bonus_product"), P.due("bonus_product"))
            for part, (t0, tn) in enumerate(T3):
                last = P.e.matmul(K.PS[:, 2 + part, 0:tn], K.head_ones[:, :], K.t_u[:, t0:t0 + tn], start=True, stop=True)
            last.then_inc(P.sem("bonus_summed"), P.adds("bonus_summed"))

    def dve(self, K, P):
        e = P.e
        for q in range(4):
            vec = lambda n: K.p[n][:, q:q + 1]
            r, k, v = K.rz[:, q, :], K.rz[:, 4 + q, :], K.rz[:, 8 + q, :]
            e.tensor_scalar(K.t_c[:, 0:1], vec("k_a"), -1.0, 1.0, ALU.mult, ALU.add).then_inc(P.sem("dve_order"), P.adds("dve_order"))
            P.e.wait_ge(P.sem("dve_order"), P.due("dve_order", 0))
            e.tensor_scalar(K.t_kk[:, :], k, vec("k_k"), None, ALU.mult).then_inc(P.sem("kk_scaled"), P.adds("kk_scaled"))
            P.e.wait_ge(P.sem("gates_open"), P.due("gates_open", 2))
            P.e.wait_ge(P.sem("kk_summed"), P.due("kk_summed"))
            e.tensor_scalar(parts(K.t_n[:, :]), both_parts(K, 0), 1e-24, None, ALU.max).then_inc(P.sem("kk_sumsq"), P.adds("kk_sumsq"))
            P.e.wait_ge(P.sem("kk_norm"), P.due("kk_norm"))
            e.reciprocal(K.t_n[:, :], K.t_n[:, :]).then_inc(P.sem("dve_order"), P.adds("dve_order"))
            P.e.wait_ge(P.sem("dve_order"), P.due("dve_order", 0))
            e.tensor_tensor(K.t_kk[:, :], K.t_kk[:, :], K.t_n[:, :], ALU.mult).then_inc(P.sem("dve_order"), P.adds("dve_order"))
            P.e.wait_ge(P.sem("dve_order"), P.due("dve_order", 0))
            for d in range(2):
                lw, al = K.t_s[:, d, :], K.t_a[:, d, :]
                e.tensor_scalar(lw, lw, -DECAY, None, ALU.mult).then_inc(P.sem("dve_order"), P.adds("dve_order"))
                P.e.wait_ge(P.sem("dve_order"), P.due("dve_order", 0))
                e.tensor_tensor_scan(K.t_bi[:, :], K.reset16[:, :], lw, 0.0, ALU.mult, ALU.add).then_inc(P.sem("dve_order"), P.adds("dve_order"))
                P.e.wait_ge(P.sem("dve_order"), P.due("dve_order", 0))
                b3 = K.t_bi[:, :].rearrange("p (n c) -> p n c", c=16)
                e.tensor_copy(K.t_bc[:, :], b3[:, :, 15]).then_inc(P.sem("dve_order"), P.adds("dve_order"))
                P.e.wait_ge(P.sem("dve_order"), P.due("dve_order", 0))
                if d == 0:
                    e.tensor_tensor(K.t_bx[:, :], K.t_bi[:, :], lw, ALU.subtract).then_inc(P.sem("decay_cumulated"), P.adds("decay_cumulated"))
                else:
                    total = K.t_bc[:, :].rearrange("p (n c) -> p n c", c=1).broadcast_to([128, N_CHUNK, 16])
                    e.tensor_tensor(K.t_bx[:, :].rearrange("p (n c) -> p n c", c=16), total, b3, ALU.subtract).then_inc(P.sem("dve_order"), P.adds("dve_order"))
                    P.e.wait_ge(P.sem("dve_order"), P.due("dve_order", 0))
                    e.tensor_tensor(K.t_bi[:, :], K.t_bx[:, :], lw, ALU.add).then_inc(P.sem("decay_cumulated"), P.adds("decay_cumulated"))
                e.tensor_scalar(K.t_k[:, d, :], al, vec("k_a"), K.t_c[:, 0:1], ALU.mult, ALU.add).then_inc(P.sem("dve_order"), P.adds("dve_order"))
                P.e.wait_ge(P.sem("dve_order"), P.due("dve_order", 0))
                e.tensor_tensor(K.t_k[:, d, :], K.t_k[:, d, :], k, ALU.mult).then_inc(P.sem("dve_order"), P.adds("dve_order"))
                P.e.wait_ge(P.sem("dve_order"), P.due("dve_order", 0))
                e.tensor_tensor(al, al, K.t_kk[:, :], ALU.mult).then_inc(P.sem("dve_order"), P.adds("dve_order"))
                P.e.wait_ge(P.sem("dve_order"), P.due("dve_order", 0))
                P.e.wait_ge(P.sem("decay_exps"), P.due("decay_exps"))
                ar = K.ar[d]
                e.scalar_tensor_tensor(ar[:, 0, q, :], K.t_kk[:, :], -1.0, K.t_bx[:, :], ALU.mult, ALU.mult)
                e.tensor_tensor(ar[:, 1, q, :], r, lw, ALU.mult)
                e.tensor_tensor(ar[:, 2, q, :], al, K.t_en[:, :], ALU.mult)
                e.tensor_tensor(ar[:, 3, q, :], K.t_k[:, d, :], K.t_en[:, :], ALU.mult).then_inc(P.sem("direction_done"), P.adds("direction_done"))
                P.e.wait_ge(P.sem("direction_done"), P.due("direction_done", 0))
            e.tensor_tensor(K.t_u[:, :], K.t_k[:, 0, :], K.t_k[:, 1, :], ALU.add).then_inc(P.sem("dve_order"), P.adds("dve_order"))
            P.e.wait_ge(P.sem("dve_order"), P.due("dve_order", 0))
            e.scalar_tensor_tensor(K.t_u[:, :], K.t_u[:, :], vec("r_k"), r, ALU.mult, ALU.mult).then_inc(P.sem("bonus_product"), P.adds("bonus_product"))
            P.e.wait_ge(P.sem("bonus_summed"), P.due("bonus_summed"))
            e.scalar_tensor_tensor(parts(K.rz[:, q, :]), both_parts(K, 2), 0.5, parts(v), ALU.mult, ALU.mult).then_inc(P.sem("bonus_done"), P.adds("bonus_done"))
            P.e.wait_ge(P.sem("bonus_done"), P.due("bonus_done", 0))


class RwkvScan(Stage):

    HALVES = [slice(0, 64), slice(64, 128)]
    BOTH = [(0, HALVES[0]), (0, HALVES[1]), (1, HALVES[0]), (1, HALVES[1])]

    def act(self, K, P):
        def stage(c, b):
            for d in range(2):
                t = sl_t(16 * c if d == 0 else (N_CHUNK - 1) * 16 - 16 * c, 16)
                P.e.activation(K.c_st[b][:, d, 0:4, :].rearrange("p a (q t) -> p a q t", q=4), K.ar[d][:, :, :, t], ACT.Copy)
                last = P.e.activation(K.c_st[b][:, d, 4, :].rearrange("p (q t) -> p q t", q=4), K.rz[:, 8:12, t], ACT.Copy)
            last.then_inc(P.sem("chunk_staged"), P.adds("chunk_staged"))

        def betas():
            P.e.wait_ge(P.sem("betas_transposed"), P.due("betas_transposed"))
            for par, half in enumerate(self.HALVES):
                last = P.e.activation(K.c_bt[half, :, :], K.PS[0:64, 5, :].rearrange("p (a q n) -> p a q n", q=2, n=64)[:, :, par, :], ACT.Copy)
            last.then_inc(P.sem("betas_ready"), P.adds("betas_ready"))

        def step(c, b, more=2):
            P.e.wait_ge(P.sem("u_done"), P.due("u_done"))
            P.e.activation(K.c_u[:, :], K.PS[:, 2, :], ACT.Copy).then_inc(P.sem("u_ready"), P.adds("u_ready"))
            P.e.wait_ge(P.sem("state_done"), P.due("state_done"))
            if more:
                betas()
            P.e.wait_ge(P.sem("y_done"), P.due("y_done"))
            if more > 1:
                stage(c + 2, b)

        def body(i):
            step(2 * i, 0)
            step(2 * i + 1, 1)

        stage(0, 0)
        stage(1, 1)
        betas()
        P.loop((N_CHUNK - 3) // 2, body, u_done=2, u_ready=2, state_done=2, y_done=2, betas_transposed=2, betas_ready=2, chunk_staged=2)
        step(N_CHUNK - 3, 0)
        step(N_CHUNK - 2, 1, more=1)
        step(N_CHUNK - 1, 0, more=0)

    def pe(self, K, P):
        mm = P.e.matmul

        def grams(b):
            P.e.wait_ge(P.sem("chunk_staged"), P.due("chunk_staged"))
            P.settle()
            st = K.c_st[b]
            for d, h in self.BOTH:
                mm(K.PS[h, d, 0:128], st[h, d, 2, :], st[h, d, 0:2, :].rearrange("p a n -> p (a n)"), start=True, stop=True)
                mm(K.PS[h, d, 128:256], st[h, d, 3, :], st[h, d, 0:2, :].rearrange("p a n -> p (a n)"), start=True, stop=True)
                last = mm(K.PS[h, d, 256:320], st[h, d, 0, :], st[h, d, 2, :], start=True, stop=True)
            last.then_inc(P.sem("grams_done"), P.adds("grams_done"))

        def transposes(b):
            st = K.c_st[b]
            for d in range(2):
                for j in range(2):
                    last = P.e.transpose(K.PS[0:64, 5, 256 * d + 128 * j:256 * d + 128 * j + 128], st[:, d, 2 + j, :], K.ident[:, :])
            last.then_inc(P.sem("betas_transposed"), P.adds("betas_transposed"))
            for d in range(2):
                last = P.e.transpose(K.PS[0:64, 6, 128 * d:128 * d + 128], st[:, d, 4, :], K.ident[:, :])
            last.then_inc(P.sem("v_rows_done"), P.adds("v_rows_done"))

        def square(n, b):
            if n == 0:
                P.e.wait_ge(P.sem("grams_masked"), P.due("grams_masked"))
            else:
                P.e.wait_ge(P.sem("squares_ready"), P.due("squares_ready"))
            P.settle()
            g = K.c_g[b]
            for d, h in self.BOTH:
                if n == 0:
                    c = 128 * d
                    mm(K.PS[h, 7, c:c + 64], g[h, d, 256:320], g[h, d, 0:64], start=True, stop=True)
                    last = mm(K.PS[h, 7, c + 64:c + 128], g[h, d, 0:64], g[h, d, 256:320], start=True, stop=True)
                elif n == 1:
                    n2, n2t = K.c_n2[h, d, 0:64], K.c_n2[h, d, 64:128]
                    mm(K.PS[h, 0, 128 * d:128 * d + 64], n2t, n2, start=True, stop=True)
                    mm(K.PS[h, 0, 128 * d + 64:128 * d + 128], n2, n2t, start=True, stop=True)
                    last = mm(K.PS[h, 0, 256 + 64 * d:320 + 64 * d], n2t, K.c_p[h, 0, d, :], start=True, stop=True)
                elif n == 2:
                    n4, n4t = K.c_n4[h, d, 0:64], K.c_n4[h, d, 64:128]
                    mm(K.PS[h, 1, 64 * d:64 * d + 64], n4, n4t, start=True, stop=True)
                    last = mm(K.PS[h, 1, 128 + 64 * d:192 + 64 * d], n4t, K.c_p[h, 1, d, :], start=True, stop=True)
                else:
                    last = mm(K.PS[h, 1, 256 + 64 * d:320 + 64 * d], K.c_n8[h, d, :], K.c_p[h, 0, d, :], start=True, stop=True)
            last.then_inc(P.sem("squares_done"), P.adds("squares_done"))

        def outputs(b, which):
            for d, h in self.BOTH:
                if d == which:
                    c = slice(256 * d, 256 * d + 256)
                    mm(K.PS[h, 4, c], K.c_st[b][h, d, 1, :], K.c_s[b][h, c], start=True, stop=False)
                    mm(K.PS[h, 4, c], K.c_g[b][h, d, 192:256], K.c_v[b][h, c], start=False, stop=False)
                    last = mm(K.PS[h, 4, c], K.c_g[b][h, d, 64:128], K.c_u[h, c], start=False, stop=True)
            return last

        def step(b, more=True, first=False):
            nb = 1 - b
            P.e.wait_ge(P.sem("state_ready"), P.due("state_ready"))
            P.e.wait_ge(P.sem("v_rows_ready"), P.due("v_rows_ready"))
            P.settle()
            for d, h in self.BOTH:
                c = slice(256 * d, 256 * d + 256)
                mm(K.PS[h, 7, c], K.c_g[b][h, d, 128:192], K.c_v[b][h, c], start=True, stop=False)
                last = mm(K.PS[h, 7, c], K.c_st[b][h, d, 0, :], K.c_s[b][h, c], start=False, stop=True)
            last.then_inc(P.sem("rhs_done"), P.adds("rhs_done"))
            P.e.wait_ge(P.sem("squares_ready"), P.due("squares_ready"))
            if more:
                grams(nb)
            P.e.wait_ge(P.sem("rhs_ready"), P.due("rhs_ready"))
            P.settle()
            for d, h in self.BOTH:
                c = slice(256 * d, 256 * d + 256)
                last = mm(K.PS[h, 2, c], K.c_p[h, 1, d, :], K.c_r[h, c], start=True, stop=True)
            last.then_inc(P.sem("u_done"), P.adds("u_done"))
            P.e.wait_ge(P.sem("betas_ready"), P.due("betas_ready"))
            if more:
                square(0, nb)
                transposes(nb)
            P.e.wait_ge(P.sem("u_ready"), P.due("u_ready"))
            P.settle()
            for d, h in self.BOTH:
                c = slice(256 * d, 256 * d + 256)
                mm(K.PS[h, 3, c], K.c_bt[h, 2 * d, :], K.c_u[h, c], start=True, stop=False)
                last = mm(K.PS[h, 3, c], K.c_bt[h, 2 * d + 1, :], K.c_v[b][h, c], start=False, stop=True)
            last.then_inc(P.sem("state_done"), P.adds("state_done"))
            if more:
                square(1, nb)
            P.e.wait_ge(P.sem("y_taken"), P.due("y_taken"))
            P.settle()
            outputs(b, 0)
            if more:
                square(2, nb)
            last = outputs(b, 1)
            last.then_inc(P.sem("y_done"), P.adds("y_done"))
            if more:
                square(3, nb)

        def body(_):
            step(0)
            step(1)

        grams(0)
        for n in range(4):
            square(n, 0)
            if n == 0:
                transposes(0)
        P.loop(N_CHUNK // 2, body, chunk_staged=2, grams_done=2, betas_transposed=2, v_rows_done=2, grams_masked=2, squares_done=8,
               squares_ready=8, v_rows_ready=2, state_ready=2, rhs_done=2, rhs_ready=2, u_done=2, u_ready=2, betas_ready=2,
               state_done=2, y_taken=2, y_done=2)
        step(0, more=False)

    def dve(self, K, P):
        e = P.e
        mask = K.block_mask[:, :].rearrange("p (a n) -> p a n", a=1).broadcast_to([128, 2, 256])
        halves = lambda ap: ap.rearrange("p (d n) -> p d n", d=2)
        e.memset(K.yt[:, :, :], 0.0)
        e.memset(K.c_s[0][:, :], 0.0).then_inc(P.sem("state_ready"), P.adds("state_ready"))
        P.e.wait_ge(P.sem("state_ready"), P.due("state_ready", 0))

        def square(n, b):
            if n < 0:
                P.e.wait_ge(P.sem("grams_done"), P.due("grams_done"))
                e.tensor_tensor(K.c_g[b][:, :, :], K.PS[:, 0:2, 0:320], K.gram_mask[:, :, :], ALU.mult).then_inc(P.sem("grams_masked"), P.adds("grams_masked"))
                P.e.wait_ge(P.sem("grams_masked"), P.due("grams_masked", 0))
                e.tensor_tensor(K.c_p[:, 0, :, :], K.c_g[b][:, :, 0:64], K.eye64[:, :, :], ALU.add)
                return
            P.e.wait_ge(P.sem("squares_done"), P.due("squares_done"))
            P.e.wait_ge(P.sem("squares_ready"), P.due("squares_ready", 0))
            if n == 0:
                last = e.tensor_copy(K.c_n2[:, :, :].rearrange("p d n -> p (d n)"), K.PS[:, 7, 0:256])
            elif n == 1:
                e.tensor_copy(K.c_n4[:, :, :].rearrange("p d n -> p (d n)"), K.PS[:, 0, 0:256])
                last = e.tensor_tensor(K.c_p[:, 1, :, :], K.PS[:, 0, 256:384].rearrange("p (d n) -> p d n", d=2), K.c_p[:, 0, :, :], ALU.add)
            elif n == 2:
                e.tensor_copy(K.c_n8[:, :, :].rearrange("p d n -> p (d n)"), K.PS[:, 1, 0:128])
                last = e.tensor_tensor(K.c_p[:, 0, :, :], K.PS[:, 1, 128:256].rearrange("p (d n) -> p d n", d=2), K.c_p[:, 1, :, :], ALU.add)
            else:
                last = e.tensor_tensor(K.c_p[:, 1, :, :], K.PS[:, 1, 256:384].rearrange("p (d n) -> p d n", d=2), K.c_p[:, 0, :, :], ALU.add)
            last.then_inc(P.sem("squares_ready"), P.adds("squares_ready"))

        def v_rows(b):
            P.e.wait_ge(P.sem("v_rows_done"), P.due("v_rows_done"))
            for par, half in enumerate(self.HALVES):
                v = K.PS[0:64, 6, 0:256].rearrange("p (d a q n) -> p d a q n", d=2, a=1, q=2)[:, :, :, par, :]
                m = K.block_mask[0:64, :].rearrange("p (q n) -> p q n", q=4)
                for d in range(2):
                    last = e.tensor_tensor(K.c_v[b][half, 256 * d:256 * d + 256].rearrange("p (q n) -> p q n", q=4),
                                           v[:, d].broadcast_to([64, 4, 64]), m, ALU.mult)
            last.then_inc(P.sem("v_rows_ready"), P.adds("v_rows_ready"))

        def step(c, b, more=True):
            nb = 1 - b
            P.e.wait_ge(P.sem("rhs_done"), P.due("rhs_done"))
            e.tensor_tensor(halves(K.c_r[:, :]), halves(K.PS[:, 7, :]), mask, ALU.mult).then_inc(P.sem("rhs_ready"), P.adds("rhs_ready"))
            if more:
                square(-1, nb)
                square(0, nb)
                v_rows(nb)
            P.e.wait_ge(P.sem("state_done"), P.due("state_done"))
            e.tensor_tensor(K.c_s[nb][:, :], K.c_s[b][:, :], K.PS[:, 3, :], ALU.add).then_inc(P.sem("dve_order"), P.adds("dve_order"))
            P.e.wait_ge(P.sem("dve_order"), P.due("dve_order", 0))
            for d in range(2):
                s4 = K.c_s[nb][:, 256 * d:256 * d + 256].rearrange("p (q n) -> p q n", q=4)
                decay = K.wc[:, d, :, sl_t(c if d == 0 else N_CHUNK - 1 - c, 1)].broadcast_to([128, 4, 64])
                last = e.tensor_tensor(s4, s4, decay, ALU.mult)
            last.then_inc(P.sem("state_ready"), P.adds("state_ready"))
            if more:
                square(1, nb)
                square(2, nb)
                square(3, nb)
            P.e.wait_ge(P.sem("y_done"), P.due("y_done"))
            e.tensor_tensor(halves(K.c_y[:, :]), halves(K.PS[:, 4, :]), mask, ALU.mult).then_inc(P.sem("y_taken"), P.adds("y_taken"))
            P.e.wait_ge(P.sem("y_taken"), P.due("y_taken", 0))
            e.reduce_sum(K.c_yr[:, :, :], K.c_y[:, :].rearrange("p (d q n) -> p d n q", d=2, q=4), AX.X).then_inc(P.sem("dve_order"), P.adds("dve_order"))
            P.e.wait_ge(P.sem("dve_order"), P.due("dve_order", 0))
            y0 = flat(K.yt[:, sl(c), :])
            y1 = flat(K.yt[:, sl_(N_CHUNK - 1 - c), :])
            e.tensor_tensor(y0, y0, K.c_yr[:, 0, :], ALU.add).then_inc(P.sem("dve_order"), P.adds("dve_order"))
            P.e.wait_ge(P.sem("dve_order"), P.due("dve_order", 0))
            e.tensor_tensor(y1, y1, K.c_yr[:, 1, :], ALU.add).then_inc(P.sem("dve_order"), P.adds("dve_order"))
            P.e.wait_ge(P.sem("dve_order"), P.due("dve_order", 0))

        def body(i):
            step(2 * i, 0)
            step(2 * i + 1, 1)

        e.memset(K.c_y[:, :], 0.0).then_inc(P.sem("y_taken"), P.adds("y_taken"))
        P.e.wait_ge(P.sem("y_taken"), P.due("y_taken", 0))
        for n in range(-1, 4):
            square(n, 0)
            if n == 0:
                v_rows(0)
        P.loop(N_CHUNK // 2, body, grams_done=2, grams_masked=2, squares_done=8, squares_ready=8, v_rows_done=2, v_rows_ready=2,
               rhs_done=2, rhs_ready=2, y_done=2, y_taken=2, state_done=2, state_ready=2, dve_order=8)
        step(N_CHUNK - 1, 0, more=False)


def sl_t(start, n):
    return slice(start, start + n) if isinstance(start, int) else bass.ds(start, n)


def sl_(i):
    return sl_t(i, 1)


class RwkvOutput(Stage):

    def dve(self, K, P):
        e = P.e
        col = lambda j: K.g_c[:, j, :]
        wide = lambda j: K.g_c[:, j, :].rearrange("p (n c) -> p n c", c=1).broadcast_to([128, N_CHUNK, 64])
        e.reduce_sum(col(0), K.yt[:, :, :], AX.X).then_inc(P.sem("dve_order"), P.adds("dve_order"))
        P.e.wait_ge(P.sem("dve_order"), P.due("dve_order", 0))
        e.tensor_scalar(col(0), col(0), 1.0 / 64, None, ALU.mult).then_inc(P.sem("dve_order"), P.adds("dve_order"))
        P.e.wait_ge(P.sem("dve_order"), P.due("dve_order", 0))
        e.tensor_tensor(K.yt[:, :, :], K.yt[:, :, :], wide(0), ALU.subtract).then_inc(P.sem("y_centred"), P.adds("y_centred"))
        P.e.wait_ge(P.sem("y_squared"), P.due("y_squared"))
        e.reduce_sum(col(1), K.y2[:, :, :], AX.X).then_inc(P.sem("dve_order"), P.adds("dve_order"))
        P.e.wait_ge(P.sem("dve_order"), P.due("dve_order", 0))
        e.tensor_scalar(col(1), col(1), 1.0 / 64, 64e-5, ALU.mult, ALU.add).then_inc(P.sem("dve_order"), P.adds("dve_order"))
        P.e.wait_ge(P.sem("dve_order"), P.due("dve_order", 0))
        e.reciprocal(col(1), col(1)).then_inc(P.sem("y_inverse"), P.adds("y_inverse"))
        P.e.wait_ge(P.sem("y_root"), P.due("y_root"))
        e.tensor_tensor(K.yt[:, :, :], K.yt[:, :, :], wide(1), ALU.mult).then_inc(P.sem("y_normed"), P.adds("y_normed"))
        P.e.wait_ge(P.sem("y_transposed"), P.due("y_transposed"))
        for b in range(8):
            for par in range(2):
                src = K.PS[0:64, b, :].rearrange("p (c a q t) -> p c a q t", c=4, a=2, q=4)[:, :, par]
                dst = K.yf[64 * par:64 * par + 64, :, 64 * b:64 * b + 64].rearrange("p q (c t) -> p c q t", c=4)
                last = e.tensor_copy(dst, src)
        last.then_inc(P.sem("y_rows"), P.adds("y_rows"))
        P.e.wait_ge(P.sem("y_rows"), P.due("y_rows", 0))
        for q in range(4):
            e.scalar_tensor_tensor(K.yf[:, q, :], K.yf[:, q, :], K.p["lnx_g"][:, q:q + 1], K.rz[:, q, META:TM], ALU.mult, ALU.add).then_inc(P.sem("y_bonus"), P.adds("y_bonus"))
        for q in range(4):
            P.e.wait_ge(P.sem("y_shifted"), P.due("y_shifted"))
            P.e.wait_ge(P.sem("gate_done"), P.due("gate_done"))
            e.tensor_tensor(K.ya[:, q, :], K.yf[:, q, :], K.PS[:, q, :], ALU.mult).then_inc(P.sem("y_gated"), P.adds("y_gated"))

    def act(self, K, P):
        P.e.activation(K.rz[:, 14, :], K.rz[:, 14, :], ACT.Sigmoid)
        P.e.activation(K.rz[0:32, 15, :], K.rz[0:32, 15, :], ACT.Sigmoid).then_inc(P.sem("gate_open"), P.adds("gate_open"))
        P.e.wait_ge(P.sem("y_centred"), P.due("y_centred"))
        P.e.activation(K.y2[:, :, :], K.yt[:, :, :], ACT.Square).then_inc(P.sem("y_squared"), P.adds("y_squared"))
        P.e.wait_ge(P.sem("y_inverse"), P.due("y_inverse"))
        P.e.activation(K.g_c[:, 1, :], K.g_c[:, 1, :], ACT.Sqrt).then_inc(P.sem("y_root"), P.adds("y_root"))
        for q in range(4):
            P.e.wait_ge(P.sem("y_bonus"), P.due("y_bonus"))
            P.e.activation(K.yf[:, q, :], K.yf[:, q, :], ACT.Identity, bias=K.p["lnx_b"][:, q:q + 1]).then_inc(P.sem("y_shifted"), P.adds("y_shifted"))

    def pe(self, K, P):
        P.e.wait_ge(P.sem("y_normed"), P.due("y_normed"))
        for b in range(8):
            for c in range(4):
                last = P.e.transpose(K.PS[0:64, b, 128 * c:128 * c + 128], K.yt[:, 1 + 4 * b + c, :], K.ident[:, :])
        last.then_inc(P.sem("y_transposed"), P.adds("y_transposed"))
        P.e.wait_ge(P.sem("y_rows"), P.due("y_rows"))
        P.e.wait_ge(P.sem("gate_open"), P.due("gate_open"))
        for q in range(4):
            c = slice(128 * q, 128 * q + 128)
            P.e.matmul(K.PS[:, q, :], K.g2a[:, c], K.rz[:, 14, META:TM], start=True, stop=False)
            P.e.matmul(K.PS[:, q, :], K.g2b[0:32, c], K.rz[0:32, 15, META:TM], start=False, stop=True).then_inc(P.sem("gate_done"), P.adds("gate_done"))


class QkNormRope(Stage):

    def tiles(self, K):
        out = [(K.a_q[:, q, :], K.p["q_norm_g"], META, ((0, S),)) for q in range(4)]
        return out + [(K.a_kv[:, 0, :], K.p["k_norm_g"], 0, T3)]

    def act(self, K, P):
        for x, g, off, toks in self.tiles(K):
            n = toks[-1][0] + toks[-1][1]
            P.e.activation(K.a_t[:, 0, 0:n], x, ACT.Square).then_inc(P.sem("qk_squared"), P.adds("qk_squared"))
            P.e.wait_ge(P.sem("qk_inverse"), P.due("qk_inverse"))
            P.e.activation(K.a_t[:, 1, 0:n], K.a_t[:, 1, 0:n], ACT.Sqrt).then_inc(P.sem("qk_root"), P.adds("qk_root"))
            P.e.wait_ge(P.sem("qk_rotated"), P.due("qk_rotated"))

    def pe(self, K, P):
        for x, g, off, toks in self.tiles(K):
            P.e.wait_ge(P.sem("qk_squared"), P.due("qk_squared"))
            for part, (t0, tn) in enumerate(toks):
                last = P.e.matmul(K.PS[:, part, 0:tn], K.head_ones2[:, :], K.a_t[:, 0, t0:t0 + tn], start=True, stop=True)
            last.then_inc(P.sem("qk_sumsq"), P.adds("qk_sumsq"))
            P.e.wait_ge(P.sem("qk_normed"), P.due("qk_normed"))
            for part, (t0, tn) in enumerate(toks):
                last = P.e.matmul(K.PS[:, 2 + part, 0:tn], K.rot[:, :], x[:, t0:t0 + tn], start=True, stop=True)
            last.then_inc(P.sem("qk_partner"), P.adds("qk_partner"))
            P.e.wait_ge(P.sem("qk_rotated"), P.due("qk_rotated"))

    def dve(self, K, P):
        e = P.e
        for x, g, off, toks in self.tiles(K):
            n = toks[-1][0] + toks[-1][1]
            P.e.wait_ge(P.sem("qk_sumsq"), P.due("qk_sumsq"))
            for part, (t0, tn) in enumerate(toks):
                last = e.tensor_scalar(K.a_t[:, 1, t0:t0 + tn], K.PS[:, part, 0:tn], 1.0 / 64, EPS, ALU.mult, ALU.add)
            last.then_inc(P.sem("dve_order"), P.adds("dve_order"))
            P.e.wait_ge(P.sem("dve_order"), P.due("dve_order", 0))
            e.reciprocal(K.a_t[:, 1, 0:n], K.a_t[:, 1, 0:n]).then_inc(P.sem("qk_inverse"), P.adds("qk_inverse"))
            P.e.wait_ge(P.sem("qk_root"), P.due("qk_root"))
            e.scalar_tensor_tensor(x, x, g[:, 0:1], K.a_t[:, 1, 0:n], ALU.mult, ALU.mult).then_inc(P.sem("qk_normed"), P.adds("qk_normed"))
            P.e.wait_ge(P.sem("qk_partner"), P.due("qk_partner"))
            for part, (t0, tn) in enumerate(toks):
                last = e.tensor_tensor(K.a_t[:, 0, t0:t0 + tn], K.PS[:, 2 + part, 0:tn], K.rope[:, 1, off + t0:off + t0 + tn], ALU.mult)
            e.tensor_tensor(x, x, K.rope[:, 0, off:off + n], ALU.mult).then_inc(P.sem("dve_order"), P.adds("dve_order"))
            P.e.wait_ge(P.sem("dve_order"), P.due("dve_order", 0))
            e.tensor_tensor(x, x, K.a_t[:, 0, 0:n], ALU.add).then_inc(P.sem("qk_rotated"), P.adds("qk_rotated"))


class GroupedAttention(Stage):

    UNITS = [(u, b) for u in range(2) for b in range(4)]
    KEYS = [(128 * j, min(128, TM - 128 * j)) for j in range(5)]

    def act(self, K, P):
        P.e.activation(K.a_ks[0:64, 0, :], K.a_kv[0:64, 0, :], ACT.Copy).then_inc(P.sem("k_staged"), P.adds("k_staged"))
        P.e.activation(K.a_ks[0:64, 1, :], K.a_kv[64:128, 0, :], ACT.Copy).then_inc(P.sem("k_staged"), P.adds("k_staged"))
        P.e.wait_ge(P.sem("v_transposed"), P.due("v_transposed"))
        P.e.activation(K.a_vT[:, 0:4, :].rearrange("p a n -> p (a n)"), K.PS[:, 7, :], ACT.Copy)
        P.e.activation(K.a_vT[0:16, 4, :], K.PS[0:16, 5, 0:128], ACT.Copy).then_inc(P.sem("vT_ready"), P.adds("vT_ready"))
        for kv in range(2):
            def body(i):
                for u in range(2):
                    P.e.activation(K.a_qs[0:64, u, :], flat(K.a_q[64 * u:64 * u + 64, sl(i + 2 * kv), :]), ACT.Copy, scale=0.125).then_inc(P.sem("qk_staged"), P.adds("qk_staged"))
                for n, (u, b) in enumerate(self.UNITS):
                    s = n % 2
                    P.e.wait_ge(P.sem("logits_done"), P.due("logits_done"))
                    P.e.wait_ge(P.sem("max_negated"), P.due("max_negated"))
                    P.e.activation(parts(K.a_p[:, s, :]), K.PS[:, 2 * s:2 * s + 2, 0:HALF_T], ACT.Exp,
                                         bias=K.a_st[:, s, 1:2], accum_out=K.a_st[:, s, 2:3]).then_inc(P.sem("exp_done"), P.adds("exp_done"))
                P.e.wait_ge(P.sem("att_out_done"), P.due("att_out_done"))
                P.e.activation(flat(K.HH[:, sl(i + 4 + 2 * kv), :]), K.PS[:, 6, :], ACT.Copy).then_inc(P.sem("att_out_hi"), P.adds("att_out_hi"))

            P.loop(2, body, qk_staged=2, logits_done=8, max_negated=8, exp_done=8, att_out_done=1, att_out_hi=1)

    def dve(self, K, P):
        e = P.e
        for kv in range(2):
            def body(i):
                for n, (u, b) in enumerate(self.UNITS):
                    s = n % 2
                    P.e.wait_ge(P.sem("logits_done"), P.due("logits_done"))
                    e.tensor_reduce(K.a_st[:, s, 0:1], K.PS[:, 2 * s:2 * s + 2, 0:HALF_T], AX.XY, ALU.max).then_inc(P.sem("dve_order"), P.adds("dve_order"))
                    P.e.wait_ge(P.sem("dve_order"), P.due("dve_order", 0))
                    e.tensor_scalar(K.a_st[:, s, 1:2], K.a_st[:, s, 0:1], -1.0, None, ALU.mult).then_inc(P.sem("max_negated"), P.adds("max_negated"))
                    P.e.wait_ge(P.sem("exp_done"), P.due("exp_done"))
                    e.reciprocal(K.a_st[:, s, 3:4], K.a_st[:, s, 2:3]).then_inc(P.sem("dve_order"), P.adds("dve_order"))
                    P.e.wait_ge(P.sem("dve_order"), P.due("dve_order", 0))
                    e.tensor_scalar(K.a_p[:, s, :], K.a_p[:, s, :], K.a_st[:, s, 3:4], None, ALU.mult).then_inc(P.sem("probs_ready"), P.adds("probs_ready"))
                    P.e.wait_ge(P.sem("probs_transposed"), P.due("probs_transposed"))
                    e.tensor_copy(K.a_pT[:, s, 0:4, :].rearrange("p a n -> p (a n)"), K.PS[:, 4, :])
                    e.tensor_copy(K.a_pT[0:16, s, 4, :], K.PS[0:16, 5, 0:128]).then_inc(P.sem("probsT_ready"), P.adds("probsT_ready"))
                P.e.wait_ge(P.sem("att_out_done"), P.due("att_out_done"))
                P.e.wait_ge(P.sem("att_out_hi"), P.due("att_out_hi"))
                h = sl(i + 4 + 2 * kv)
                e.tensor_tensor(flat(K.HL[:, h, :]), K.PS[:, 6, :], flat(K.HH[:, h, :]).bitcast(F32), ALU.subtract).then_inc(P.sem("att_out_lo"), P.adds("att_out_lo"))

            P.loop(2, body, dve_order=16, logits_done=8, max_negated=8, exp_done=8, probs_ready=8, probs_transposed=8,
                   probsT_ready=8, att_out_done=1, att_out_hi=1, att_out_lo=1)

    def pe(self, K, P):
        for j, (k0, kn) in enumerate(self.KEYS):
            out = K.PS[0:kn, 7, k0:k0 + 128] if j < 4 else K.PS[0:kn, 5, 0:128]
            last = P.e.transpose(out, K.a_kv[:, 1, k0:k0 + kn], K.ident[:, :])
        last.then_inc(P.sem("v_transposed"), P.adds("v_transposed"))
        P.e.wait_ge(P.sem("k_staged"), P.due("k_staged", 2))
        for kv in range(2):
            def logits(n):
                u, b = self.UNITS[n]
                for part, (t0, tn) in enumerate(T3):
                    last = P.e.matmul(K.PS[:, 2 * (n % 2) + part, 0:tn], K.a_qs[0:64, u, 128 * b:128 * b + 128],
                                      K.a_ks[0:64, kv, t0:t0 + tn], start=True, stop=True)
                last.then_inc(P.sem("logits_done"), P.adds("logits_done"))

            def body(i):
                P.e.wait_ge(P.sem("qk_staged"), P.due("qk_staged", 2))
                logits(0)
                for n, (u, b) in enumerate(self.UNITS):
                    if n + 1 < len(self.UNITS):
                        if n >= 1:
                            P.e.wait_ge(P.sem("exp_done"), P.due("exp_done", 0))
                        logits(n + 1)
                    s = n % 2
                    P.e.wait_ge(P.sem("probs_ready"), P.due("probs_ready"))
                    P.e.wait_ge(P.sem("exp_done"), P.due("exp_done"))
                    if n:
                        P.e.wait_ge(P.sem("probsT_ready"), P.due("probsT_ready", 0))
                    for j, (k0, kn) in enumerate(self.KEYS):
                        out = K.PS[0:kn, 4, k0:k0 + 128] if j < 4 else K.PS[0:kn, 5, 0:128]
                        last = P.e.transpose(out, K.a_p[:, s, k0:k0 + kn], K.ident[:, :])
                    last.then_inc(P.sem("probs_transposed"), P.adds("probs_transposed"))
                    P.e.wait_ge(P.sem("probsT_ready"), P.due("probsT_ready"))
                    if n == 0 and kv == 0 and isinstance(i, int):
                        pass
                    for j, (k0, kn) in enumerate(self.KEYS):
                        last = P.e.matmul(K.PS[64 * u:64 * u + 64, 6, 128 * b:128 * b + 128],
                                          K.a_vT[0:kn, j, 64 * kv:64 * kv + 64], K.a_pT[0:kn, s, j, :],
                                          start=(j == 0), stop=(j == 4))
                last.then_inc(P.sem("att_out_done"), P.adds("att_out_done"))
                P.e.wait_ge(P.sem("att_out_lo"), P.due("att_out_lo"))

            if kv == 0:
                P.e.wait_ge(P.sem("vT_ready"), P.due("vT_ready"))
            P.loop(2, body, qk_staged=2, logits_done=8, exp_done=8, probs_ready=8, probs_transposed=8, probsT_ready=8,
                   att_out_done=1, att_out_lo=1)


class SplitYa(Stage):

    def act(self, K, P):
        P.e.activation(K.HH[:, 0:4, :], K.ya[:, :, :], ACT.Copy).then_inc(P.sem("ya_hi"), P.adds("ya_hi"))

    def dve(self, K, P):
        P.e.wait_ge(P.sem("ya_hi"), P.due("ya_hi"))
        P.e.tensor_tensor(K.HL[:, 0:4, :], K.ya[:, :, :], K.HH[:, 0:4, :].bitcast(F32), ALU.subtract)


class GatedNarrow(Narrow):

    def __init__(self, nk, xh, xl, gate):
        super().__init__(nk, xh, xl, gate)

    def act(self, K, P):
        narrow_split(K, P, self.nk, split_act)
        split_last(K, P, split_act)

    def dve(self, K, P):
        narrow_split(K, P, self.nk, split_dve)
        for t in range(8):
            sum_wait(P, t)
            P.e.tensor_tensor(self.dst[:, t, :], self.dst[:, t, :], K.PS[:, t, 0:S], ALU.mult).then_inc(P.sem("sum_stored"), P.adds("sum_stored"))
        split_last(K, P, split_dve)


class Merge(Stage):

    def dve(self, K, P):
        for t in range(8):
            P.e.tensor_tensor(K.gates[:, t, :], K.gates[:, t, :], K.gates[:, 8 + t, :], ALU.add).then_inc(P.sem("merged"), P.adds("merged"))
        for t in range(8):
            P.e.wait_ge(P.sem("merged_hi"), P.due("merged_hi"))
            P.e.wait_ge(P.sem("merged"), P.due("merged", 0))
            P.e.tensor_tensor(K.XL[:, t, 0:S], K.gates[:, t, :], K.XH[:, t, 0:S].bitcast(F32), ALU.subtract)

    def act(self, K, P):
        for t in range(8):
            P.e.wait_ge(P.sem("merged"), P.due("merged"))
            P.e.activation(K.XH[:, t, 0:S], K.gates[:, t, :], ACT.Copy).then_inc(P.sem("merged_hi"), P.adds("merged_hi"))


def block3(K):
    real = ((META, S),)
    st = [Load(K.loads3), RmsNorm(K.XM, K.p["mix_norm_g"], T3), GateRows(), Store(7, K.XH, K.XL, K.rp, toks=T3),
          CentredShift(), Load(K.loads3b), RwkvPrepare(), Load(K.loads3c), RwkvScan(), Load(K.loads3d), RwkvOutput(),
          RmsNorm(K.XM, K.p["mix_norm_g"], T3), Load(K.loads3e), Store(2, K.XH, K.XL, K.a_q, toks=real, off=META),
          Store(1, K.XH, K.XL, K.a_kv, toks=T3), QkNormRope(), GroupedAttention(), SplitYa(),
          Store(8, K.XH, K.XL, K.gates, toks=real, off=META, func=ACT.Sigmoid),
          GatedNarrow(4, K.HH, K.HL, K.gates[:, 0:8, :]), GatedNarrow(4, K.HH[:, 4:8, :], K.HL[:, 4:8, :], K.gates[:, 8:16, :]),
          Merge(), Narrow(8, K.XH, K.XL, K.X), RmsNorm(K.X, K.p["ffn3_norm_g"])]
    for c0, n in FF3_CHUNKS:
        st += [SquaredReluUp(n // 2, K.XH, K.XL), Narrow(n, K.HH, K.HL, K.X)]
    return st + [RmsNorm(K.X, K.p["final3_norm_g"], out=K.X)]


def specs3():
    v = [("mix_norm_g", "mix_norm_g_3", 0), ("ffn3_norm_g", "ffn_norm_g_3", 0), ("final3_norm_g", "final_norm_g_3", None),
         ("k_k", "k_k_3", 0), ("k_a", "k_a_3", 0), ("r_k", "r_k_3", 0), ("lnx_g", "lnx_g_3", 0), ("lnx_b", "lnx_b_3", 0)]
    v += [(f"decay_w0{d}", "decay_w0_3", (0, d)) for d in range(2)] + [(f"icl_a0{d}", "icl_a0_3", (0, d)) for d in range(2)]
    v += [("q_norm_g", "q_norm_g_3", 0), ("k_norm_g", "k_norm_g_3", 0)]
    return v


def weights3(a):
    w = a["w_in_3"][0]
    rk = 1952
    out = [wide_panels(w[:, 0:1792]), wide_panels(w[:, rk:rk + 512]), wide_panels(w[:, rk + 512:rk + 768]),
           wide_panels(w[:, rk + 768:]), narrow_panels(a["w_branch_rwkv_3"][0]), narrow_panels(a["w_branch_attn_3"][0]),
           narrow_panels(a["w_out_3"][0])]
    for c0, n in FF3_CHUNKS:
        c = slice(128 * c0, 128 * (c0 + n))
        out += [wide_panels(a["w_ff1_3"][0][:, c]), narrow_panels(a["w_ff2_3"][0][c])]
    return out


def consts3():
    r = np.arange(128)
    tile, tok = (r % 64) // 16, r % 16
    ct, ck = np.arange(64) // 16, np.arange(64) % 16
    same = tile[:, None] == ct[None, :]
    gram = []
    for d in range(2):
        before = (tok[:, None] < ck[None, :]) if d == 0 else (tok[:, None] > ck[None, :])
        after = (tok[:, None] > ck[None, :]) if d == 0 else (tok[:, None] < ck[None, :])
        here = before | (tok[:, None] == ck[None, :])
        gram += [same & before, same & here, same & before, same & here, same & after]
    block = np.repeat(tile[:, None] == np.arange(4)[None, :], 64, axis=1)
    eye = np.tile(np.eye(64), (2, 2))
    head = (r[:, None] // 64) == (r[None, :] // 64)
    rot = np.zeros((128, 128))
    for d in range(128):
        if (d % 32) < 16:
            rot[d + 16, d] = -1.0
        else:
            rot[d - 16, d] = 1.0
    inv = np.float32(10000.0) ** (-np.arange(16, dtype=np.float32) * np.float32(2.0) / np.float32(32))
    t = np.arange(S)
    row, colu = (t // 64).astype(np.float32), (t % 64).astype(np.float32)
    ang = np.zeros((128, TM), np.float32)
    for d in range(128):
        pos = row if (d % 64) < 32 else colu
        ang[d, META:] = pos * inv[d % 16]
    reset = np.broadcast_to((np.arange(TM) % 16 != 0), (128, TM))
    f = lambda x: np.ascontiguousarray(x.astype(np.float32))
    return {"gram_mask": f(np.concatenate(gram, axis=1).reshape(128, 2, 320)), "block_mask": f(block), "eye64": f(eye.reshape(128, 2, 64)),
            "head_ones": f(head), "rot": f(rot), "rope": f(np.stack([np.cos(ang), np.sin(ang)], axis=1)), "reset16": f(reset)}


class Prologue(Stage):

    def act(self, K, P):
        for dst, src in K.loads:
            P.e.dma_start(dst, src).then_inc(P.sem("inputs_loaded"), P.adds("inputs_loaded", 16))
        P.e.wait_ge(P.sem("inputs_loaded"), P.due("inputs_loaded", 0))
        for _ in range(2):
            split_act(K, P)

    def dve(self, K, P):
        for t in range(2):
            P.e.memset(K.zero_credit[:, t:t + 1], 0.0).then_inc(P.sem(f"tile_evacuated{t}"), 2)
        for _ in range(2):
            split_dve(K, P)
        


class Epilogue(Stage):

    def __init__(self, src):
        self.src = src

    def act(self, K, P):
        P.e.dma_start(K.out, self.src).then_inc(P.sem("output_stored"), P.adds("output_stored", 16))
        P.e.wait_ge(P.sem("output_stored"), P.due("output_stored", 0))


def block1(K):
    g1, hh, hl = K.p, K.HH, K.HL
    st = [RmsNorm(K.X, g1["att_norm_g"]), ForgetGates(K.w_fl, 16),
          Store(4, K.XH, K.XL, K.q1), Store(4, K.XH, K.XL, K.k1), Store(4, K.XH, K.XL, K.v1),
          ForgettingAttention(), Narrow(8, K.XH, K.XL, K.X)]
    st += ffn1(K, 0)
    st += [RmsNorm(K.X, g1["hgrn_norm_g"]), LowerBounds(),
           Store(4, K.XH, K.XL, K.q1h, func=ACT.Silu), Store(4, K.XH, K.XL, K.g1, func=ACT.Silu),
           Store(4, K.XH, K.XL, K.f1, func=ACT.Sigmoid), Store(4, K.XH, K.XL, K.i1),
           Hgrn(), Narrow(8, K.XH, K.XL, K.X)]
    st += ffn1(K, 1)
    st += [RmsNorm(K.X, g1["final_norm_g"], out=K.X)]
    return st


def ffn1(K, layer):
    conv = ([K.p[f"ffn_conv_w{layer}{j}"] for j in range(3)], K.p[f"ffn_conv_b{layer}"])
    st = [RmsNorm(K.X, K.p[f"ffn_norm_g{layer}"])]
    for c0, n in FFN_CHUNKS:
        up = GatedUp(n, c0, conv)
        up.xh, up.xl = K.XH, K.XL
        st += [up, Narrow(n, K.HH, K.HL, K.X)]
    return st


def vec_specs():
    v = [("att_norm_g", "att_norm_g", 0), ("hgrn_norm_g", "hgrn_norm_g", 0), ("hgrn_onorm_g", "hgrn_onorm_g", 0),
         ("final_norm_g", "final_norm_g", None)]
    for l in range(2):
        v += [(f"ffn_norm_g{l}", "ffn_norm_g", l), (f"ffn_conv_b{l}", "ffn_conv_b", l)]
        v += [(f"ffn_conv_w{l}{j}", "ffn_conv_w", (l, j)) for j in range(3)]
    return v


CONSTS = [("ident", 128), ("inv_d", 128), ("inv_dv", 128), ("causal", 128), ("ones_row", 512), ("reset64", 512),
          ("causal64", 256), ("one_col", 2), ("flip", 128), ("keep_upper", 128)]


def program(nc, args, out):
    n_panels = args["weights"].shape[0]
    with ExitStack() as ctx:
        K, M = Bufs(), Mem(nc)
        K.XM, _ = M.new("X", [128, KT, TM])
        K.X = K.XM[:, :, META:TM]
        K.XH, xa = M.new("XH", [128, KT, TM], F32R)
        K.XL, xb = M.new("XL", [128, KT, TM], F32R)
        K.W, _ = M.new("W", [128, 2, PANEL])
        K.WH, _ = M.new("WH", [128, 2, PANEL], F32R)
        K.WL, _ = M.new("WL", [128, 2, PANEL], F32R)
        K.HH, ha = M.new("HH", [128, 12, S], F32R)
        K.HL, _ = M.new("HL", [128, 12, S], F32R)
        consts, _ = M.new("consts", [128, sum(n for _, n in CONSTS)])
        params, _ = M.new("params", [128, args["params"].shape[1]])
        K.R, _ = M.new("R", [128, TM])
        K.zero_credit, _ = M.new("zero_credit", [128, 8])
        K.att_b_f, _ = M.new("att_b_f", [16, 1])
        K.lb_logits, _ = M.new("lb_logits", [128, 16])
        K.lbt, _ = M.new("lbt", [128, 24])
        K.lb, _ = M.new("lb", [128, 16])
        K.PS = ctx.enter_context(nc.psum_tensor("PS", [128, 8, 512], F32))
        at = 0
        cols = {}
        for name, n in CONSTS:
            cols[name] = consts[:, at:at + n]
            at += n
        K.ident, K.inv_d, K.inv_dv, K.causal = cols["ident"], cols["inv_d"], cols["inv_dv"], cols["causal"]
        K.ones_row, K.reset64, K.causal64, K.one_col = cols["ones_row"], cols["reset64"], cols["causal64"], cols["one_col"]
        K.flip, K.keep_upper = cols["flip"], cols["keep_upper"]
        K.p, at = {}, 0
        for name, n in args["param_tiles"]:
            K.p[name] = params[:, at:at + n]
            at += n
        scr = M.at
        room = (M.end - scr) // 32 * 8

        def v(name, shape, words, base=None, dt=F32):
            assert words + int(np.prod(shape[1:])) <= (room if base is None else 24 * S), (name, room)
            return nc.alloc_sbuf_tensor_at(name, shape, dt, offset=(scr if base is None else base) + 4 * words)

        K.Y = v("Y", [128, KT, TM], 0)
        K.w_fl = v("w_fl", [128, KT, 16], 4224)
        K.q1, K.k1 = v("q1", [128, 8, S], 0, ha), v("k1", [128, 8, S], 4096, ha)
        K.qs, K.ks = v("qs", [128, 2, S], 8192, ha), v("ks", [128, 2, S], 9216, ha)
        K.vs, K.vT = v("vs", [128, S], 10240, ha), v("vT", [128, S], 10752, ha)
        K.v1 = v("v1", [128, 8, S], 0)
        K.c_rows, K.gate_rows = v("c_rows", [16, S], 4608), v("gate_rows", [16, 2, S], 5120)
        K.cm, K.ncm = v("cm", [16, 2, S], 6144), v("ncm", [16, 2, S], 7168)
        K.pr, K.pT, K.st = v("pr", [128, 2, S], 8192), v("pT", [128, 2, S], 9216), v("st", [128, 2, 4], 10240)
        K.one_row16 = v("one_row16", [16, S], 10256)

        K.q1h, K.f1 = v("q1h", [128, 8, S], 0), v("f1", [128, 8, S], 4096)
        K.i1, K.g1 = v("i1", [128, 8, S], 0, ha), v("g1", [128, 8, S], 4096, ha)
        (K.h_f, K.h_k, K.h_lf, K.h_b, K.h_eb, K.h_en, K.h_qd, K.h_ki) = (v(f"head{j}", [128, S], 8192 + 512 * j) for j in range(8))
        K.aT = v("aT", [128, 256], 12288)
        K.h_ks, K.h_i = v("h_ks", [128, S], 8192, ha), v("h_i", [128, S], 8704, ha)
        K.iT, K.ksT = v("iT", [128, 4, 128], 9216, ha), v("ksT", [128, 4, 128], 10240, ha)
        K.sp = v("sp", [128, 8, 128], 11264, ha)

        K.CV, K.CF = v("CV", [128, 2, 2, S], 4224), v("CF", [128, 2, 2, S], 6272)
        K.SG, K.HF = v("SG", [128, 2, S], 6272), v("HF", [128, 2, S], 7296)

        K.F = v("F", [128, KT, S], 8320)
        K.in2 = v("in2", [128, 24, S], 0, ha)
        K.d_q, K.d_k = v("d_q", [128, 2, S], 0), v("d_k", [128, 2, S], 1024)
        K.d_vs, K.d_vT = v("d_vs", [128, S], 2048), v("d_vT", [128, S], 2560)
        K.d_p, K.d_pT = v("d_p", [128, 2, S], 3072), v("d_pT", [128, 2, S], 4096)
        K.bias, K.d_st, K.lam = v("bias", [128, 4, 512], 5120), v("d_st", [128, 2, 4], 7168), v("lam", [128, 256], 7184)
        K.lamt, K.bias_t, K.onehot = v("lamt", [128, 8], 7440), v("bias_t", [33, 4], 7448), v("onehot", [33, BIAS_W], 7456)
        K.d_cz, K.d_cy, K.d_sq = v("d_cz", [128, S], 8104), v("d_cy", [128, S], 8616), v("d_sq", [128, S], 9128)
        K.bias_rows, K.lam_prod = v("bias_rows", [4, BIAS_W], 9640), v("lam_prod", [128, 128], 10280)
        K.bias_dram = nc.dram_tensor("bias_spread", (4, BIAS_W), F32, kind="Internal").ap()
        K.uv2 = v("uv2", [128, 16, S], 0, ha)
        K.u2, K.v2 = K.uv2[:, 0:8, :], K.uv2[:, 8:16, :]
        K.ws, K.sgu_b, K.one_row2 = v("ws", [128, 8, 128], 4224), v("sgu_b", [1, 8, 128], 5248), K.ones_row
        K.s_a, K.s_b, K.s_vT, K.s_o = (v("s_" + n, [128, S], 6272 + 512 * j) for j, n in enumerate(("a", "b", "vT", "o")))

        if 3 in BLOCKS:
            rest = 4 * 4 * TM
            K.w_gd = v("w_gd", [128, KT, 160], 4224)
            K.mu, K.mu_rest = v("mu", [128, 16, 2], 5504), v("mu_rest", [128, 16], 5536)
            K.rp = v("rp", [128, 16, TM], 0, ha)
            rz = nc.alloc_sbuf_tensor_at("rz", [128, 16 * TM], F32, offset=xa)
            K.rz = rz[:, :].rearrange("p (q t) -> p q t", q=16)
            K.yt = rz[:, 4 * TM:8 * TM].rearrange("p (n c) -> p n c", c=64)
            K.ar = [v("ar0", [128, 4, 4, TM], 0, ha), v("ar1", [128, 4, 4, TM], 0)]
            K.t_s, K.t_a = v("t_s", [128, 2, TM], rest, ha), v("t_a", [128, 2, TM], rest + 2 * TM, ha)
            K.t_k, K.t_n = v("t_k", [128, 2, TM], rest + 4 * TM, ha), v("t_n", [128, TM], rest + 6 * TM, ha)
            K.head_ones = v("head_ones", [128, 128], rest + 7 * TM, ha)
            K.wc = v("wc", [128, 2, 4, N_CHUNK], rest)
            K.reset16, K.t_kk, K.t_bi, K.t_bx, K.t_en = (v(f"prepare{j}", [128, TM], rest + 264 + TM * j) for j in range(5))
            K.t_u = K.t_en
            at = rest + 264 + 5 * TM
            K.w2, K.a2 = v("w2", [128, 512], at), v("a2", [128, 512], at + 512)
            K.t_bc, K.t_c = v("t_bc", [128, N_CHUNK], at + 1024), v("t_c", [128, 2], at + 1064)

            def row(base, at, *named):
                out = []
                for name, shape in named:
                    out.append(v(name, shape, at, base))
                    at += int(np.prod(shape[1:]))
                return out

            (c_st0, c_g0, K.c_n2, K.c_n4, K.c_n8, K.c_p, K.c_bt, c_v0, K.c_r) = row(ha, rest, ("c_st", [128, 2, 5, 64]), ("c_g", [128, 2, 320]), ("c_n2", [128, 2, 128]), ("c_n4", [128, 2, 128]),
                                ("c_n8", [128, 2, 64]), ("c_p", [128, 2, 2, 64]), ("c_bt", [128, 4, 64]), ("c_v", [128, 512]),
                                ("c_r", [128, 512]))
            (K.c_u, c_s0, K.c_y, K.c_yr, K.gram_mask, K.block_mask, K.eye64, c_st1, c_g1) = row(None, rest + 264, ("c_u", [128, 512]), ("c_s", [128, 512]), ("c_y", [128, 512]), ("c_yr", [128, 2, 64]),
                                ("gram_mask", [128, 2, 320]), ("block_mask", [128, 256]), ("eye64", [128, 2, 64]),
                                ("c_st1", [128, 2, 5, 64]), ("c_g1", [128, 2, 320]))
            c_v1 = nc.alloc_sbuf_tensor_at("c_v1", [128, 512], F32, offset=xa + 4 * 12 * TM)
            c_s1 = nc.alloc_sbuf_tensor_at("c_s1", [128, 512], F32, offset=xa + 4 * (12 * TM + 512))
            K.c_s = (c_s0, c_s1)
            K.c_st, K.c_g, K.c_v = (c_st0, c_st1), (c_g0, c_g1), (c_v0, c_v1)
            K.ya = v("ya", [128, 4, S], room - 2048 - 8)
            K.y2, K.yf = v("y2", [128, N_CHUNK, 64], 0, ha), v("yf", [128, 4, S], 2112, ha)
            K.g_c = v("g_c", [128, 2, N_CHUNK], 4160, ha)
            K.g2a, K.g2b = v("g2a", [128, 512], 0), v("g2b", [32, 512], 512)
            (K.a_q, K.a_kv, K.a_t, K.rope, K.rot, K.a_ks, K.a_vT, K.a_qs, K.a_p, K.a_st, K.a_pT, K.head_ones2) = row(None, 0, ("a_q", [128, 4, S]), ("a_kv", [128, 2, TM]), ("a_t", [128, 2, TM]), ("rope", [128, 2, TM]),
                                ("rot", [128, 128]), ("a_ks", [64, 2, TM]), ("a_vT", [128, 5, 128]), ("a_qs", [64, 2, S]),
                                ("a_p", [128, 2, TM]), ("a_st", [128, 2, 4]), ("a_pT", [128, 2, 5, 128]), ("head_ones2", [128, 128]))
            K.gates = v("gates", [128, 16, S], 0)
            A = args
            K.loads3 = [(K.w_gd[:, :, :], A["w_gd"]), (K.mu[:, 0:15, :], A["mu"]), (K.mu[0:32, 15:16, :], A["mu_tail"]),
                        (K.XM[:, :, 0:META], A["meta"])]
            K.loads3b = [(K.w2[:, :], A["w2"]), (K.a2[:, :], A["a2"]), (K.reset16[:, :], A["c3_reset16"]), (K.head_ones[:, :], A["c3_head_ones"])]
            K.loads3c = [(K.gram_mask[:, :, :], A["c3_gram_mask"]), (K.block_mask[:, :], A["c3_block_mask"]), (K.eye64[:, :, :], A["c3_eye64"])]
            K.loads3d = [(K.g2a[:, :], A["g2"][0:128, :]), (K.g2b[:, :], A["g2"][128:160, :])]
            K.loads3e = [(K.rope[:, :, :], A["c3_rope"]), (K.rot[:, :], A["c3_rot"]), (K.head_ones2[:, :], A["c3_head_ones"])]

        K.halves = lambda t, u: t[:, 0:S].rearrange("p (j u c) -> p u j c", u=2, c=64)[:, u]
        K.halves_ps = lambda u: K.PS[:, (7, 3)[u], 0:256].rearrange("p (j c) -> p j c", c=64)
        K.weights = args["weights"]
        K.out = out
        K.loads = [(consts[:, :], args["consts"]), (params[:, :], args["params"]), (K.X[:, :, 0:S], args["x"])]
        if 1 in BLOCKS:
            K.loads += [(K.att_b_f[:, :], args["att_b_f"]), (K.lb_logits[:, :], args["lb_logits"]),
                        (K.w_fl[:, :, :], args["w_fl"])]
        if 2 in BLOCKS:
            K.loads2 = [(K.lam[:, :], args["lam"].partition_broadcast(128)), (K.bias_t[0:32, :], args["rel_bias"]),
                        (K.onehot[:, :], args["onehot"])]
            K.loads2b = [(K.ws[:, :, :], args["ws"]), (K.sgu_b[0:1, :, :], args["sgu_b"])]
        stages = [Prologue()]
        if 1 in BLOCKS:
            stages += block1(K)
        if 2 in BLOCKS:
            stages += block2(K)
        if 3 in BLOCKS:
            stages += block3(K)
        stages += [Epilogue(K.X[:, :, 0:S])]

        sems = {}
        block = ctx.enter_context(nc.Block())

        def engine(e, tag):
            P = Engine(ctx, nc, sems, e, tag)
            P.split_left, P.split_par = n_panels, 0
            return P

        def left_after_prologue(P, stage):
            if isinstance(stage, Prologue):
                P.split_left = n_panels - 2

        @block.sync
        def _(e):
            stream_sync(K, engine(e, "sync"), n_panels)

        pairs = list(zip(stages, stages[1:]))
        for st, after in pairs:
            if isinstance(after, Wide) and after.n >= 3:
                after.after_norm = st.before_panels = st.gives_normed
                after.after_narrow = st.gives_sums
            if isinstance(after, RmsNorm) and st.gives_sums:
                after.after_sums = st.before_norm = True
            if isinstance(after, Narrow) and isinstance(st, (GatedUp, SquaredReluUp)):
                after.after_wide = True

        @block.tensor
        def _(e):
            P = engine(e, "pe")
            for st, after in pairs + [(stages[-1], None)]:
                st.pe(K, P)
                onto_wide = isinstance(after, Wide) and after.n >= 3 and (st.gives_normed or st.gives_sums or st.gives_banks)
                if onto_wide or (isinstance(after, Narrow) and after.after_wide):
                    P.stage_end_open()
                else:
                    P.stage_end()

        @block.scalar
        def _(e):
            P = engine(e, "act")
            for st, after in pairs + [(stages[-1], None)]:
                st.act(K, P)
                left_after_prologue(P, st)
                if isinstance(after, RmsNorm) and after.after_sums:
                    P.stage_end_open()
                else:
                    P.stage_end()
                    P.count("sum_stored", 8 if st.gives_sums else 0)

        @block.vector
        def _(e):
            P = engine(e, "dve")
            for st in stages:
                st.dve(K, P)
                left_after_prologue(P, st)
                P.stage_end()


def wide_panels(w):
    return w.reshape(KT, 128, -1, 256).transpose(2, 1, 0, 3).reshape(-1, 128, PANEL)


def narrow_panels(w):
    return w.reshape(-1, 2, 128, D).transpose(0, 2, 1, 3).reshape(-1, 128, PANEL)


def paired_panels(gate, value):
    g = gate.reshape(KT, 128, -1, 1, 128)
    v = value.reshape(KT, 128, -1, 1, 128)
    return np.concatenate([g, v], axis=3).transpose(2, 1, 0, 3, 4).reshape(-1, 128, PANEL)


def ffn_panels(gate, value, down, chunks):
    out = []
    for c0, n in chunks:
        c = slice(128 * c0, 128 * (c0 + n))
        out += [paired_panels(gate[:, c], value[:, c]), narrow_panels(down[c])]
    return out


def weights1(a):
    w = a["att_w_in"][0]
    out = [wide_panels(w[:, 0:3 * D]), narrow_panels(a["att_w_out"][0])]
    up, down = a["ffn_w_up"], a["ffn_w_down"]
    out += ffn_panels(up[0][:, :FFN], up[0][:, FFN:], down[0], FFN_CHUNKS)
    w = a["hgrn_w_in"][0]
    out += [wide_panels(w[:, c * D:(c + 1) * D]) for c in (0, 3, 1, 2)] + [narrow_panels(a["hgrn_w_out"][0])]
    out += ffn_panels(up[1][:, :FFN], up[1][:, FFN:], down[1], FFN_CHUNKS)
    return out


def make_consts():
    r = np.arange(128)
    c = {
        "ident": np.eye(128),
        "inv_d": np.full((128, 128), 1.0 / D),
        "inv_dv": np.full((128, 128), 1.0 / 128),
        "causal": np.where(r[None, :] <= r[:, None], 0.0, NEG),
        "ones_row": np.ones((128, 512)),
        "reset64": np.broadcast_to((np.arange(512) % 64 != 0).astype(np.float32), (128, 512)),
        "causal64": (np.arange(256)[None, :] % 64 >= (r % 64)[:, None]).astype(np.float32),
        "one_col": np.ones((128, 2)),
        "flip": np.eye(128)[::-1],
        "keep_upper": (r[:, None] <= r[None, :]).astype(np.float32),
    }
    return np.ascontiguousarray(np.concatenate([c[n].astype(np.float32) for n, _ in CONSTS], axis=1))


def kernel(**inputs):
    import concourse.bacc as bacc
    from concourse.bass_utils import run_bass_kernel_spmd

    a = {k: np.asarray(v) for k, v in inputs.items()}
    cols, tiles = [], []
    for name, key, idx in (vec_specs() if 1 in BLOCKS else []) + (specs2() if 2 in BLOCKS else []) + (specs3() if 3 in BLOCKS else []):
        x = a[key] if idx is None else a[key][idx]
        if x.size == 64:
            x = np.concatenate([x, x])
        cols.append(x.reshape(-1, 128).T)
        tiles.append((name, cols[-1].shape[1]))
    weights = []
    if 1 in BLOCKS:
        weights += weights1(a)
    if 2 in BLOCKS:
        weights += weights2(a)
    if 3 in BLOCKS:
        weights += weights3(a)
    arrays = {
        "weights": np.concatenate(weights, axis=0),
        "x": a["x"][0].T.reshape(KT, 128, S).transpose(1, 0, 2),
        "params": np.concatenate(cols, axis=1),
        "consts": make_consts(),
    }
    if 1 in BLOCKS:
        arrays["att_b_f"] = a["att_b_f"].reshape(16, 1)
        arrays["lb_logits"] = a["hgrn_lb_logits"].reshape(2, KT, 128).transpose(2, 0, 1).reshape(128, 16)
        arrays["w_fl"] = a["att_w_in"][0][:, 3 * D:].reshape(KT, 128, 16).transpose(1, 0, 2)
    if 2 in BLOCKS:
        arrays["lam"] = a["diff_lambda_2"].reshape(256)
        arrays["rel_bias"] = a["rel_bias_2"]
        arrays["onehot"] = bucket_onehot()
        arrays["ws"] = a["sgu_w_2"][0].transpose(2, 0, 1)
        arrays["sgu_b"] = a["sgu_b_2"]
    if 3 in BLOCKS:
        w, mu = a["w_in_3"][0], a["rwkv_shift_3"][0]
        arrays["w_gd"] = w[:, 1792:1952].reshape(KT, 128, 160).transpose(1, 0, 2)
        arrays["mu"] = mu[:, 0:1920].reshape(2, 15, 128).transpose(2, 1, 0)
        arrays["mu_tail"] = mu[:, 1920:].T.reshape(32, 1, 2)
        arrays["meta"] = a["meta_tokens_3"].T.reshape(KT, 128, META).transpose(1, 0, 2)
        arrays["w2"] = a["decay_w2_3"].reshape(128, 512)
        arrays["a2"] = a["icl_a2_3"].reshape(128, 512)
        arrays["g2"] = a["gate_w2_3"].reshape(160, 512)
        for name, x in consts3().items():
            arrays["c3_" + name] = x
    nc = bacc.Bacc("TRN2", target_bir_lowering=False, num_devices=1)
    sent, args = {}, {}
    for name, x in arrays.items():
        sent["in_" + name] = np.ascontiguousarray(x)
        args[name] = nc.dram_tensor("in_" + name, x.shape, mybir.dt.from_np(x.dtype), kind="ExternalInput").ap()
    args["param_tiles"] = tiles
    out = nc.dram_tensor("out_0", (128, KT, S), F32, kind="ExternalOutput").ap()
    program(nc, args, out)
    r = run_bass_kernel_spmd(nc, [sent], core_ids=[0])
    y = r.results[0]["out_0"]
    return y.transpose(1, 0, 2).reshape(D, S).T.reshape(1, S, D)
```

```python
from contextlib import ExitStack

import numpy as np

import concourse.bass as bass
from concourse import mybir

F32 = mybir.dt.float32
F32R = mybir.dt.float32r
I32 = mybir.dt.int32
ALU = mybir.AluOpType
ACT = mybir.ActivationFunctionType
AX = mybir.AxisListType

BLOCKS = (1, 2, 3)
D = 1024
S = 512
KT = D // 128
PANEL = 2048
META = 16
TM = S + META
FFN = 2816
FT = FFN // 128
FFN_CHUNKS = ((0, 12), (12, 10))
FF3_CHUNKS = ((0, 12), (12, 12), (24, 8))
EPS = 1e-6
NEG = -1e30


class Engine:

    def __init__(self, ctx, nc, sems, e, tag):
        self.ctx, self.nc, self.sems, self.e, self.tag = ctx, nc, sems, e, tag
        self.n, self.off = {}, {}
        self.parity = 0
        self.split_later = False

    def sem(self, name):
        if name not in self.sems:
            self.sems[name] = self.ctx.enter_context(self.nc.semaphore(name))
        return self.sems[name]

    def count(self, name, k):
        self.n[name] = self.n.get(name, 0) + k

    def adds(self, name, by=1):
        self.count(name, by)
        return by

    def due(self, name, k=1, less=0):
        self.count(name, k)
        return self.off.get(name, 0) + (self.n[name] - less)

    def settle(self):
        self.e.sem_inc(self.sem(self.tag + "_passed_waits"), 1)

    def loop(self, times, body, **per):
        if times <= 0:
            return
        if times == 1:
            body(0)
            return
        start = dict(self.n)
        with self.e.Fori(0, times) as i:
            for name, k in per.items():
                self.off[name] = i * k
            body(i)
            self.off = {}
        got = {k: v - start.get(k, 0) for k, v in self.n.items() if v != start.get(k, 0)}
        assert got == {k: v for k, v in per.items() if v}, f"{self.tag} loop counts {got}"
        for name, k in per.items():
            self.n[name] = start.get(name, 0) + times * k

    def stage_end(self):
        self.e.drain().then_inc(self.sem("stage_done"), 1)
        self.e.wait_ge(self.sem("stage_done"), self.due("stage_done", 3))

    def stage_end_open(self):
        self.e.drain().then_inc(self.sem("stage_done"), 1)
        self.count("stage_done", 3)


class Mem:

    def __init__(self, nc):
        self.nc, self.at = nc, (nc.sbuf_base + 31) // 32 * 32
        self.end = nc.sbuf_usable_end

    def new(self, name, shape, dt=F32):
        words = int(np.prod(shape[1:]))
        t = self.nc.alloc_sbuf_tensor_at(name, shape, dt, offset=self.at)
        t_at = self.at
        self.at += (4 * words + 31) // 32 * 32
        assert self.at <= self.end, (name, self.at, self.end)
        return t, t_at


def sl(i, k=1):
    return slice(i, i + k) if isinstance(i, int) else bass.ds(i, k)


class Places:
    pass


def split_act(K, P):
    if P.split_left <= 0:
        return
    s = P.split_par
    P.e.wait_ge(P.sem(f"weights_loaded{s}"), P.due(f"weights_loaded{s}", 16))
    P.e.activation(K.WH[:, s, :], K.W[:, s, :], ACT.Copy).then_inc(P.sem("hi_ready"), P.adds("hi_ready"))
    P.split_par ^= 1


def split_dve(K, P):
    if P.split_left <= 0:
        return
    s = P.split_par
    P.e.wait_ge(P.sem("hi_ready"), P.due("hi_ready"))
    P.e.tensor_tensor(K.WL[:, s, :], K.W[:, s, :], K.WH[:, s, :].bitcast(F32), ALU.subtract).then_inc(P.sem("weights_split"), P.adds("weights_split"))
    P.split_par ^= 1


def stream_sync(K, P, n_panels):
    for s in range(2):
        P.e.dma_start(K.W[:, s, :], K.weights[s]).then_inc(P.sem(f"weights_loaded{s}"), P.adds(f"weights_loaded{s}", 16))

    def body(i):
        for s in range(2):
            P.e.wait_ge(P.sem("weights_split"), P.due("weights_split"))
            src = K.weights[sl(2 * i + 2 + s)].rearrange("a p n -> (a p) n")
            P.e.dma_start(K.W[:, s, :], src).then_inc(P.sem(f"weights_loaded{s}"), P.adds(f"weights_loaded{s}", 16))

    pairs = (n_panels - 2) // 2
    P.loop(pairs, body, weights_split=2, weights_loaded0=16, weights_loaded1=16)
    for s in range((n_panels - 2) % 2):
        P.e.wait_ge(P.sem("weights_split"), P.due("weights_split"))
        P.e.dma_start(K.W[:, s, :], K.weights[2 * pairs + 2 + s]).then_inc(P.sem(f"weights_loaded{s}"), P.adds(f"weights_loaded{s}", 16))


def wide_pe(K, P, n, xh, xl, toks, after_norm, after_narrow):
    def panel(i, first=False, sums=0):
        s = P.parity
        P.e.wait_ge(P.sem("weights_split"), P.due("weights_split"))
        wh = K.WH[:, s, :].rearrange("p (k n) -> p k n", k=KT)
        wl = K.WL[:, s, :].rearrange("p (k n) -> p k n", k=KT)
        for t in range(2):
            P.e.wait_ge(P.sem(f"tile_evacuated{t}"), P.due(f"tile_evacuated{t}"))
            bank = 2 * (2 * s + t)
            if sums:
                P.e.wait_ge(P.sem("sum_stored"), P.due("sum_stored", 0, less=7 - bank))
            c = slice(128 * t, 128 * t + 128)
            for part, (t0, tn) in enumerate(toks):
                out = K.PS[:, bank + part, 0:tn]
                for k in range(KT):
                    r = slice(t0, t0 + tn)
                    if first and t == 0 and part == 0:
                        P.e.wait_ge(P.sem("norm_lo"), P.due("norm_lo"))
                    P.e.matmul(out, wh[:, k, c], xh[:, k, r], start=(k == 0), stop=False)
                    P.e.matmul(out, wh[:, k, c], xl[:, k, r], start=False, stop=False)
                    last = P.e.matmul(out, wl[:, k, c], xh[:, k, r], start=False, stop=(k == KT - 1))
            last.then_inc(P.sem("tile_done"), P.adds("tile_done"))
        P.parity ^= 1

    def body(i):
        panel(i)
        panel(i)

    peeled = 2 if after_narrow else (2 if n % 2 == 0 else 1) if after_norm else 0
    for p in range(peeled):
        panel(0, after_norm and p == 0, after_narrow)
    P.loop((n - peeled) // 2, body, weights_split=2, tile_evacuated0=2, tile_evacuated1=2, tile_done=4)
    if (n - peeled) % 2:
        panel(0)


def wide_evac(K, P, n, evac, split, per):
    def panel(p, s):
        evac(P, p, s, "first")
        split(K, P)
        evac(P, p, s, "rest")
        P.count("tile_evacuated0", 1)
        P.count("tile_evacuated1", 1)

    def body(i):
        panel(2 * i, P.parity)
        panel(2 * i + 1, P.parity ^ 1)

    counts = {k: 2 * v for k, v in dict(per, tile_evacuated0=1, tile_evacuated1=1).items()}
    if split is split_act:
        counts.update(hi_ready=2, weights_loaded0=16, weights_loaded1=16)
    else:
        counts.update(hi_ready=2, weights_split=2)
    left = P.split_left
    whole = min(n, left) if min(n, left) % 2 == 0 else min(n, left) - 1
    P.loop(whole // 2, body, **counts)
    P.split_left = left - whole
    for p in range(whole, n):
        panel(p, P.parity)
        P.parity ^= 1
        P.split_left -= 1


def narrow_pe(K, P, nk, xh, xl, after_wide):
    def panel(k0, first, last_panel):
        s = P.parity
        P.e.wait_ge(P.sem("weights_split"), P.due("weights_split"))
        order = [(kk, t) for kk in range(2) for t in range(8)]
        if first and after_wide:
            order = [(kk, t) for t0 in (1, 0) for kk in range(2) for t in range(t0, 8, 2)]
        if last_panel and after_wide:
            P.e.wait_ge(P.sem("stage_done"), P.due("stage_done", 0))
        for kk, t in order:
            if first and after_wide and kk == 0 and t == 0:
                for j in range(2):
                    P.e.wait_ge(P.sem(f"tile_evacuated{j}"), P.due(f"tile_evacuated{j}", 0, less=-2))
            c = slice(kk * D + 128 * t, kk * D + 128 * t + 128)
            out = K.PS[:, t, 0:S]
            k = sl(k0 + kk)
            h = xh[:, k, 0:S].rearrange("p a n -> p (a n)")
            l = xl[:, k, 0:S].rearrange("p a n -> p (a n)")
            P.e.matmul(out, K.WH[:, s, c], h, start=(first and kk == 0), stop=False)
            P.e.matmul(out, K.WH[:, s, c], l, start=False, stop=False)
            last = P.e.matmul(out, K.WL[:, s, c], h, start=False, stop=(last_panel and kk == 1))
            if last_panel and kk == 1 and t < 7:
                last.then_inc(P.sem("sum_done"), P.adds("sum_done"))
            elif (kk, t) == order[len(order) // 2 - 1] or (kk, t) == order[-1]:
                last.then_inc(P.sem("tile_done"), P.adds("tile_done"))
        P.parity ^= 1

    n = nk // 2
    panel(0, True, n == 1)
    pairs = max(0, (n - 2) // 2)

    def body(i):
        panel(4 * i + 2, False, False)
        panel(4 * i + 4, False, False)

    P.loop(pairs, body, weights_split=2, tile_done=4)
    for p in range(1 + 2 * pairs, n):
        panel(2 * p, False, p == n - 1)


def narrow_split(K, P, nk, split):
    def panel():
        if split is split_act:
            P.e.wait_ge(P.sem("tile_done"), P.due("tile_done", 2))
        split(K, P)
        P.parity ^= 1

    def body(i):
        panel()
        panel()

    left = P.split_left
    n = nk // 2
    P.split_later = min(n, left) == n
    whole = (min(n, left) - P.split_later) // 2 * 2
    if split is split_act:
        P.loop(whole // 2, body, tile_done=4, hi_ready=2, weights_loaded0=16, weights_loaded1=16)
    else:
        P.loop(whole // 2, body, hi_ready=2, weights_split=2)
    P.split_left = left - whole
    for p in range(whole, n - P.split_later):
        panel()
        P.split_left -= 1
    if split is split_dve:
        P.count("tile_done", nk)


def split_last(K, P, split):
    if P.split_later:
        if split is split_act:
            P.e.wait_ge(P.sem("tile_done"), P.due("tile_done", 2))
        split(K, P)
        P.parity ^= 1
        P.split_left -= 1
        P.split_later = False


def sum_wait(P, t):
    if t < 7:
        P.e.wait_ge(P.sem("sum_done"), P.due("sum_done"))
    else:
        P.e.wait_ge(P.sem("tile_done"), P.due("tile_done", 0))


class Stage:

    gives_normed = gives_sums = gives_banks = False

    def pe(self, K, P):
        pass

    def act(self, K, P):
        pass

    def dve(self, K, P):
        pass


class Wide(Stage):

    def __init__(self, n, xh, xl, toks=((0, S),)):
        self.n, self.xh, self.xl, self.toks = n, xh, xl, toks

    gives_banks = True
    after_norm = after_narrow = False
    per_act = {}
    per_dve = {}

    def pe(self, K, P):
        wide_pe(K, P, self.n, self.xh, self.xl, self.toks, self.after_norm, self.after_narrow)

    def act(self, K, P):
        wide_evac(K, P, self.n, lambda P, p, s, when: self.evac_act(K, P, p, s, when), split_act,
                  dict(self.per_act, tile_done=2))

    def dve(self, K, P):
        wide_evac(K, P, self.n, lambda P, p, s, when: self.evac_dve(K, P, p, s, when), split_dve,
                  dict(self.per_dve, tile_done=2))

    def evac_act(self, K, P, p, s, when):
        if when == "first":
            P.e.wait_ge(P.sem("tile_done"), P.due("tile_done", 2))

    def evac_dve(self, K, P, p, s, when):
        if when == "first":
            P.e.wait_ge(P.sem("tile_done"), P.due("tile_done", 2))


class Store(Wide):

    def __init__(self, n, xh, xl, dst, first=0, func=None, toks=((0, S),), off=0):
        super().__init__(n, xh, xl, toks)
        self.off = off
        self.dst, self.first, self.func = dst, first, func

    def both(self):
        return self.func is not None

    def evac_act(self, K, P, p, s, when):
        if when != "first":
            return
        for t in range(2):
            P.e.wait_ge(P.sem("tile_done"), P.due("tile_done"))
            if t and not self.both():
                continue
            for part, (t0, tn) in enumerate(self.toks):
                last = P.e.activation(self.dst[:, sl(2 * p + t + self.first), t0 - self.off:t0 - self.off + tn].rearrange("p a n -> p (a n)"),
                                      K.PS[:, 2 * (2 * s + t) + part, 0:tn], self.func or ACT.Copy)
            last.then_inc(P.sem(f"tile_evacuated{t}"), 1)

    def evac_dve(self, K, P, p, s, when):
        if when != "first":
            return
        P.e.wait_ge(P.sem("tile_done"), P.due("tile_done", 2))
        if self.both():
            return
        for part, (t0, tn) in enumerate(self.toks):
            last = P.e.tensor_copy(self.dst[:, sl(2 * p + 1 + self.first), t0 - self.off:t0 - self.off + tn].rearrange("p a n -> p (a n)"),
                                   K.PS[:, 2 * (2 * s + 1) + part, 0:tn])
        last.then_inc(P.sem("tile_evacuated1"), 1)


class Narrow(Stage):

    gives_sums = True
    before_norm = after_wide = False

    def __init__(self, nk, xh, xl, dst, add=True, off=0):
        self.nk, self.xh, self.xl, self.dst, self.add, self.off = nk, xh, xl, dst, add, off

    def pe(self, K, P):
        narrow_pe(K, P, self.nk, self.xh, self.xl, self.after_wide)
        P.count("sum_stored", 8)

    def act(self, K, P):
        narrow_split(K, P, self.nk, split_act)
        if not self.before_norm:
            split_last(K, P, split_act)

    def dve(self, K, P):
        narrow_split(K, P, self.nk, split_dve)
        for t in range(8):
            d = self.dst[:, t, self.off:self.off + S]
            sum_wait(P, t)
            if self.add:
                last = P.e.tensor_tensor(d, d, K.PS[:, t, 0:S], ALU.add)
            else:
                last = P.e.tensor_copy(d, K.PS[:, t, 0:S])
            last.then_inc(P.sem("sum_stored"), P.adds("sum_stored"))
        if not self.before_norm:
            split_last(K, P, split_dve)


class Small(Stage):

    def __init__(self, w, m, bank=0, toks=((0, S),)):
        self.w, self.m, self.bank, self.toks = w, m, bank, toks

    def pe(self, K, P):
        for part, (t0, tn) in enumerate(self.toks):
            for k in range(KT):
                P.e.matmul(K.PS[0:self.m, self.bank + part, 0:tn], self.w[:, k, :], K.Y[:, k, t0:t0 + tn],
                           start=(k == 0), stop=(k == KT - 1))


class RmsNorm(Stage):

    def __init__(self, src, gain, toks=((0, S),), out=None, add=False, out_off=0, eps=EPS):
        self.src, self.gain, self.toks, self.out, self.add, self.eps = src, gain, toks, out, add, eps
        self.t0, self.t1 = toks[0][0], toks[-1][0] + toks[-1][1]
        self.out_off = out_off

    gives_normed = property(lambda self: self.out is None)
    gives_sums = property(lambda self: self.add)
    before_norm = False
    after_sums = before_panels = False

    def blocks(self):
        out = [(part, c, min(128, tn - c)) for part, (t0, tn) in enumerate(self.toks) for c in range(0, tn, 128)]
        return sorted(out, key=lambda b: -b[2])

    def columns(self, K):
        n, rows = len(self.blocks()), self.blocks()[-1][2]
        return [K.R[:, 0:4]] + ([K.R[0:rows, 4:n]] if n > 4 else [])

    def act(self, K, P):
        for k in range(KT):
            if self.after_sums:
                P.e.wait_ge(P.sem("sum_stored"), P.due("sum_stored"))
            P.e.activation(K.Y[:, k, self.t0:self.t1], self.src[:, k, self.t0:self.t1], ACT.Square).then_inc(P.sem("norm_squared"), P.adds("norm_squared"))
        split_last(K, P, split_act)
        P.e.wait_ge(P.sem("norm_inverse"), P.due("norm_inverse"))
        for r in self.columns(K):
            last = P.e.activation(r, r, ACT.Sqrt)
        last.then_inc(P.sem("norm_root"), P.adds("norm_root"))
        if self.out is None:
            for k in range(KT):
                P.e.wait_ge(P.sem("norm_scaled"), P.due("norm_scaled"))
                P.e.activation(K.XH[:, k, self.t0:self.t1], K.Y[:, k, self.t0:self.t1], ACT.Copy).then_inc(P.sem("norm_hi"), P.adds("norm_hi"))

    def pe(self, K, P):
        P.e.wait_ge(P.sem("norm_summed"), P.due("norm_summed"))
        for j, (part, c, n) in enumerate(self.blocks()):
            t = self.toks[part][0] + c
            for half in range(2):
                last = P.e.matmul(K.PS[0:n, 0, 2 * j:2 * j + 2], K.Y[:, half, t:t + n], K.inv_d[:, 0:2], start=(half == 0), stop=(half == 1))
        last.then_inc(P.sem("norm_mean"), P.adds("norm_mean"))
        for j, (part, c, n) in enumerate(self.blocks()):
            P.e.wait_ge(P.sem("norm_diagonal"), P.due("norm_diagonal"))
            last = P.e.matmul(K.PS[:, 6 + part, c:c + n], K.ones_row[0:n, 0:128], K.R[0:n, 16 + 128 * (j % 4):16 + 128 * (j % 4) + n], start=True, stop=True)
            last.then_inc(P.sem("norm_spread"), P.adds("norm_spread"))
        if self.out is None and not self.before_panels:
            P.count("norm_lo", KT)
        if self.add:
            P.count("sum_stored", KT)

    def dve(self, K, P):
        for k in range(2, KT):
            P.e.wait_ge(P.sem("norm_squared"), P.due("norm_squared", 3 if k == 2 else 1))
            if k >= 4:
                P.e.wait_ge(P.sem("norm_partial"), P.due("norm_partial", 0, less=1))
            y = K.Y[:, k % 2, self.t0:self.t1]
            last = P.e.tensor_tensor(y, y, K.Y[:, k, self.t0:self.t1], ALU.add)
            last.then_inc(P.sem("norm_summed" if k == KT - 1 else "norm_partial"), P.adds("norm_summed" if k == KT - 1 else "norm_partial"))
        split_last(K, P, split_dve)
        blocks = self.blocks()
        P.e.wait_ge(P.sem("norm_mean"), P.due("norm_mean"))
        for j, (part, c, n) in enumerate(blocks):
            last = P.e.tensor_scalar(K.R[0:n, j:j + 1], K.PS[0:n, 0, 2 * j:2 * j + 1], self.eps, None, ALU.add)
        last.then_inc(P.sem("dve_order"), P.adds("dve_order"))
        P.e.wait_ge(P.sem("dve_order"), P.due("dve_order", 0))
        for r in self.columns(K):
            last = P.e.reciprocal(r, r)
        last.then_inc(P.sem("norm_inverse"), P.adds("norm_inverse"))
        P.e.wait_ge(P.sem("norm_root"), P.due("norm_root"))
        for j, (part, c, n) in enumerate(blocks):
            if j >= 4:
                P.e.wait_ge(P.sem("norm_spread"), P.due("norm_spread"))
            at = 16 + 128 * (j % 4)
            P.e.tensor_scalar(K.R[0:n, at:at + n], K.ident[0:n, 0:n], K.R[0:n, j:j + 1], None, ALU.mult).then_inc(P.sem("norm_diagonal"), P.adds("norm_diagonal"))
        P.e.wait_ge(P.sem("norm_spread"), P.due("norm_spread", min(4, len(blocks))))
        two = len(self.toks) == 2
        r = K.PS[:, 6:8, 0:self.toks[0][1]] if two else K.PS[:, 6, 0:self.toks[0][1]]
        view = (lambda ap: ap.rearrange("p (a n) -> p a n", a=2)) if two else (lambda ap: ap)
        lag = 2
        for k in range(KT + lag):
            if k < KT:
                src = view(self.src[:, k, self.t0:self.t1])
                g = self.gain[:, k:k + 1]
                y = view(K.Y[:, k, self.t0:self.t1])
                if self.out is None:
                    P.e.scalar_tensor_tensor(y, src, g, r, ALU.mult, ALU.mult).then_inc(P.sem("norm_scaled"), P.adds("norm_scaled"))
                elif self.add:
                    P.e.scalar_tensor_tensor(y, src, g, r, ALU.mult, ALU.mult).then_inc(P.sem("norm_term"), P.adds("norm_term"))
                else:
                    P.e.scalar_tensor_tensor(view(self.out[:, k, 0:self.t1 - self.t0]), src, g, r, ALU.mult, ALU.mult)
            if k >= lag:
                y = K.Y[:, k - lag, self.t0:self.t1]
                if self.out is None:
                    P.e.wait_ge(P.sem("norm_hi"), P.due("norm_hi"))
                    P.e.tensor_tensor(K.XL[:, k - lag, self.t0:self.t1], y,
                                      K.XH[:, k - lag, self.t0:self.t1].bitcast(F32), ALU.subtract).then_inc(P.sem("norm_lo"), P.adds("norm_lo"))
                elif self.add:
                    P.e.wait_ge(P.sem("norm_term"), P.due("norm_term", 0, less=min(lag, KT - 1 - (k - lag))))
                    o = self.out[:, k - lag, self.out_off + self.t0:self.out_off + self.t1]
                    P.e.tensor_tensor(o, o, y, ALU.add).then_inc(P.sem("sum_stored"), P.adds("sum_stored"))


class GatedUp(Wide):

    def __init__(self, n, first, conv=None):
        super().__init__(n, None, None)
        self.c0, self.conv = first, conv
        if conv is None:
            self.per_act = self.per_dve = {"hidden_hi": 1}
        else:
            self.per_act = {"conv_seeded": 2, "gate_activated": 1, "hidden_ready": 1, "hidden_hi": 1}
            self.per_dve = dict(self.per_act, dve_order=2)

    def evac_act(self, K, P, p, s, when):
        ps = [K.PS[:, 2 * (2 * s + t), 0:S] for t in range(2)]
        if when == "first":
            if self.conv is None:
                P.e.wait_ge(P.sem("tile_done"), P.due("tile_done"))
                P.e.activation(K.SG[:, s, :], ps[0], ACT.Silu).then_inc(P.sem("tile_evacuated0"), 1)
                P.e.wait_ge(P.sem("tile_done"), P.due("tile_done"))
                return
            w, b = self.conv
            for t in range(2):
                c = sl(t * FT + self.c0 + p)
                P.e.wait_ge(P.sem("tile_done"), P.due("tile_done"))
                P.e.activation(K.CV[:, s, t, :], ps[t], ACT.Identity, bias=b[:, c], scale=w[2][:, c]).then_inc(P.sem("conv_seeded"), P.adds("conv_seeded"))
            P.e.wait_ge(P.sem("tile_evacuated0"), P.due("tile_evacuated0", 0, less=-3))
            P.e.activation(K.SG[:, s, :], K.CV[:, s, 0, :], ACT.Silu).then_inc(P.sem("gate_activated"), P.adds("gate_activated"))
        else:
            if self.conv is None:
                P.e.wait_ge(P.sem("tile_evacuated1"), P.due("tile_evacuated1", 0, less=-3))
            else:
                P.e.wait_ge(P.sem("hidden_ready"), P.due("hidden_ready"))
            P.e.activation(K.HH[:, sl(p), :].rearrange("p a n -> p (a n)"), K.HF[:, s, :], ACT.Copy).then_inc(P.sem("hidden_hi"), P.adds("hidden_hi"))

    def evac_dve(self, K, P, p, s, when):
        ps = [K.PS[:, 2 * (2 * s + t), 0:S] for t in range(2)]
        if when == "first":
            P.e.wait_ge(P.sem("tile_done"), P.due("tile_done", 2))
            if self.conv is None:
                P.e.wait_ge(P.sem("tile_evacuated0"), P.due("tile_evacuated0", 0, less=-3))
                last = P.e.tensor_tensor(K.HF[:, s, :], K.SG[:, s, :], ps[1], ALU.mult)
                last.then_inc(P.sem("tile_evacuated1"), 1)
            else:
                w, b = self.conv
                for t in range(2):
                    c = sl(t * FT + self.c0 + p)
                    y = K.CV[:, s, t, :]
                    P.e.wait_ge(P.sem("conv_seeded"), P.due("conv_seeded"))
                    P.e.scalar_tensor_tensor(y[:, 1:S], ps[t][:, 0:S - 1], w[1][:, c], y[:, 1:S], ALU.mult, ALU.add).then_inc(P.sem("dve_order"), P.adds("dve_order"))
                    P.e.wait_ge(P.sem("dve_order"), P.due("dve_order", 0))
                    last = P.e.scalar_tensor_tensor(y[:, 2:S], ps[t][:, 0:S - 2], w[0][:, c], y[:, 2:S], ALU.mult, ALU.add)
                    last.then_inc(P.sem(f"tile_evacuated{t}"), 1)
                P.e.wait_ge(P.sem("tile_evacuated1"), P.due("tile_evacuated1", 0, less=-3))
                P.e.wait_ge(P.sem("gate_activated"), P.due("gate_activated"))
                P.e.tensor_tensor(K.HF[:, s, :], K.SG[:, s, :], K.CV[:, s, 1, :], ALU.mult).then_inc(P.sem("hidden_ready"), P.adds("hidden_ready"))
        else:
            P.e.wait_ge(P.sem("hidden_hi"), P.due("hidden_hi"))
            h = sl(p)
            P.e.tensor_tensor(K.HL[:, h, :].rearrange("p a n -> p (a n)"), K.HF[:, s, :],
                              K.HH[:, h, :].rearrange("p a n -> p (a n)").bitcast(F32), ALU.subtract)


class SquaredReluUp(Wide):

    per_act = per_dve = {"hidden_ready": 2, "hidden_hi": 2}

    def evac_act(self, K, P, p, s, when):
        if when == "first":
            for t in range(2):
                P.e.wait_ge(P.sem("tile_done"), P.due("tile_done"))
                P.e.activation(K.CV[:, s, t, :], K.PS[:, 2 * (2 * s + t), 0:S], ACT.Relu)\
                   .then_inc(P.sem(f"tile_evacuated{t}"), 1)
        else:
            for t in range(2):
                P.e.wait_ge(P.sem("hidden_ready"), P.due("hidden_ready"))
                P.e.activation(K.HH[:, sl(2 * p + t), :].rearrange("p a n -> p (a n)"), K.CF[:, s, t, :], ACT.Copy).then_inc(P.sem("hidden_hi"), P.adds("hidden_hi"))

    def evac_dve(self, K, P, p, s, when):
        if when == "first":
            for t in range(2):
                P.e.wait_ge(P.sem("tile_done"), P.due("tile_done"))
                P.e.wait_ge(P.sem(f"tile_evacuated{t}"), P.due(f"tile_evacuated{t}", 0, less=-3))
                P.e.tensor_tensor(K.CF[:, s, t, :], K.CV[:, s, t, :], K.CV[:, s, t, :], ALU.mult).then_inc(P.sem("hidden_ready"), P.adds("hidden_ready"))
        else:
            for t in range(2):
                P.e.wait_ge(P.sem("hidden_hi"), P.due("hidden_hi"))
                h = sl(2 * p + t)
                P.e.tensor_tensor(K.HL[:, h, :].rearrange("p a n -> p (a n)"), K.CF[:, s, t, :],
                                  K.HH[:, h, :].rearrange("p a n -> p (a n)").bitcast(F32), ALU.subtract)


class ForgetGates(Small):

    def pe(self, K, P):
        super().pe(K, P)
        P.e.matmul(K.PS[0:16, 7, 0:2], K.ident[:, 0:16], K.ident[:, 0:2], start=True, stop=True).then_inc(P.sem("gates_projected"), P.adds("gates_projected"))

    def act(self, K, P):
        g = K.gate_rows
        P.e.wait_ge(P.sem("gates_projected"), P.due("gates_projected"))
        P.e.activation(g[0:16, 0, :], K.PS[0:16, 0, 0:S], ACT.Abs, bias=K.att_b_f[0:16, 0:1]).then_inc(P.sem("act_order"), P.adds("act_order"))
        P.e.wait_ge(P.sem("act_order"), P.due("act_order", 0))
        P.e.activation(g[0:16, 0, :], g[0:16, 0, :], ACT.Exp, scale=-1.0).then_inc(P.sem("act_order"), P.adds("act_order"))
        P.e.wait_ge(P.sem("act_order"), P.due("act_order", 0))
        P.e.activation(g[0:16, 0, :], g[0:16, 0, :], ACT.Ln, bias=K.one_col[0:16, 0:1]).then_inc(P.sem("log_term"), P.adds("log_term"))

    def dve(self, K, P):
        g = K.gate_rows
        P.e.wait_ge(P.sem("gates_projected"), P.due("gates_projected"))
        P.e.wait_ge(P.sem("log_term"), P.due("log_term"))
        P.e.tensor_scalar(g[0:16, 1, :], K.PS[0:16, 0, 0:S], K.att_b_f[0:16, 0:1], 0.0, ALU.add, ALU.min).then_inc(P.sem("dve_order"), P.adds("dve_order"))
        P.e.wait_ge(P.sem("dve_order"), P.due("dve_order", 0))
        P.e.tensor_tensor(g[0:16, 1, :], g[0:16, 1, :], g[0:16, 0, :], ALU.subtract).then_inc(P.sem("dve_order"), P.adds("dve_order"))
        P.e.wait_ge(P.sem("dve_order"), P.due("dve_order", 0))
        P.e.tensor_tensor_scan(K.c_rows[0:16, :], K.ones_row[0:16, :], g[0:16, 1, :], 0.0, ALU.mult, ALU.add)


class ForgettingAttention(Stage):

    UNITS = [(pair, u, b) for pair in range(2) for u in range(2) for b in range(S // 128)]
    N = len(UNITS)

    def dve(self, K, P):
        def stage(t, pair):
            for u in range(2):
                h = sl(2 * t + u)
                last = P.e.tensor_scalar(K.ka[96:112, 2 * pair + u, :], K.c_rows[0:16, :], K.ident[0:16, h], -1.0, ALU.mult, ALU.mult)
            last.then_inc(P.sem("c_staged"), P.adds("c_staged"))

        def low_part(t, pair):
            P.e.wait_ge(P.sem("att_out_done"), P.due("att_out_done"))
            P.e.wait_ge(P.sem("att_out_hi"), P.due("att_out_hi"))
            P.e.tensor_tensor(flat(K.XL[:, sl(t), 0:S]), K.PS[:, (4, 7)[pair], 0:S], flat(K.XH[:, sl(t), 0:S]).bitcast(F32),
                              ALU.subtract).then_inc(P.sem("att_out_lo"), P.adds("att_out_lo"))

        def body(i, more=True):
            for n in range(self.N + 2):
                if n < self.N:
                    pair, u, b = self.UNITS[n]
                    s, nk = n % 3, 128 * (b + 1)
                    P.e.wait_ge(P.sem("logits_done"), P.due("logits_done"))
                    P.e.reduce_max(K.st[:, s, 0:1], K.PS[:, s, 0:nk], AX.X).then_inc(P.sem("dve_order"), P.adds("dve_order"))
                    P.e.wait_ge(P.sem("dve_order"), P.due("dve_order", 0))
                    P.e.tensor_scalar(K.st[:, s, 1:2], K.st[:, s, 0:1], -1.0, None, ALU.mult).then_inc(P.sem("max_negated"), P.adds("max_negated"))
                if 1 <= n <= self.N:
                    s, nk = (n - 1) % 3, 128 * (self.UNITS[n - 1][2] + 1)
                    P.e.wait_ge(P.sem("exp_done"), P.due("exp_done"))
                    P.e.reciprocal(K.st[:, s, 3:4], K.st[:, s, 2:3]).then_inc(P.sem("dve_order"), P.adds("dve_order"))
                    P.e.wait_ge(P.sem("dve_order"), P.due("dve_order", 0))
                    P.e.tensor_scalar(K.pr[:, s, 0:nk], K.pr[:, s, 0:nk], K.st[:, s, 3:4], None, ALU.mult).then_inc(P.sem("probs_ready"), P.adds("probs_ready"))
                if n >= 2:
                    s, nk = n % 2, 128 * (self.UNITS[n - 2][2] + 1)
                    P.e.wait_ge(P.sem("probs_transposed"), P.due("probs_transposed"))
                    P.e.tensor_copy(K.pT[:, s, 0:nk], K.PS[:, (3, 6)[s], 0:nk]).then_inc(P.sem("probsT_ready"), P.adds("probsT_ready"))
                if n % 8 == 4 and (n < 8 or more):
                    stage(2 * i + 1 + n // 8, 1 - n // 8)
                if n == 11:
                    low_part(2 * i, 0)
            low_part(2 * i + 1, 1)

        for x, ones in ((K.qa, slice(96, 112)), (K.ka, slice(64, 80))):
            P.e.memset(x[64:128, :, :], 0.0).then_inc(P.sem("dve_order"), P.adds("dve_order"))
            P.e.wait_ge(P.sem("dve_order"), P.due("dve_order", 0))
            for j in range(4):
                last = P.e.tensor_copy(x[ones, j, :], K.ones_row[ones, :])
            last.then_inc(P.sem("rows_filled"), P.adds("rows_filled"))
        P.e.wait_ge(P.sem("rows_filled"), P.due("rows_filled", 0))
        for pair in range(2):
            P.e.memset(K.zero_credit[:, pair:pair + 1], 0.0).then_inc(P.sem("att_out_lo"), P.adds("att_out_lo"))
        stage(0, 0)
        P.loop(3, body, dve_order=32, logits_done=16, max_negated=16, exp_done=16, probs_ready=16,
               probs_transposed=16, probsT_ready=16, c_staged=2, att_out_done=2, att_out_hi=2, att_out_lo=2)
        body(3, more=False)

    def act(self, K, P):
        def stage(t, pair):
            for u in range(2):
                half, j = slice(64 * u, 64 * u + 64), 2 * pair + u
                P.e.activation(K.qa[0:64, j, :], flat(K.q1[half, sl(t), :]), ACT.Copy, scale=0.125)
                P.e.activation(K.ka[0:64, j, :], flat(K.k1[half, sl(t), :]), ACT.Copy)
                last = P.e.activation(K.qa[64:80, j, :], K.c_rows[0:16, :], ACT.Copy, scale=K.ident[0:16, sl(2 * t + u)])
            last.then_inc(P.sem("qk_staged"), P.adds("qk_staged"))
            P.e.activation(K.vs[:, :], flat(K.v1[:, sl(t), :]), ACT.Copy).then_inc(P.sem("v_staged"), P.adds("v_staged"))

        def high_part(t, pair):
            P.e.wait_ge(P.sem("att_out_done"), P.due("att_out_done"))
            P.e.activation(flat(K.XH[:, sl(t), 0:S]), K.PS[:, (4, 7)[pair], 0:S], ACT.Copy).then_inc(P.sem("att_out_hi"), P.adds("att_out_hi"))

        def body(i, more=True):
            for n, (pair, u, b) in enumerate(self.UNITS):
                s, nk = n % 3, 128 * (b + 1)
                if n % 8 == 0:
                    P.e.wait_ge(P.sem("v_transposed"), P.due("v_transposed"))
                    P.e.activation(K.vT[:, pair, :], K.PS[:, 5, :], ACT.Copy).then_inc(P.sem("vT_ready"), P.adds("vT_ready"))
                P.e.wait_ge(P.sem("logits_done"), P.due("logits_done"))
                P.e.wait_ge(P.sem("max_negated"), P.due("max_negated"))
                P.e.activation(K.pr[:, s, 0:nk], K.PS[:, s, 0:nk], ACT.Exp, bias=K.st[:, s, 1:2],
                               accum_out=K.st[:, s, 2:3]).then_inc(P.sem("exp_done"), P.adds("exp_done"))
                if n % 8 == 4 and (n < 8 or more):
                    stage(2 * i + 1 + n // 8, 1 - n // 8)
                if n == 11:
                    high_part(2 * i, 0)
            high_part(2 * i + 1, 1)

        P.e.wait_ge(P.sem("rows_filled"), P.due("rows_filled", 2))
        stage(0, 0)
        P.loop(3, body, qk_staged=2, v_staged=2, v_transposed=2, vT_ready=2, logits_done=16, max_negated=16, exp_done=16,
               att_out_done=2, att_out_hi=2)
        body(3, more=False)

    def pe(self, K, P):
        def body(i):
            for n in range(self.N + 3):
                if n < self.N:
                    pair, u, b = self.UNITS[n]
                    j, s, nk, q = 2 * pair + u, n % 3, 128 * (b + 1), slice(128 * b, 128 * b + 128)
                    if n % 8 == 0:
                        P.e.wait_ge(P.sem("v_staged"), P.due("v_staged"))
                        for c in range(4):
                            last = P.e.transpose(K.PS[:, 5, 128 * c:128 * c + 128], K.vs[:, 128 * c:128 * c + 128], K.ident[:, :])
                        last.then_inc(P.sem("v_transposed"), P.adds("v_transposed"))
                        P.e.wait_ge(P.sem("qk_staged"), P.due("qk_staged"))
                        P.e.wait_ge(P.sem("c_staged"), P.due("c_staged"))
                    P.e.matmul(K.PS[:, s, 0:nk], K.qa[:, j, q], K.ka[:, j, 0:nk], start=True, stop=False)
                    P.e.matmul(K.PS[:, s, nk - 128:nk], K.ident[:, :], K.causal[:, :], start=False, stop=True).then_inc(P.sem("logits_done"), P.adds("logits_done"))
                if 2 <= n < self.N + 2:
                    m = n - 2
                    P.e.wait_ge(P.sem("probs_ready"), P.due("probs_ready"))
                    for kb in range(self.UNITS[m][2] + 1):
                        c = slice(128 * kb, 128 * kb + 128)
                        last = P.e.transpose(K.PS[:, (3, 6)[m % 2], c], K.pr[:, m % 3, c], K.ident[:, :])
                    last.then_inc(P.sem("probs_transposed"), P.adds("probs_transposed"))
                if n >= 3:
                    m = n - 3
                    pair, u, b = self.UNITS[m]
                    if m % 8 == 0:
                        P.e.wait_ge(P.sem("vT_ready"), P.due("vT_ready"))
                        P.e.wait_ge(P.sem("att_out_lo"), P.due("att_out_lo"))
                    P.e.wait_ge(P.sem("probsT_ready"), P.due("probsT_ready"))
                    for kb in range(b + 1):
                        last = P.e.matmul(K.PS[64 * u:64 * u + 64, (4, 7)[pair], 128 * b:128 * b + 128],
                                          K.vT[:, pair, 128 * kb + 64 * u:128 * kb + 64 * u + 64],
                                          K.pT[:, m % 2, 128 * kb:128 * kb + 128], start=(kb == 0), stop=(kb == b))
                    if m % 8 == 7:
                        last.then_inc(P.sem("att_out_done"), P.adds("att_out_done"))

        P.loop(4, body, v_staged=2, v_transposed=2, qk_staged=2, c_staged=2, logits_done=16,
               probs_ready=16, probs_transposed=16, probsT_ready=16, vT_ready=2, att_out_done=2, att_out_lo=2)
        P.count("att_out_lo", 2)
        P.count("exp_done", 4 * self.N)


class LowerBounds(Stage):

    def dve(self, K, P):
        a, b, m, t = K.lb_logits[:, 0:8], K.lb_logits[:, 8:16], K.lbt[:, 0:8], K.lbt
        P.e.tensor_tensor(m, a, b, ALU.max).then_inc(P.sem("dve_order"), P.adds("dve_order"))
        P.e.wait_ge(P.sem("dve_order"), P.due("dve_order", 0))
        P.e.tensor_tensor(t[:, 8:16], a, m, ALU.subtract)
        P.e.tensor_tensor(t[:, 16:24], b, m, ALU.subtract).then_inc(P.sem("lb_shifted"), P.adds("lb_shifted"))
        P.e.wait_ge(P.sem("lb_exp"), P.due("lb_exp"))
        P.e.tensor_tensor(t[:, 0:8], t[:, 8:16], t[:, 16:24], ALU.add).then_inc(P.sem("dve_order"), P.adds("dve_order"))
        P.e.wait_ge(P.sem("dve_order"), P.due("dve_order", 0))
        P.e.reciprocal(t[:, 0:8], t[:, 0:8]).then_inc(P.sem("dve_order"), P.adds("dve_order"))
        P.e.wait_ge(P.sem("dve_order"), P.due("dve_order", 0))
        P.e.tensor_tensor(K.lb[:, 0:8], t[:, 16:24], t[:, 0:8], ALU.mult)
        P.e.tensor_tensor(K.lb[:, 8:16], t[:, 8:16], t[:, 0:8], ALU.mult)

    def act(self, K, P):
        P.e.wait_ge(P.sem("lb_shifted"), P.due("lb_shifted"))
        P.e.activation(K.lbt[:, 8:24], K.lbt[:, 8:24], ACT.Exp).then_inc(P.sem("lb_exp"), P.adds("lb_exp"))


class Hgrn(Stage):

    def dve(self, K, P):
        def decays(t):
            P.e.tensor_scalar(K.h_k[:, :], flat(K.f1[:, sl(t), :]), 1.0, K.lbt[:, sl(t)], ALU.subtract, ALU.mult)
            P.e.wait_ge(P.sem("logf_ready"), P.due("logf_ready"))
            P.e.tensor_tensor_scan(K.h_b[:, :], K.reset64[:, :], flat(K.lf[:, sl(t), :]), 0.0, ALU.mult, ALU.add).then_inc(P.sem("dve_order"), P.adds("dve_order"))

        def to_chunk_end(b):
            P.e.wait_ge(P.sem("dve_order"), P.due("dve_order", 0))
            b3 = K.h_b[:, :].rearrange("p (n c) -> p n c", c=64)
            P.e.tensor_tensor(K.h_ks[:, b, :].rearrange("p (n c) -> p n c", c=64),
                              b3[:, :, 63:64].broadcast_to([128, 8, 64]), b3, ALU.subtract).then_inc(P.sem("b_ready"), P.adds("b_ready"))

        def keys(t, b):
            P.e.wait_ge(P.sem("exps_ready"), P.due("exps_ready"))
            P.e.tensor_tensor(K.h_ks[:, b, :], K.h_k[:, :], K.h_ks[:, b, :], ALU.mult)
            P.e.tensor_tensor(K.h_qd[:, b, :], flat(K.q1h[:, sl(t), :]), K.h_eb[:, b, :], ALU.mult)
            P.e.tensor_tensor(K.h_ki[:, b, :], K.h_k[:, :], K.h_ki[:, b, :], ALU.mult).then_inc(P.sem("keys_ready"), P.adds("keys_ready"))
            P.e.wait_ge(P.sem("keys_ready"), P.due("keys_ready", 0))

        def keep_mean(t):
            P.e.wait_ge(P.sem("o_mean"), P.due("o_mean"))
            P.e.tensor_copy(K.R[:, sl(4 * t, 4)], K.PS[:, 1, 0:8].rearrange("p (j c) -> p j c", c=2)[:, :, 0]).then_inc(P.sem("mean_kept"), P.adds("mean_kept"))

        def step(t, b, more=True, first=False):
            if more:
                decays(t + 1)
            P.e.wait_ge(P.sem("ksT_done"), P.due("ksT_done"))
            P.e.tensor_copy(K.ksT[:, :, :].rearrange("p n c -> p (n c)"), K.PS[:, 2, :]).then_inc(P.sem("ksT_ready"), P.adds("ksT_ready"))
            if more:
                to_chunk_end(1 - b)
            P.e.wait_ge(P.sem("A_done"), P.due("A_done"))
            P.e.tensor_tensor(K.aT[:, :], K.PS[:, 4, 0:256], K.causal64[:, 0:256], ALU.mult).then_inc(P.sem("A_ready"), P.adds("A_ready"))
            P.e.wait_ge(P.sem("U_done"), P.due("U_done"))
            for n in range(7):
                ins = P.e.scalar_tensor_tensor(K.sp[:, n + 1, :], K.sp[:, n, :], K.h_eb[:, b, 64 * n + 63:64 * n + 64],
                                               K.PS[:, 5 + n % 2, 128 * (n // 2):128 * (n // 2) + 128], ALU.mult, ALU.add)
                if n < 6:
                    ins.then_inc(P.sem("dve_order"), P.adds("dve_order"))
                    P.e.wait_ge(P.sem("dve_order"), P.due("dve_order", 0))
                else:
                    ins.then_inc(P.sem("states_ready"), P.adds("states_ready"))
            if more:
                keys(t + 1, 1 - b)
            if not first:
                keep_mean(t - 1)

        def body(i):
            step(2 * i + 2, 0)
            step(2 * i + 3, 1)

        P.e.memset(K.sp[:, 0, :], 0.0)
        P.e.tensor_scalar(K.lbt[:, 0:8], K.lb[:, 8:16], -1.0, None, ALU.mult).then_inc(P.sem("dve_order"), P.adds("dve_order"))
        P.e.wait_ge(P.sem("dve_order"), P.due("dve_order", 0))
        decays(0)
        to_chunk_end(0)
        keys(0, 0)
        step(0, 0, first=True)
        step(1, 1)
        P.loop(2, body, logf_ready=2, dve_order=14, b_ready=2, exps_ready=2, keys_ready=2, ksT_done=2, ksT_ready=2,
               A_done=2, A_ready=2, U_done=2, states_ready=2, o_mean=2, mean_kept=2)
        step(6, 0)
        step(7, 1, more=False)
        keep_mean(7)

        r = K.R[:, 0:32]
        P.e.wait_ge(P.sem("mean_kept"), P.due("mean_kept", 0))
        P.e.tensor_scalar(r, r, EPS, None, ALU.add).then_inc(P.sem("dve_order"), P.adds("dve_order"))
        P.e.wait_ge(P.sem("dve_order"), P.due("dve_order", 0))
        P.e.reciprocal(r, r).then_inc(P.sem("o_inverse"), P.adds("o_inverse"))
        P.e.wait_ge(P.sem("o_root"), P.due("o_root"))

        def diagonals(t):
            for j in range(4):
                last = P.e.tensor_scalar(K.diag[:, t % 2, 128 * j:128 * j + 128], K.ident[:, :], K.R[:, 4 * t + j:4 * t + j + 1], None, ALU.mult)
            last.then_inc(P.sem("o_diagonals"), P.adds("o_diagonals"))

        def low_part(t):
            P.e.wait_ge(P.sem("o_hi"), P.due("o_hi"))
            P.e.tensor_tensor(K.XL[:, t, 0:S], K.f1[:, t, :], K.XH[:, t, 0:S].bitcast(F32), ALU.subtract)

        diagonals(0)
        for t in range(8):
            if t < 7:
                diagonals(t + 1)
            P.e.wait_ge(P.sem("o_spread"), P.due("o_spread"))
            o = K.f1[:, t, :]
            P.e.scalar_tensor_tensor(o, o, K.p["hgrn_onorm_g"][:, t:t + 1], K.PS[:, 5 + t % 2, :], ALU.mult, ALU.mult).then_inc(P.sem("o_normed"), P.adds("o_normed"))
            P.e.wait_ge(P.sem("o_normed"), P.due("o_normed", 0))
            P.e.tensor_tensor(o, o, K.g1[:, t, :], ALU.mult).then_inc(P.sem("o_gated"), P.adds("o_gated"))
            if t:
                low_part(t - 1)
        low_part(7)

    def act(self, K, P):
        for t in range(8):
            P.e.activation(K.lf[:, t, :], K.f1[:, t, :], ACT.Ln, scale=K.lb[:, 8 + t:9 + t], bias=K.lb[:, t:t + 1]).then_inc(P.sem("logf_ready"), P.adds("logf_ready"))

        def stage(t):
            P.e.activation(K.h_i[:, :], flat(K.i1[:, sl(t), :]), ACT.Copy).then_inc(P.sem("i_staged"), P.adds("i_staged"))

        def exps(b):
            P.e.wait_ge(P.sem("b_ready"), P.due("b_ready"))
            P.e.activation(K.h_eb[:, b, :], K.h_b[:, :], ACT.Exp)
            P.e.activation(K.h_ki[:, b, :], K.h_b[:, :], ACT.Exp, scale=-1.0)
            P.e.activation(K.h_ks[:, b, :], K.h_ks[:, b, :], ACT.Exp).then_inc(P.sem("exps_ready"), P.adds("exps_ready"))

        def step(t, b, more=True):
            P.e.wait_ge(P.sem("iT_done"), P.due("iT_done"))
            P.e.activation(K.iT[:, :, :].rearrange("p n c -> p (n c)"), K.PS[:, 0, :], ACT.Copy).then_inc(P.sem("iT_ready"), P.adds("iT_ready"))
            if more:
                stage(t + 1)
                exps(1 - b)
            P.e.wait_ge(P.sem("o_done"), P.due("o_done"))
            for u in range(2):
                P.e.activation(K.halves(K.o_sq, u), K.halves_ps(u), ACT.Square)
                last = P.e.activation(flat(K.f1[:, sl(t), :]).rearrange("p (j u c) -> p u j c", u=2, c=64)[:, u], K.halves_ps(u), ACT.Copy)
            last.then_inc(P.sem("o_squared"), P.adds("o_squared"))

        def body(i):
            step(2 * i, 0)
            step(2 * i + 1, 1)

        stage(0)
        exps(0)
        P.loop(3, body, i_staged=2, b_ready=2, exps_ready=2, iT_done=2, iT_ready=2, o_done=2, o_squared=2)
        step(6, 0)
        step(7, 1, more=False)
        P.e.wait_ge(P.sem("o_inverse"), P.due("o_inverse"))
        P.e.activation(K.R[:, 0:32], K.R[:, 0:32], ACT.Sqrt).then_inc(P.sem("o_root"), P.adds("o_root"))
        for t in range(8):
            P.e.wait_ge(P.sem("o_gated"), P.due("o_gated"))
            P.e.activation(K.XH[:, t, 0:S], K.f1[:, t, :], ACT.Copy).then_inc(P.sem("o_hi"), P.adds("o_hi"))
        P.count("o_normed", 8)

    def pe(self, K, P):
        def means():
            P.e.wait_ge(P.sem("o_squared"), P.due("o_squared"))
            for j in range(4):
                last = P.e.matmul(K.PS[:, 1, 2 * j:2 * j + 2], K.o_sq[:, 128 * j:128 * j + 128], K.inv_dv[:, 0:2], start=True, stop=True)
            last.then_inc(P.sem("o_mean"), P.adds("o_mean"))

        def step(b, first=False):
            P.e.wait_ge(P.sem("i_staged"), P.due("i_staged"))
            for j in range(4):
                c = slice(128 * j, 128 * j + 128)
                last = P.e.transpose(K.PS[:, 0, c], K.h_i[:, c], K.ident[:, :])
            last.then_inc(P.sem("iT_done"), P.adds("iT_done"))
            P.e.wait_ge(P.sem("keys_ready"), P.due("keys_ready"))
            for j in range(4):
                c = slice(128 * j, 128 * j + 128)
                last = P.e.transpose(K.PS[:, 2, c], K.h_ks[:, b, c], K.ident[:, :])
            last.then_inc(P.sem("ksT_done"), P.adds("ksT_done"))
            chunks = [(n, slice(64 * (n % 2), 64 * (n % 2) + 64), n // 2, slice(64 * n, 64 * n + 64)) for n in range(8)]
            for n, half, j, c in chunks:
                last = P.e.matmul(K.PS[half, 4, 64 * j:64 * j + 64], K.h_ki[:, b, c], K.h_qd[:, b, c], start=True, stop=True)
            last.then_inc(P.sem("A_done"), P.adds("A_done"))
            P.e.wait_ge(P.sem("iT_ready"), P.due("iT_ready"))
            P.e.wait_ge(P.sem("ksT_ready"), P.due("ksT_ready"))
            for n, half, j, c in chunks[:7]:
                last = P.e.matmul(K.PS[:, 5 + n % 2, 128 * j:128 * j + 128], K.ksT[half, j, :], K.iT[half, j, :],
                                  start=True, stop=True)
            last.then_inc(P.sem("U_done"), P.adds("U_done"))
            if not first:
                means()
            P.e.wait_ge(P.sem("A_ready"), P.due("A_ready"))
            P.e.wait_ge(P.sem("states_ready"), P.due("states_ready"))
            for n, half, j, c in chunks:
                out = K.PS[:, (7, 3)[n % 2], 64 * j:64 * j + 64]
                P.e.matmul(out, K.iT[half, j, :], K.aT[half, 64 * j:64 * j + 64], start=True, stop=False)
                last = P.e.matmul(out, K.sp[:, n, :], K.h_qd[:, b, c], start=False, stop=True)
            last.then_inc(P.sem("o_done"), P.adds("o_done"))

        def body(i):
            step(0)
            step(1)

        step(0, first=True)
        step(1)
        P.loop(3, body, i_staged=2, iT_done=2, keys_ready=2, ksT_done=2, A_done=2, iT_ready=2, ksT_ready=2, U_done=2,
               A_ready=2, states_ready=2, o_done=2, o_squared=2, o_mean=2)
        P.e.wait_ge(P.sem("mean_kept"), P.due("mean_kept", 7))
        means()
        for t in range(8):
            P.e.wait_ge(P.sem("o_diagonals"), P.due("o_diagonals"))
            if t >= 2:
                P.e.wait_ge(P.sem("o_normed"), P.due("o_normed"))
            for j in range(4):
                c = slice(128 * j, 128 * j + 128)
                last = P.e.matmul(K.PS[:, 5 + t % 2, c], K.ones_row[:, 0:128], K.diag[:, t % 2, c], start=True, stop=True)
            last.then_inc(P.sem("o_spread"), P.adds("o_spread"))
        P.count("o_normed", 2)
        P.count("mean_kept", 1)


BIAS_W = 640


class Load(Stage):

    def __init__(self, loads):
        self.loads = loads

    def act(self, K, P):
        for dst, src in self.loads:
            P.e.dma_start(dst, src).then_inc(P.sem("inputs_loaded"), P.adds("inputs_loaded", 16))
        P.e.wait_ge(P.sem("inputs_loaded"), P.due("inputs_loaded", 0))


class BiasTable(Stage):

    def dve(self, K, P):
        P.e.memset(K.bias_t[32:33, :], NEG).then_inc(P.sem("bias_staged"), P.adds("bias_staged"))
        P.e.wait_ge(P.sem("bias_rows_done"), P.due("bias_rows_done"))
        P.e.tensor_copy(K.bias_rows[0:4, 0:512], K.PS[0:4, 0, :])
        P.e.tensor_copy(K.bias_rows[0:4, 512:BIAS_W], K.PS[0:4, 1, 0:BIAS_W - 512]).then_inc(P.sem("bias_rows_ready"), P.adds("bias_rows_ready"))
        lam = K.lam[:, :].rearrange("p (a b c) -> p a b c", a=2, b=2)
        P.e.tensor_tensor(K.lam_prod[:, :].rearrange("p (a c) -> p a c", a=2), lam[:, :, 0, :], lam[:, :, 1, :], ALU.mult).then_inc(P.sem("dve_order"), P.adds("dve_order"))
        P.e.wait_ge(P.sem("dve_order"), P.due("dve_order", 0))
        P.e.reduce_sum(K.lamt[:, 0:2], K.lam_prod[:, :].rearrange("p (a c) -> p a c", a=2), AX.X).then_inc(P.sem("lambda_dots"), P.adds("lambda_dots"))
        P.e.wait_ge(P.sem("lambda_exps"), P.due("lambda_exps"))
        P.e.tensor_tensor(K.lamt[:, 4:5], K.lamt[:, 3:4], K.lamt[:, 2:3], ALU.subtract).then_inc(P.sem("dve_order"), P.adds("dve_order"))
        P.e.wait_ge(P.sem("dve_order"), P.due("dve_order", 0))
        P.e.tensor_scalar(K.lamt[:, 5:6], K.lamt[:, 4:5], -0.2, None, ALU.add)

    def act(self, K, P):
        P.e.wait_ge(P.sem("lambda_dots"), P.due("lambda_dots"))
        P.e.activation(K.lamt[:, 2:4], K.lamt[:, 0:2], ACT.Exp).then_inc(P.sem("lambda_exps"), P.adds("lambda_exps"))
        P.e.wait_ge(P.sem("bias_rows_ready"), P.due("bias_rows_ready"))
        P.e.dma_start(K.bias_dram, K.bias_rows[0:4, :]).then_inc(P.sem("bias_moved"), P.adds("bias_moved", 16))
        P.e.wait_ge(P.sem("bias_moved"), P.due("bias_moved", 0))
        for h in range(4):
            src = bass.AP(tensor=K.bias_dram.tensor, offset=h * BIAS_W, ap=[[1, 128], [1, 512]])
            P.e.dma_start(K.bias[:, h, :], src).then_inc(P.sem("bias_moved"), P.adds("bias_moved", 16))
        P.e.wait_ge(P.sem("bias_moved"), P.due("bias_moved", 0))

    def pe(self, K, P):
        P.e.wait_ge(P.sem("bias_staged"), P.due("bias_staged"))
        P.e.matmul(K.PS[0:4, 0, :], K.bias_t[0:33, :], K.onehot[0:33, 0:512], start=True, stop=True)
        P.e.matmul(K.PS[0:4, 1, 0:BIAS_W - 512], K.bias_t[0:33, :], K.onehot[0:33, 512:BIAS_W], start=True, stop=True).then_inc(P.sem("bias_rows_done"), P.adds("bias_rows_done"))


class DiffAttention(Stage):

    UNITS = [(h, b) for h in range(4) for b in range(4)]
    N = len(UNITS)

    def act(self, K, P):
        def stage(h):
            for m in range(2):
                half = slice(64 * m, 64 * m + 64)
                P.e.activation(K.d_q[0:64, h % 2, m, :], K.in2[half, h, :], ACT.Copy, scale=0.125)
                last = P.e.activation(K.d_k[0:64, h % 2, m, :], K.in2[half, h + 4, :], ACT.Copy)
            last.then_inc(P.sem("qk_staged"), P.adds("qk_staged"))

        def take_out(h):
            P.e.wait_ge(P.sem("att_out_done"), P.due("att_out_done"))
            P.e.activation(K.in2[:, h, :], K.PS[:, (4, 7)[h % 2], :], ACT.Copy)
            P.e.activation(K.d_sq[:, :], K.PS[:, (4, 7)[h % 2], :], ACT.Square).then_inc(P.sem("o_squared"), P.adds("o_squared"))

        stage(0)
        for n, (h, b) in enumerate(self.UNITS):
            nk = 128 * (b + 1)
            if b == 0:
                P.e.wait_ge(P.sem("v_transposed"), P.due("v_transposed"))
                P.e.activation(K.d_vT[:, h % 2, :], K.PS[:, (4, 7)[h % 2], :], ACT.Copy).then_inc(P.sem("vT_ready"), P.adds("vT_ready"))
            for m in range(2):
                P.e.wait_ge(P.sem("logits_done"), P.due("logits_done"))
                P.e.wait_ge(P.sem("max_negated"), P.due("max_negated"))
                P.e.activation(K.d_p[:, m, n % 3, 0:nk], K.PS[:, 2 * (n % 2) + m, 0:nk], ACT.Exp, bias=K.d_st[:, n % 3, m, 1:2],
                               accum_out=K.d_st[:, n % 3, m, 2:3]).then_inc(P.sem("exp_done"), P.adds("exp_done"))
            if b == 1 and h < 3:
                stage(h + 1)
            if b == 2 and h:
                take_out(h - 1)
        take_out(3)

        P.e.wait_ge(P.sem("conv_z"), P.due("conv_z"))
        for i in range(4):
            P.e.activation(K.in2[:, 20 + i, :], K.in2[:, 16 + i, :], ACT.Copy, scale=K.p["conv2_w2"][:, i:i + 1]).then_inc(P.sem("conv_seeded"), P.adds("conv_seeded"))
        P.e.wait_ge(P.sem("o_inverse"), P.due("o_inverse"))
        P.e.activation(K.R[:, 0:16], K.R[:, 0:16], ACT.Sqrt).then_inc(P.sem("o_root"), P.adds("o_root"))
        P.e.wait_ge(P.sem("conv_gated"), P.due("conv_gated"))
        P.e.activation(K.XH[:, 4:8, 0:S], K.in2[:, 16:20, :], ACT.Copy).then_inc(P.sem("conv_hi"), P.adds("conv_hi"))
        for h in range(4):
            P.e.wait_ge(P.sem("o_normed"), P.due("o_normed"))
            P.e.activation(K.XH[:, h, 0:S], K.in2[:, h, :], ACT.Copy).then_inc(P.sem("o_hi"), P.adds("o_hi"))

    def dve(self, K, P):
        e = P.e
        for n in range(self.N + 2):
            if n >= 8 and n % 4 == 0:
                self.keep_mean(K, P, n // 4 - 2)
            if n < self.N:
                h, b = self.UNITS[n]
                nk, st = 128 * (b + 1), K.d_st[:, n % 3]
                for m in range(2):
                    P.e.wait_ge(P.sem("logits_done"), P.due("logits_done"))
                    e.reduce_max(st[:, m, 0:1], K.PS[:, 2 * (n % 2) + m, 0:nk], AX.X).then_inc(P.sem("dve_order"), P.adds("dve_order"))
                    P.e.wait_ge(P.sem("dve_order"), P.due("dve_order", 0))
                    e.tensor_scalar(st[:, m, 1:2], st[:, m, 0:1], -1.0, None, ALU.mult).then_inc(P.sem("max_negated"), P.adds("max_negated"))
            if 1 <= n <= self.N:
                nk, st = 128 * (self.UNITS[n - 1][1] + 1), K.d_st[:, (n - 1) % 3]
                p0, p1 = (K.d_p[:, m, (n - 1) % 3, 0:nk] for m in range(2))
                P.e.wait_ge(P.sem("exp_done"), P.due("exp_done", 2))
                e.reciprocal(st[:, :, 3:4], st[:, :, 2:3]).then_inc(P.sem("dve_order"), P.adds("dve_order"))
                P.e.wait_ge(P.sem("dve_order"), P.due("dve_order", 0))
                e.tensor_scalar(p0, p0, st[:, 0, 3:4], None, ALU.mult)
                e.tensor_scalar(st[:, 1, 3:4], st[:, 1, 3:4], K.lamt[:, 5:6], None, ALU.mult).then_inc(P.sem("dve_order"), P.adds("dve_order"))
                P.e.wait_ge(P.sem("dve_order"), P.due("dve_order", 0))
                e.scalar_tensor_tensor(p0, p1, st[:, 1, 3:4], p0, ALU.mult, ALU.add).then_inc(P.sem("probs_ready"), P.adds("probs_ready"))
            if n >= 2:
                nk = 128 * (self.UNITS[n - 2][1] + 1)
                P.e.wait_ge(P.sem("probs_transposed"), P.due("probs_transposed"))
                e.tensor_copy(K.d_pT[:, n % 2, 0:nk], K.PS[:, 5 + n % 2, 0:nk]).then_inc(P.sem("probsT_ready"), P.adds("probsT_ready"))
        e.tensor_tensor(K.in2[:, 16:20, :], K.in2[:, 16:20, :], K.in2[:, 20:24, :], ALU.mult).then_inc(P.sem("conv_z"), P.adds("conv_z"))
        self.keep_mean(K, P, 3)
        r = K.R[:, 0:16]
        P.e.wait_ge(P.sem("mean_kept"), P.due("mean_kept", 0))
        e.tensor_scalar(r, r, 1e-5, None, ALU.add).then_inc(P.sem("dve_order"), P.adds("dve_order"))
        P.e.wait_ge(P.sem("dve_order"), P.due("dve_order", 0))
        e.reciprocal(r, r).then_inc(P.sem("o_inverse"), P.adds("o_inverse"))
        for i in range(4):
            z, y = K.in2[:, 16 + i, :], K.in2[:, 20 + i, :]
            P.e.wait_ge(P.sem("conv_seeded"), P.due("conv_seeded"))
            e.scalar_tensor_tensor(y[:, 1:S], z[:, 0:S - 1], K.p["conv2_w1"][:, i:i + 1], y[:, 1:S], ALU.mult, ALU.add).then_inc(P.sem("dve_order"), P.adds("dve_order"))
            P.e.wait_ge(P.sem("dve_order"), P.due("dve_order", 0))
            e.scalar_tensor_tensor(y[:, 2:S], z[:, 0:S - 2], K.p["conv2_w0"][:, i:i + 1], y[:, 2:S], ALU.mult, ALU.add).then_inc(P.sem("dve_order"), P.adds("dve_order"))
        P.e.wait_ge(P.sem("dve_order"), P.due("dve_order", 0))
        e.tensor_tensor(K.in2[:, 16:20, :], K.in2[:, 20:24, :], K.in2[:, 12:16, :], ALU.mult).then_inc(P.sem("conv_gated"), P.adds("conv_gated"))
        P.e.wait_ge(P.sem("o_root"), P.due("o_root"))
        e.tensor_scalar(r, r, 0.8, None, ALU.mult).then_inc(P.sem("dve_order"), P.adds("dve_order"))
        P.e.wait_ge(P.sem("dve_order"), P.due("dve_order", 0))
        for h in range(4):
            for j in range(4):
                last = e.tensor_scalar(K.d_diag[:, h, 128 * j:128 * j + 128], K.ident[:, :], K.R[:, 4 * h + j:4 * h + j + 1], None, ALU.mult)
            last.then_inc(P.sem("o_diagonals"), P.adds("o_diagonals"))
        for h in range(4):
            P.e.wait_ge(P.sem("o_spread"), P.due("o_spread"))
            o = K.in2[:, h, :]
            e.scalar_tensor_tensor(o, o, K.p["subln_g"][:, 0:1], K.PS[:, h, :], ALU.mult, ALU.mult).then_inc(P.sem("o_normed"), P.adds("o_normed"))
        P.e.wait_ge(P.sem("conv_hi"), P.due("conv_hi"))
        e.tensor_tensor(K.XL[:, 4:8, 0:S], K.in2[:, 16:20, :], K.XH[:, 4:8, 0:S].bitcast(F32), ALU.subtract)
        for h in range(4):
            P.e.wait_ge(P.sem("o_hi"), P.due("o_hi"))
            e.tensor_tensor(K.XL[:, h, 0:S], K.in2[:, h, :], K.XH[:, h, 0:S].bitcast(F32), ALU.subtract)
        P.count("att_out_done", 4)

    def keep_mean(self, K, P, h):
        P.e.wait_ge(P.sem("o_mean"), P.due("o_mean"))
        P.e.tensor_copy(K.R[:, 4 * h:4 * h + 4], K.PS[:, (4, 7)[h % 2], 0:8].rearrange("p (j c) -> p j c", c=2)[:, :, 0]).then_inc(P.sem("mean_kept"), P.adds("mean_kept"))

    def pe(self, K, P):
        def means(h):
            P.e.wait_ge(P.sem("o_squared"), P.due("o_squared"))
            for j in range(4):
                last = P.e.matmul(K.PS[:, (4, 7)[h % 2], 2 * j:2 * j + 2], K.d_sq[:, 128 * j:128 * j + 128], K.inv_dv[:, 0:2], start=True, stop=True)
            last.then_inc(P.sem("o_mean"), P.adds("o_mean"))

        for n in range(self.N + 3):
            if n < self.N:
                h, b = self.UNITS[n]
                nk = 128 * (b + 1)
                if b == 0:
                    if h >= 2:
                        P.e.wait_ge(P.sem("mean_kept"), P.due("mean_kept"))
                    for j in range(4):
                        last = P.e.transpose(K.PS[:, (4, 7)[h % 2], 128 * j:128 * j + 128], K.in2[:, h + 8, 128 * j:128 * j + 128], K.ident[:, :])
                    last.then_inc(P.sem("v_transposed"), P.adds("v_transposed"))
                    P.e.wait_ge(P.sem("qk_staged"), P.due("qk_staged"))
                if n >= 2:
                    P.e.wait_ge(P.sem("exp_done"), P.due("exp_done", 2))
                for m in range(2):
                    out = K.PS[:, 2 * (n % 2) + m, 0:nk]
                    P.e.matmul(out, K.d_q[0:64, h % 2, m, 128 * b:128 * b + 128], K.d_k[0:64, h % 2, m, 0:nk], start=True, stop=False)
                    P.e.matmul(out, K.flip[:, :], K.bias[:, h, 512 - nk:512], start=False, stop=True).then_inc(P.sem("logits_done"), P.adds("logits_done"))
            if 2 <= n < self.N + 2:
                m = n - 2
                P.e.wait_ge(P.sem("probs_ready"), P.due("probs_ready"))
                for kb in range(self.UNITS[m][1] + 1):
                    c = slice(128 * kb, 128 * kb + 128)
                    last = P.e.transpose(K.PS[:, 5 + m % 2, c], K.d_p[:, 0, m % 3, c], K.ident[:, :])
                last.then_inc(P.sem("probs_transposed"), P.adds("probs_transposed"))
            if n >= 3:
                h, b = self.UNITS[n - 3]
                if b == 0:
                    P.e.wait_ge(P.sem("vT_ready"), P.due("vT_ready"))
                P.e.wait_ge(P.sem("probsT_ready"), P.due("probsT_ready"))
                for kb in range(b + 1):
                    c = slice(128 * kb, 128 * kb + 128)
                    last = P.e.matmul(K.PS[:, (4, 7)[h % 2], 128 * b:128 * b + 128], K.d_vT[:, h % 2, c],
                                      K.d_pT[:, (n - 3) % 2, c], start=(kb == 0), stop=(kb == b))
                if b == 3:
                    last.then_inc(P.sem("att_out_done"), P.adds("att_out_done"))
            if n >= 7 and n % 4 == 3:
                means(n // 4 - 1)
        P.count("exp_done", 4)
        means(3)
        for h in range(4):
            P.e.wait_ge(P.sem("o_diagonals"), P.due("o_diagonals"))
            for j in range(4):
                c = slice(128 * j, 128 * j + 128)
                last = P.e.matmul(K.PS[:, h, c], K.ones_row[:, 0:128], K.d_diag[:, h, c], start=True, stop=True)
            last.then_inc(P.sem("o_spread"), P.adds("o_spread"))
        P.count("mean_kept", 2)


class CentreV(Stage):

    def pe(self, K, P):
        for k in range(KT):
            last = P.e.matmul(K.PS[:, 0, :], K.inv_d[:, :], K.v2[:, k, :], start=(k == 0), stop=(k == KT - 1))
        last.then_inc(P.sem("v_mean"), P.adds("v_mean"))
        for k in range(KT):
            P.e.wait_ge(P.sem("v_squared"), P.due("v_squared"))
            last = P.e.matmul(K.PS[:, 1, :], K.inv_d[:, :], K.Y[:, k, 0:S], start=(k == 0), stop=(k == KT - 1))
        last.then_inc(P.sem("norm_mean"), P.adds("norm_mean"))

    def act(self, K, P):
        for k in range(KT):
            P.e.wait_ge(P.sem("v_centred"), P.due("v_centred"))
            P.e.activation(K.Y[:, k, 0:S], K.v2[:, k, :], ACT.Square).then_inc(P.sem("v_squared"), P.adds("v_squared"))
        P.e.wait_ge(P.sem("norm_inverse"), P.due("norm_inverse"))
        P.e.activation(K.R[:, 0:S], K.R[:, 0:S], ACT.Sqrt).then_inc(P.sem("norm_root"), P.adds("norm_root"))

    def dve(self, K, P):
        P.e.wait_ge(P.sem("v_mean"), P.due("v_mean"))
        for k in range(KT):
            P.e.tensor_tensor(K.v2[:, k, :], K.v2[:, k, :], K.PS[:, 0, :], ALU.subtract).then_inc(P.sem("v_centred"), P.adds("v_centred"))
        P.e.tensor_tensor(K.ws[:, :, :], K.ws[:, :, :],
                          K.keep_upper[:, :].rearrange("p (a n) -> p a n", a=1).broadcast_to([128, 8, 128]), ALU.mult)
        P.e.wait_ge(P.sem("norm_mean"), P.due("norm_mean"))
        P.e.tensor_scalar(K.R[:, 0:S], K.PS[:, 1, :], 1e-5, None, ALU.add).then_inc(P.sem("dve_order"), P.adds("dve_order"))
        P.e.wait_ge(P.sem("dve_order"), P.due("dve_order", 0))
        P.e.reciprocal(K.R[:, 0:S], K.R[:, 0:S]).then_inc(P.sem("norm_inverse"), P.adds("norm_inverse"))
        P.e.wait_ge(P.sem("norm_root"), P.due("norm_root"))


class SpatialGate(Stage):

    def dve(self, K, P):
        def scaled(t):
            v = K.v2[:, t, :]
            P.e.scalar_tensor_tensor(v, v, K.p["sgu_ln_g"][:, t:t + 1], K.R[:, 0:S], ALU.mult, ALU.mult).then_inc(P.sem("sgu_scaled"), P.adds("sgu_scaled"))

        scaled(0)
        scaled(1)
        for t in range(KT + 2):
            if t + 2 < KT:
                scaled(t + 2)
            if t < KT:
                P.e.wait_ge(P.sem("sgu_transposed"), P.due("sgu_transposed"))
                P.e.tensor_copy(K.s_vT[:, t % 2, :], K.PS[:, t % 2, :]).then_inc(P.sem("sgu_vT"), P.adds("sgu_vT"))
            if 1 <= t <= KT:
                P.e.wait_ge(P.sem("sgu_mixed"), P.due("sgu_mixed"))
                P.e.tensor_tensor(K.v2[:, t - 1, :], K.PS[:, 2 + (t - 1) % 2, :], K.u2[:, t - 1, :], ALU.mult).then_inc(P.sem("sgu_gated"), P.adds("sgu_gated"))
            if t >= 2:
                P.e.wait_ge(P.sem("sgu_hi"), P.due("sgu_hi"))
                P.e.tensor_tensor(K.XL[:, t - 2, 0:S], K.v2[:, t - 2, :], K.XH[:, t - 2, 0:S].bitcast(F32), ALU.subtract)

    def act(self, K, P):
        for t in range(KT + 2):
            if t < KT:
                v = K.v2[:, t, :]
                P.e.wait_ge(P.sem("sgu_scaled"), P.due("sgu_scaled"))
                P.e.activation(v, v, ACT.Identity, bias=K.p["sgu_ln_b"][:, t:t + 1]).then_inc(P.sem("sgu_normed"), P.adds("sgu_normed"))
            if t >= 2:
                P.e.wait_ge(P.sem("sgu_gated"), P.due("sgu_gated"))
                P.e.activation(K.XH[:, t - 2, 0:S], K.v2[:, t - 2, :], ACT.Copy).then_inc(P.sem("sgu_hi"), P.adds("sgu_hi"))

    def pe(self, K, P):
        for t in range(KT + 1):
            if t < KT:
                P.e.wait_ge(P.sem("sgu_normed"), P.due("sgu_normed"))
                for n in range(4):
                    c = slice(128 * n, 128 * n + 128)
                    last = P.e.transpose(K.PS[:, t % 2, c], K.v2[:, t, c], K.ident[:, :])
                last.then_inc(P.sem("sgu_transposed"), P.adds("sgu_transposed"))
            if t:
                P.e.wait_ge(P.sem("sgu_vT"), P.due("sgu_vT"))
                if t >= 3:
                    P.e.wait_ge(P.sem("sgu_gated"), P.due("sgu_gated"))
                for n in range(4):
                    c = slice(128 * n, 128 * n + 128)
                    out = K.PS[:, 2 + (t - 1) % 2, c]
                    P.e.matmul(out, K.s_vT[:, (t - 1) % 2, c], K.ws[:, t - 1, :], start=True, stop=False)
                    last = P.e.matmul(out, K.one_row2[0:1, 0:128], K.sgu_b[0:1, t - 1, :], start=False, stop=True)
                last.then_inc(P.sem("sgu_mixed"), P.adds("sgu_mixed"))


def ffn2(K, layer):
    g = [K.p[f"norm2_g{layer}{j}"] for j in range(4)]
    st = [RmsNorm(K.X, g[2])]
    for c0, n in FFN_CHUNKS:
        up = GatedUp(n, c0)
        up.xh, up.xl = K.XH, K.XL
        st += [up, Narrow(n, K.HH, K.HL, K.F, add=c0 > 0)]
    return st + [RmsNorm(K.F, g[3], out=K.X, add=True)]


def block2(K):
    g = [[K.p[f"norm2_g{i}{j}"] for j in range(4)] for i in range(2)]
    st = [Load(K.loads2), RmsNorm(K.X, g[0][0]), Store(12, K.XH, K.XL, K.in2), BiasTable(), DiffAttention(),
          Narrow(8, K.XH, K.XL, K.F, add=False), RmsNorm(K.F, g[0][1], out=K.X, add=True)] + ffn2(K, 0)
    st += [Load(K.loads2b), RmsNorm(K.X, g[1][0]), Store(8, K.XH, K.XL, K.uv2, func=ACT.Gelu), CentreV(), SpatialGate(),
           Narrow(8, K.XH, K.XL, K.F, add=False), RmsNorm(K.F, g[1][1], out=K.X, add=True)] + ffn2(K, 1)
    return st


def specs2():
    v = [("subln_g", "diff_subln_g_2", 0), ("sgu_ln_g", "sgu_ln_g_2", 0), ("sgu_ln_b", "sgu_ln_b_2", 0)]
    v += [(f"norm2_g{i}{j}", "norm_g_2", (i, j)) for i in range(2) for j in range(4)]
    return v + [(f"conv2_w{j}", "conv_w_2", (0, j)) for j in range(3)]


def weights2(a):
    out = [wide_panels(a["w_in_even_2"][0]), narrow_panels(a["w_out_even_2"][0])]
    out += ffn_panels(a["w_gate_2"][0], a["w_up_2"][0], a["w_down_2"][0], FFN_CHUNKS)
    out += [wide_panels(a["w_in_odd_2"][0]), narrow_panels(a["w_out_odd_2"][0])]
    return out + ffn_panels(a["w_gate_2"][1], a["w_up_2"][1], a["w_down_2"][1], FFN_CHUNKS)


def bucket_onehot():
    n = 511 - np.arange(BIAS_W)
    nf = np.maximum(n, 1).astype(np.float32)
    large = 16 + (np.log(nf / np.float32(16)) / np.float32(np.log(8.0)) * np.float32(16)).astype(np.int32)
    b = np.where(n < 0, 32, np.where(n < 16, n, np.minimum(large, 31)))
    return (b[None, :] == np.arange(33)[:, None]).astype(np.float32)


T3 = ((0, TM // 2), (TM // 2, TM // 2))
HALF_T = TM // 2
N_CHUNK = TM // 16
DECAY = float(np.exp(-0.5))


def flat(ap):
    return ap.rearrange("p a n -> p (a n)")


def both_parts(K, bank, lo=0, hi=128):
    return K.PS[lo:hi, bank:bank + 2, 0:HALF_T]


def parts(ap):
    return ap.rearrange("p (a n) -> p a n", a=2)


class GateRows(Stage):

    def pe(self, K, P):
        for m, (c0, cn) in enumerate(((0, 128), (128, 32))):
            for part, (t0, tn) in enumerate(T3):
                for k in range(KT):
                    last = P.e.matmul(K.PS[0:cn, 2 * m + part, 0:tn], K.w_gd[:, k, c0:c0 + cn], K.Y[:, k, t0:t0 + tn],
                                      start=(k == 0), stop=(k == KT - 1))
        last.then_inc(P.sem("gate_rows_done"), P.adds("gate_rows_done"))

    def dve(self, K, P):
        P.e.wait_ge(P.sem("gate_rows_done"), P.due("gate_rows_done"))
        P.e.tensor_copy(parts(K.rp[:, 14, :]), both_parts(K, 0))
        P.e.tensor_copy(parts(K.rp[0:32, 15, :]), both_parts(K, 2, 0, 32))


class CentredShift(Stage):

    def dve(self, K, P):
        mu0, mu1, c = K.mu[:, :, 0], K.mu[:, :, 1], K.mu_rest
        areas = ((slice(0, 128), slice(0, 15)), (slice(0, 32), slice(15, 16)))
        for r, q in areas:
            P.e.tensor_tensor(c[r, q], mu0[r, q], mu1[r, q], ALU.add).then_inc(P.sem("dve_order"), P.adds("dve_order"))
            P.e.wait_ge(P.sem("dve_order"), P.due("dve_order", 0))
        for r, q in areas:
            P.e.tensor_scalar(c[r, q], c[r, q], -1.0, 1.0, ALU.mult, ALU.add).then_inc(P.sem("shift_weights"), P.adds("shift_weights"))
        for q in range(16):
            r = slice(0, 128 if q < 15 else 32)
            P.e.wait_ge(P.sem("shift_seeded"), P.due("shift_seeded"))
            z, p = K.rz[r, q, :], K.rp[r, q, :]
            P.e.scalar_tensor_tensor(z[:, 1:TM], p[:, 0:TM - 1], mu0[r, q:q + 1], z[:, 1:TM], ALU.mult, ALU.add).then_inc(P.sem("dve_order"), P.adds("dve_order"))
            P.e.wait_ge(P.sem("dve_order"), P.due("dve_order", 0))
            P.e.scalar_tensor_tensor(z[:, 0:TM - 1], p[:, 1:TM], mu1[r, q:q + 1], z[:, 0:TM - 1], ALU.mult, ALU.add)

    def act(self, K, P):
        P.e.wait_ge(P.sem("shift_weights"), P.due("shift_weights", 2))
        for q in range(16):
            r = slice(0, 128 if q < 15 else 32)
            P.e.activation(K.rz[r, q, :], K.rp[r, q, :], ACT.Copy, scale=K.mu_rest[r, q:q + 1]).then_inc(P.sem("shift_seeded"), P.adds("shift_seeded"))


class RwkvPrepare(Stage):

    def act(self, K, P):
        P.e.activation(K.rz[:, 12, :], K.rz[:, 12, :], ACT.Tanh).then_inc(P.sem("wd_tanh"), P.adds("wd_tanh"))
        def square(q):
            P.e.wait_ge(P.sem("kk_scaled"), P.due("kk_scaled"))
            P.e.activation(K.t_n[:, :], K.t_kk[q % 2][:, :], ACT.Square).then_inc(P.sem("kk_squared"), P.adds("kk_squared"))

        def root():
            P.e.wait_ge(P.sem("kk_sumsq"), P.due("kk_sumsq"))
            P.e.activation(K.t_n[:, :], K.t_n[:, :], ACT.Sqrt).then_inc(P.sem("kk_norm"), P.adds("kk_norm"))

        square(0)
        root()
        for q in range(4):
            if q < 3:
                square(q + 1)
            for d in range(2):
                P.e.wait_ge(P.sem("lora_done"), P.due("lora_done", 2))
                P.e.activation(parts(K.t_s[:, d, :]), both_parts(K, 2 * d), ACT.Sigmoid, bias=K.p[f"decay_w0{d}"][:, q:q + 1])
                P.e.activation(parts(K.t_a[:, d, :]), both_parts(K, 4 + 2 * d), ACT.Sigmoid,
                                     bias=K.p[f"icl_a0{d}"][:, q:q + 1]).then_inc(P.sem("gates_open"), P.adds("gates_open"))
            if q < 3:
                root()
            for d in range(2):
                P.e.wait_ge(P.sem("decay_cumulated"), P.due("decay_cumulated"))
                P.e.activation(K.t_s[:, d, :], K.t_bi[:, :], ACT.Exp)
                P.e.activation(K.wc[:, d, q, :], K.t_bc[:, :], ACT.Exp)
                P.e.activation(K.t_en[:, :], K.t_bi[:, :], ACT.Exp, scale=-1.0)
                P.e.activation(K.t_bx[:, :], K.t_bx[:, :], ACT.Exp).then_inc(P.sem("decay_exps"), P.adds("decay_exps"))
                P.e.wait_ge(P.sem("direction_done"), P.due("direction_done"))

    def pe(self, K, P):
        def head_sums():
            P.e.wait_ge(P.sem("kk_squared"), P.due("kk_squared"))
            for part, (t0, tn) in enumerate(T3):
                last = P.e.matmul(K.PS[:, part, 0:tn], K.head_ones[:, :], K.t_n[:, t0:t0 + tn], start=True, stop=True)
            last.then_inc(P.sem("kk_summed"), P.adds("kk_summed"))

        head_sums()
        P.e.wait_ge(P.sem("wd_tanh"), P.due("wd_tanh"))
        P.e.wait_ge(P.sem("kk_sumsq"), P.due("kk_sumsq"))
        for q in range(4):
            if q:
                P.e.wait_ge(P.sem("direction_done"), P.due("direction_done", 2))
                P.e.wait_ge(P.sem("bonus_done"), P.due("bonus_done"))
            c = slice(128 * q, 128 * q + 128)
            for d in range(2):
                rows = slice(64 * d, 64 * d + 64)
                for w, tile, bank in ((K.w2, 12, 2 * d), (K.a2, 13, 4 + 2 * d)):
                    for part, (t0, tn) in enumerate(T3):
                        last = P.e.matmul(K.PS[:, bank + part, 0:tn], w[rows, c], K.rz[rows, tile, t0:t0 + tn], start=True, stop=True)
                    last.then_inc(P.sem("lora_done"), P.adds("lora_done"))
            if q < 3:
                P.e.wait_ge(P.sem("gates_open"), P.due("gates_open"))
                P.count("gates_open", 1)
                head_sums()
            P.e.wait_ge(P.sem("bonus_product"), P.due("bonus_product"))
            for part, (t0, tn) in enumerate(T3):
                last = P.e.matmul(K.PS[:, 2 + part, 0:tn], K.head_ones[:, :], K.t_u[:, t0:t0 + tn], start=True, stop=True)
            last.then_inc(P.sem("bonus_summed"), P.adds("bonus_summed"))

    def dve(self, K, P):
        e = P.e

        def scale(q):
            P.e.wait_ge(P.sem("bonus_done"), P.due("bonus_done", 0))
            e.tensor_scalar(K.t_kk[q % 2][:, :], K.rz[:, 4 + q, :], K.p["k_k"][:, q:q + 1], None, ALU.mult).then_inc(P.sem("kk_scaled"), P.adds("kk_scaled"))

        def sums():
            P.e.wait_ge(P.sem("kk_summed"), P.due("kk_summed"))
            e.tensor_scalar(parts(K.t_n[:, :]), both_parts(K, 0), 1e-24, None, ALU.max).then_inc(P.sem("kk_sumsq"), P.adds("kk_sumsq"))

        def normalise(q):
            kk = K.t_kk[q % 2][:, :]
            P.e.wait_ge(P.sem("kk_norm"), P.due("kk_norm"))
            e.reciprocal(K.t_n[:, :], K.t_n[:, :]).then_inc(P.sem("dve_order"), P.adds("dve_order"))
            P.e.wait_ge(P.sem("dve_order"), P.due("dve_order", 0))
            e.tensor_tensor(kk, kk, K.t_n[:, :], ALU.mult).then_inc(P.sem("kk_unit"), P.adds("kk_unit"))
            P.e.wait_ge(P.sem("kk_unit"), P.due("kk_unit", 0))

        scale(0)
        sums()
        normalise(0)
        scale(1)
        for q in range(4):
            kk = K.t_kk[q % 2]
            vec = lambda n: K.p[n][:, q:q + 1]
            r, k, v = K.rz[:, q, :], K.rz[:, 4 + q, :], K.rz[:, 8 + q, :]
            e.tensor_scalar(K.t_c[:, 0:1], vec("k_a"), -1.0, 1.0, ALU.mult, ALU.add).then_inc(P.sem("dve_order"), P.adds("dve_order"))
            P.e.wait_ge(P.sem("dve_order"), P.due("dve_order", 0))
            P.e.wait_ge(P.sem("gates_open"), P.due("gates_open", 2))
            if q < 3:
                sums()
            for d in range(2):
                lw, al = K.t_s[:, d, :], K.t_a[:, d, :]
                e.tensor_scalar(lw, lw, -DECAY, None, ALU.mult).then_inc(P.sem("dve_order"), P.adds("dve_order"))
                P.e.wait_ge(P.sem("dve_order"), P.due("dve_order", 0))
                e.tensor_tensor_scan(K.t_bi[:, :], K.reset16[:, :], lw, 0.0, ALU.mult, ALU.add).then_inc(P.sem("dve_order"), P.adds("dve_order"))
                P.e.wait_ge(P.sem("dve_order"), P.due("dve_order", 0))
                b3 = K.t_bi[:, :].rearrange("p (n c) -> p n c", c=16)
                e.tensor_copy(K.t_bc[:, :], b3[:, :, 15]).then_inc(P.sem("dve_order"), P.adds("dve_order"))
                P.e.wait_ge(P.sem("dve_order"), P.due("dve_order", 0))
                if d == 0:
                    e.tensor_tensor(K.t_bx[:, :], K.t_bi[:, :], lw, ALU.subtract).then_inc(P.sem("decay_cumulated"), P.adds("decay_cumulated"))
                else:
                    total = K.t_bc[:, :].rearrange("p (n c) -> p n c", c=1).broadcast_to([128, N_CHUNK, 16])
                    e.tensor_tensor(K.t_bx[:, :].rearrange("p (n c) -> p n c", c=16), total, b3, ALU.subtract).then_inc(P.sem("dve_order"), P.adds("dve_order"))
                    P.e.wait_ge(P.sem("dve_order"), P.due("dve_order", 0))
                    e.tensor_tensor(K.t_bi[:, :], K.t_bx[:, :], lw, ALU.add).then_inc(P.sem("decay_cumulated"), P.adds("decay_cumulated"))
                if d == 0 and q < 3:
                    normalise(q + 1)
                e.tensor_scalar(K.t_k[:, d, :], al, vec("k_a"), K.t_c[:, 0:1], ALU.mult, ALU.add).then_inc(P.sem("dve_order"), P.adds("dve_order"))
                P.e.wait_ge(P.sem("dve_order"), P.due("dve_order", 0))
                e.tensor_tensor(K.t_k[:, d, :], K.t_k[:, d, :], k, ALU.mult).then_inc(P.sem("dve_order"), P.adds("dve_order"))
                P.e.wait_ge(P.sem("dve_order"), P.due("dve_order", 0))
                e.tensor_tensor(al, al, kk[:, :], ALU.mult).then_inc(P.sem("dve_order"), P.adds("dve_order"))
                P.e.wait_ge(P.sem("dve_order"), P.due("dve_order", 0))
                P.e.wait_ge(P.sem("decay_exps"), P.due("decay_exps"))
                ar = K.ar[d]
                e.scalar_tensor_tensor(ar[:, 0, q, :], kk[:, :], -1.0, K.t_bx[:, :], ALU.mult, ALU.mult)
                e.tensor_tensor(ar[:, 1, q, :], r, lw, ALU.mult)
                e.tensor_tensor(ar[:, 2, q, :], al, K.t_en[:, :], ALU.mult)
                e.tensor_tensor(ar[:, 3, q, :], K.t_k[:, d, :], K.t_en[:, :], ALU.mult).then_inc(P.sem("direction_done"), P.adds("direction_done"))
                P.e.wait_ge(P.sem("direction_done"), P.due("direction_done", 0))
            e.tensor_tensor(K.t_u[:, :], K.t_k[:, 0, :], K.t_k[:, 1, :], ALU.add).then_inc(P.sem("dve_order"), P.adds("dve_order"))
            P.e.wait_ge(P.sem("dve_order"), P.due("dve_order", 0))
            e.scalar_tensor_tensor(K.t_u[:, :], K.t_u[:, :], vec("r_k"), r, ALU.mult, ALU.mult).then_inc(P.sem("bonus_product"), P.adds("bonus_product"))
            P.e.wait_ge(P.sem("bonus_summed"), P.due("bonus_summed"))
            e.scalar_tensor_tensor(parts(K.rz[:, q, :]), both_parts(K, 2), 0.5, parts(v), ALU.mult, ALU.mult).then_inc(P.sem("bonus_done"), P.adds("bonus_done"))
            if q < 2:
                scale(q + 2)
            P.e.wait_ge(P.sem("bonus_done"), P.due("bonus_done", 0))


class RwkvScan(Stage):

    HALVES = [slice(0, 64), slice(64, 128)]
    BOTH = [(0, HALVES[0]), (0, HALVES[1]), (1, HALVES[0]), (1, HALVES[1])]

    def act(self, K, P):
        def stage(c, b):
            for d in range(2):
                t = sl_t(16 * c if d == 0 else (N_CHUNK - 1) * 16 - 16 * c, 16)
                P.e.activation(K.c_st[b][:, d, 0:4, :].rearrange("p a (q t) -> p a q t", q=4), K.ar[d][:, :, :, t], ACT.Copy)
                last = P.e.activation(K.c_st[b][:, d, 4, :].rearrange("p (q t) -> p q t", q=4), K.rz[:, 8:12, t], ACT.Copy)
            last.then_inc(P.sem("chunk_staged"), P.adds("chunk_staged"))

        def betas():
            P.e.wait_ge(P.sem("betas_transposed"), P.due("betas_transposed"))
            for par, half in enumerate(self.HALVES):
                last = P.e.activation(K.c_bt[half, :, :], K.PS[0:64, 5, :].rearrange("p (a q n) -> p a q n", q=2, n=64)[:, :, par, :], ACT.Copy)
            last.then_inc(P.sem("betas_ready"), P.adds("betas_ready"))

        def step(c, b, more=2):
            P.e.wait_ge(P.sem("u_done"), P.due("u_done"))
            P.e.activation(K.c_u[:, :], K.PS[:, 2, :], ACT.Copy).then_inc(P.sem("u_ready"), P.adds("u_ready"))
            P.e.wait_ge(P.sem("state_done"), P.due("state_done"))
            if more:
                betas()
            P.e.wait_ge(P.sem("y_done"), P.due("y_done"))
            if more > 1:
                stage(c + 2, b)

        def body(i):
            step(2 * i, 0)
            step(2 * i + 1, 1)

        stage(0, 0)
        stage(1, 1)
        betas()
        P.loop((N_CHUNK - 3) // 2, body, u_done=2, u_ready=2, state_done=2, y_done=2, betas_transposed=2, betas_ready=2, chunk_staged=2)
        step(N_CHUNK - 3, 0)
        step(N_CHUNK - 2, 1, more=1)
        step(N_CHUNK - 1, 0, more=0)

    def pe(self, K, P):
        mm = P.e.matmul

        def grams(b):
            P.e.wait_ge(P.sem("chunk_staged"), P.due("chunk_staged"))
            P.settle()
            st = K.c_st[b]
            for d, h in self.BOTH:
                mm(K.PS[h, d, 0:128], st[h, d, 2, :], st[h, d, 0:2, :].rearrange("p a n -> p (a n)"), start=True, stop=True)
                mm(K.PS[h, d, 128:256], st[h, d, 3, :], st[h, d, 0:2, :].rearrange("p a n -> p (a n)"), start=True, stop=True)
                last = mm(K.PS[h, d, 256:320], st[h, d, 0, :], st[h, d, 2, :], start=True, stop=True)
            last.then_inc(P.sem("grams_done"), P.adds("grams_done"))

        def transposes(b):
            st = K.c_st[b]
            for d in range(2):
                for j in range(2):
                    last = P.e.transpose(K.PS[0:64, 5, 256 * d + 128 * j:256 * d + 128 * j + 128], st[:, d, 2 + j, :], K.ident[:, :])
            last.then_inc(P.sem("betas_transposed"), P.adds("betas_transposed"))
            for d in range(2):
                last = P.e.transpose(K.PS[0:64, 6, 128 * d:128 * d + 128], st[:, d, 4, :], K.ident[:, :])
            last.then_inc(P.sem("v_rows_done"), P.adds("v_rows_done"))

        def square(n, b):
            if n == 0:
                P.e.wait_ge(P.sem("grams_masked"), P.due("grams_masked"))
            else:
                P.e.wait_ge(P.sem("squares_ready"), P.due("squares_ready"))
            P.settle()
            g = K.c_g[b]
            for d, h in self.BOTH:
                if n == 0:
                    c = 128 * d
                    mm(K.PS[h, 7, c:c + 64], g[h, d, 256:320], g[h, d, 0:64], start=True, stop=True)
                    last = mm(K.PS[h, 7, c + 64:c + 128], g[h, d, 0:64], g[h, d, 256:320], start=True, stop=True)
                elif n == 1:
                    n2, n2t = K.c_n2[h, d, 0:64], K.c_n2[h, d, 64:128]
                    mm(K.PS[h, 0, 128 * d:128 * d + 64], n2t, n2, start=True, stop=True)
                    mm(K.PS[h, 0, 128 * d + 64:128 * d + 128], n2, n2t, start=True, stop=True)
                    last = mm(K.PS[h, 0, 256 + 64 * d:320 + 64 * d], n2t, K.c_p[h, 0, d, :], start=True, stop=True)
                elif n == 2:
                    n4, n4t = K.c_n4[h, d, 0:64], K.c_n4[h, d, 64:128]
                    mm(K.PS[h, 1, 64 * d:64 * d + 64], n4, n4t, start=True, stop=True)
                    last = mm(K.PS[h, 1, 128 + 64 * d:192 + 64 * d], n4t, K.c_p[h, 1, d, :], start=True, stop=True)
                else:
                    last = mm(K.PS[h, 1, 256 + 64 * d:320 + 64 * d], K.c_n8[h, d, :], K.c_p[h, 0, d, :], start=True, stop=True)
            last.then_inc(P.sem("squares_done"), P.adds("squares_done"))

        def outputs(b, which):
            for d, h in self.BOTH:
                if d == which:
                    c = slice(256 * d, 256 * d + 256)
                    mm(K.PS[h, 4, c], K.c_st[b][h, d, 1, :], K.c_s[b][h, c], start=True, stop=False)
                    mm(K.PS[h, 4, c], K.c_g[b][h, d, 192:256], K.c_v[b][h, c], start=False, stop=False)
                    last = mm(K.PS[h, 4, c], K.c_g[b][h, d, 64:128], K.c_u[h, c], start=False, stop=True)
            return last

        def step(b, more=True, first=False):
            nb = 1 - b
            P.e.wait_ge(P.sem("state_ready"), P.due("state_ready"))
            P.e.wait_ge(P.sem("v_rows_ready"), P.due("v_rows_ready"))
            P.settle()
            for d, h in self.BOTH:
                c = slice(256 * d, 256 * d + 256)
                mm(K.PS[h, 7, c], K.c_g[b][h, d, 128:192], K.c_v[b][h, c], start=True, stop=False)
                last = mm(K.PS[h, 7, c], K.c_st[b][h, d, 0, :], K.c_s[b][h, c], start=False, stop=True)
            last.then_inc(P.sem("rhs_done"), P.adds("rhs_done"))
            P.e.wait_ge(P.sem("squares_ready"), P.due("squares_ready"))
            if more:
                grams(nb)
            P.e.wait_ge(P.sem("rhs_ready"), P.due("rhs_ready"))
            P.settle()
            for d, h in self.BOTH:
                c = slice(256 * d, 256 * d + 256)
                last = mm(K.PS[h, 2, c], K.c_p[h, 1, d, :], K.c_r[h, c], start=True, stop=True)
            last.then_inc(P.sem("u_done"), P.adds("u_done"))
            P.e.wait_ge(P.sem("betas_ready"), P.due("betas_ready"))
            if more:
                square(0, nb)
                transposes(nb)
            P.e.wait_ge(P.sem("u_ready"), P.due("u_ready"))
            P.settle()
            for d, h in self.BOTH:
                c = slice(256 * d, 256 * d + 256)
                mm(K.PS[h, 3, c], K.c_bt[h, 2 * d, :], K.c_u[h, c], start=True, stop=False)
                last = mm(K.PS[h, 3, c], K.c_bt[h, 2 * d + 1, :], K.c_v[b][h, c], start=False, stop=True)
            last.then_inc(P.sem("state_done"), P.adds("state_done"))
            if more:
                square(1, nb)
            P.e.wait_ge(P.sem("y_taken"), P.due("y_taken"))
            P.settle()
            outputs(b, 0)
            if more:
                square(2, nb)
            last = outputs(b, 1)
            last.then_inc(P.sem("y_done"), P.adds("y_done"))
            if more:
                square(3, nb)

        def body(_):
            step(0)
            step(1)

        grams(0)
        for n in range(4):
            square(n, 0)
            if n == 0:
                transposes(0)
        P.loop(N_CHUNK // 2, body, chunk_staged=2, grams_done=2, betas_transposed=2, v_rows_done=2, grams_masked=2, squares_done=8,
               squares_ready=8, v_rows_ready=2, state_ready=2, rhs_done=2, rhs_ready=2, u_done=2, u_ready=2, betas_ready=2,
               state_done=2, y_taken=2, y_done=2)
        step(0, more=False)

    def dve(self, K, P):
        e = P.e
        mask = K.block_mask[:, :].rearrange("p (a n) -> p a n", a=1).broadcast_to([128, 2, 256])
        halves = lambda ap: ap.rearrange("p (d n) -> p d n", d=2)
        e.memset(K.yt[:, :, :], 0.0)
        e.memset(K.c_s[0][:, :], 0.0).then_inc(P.sem("state_ready"), P.adds("state_ready"))
        P.e.wait_ge(P.sem("state_ready"), P.due("state_ready", 0))

        def square(n, b):
            if n < 0:
                P.e.wait_ge(P.sem("grams_done"), P.due("grams_done"))
                e.tensor_tensor(K.c_g[b][:, :, :], K.PS[:, 0:2, 0:320], K.gram_mask[:, :, :], ALU.mult).then_inc(P.sem("grams_masked"), P.adds("grams_masked"))
                P.e.wait_ge(P.sem("grams_masked"), P.due("grams_masked", 0))
                e.tensor_tensor(K.c_p[:, 0, :, :], K.c_g[b][:, :, 0:64], K.eye64[:, :, :], ALU.add)
                return
            P.e.wait_ge(P.sem("squares_done"), P.due("squares_done"))
            P.e.wait_ge(P.sem("squares_ready"), P.due("squares_ready", 0))
            if n == 0:
                last = e.tensor_copy(K.c_n2[:, :, :].rearrange("p d n -> p (d n)"), K.PS[:, 7, 0:256])
            elif n == 1:
                e.tensor_copy(K.c_n4[:, :, :].rearrange("p d n -> p (d n)"), K.PS[:, 0, 0:256])
                last = e.tensor_tensor(K.c_p[:, 1, :, :], K.PS[:, 0, 256:384].rearrange("p (d n) -> p d n", d=2), K.c_p[:, 0, :, :], ALU.add)
            elif n == 2:
                e.tensor_copy(K.c_n8[:, :, :].rearrange("p d n -> p (d n)"), K.PS[:, 1, 0:128])
                last = e.tensor_tensor(K.c_p[:, 0, :, :], K.PS[:, 1, 128:256].rearrange("p (d n) -> p d n", d=2), K.c_p[:, 1, :, :], ALU.add)
            else:
                last = e.tensor_tensor(K.c_p[:, 1, :, :], K.PS[:, 1, 256:384].rearrange("p (d n) -> p d n", d=2), K.c_p[:, 0, :, :], ALU.add)
            last.then_inc(P.sem("squares_ready"), P.adds("squares_ready"))

        def v_rows(b):
            P.e.wait_ge(P.sem("v_rows_done"), P.due("v_rows_done"))
            for par, half in enumerate(self.HALVES):
                v = K.PS[0:64, 6, 0:256].rearrange("p (d a q n) -> p d a q n", d=2, a=1, q=2)[:, :, :, par, :]
                m = K.block_mask[0:64, :].rearrange("p (q n) -> p q n", q=4)
                for d in range(2):
                    last = e.tensor_tensor(K.c_v[b][half, 256 * d:256 * d + 256].rearrange("p (q n) -> p q n", q=4),
                                           v[:, d].broadcast_to([64, 4, 64]), m, ALU.mult)
            last.then_inc(P.sem("v_rows_ready"), P.adds("v_rows_ready"))

        def step(c, b, more=True):
            nb = 1 - b
            P.e.wait_ge(P.sem("rhs_done"), P.due("rhs_done"))
            e.tensor_tensor(halves(K.c_r[:, :]), halves(K.PS[:, 7, :]), mask, ALU.mult).then_inc(P.sem("rhs_ready"), P.adds("rhs_ready"))
            if more:
                square(-1, nb)
                square(0, nb)
                v_rows(nb)
            P.e.wait_ge(P.sem("state_done"), P.due("state_done"))
            e.tensor_tensor(K.c_s[nb][:, :], K.c_s[b][:, :], K.PS[:, 3, :], ALU.add).then_inc(P.sem("dve_order"), P.adds("dve_order"))
            P.e.wait_ge(P.sem("dve_order"), P.due("dve_order", 0))
            for d in range(2):
                s4 = K.c_s[nb][:, 256 * d:256 * d + 256].rearrange("p (q n) -> p q n", q=4)
                decay = K.wc[:, d, :, sl_t(c if d == 0 else N_CHUNK - 1 - c, 1)].broadcast_to([128, 4, 64])
                last = e.tensor_tensor(s4, s4, decay, ALU.mult)
            last.then_inc(P.sem("state_ready"), P.adds("state_ready"))
            if more:
                square(1, nb)
                square(2, nb)
                square(3, nb)
            P.e.wait_ge(P.sem("y_done"), P.due("y_done"))
            e.tensor_tensor(halves(K.c_y[:, :]), halves(K.PS[:, 4, :]), mask, ALU.mult).then_inc(P.sem("y_taken"), P.adds("y_taken"))
            P.e.wait_ge(P.sem("y_taken"), P.due("y_taken", 0))
            e.reduce_sum(K.c_yr[:, :, :], K.c_y[:, :].rearrange("p (d q n) -> p d n q", d=2, q=4), AX.X).then_inc(P.sem("dve_order"), P.adds("dve_order"))
            P.e.wait_ge(P.sem("dve_order"), P.due("dve_order", 0))
            y0 = flat(K.yt[:, sl(c), :])
            y1 = flat(K.yt[:, sl_(N_CHUNK - 1 - c), :])
            e.tensor_tensor(y0, y0, K.c_yr[:, 0, :], ALU.add).then_inc(P.sem("dve_order"), P.adds("dve_order"))
            P.e.wait_ge(P.sem("dve_order"), P.due("dve_order", 0))
            e.tensor_tensor(y1, y1, K.c_yr[:, 1, :], ALU.add).then_inc(P.sem("dve_order"), P.adds("dve_order"))
            P.e.wait_ge(P.sem("dve_order"), P.due("dve_order", 0))

        def body(i):
            step(2 * i, 0)
            step(2 * i + 1, 1)

        e.memset(K.c_y[:, :], 0.0).then_inc(P.sem("y_taken"), P.adds("y_taken"))
        P.e.wait_ge(P.sem("y_taken"), P.due("y_taken", 0))
        for n in range(-1, 4):
            square(n, 0)
            if n == 0:
                v_rows(0)
        P.loop(N_CHUNK // 2, body, grams_done=2, grams_masked=2, squares_done=8, squares_ready=8, v_rows_done=2, v_rows_ready=2,
               rhs_done=2, rhs_ready=2, y_done=2, y_taken=2, state_done=2, state_ready=2, dve_order=8)
        step(N_CHUNK - 1, 0, more=False)


def sl_t(start, n):
    return slice(start, start + n) if isinstance(start, int) else bass.ds(start, n)


def sl_(i):
    return sl_t(i, 1)


class RwkvOutput(Stage):

    def dve(self, K, P):
        e = P.e
        col = lambda j: K.g_c[:, j, :]
        wide = lambda j: K.g_c[:, j, :].rearrange("p (n c) -> p n c", c=1).broadcast_to([128, N_CHUNK, 64])
        e.reduce_sum(col(0), K.yt[:, :, :], AX.X).then_inc(P.sem("dve_order"), P.adds("dve_order"))
        P.e.wait_ge(P.sem("dve_order"), P.due("dve_order", 0))
        e.tensor_scalar(col(0), col(0), 1.0 / 64, None, ALU.mult).then_inc(P.sem("dve_order"), P.adds("dve_order"))
        P.e.wait_ge(P.sem("dve_order"), P.due("dve_order", 0))
        e.tensor_tensor(K.yt[:, :, :], K.yt[:, :, :], wide(0), ALU.subtract).then_inc(P.sem("y_centred"), P.adds("y_centred"))
        P.e.wait_ge(P.sem("y_squared"), P.due("y_squared"))
        e.reduce_sum(col(1), K.y2[:, :, :], AX.X).then_inc(P.sem("dve_order"), P.adds("dve_order"))
        P.e.wait_ge(P.sem("dve_order"), P.due("dve_order", 0))
        e.tensor_scalar(col(1), col(1), 1.0 / 64, 64e-5, ALU.mult, ALU.add).then_inc(P.sem("dve_order"), P.adds("dve_order"))
        P.e.wait_ge(P.sem("dve_order"), P.due("dve_order", 0))
        e.reciprocal(col(1), col(1)).then_inc(P.sem("y_inverse"), P.adds("y_inverse"))
        P.e.wait_ge(P.sem("y_root"), P.due("y_root"))
        e.tensor_tensor(K.yt[:, :, :], K.yt[:, :, :], wide(1), ALU.mult).then_inc(P.sem("y_normed"), P.adds("y_normed"))
        P.e.wait_ge(P.sem("y_transposed"), P.due("y_transposed"))
        for b in range(8):
            for par in range(2):
                src = K.PS[0:64, b, :].rearrange("p (c a q t) -> p c a q t", c=4, a=2, q=4)[:, :, par]
                dst = K.yf[64 * par:64 * par + 64, :, 64 * b:64 * b + 64].rearrange("p q (c t) -> p c q t", c=4)
                last = e.tensor_copy(dst, src)
        last.then_inc(P.sem("y_rows"), P.adds("y_rows"))
        P.e.wait_ge(P.sem("y_rows"), P.due("y_rows", 0))
        for q in range(4):
            e.scalar_tensor_tensor(K.yf[:, q, :], K.yf[:, q, :], K.p["lnx_g"][:, q:q + 1], K.rz[:, q, META:TM], ALU.mult, ALU.add).then_inc(P.sem("y_bonus"), P.adds("y_bonus"))
        for q in range(4):
            P.e.wait_ge(P.sem("y_shifted"), P.due("y_shifted"))
            P.e.wait_ge(P.sem("gate_done"), P.due("gate_done"))
            e.tensor_tensor(K.ya[:, q, :], K.yf[:, q, :], K.PS[:, q, :], ALU.mult).then_inc(P.sem("y_gated"), P.adds("y_gated"))

    def act(self, K, P):
        P.e.activation(K.rz[:, 14, :], K.rz[:, 14, :], ACT.Sigmoid)
        P.e.activation(K.rz[0:32, 15, :], K.rz[0:32, 15, :], ACT.Sigmoid).then_inc(P.sem("gate_open"), P.adds("gate_open"))
        P.e.wait_ge(P.sem("y_centred"), P.due("y_centred"))
        P.e.activation(K.y2[:, :, :], K.yt[:, :, :], ACT.Square).then_inc(P.sem("y_squared"), P.adds("y_squared"))
        P.e.wait_ge(P.sem("y_inverse"), P.due("y_inverse"))
        P.e.activation(K.g_c[:, 1, :], K.g_c[:, 1, :], ACT.Sqrt).then_inc(P.sem("y_root"), P.adds("y_root"))
        for q in range(4):
            P.e.wait_ge(P.sem("y_bonus"), P.due("y_bonus"))
            P.e.activation(K.yf[:, q, :], K.yf[:, q, :], ACT.Identity, bias=K.p["lnx_b"][:, q:q + 1]).then_inc(P.sem("y_shifted"), P.adds("y_shifted"))

    def pe(self, K, P):
        P.e.wait_ge(P.sem("y_normed"), P.due("y_normed"))
        for b in range(8):
            for c in range(4):
                last = P.e.transpose(K.PS[0:64, b, 128 * c:128 * c + 128], K.yt[:, 1 + 4 * b + c, :], K.ident[:, :])
        last.then_inc(P.sem("y_transposed"), P.adds("y_transposed"))
        P.e.wait_ge(P.sem("y_rows"), P.due("y_rows"))
        P.e.wait_ge(P.sem("gate_open"), P.due("gate_open"))
        for q in range(4):
            c = slice(128 * q, 128 * q + 128)
            P.e.matmul(K.PS[:, q, :], K.g2a[:, c], K.rz[:, 14, META:TM], start=True, stop=False)
            P.e.matmul(K.PS[:, q, :], K.g2b[0:32, c], K.rz[0:32, 15, META:TM], start=False, stop=True).then_inc(P.sem("gate_done"), P.adds("gate_done"))


class QkNormRope(Stage):

    def tiles(self, K):
        out = [(K.a_q[:, q, :], K.p["q_norm_g"], META, ((0, S),)) for q in range(4)]
        return out + [(K.a_kv[:, 0, :], K.p["k_norm_g"], 0, T3)]

    def act(self, K, P):
        tiles = self.tiles(K)

        def square(j):
            x, n = tiles[j][0], tiles[j][3][-1][0] + tiles[j][3][-1][1]
            P.e.activation(K.a_t[:, j % 2, 0:n], x, ACT.Square).then_inc(P.sem("qk_squared"), P.adds("qk_squared"))

        square(0)
        for j, (x, g, off, toks) in enumerate(tiles):
            n = toks[-1][0] + toks[-1][1]
            if j + 1 < len(tiles):
                if j:
                    P.e.wait_ge(P.sem("qk_sumsq"), P.due("qk_sumsq"))
                square(j + 1)
            P.e.wait_ge(P.sem("qk_inverse"), P.due("qk_inverse"))
            P.e.activation(K.a_p[:, j % 2, 0:n], K.a_p[:, j % 2, 0:n], ACT.Sqrt).then_inc(P.sem("qk_root"), P.adds("qk_root"))

    def pe(self, K, P):
        tiles = self.tiles(K)

        def sums(j):
            P.e.wait_ge(P.sem("qk_squared"), P.due("qk_squared"))
            for part, (t0, tn) in enumerate(tiles[j][3]):
                last = P.e.matmul(K.PS[:, 4 * (j % 2) + part, 0:tn], K.head_ones2[:, :], K.a_t[:, j % 2, t0:t0 + tn], start=True, stop=True)
            last.then_inc(P.sem("qk_sumsq"), P.adds("qk_sumsq"))

        sums(0)
        for j, (x, g, off, toks) in enumerate(tiles):
            if j + 1 < len(tiles):
                sums(j + 1)
            P.e.wait_ge(P.sem("qk_normed"), P.due("qk_normed"))
            for part, (t0, tn) in enumerate(toks):
                last = P.e.matmul(K.PS[:, 4 * (j % 2) + 2 + part, 0:tn], K.rot[:, :], x[:, t0:t0 + tn], start=True, stop=True)
            last.then_inc(P.sem("qk_partner"), P.adds("qk_partner"))

    def dve(self, K, P):
        e, tiles = P.e, self.tiles(K)

        def rotate(j):
            x, g, off, toks = tiles[j]
            n = toks[-1][0] + toks[-1][1]
            P.e.wait_ge(P.sem("qk_partner"), P.due("qk_partner"))
            for part, (t0, tn) in enumerate(toks):
                e.tensor_tensor(K.a_p[:, 2, t0:t0 + tn], K.PS[:, 4 * (j % 2) + 2 + part, 0:tn], K.rope[:, 1, off + t0:off + t0 + tn], ALU.mult)
            e.tensor_tensor(x, x, K.rope[:, 0, off:off + n], ALU.mult).then_inc(P.sem("dve_order"), P.adds("dve_order"))
            P.e.wait_ge(P.sem("dve_order"), P.due("dve_order", 0))
            e.tensor_tensor(x, x, K.a_p[:, 2, 0:n], ALU.add).then_inc(P.sem("qk_rotated"), P.adds("qk_rotated"))
            P.e.wait_ge(P.sem("qk_rotated"), P.due("qk_rotated", 0))

        for j, (x, g, off, toks) in enumerate(tiles):
            n = toks[-1][0] + toks[-1][1]
            r = K.a_p[:, j % 2, 0:n]
            P.e.wait_ge(P.sem("qk_sumsq"), P.due("qk_sumsq"))
            for part, (t0, tn) in enumerate(toks):
                last = e.tensor_scalar(K.a_p[:, j % 2, t0:t0 + tn], K.PS[:, 4 * (j % 2) + part, 0:tn], 1.0 / 64, EPS, ALU.mult, ALU.add)
            last.then_inc(P.sem("dve_order"), P.adds("dve_order"))
            P.e.wait_ge(P.sem("dve_order"), P.due("dve_order", 0))
            e.reciprocal(r, r).then_inc(P.sem("qk_inverse"), P.adds("qk_inverse"))
            if j:
                rotate(j - 1)
            P.e.wait_ge(P.sem("qk_root"), P.due("qk_root"))
            e.scalar_tensor_tensor(x, x, g[:, 0:1], r, ALU.mult, ALU.mult).then_inc(P.sem("qk_normed"), P.adds("qk_normed"))
        rotate(len(tiles) - 1)


class GroupedAttention(Stage):

    UNITS = [(t, u, b) for t in range(2) for u in range(2) for b in range(4)]
    N = len(UNITS)
    KEYS = [(128 * j, min(128, TM - 128 * j)) for j in range(5)]

    def act(self, K, P):
        P.e.activation(K.a_ks[0:64, 0, :], K.a_kv[0:64, 0, :], ACT.Copy).then_inc(P.sem("k_staged"), P.adds("k_staged"))
        P.e.activation(K.a_ks[0:64, 1, :], K.a_kv[64:128, 0, :], ACT.Copy).then_inc(P.sem("k_staged"), P.adds("k_staged"))
        P.e.wait_ge(P.sem("v_transposed"), P.due("v_transposed"))
        P.e.activation(K.a_vT[:, 0:4, :].rearrange("p a n -> p (a n)"), K.PS[:, 7, :], ACT.Copy).then_inc(P.sem("act_order"), P.adds("act_order"))
        P.e.activation(K.a_vT[0:16, 4, :], K.PS[0:16, 5, 0:128], ACT.Copy).then_inc(P.sem("act_order"), P.adds("act_order"))
        P.e.wait_ge(P.sem("act_order"), P.due("act_order", 0))

        def stage(i, t):
            for u in range(2):
                last = P.e.activation(K.a_qs[0:64, 2 * t + u, :], flat(K.a_q[64 * u:64 * u + 64, sl(2 * i + t), :]), ACT.Copy, scale=0.125)
            last.then_inc(P.sem("qk_staged"), P.adds("qk_staged"))

        def body(i):
            stage(i, 0)
            v = slice(64 * i, 64 * i + 64) if isinstance(i, int) else bass.ds(64 * i, 64)
            P.e.activation(K.a_v64[:, 0:4, :], K.a_vT[:, 0:4, v], ACT.Copy)
            P.e.activation(K.a_v64[0:16, 4, :], K.a_vT[0:16, 4, v], ACT.Copy).then_inc(P.sem("vT_ready"), P.adds("vT_ready"))
            stage(i, 1)
            for n in range(self.N):
                P.e.wait_ge(P.sem("logits_done"), P.due("logits_done"))
                P.e.wait_ge(P.sem("max_negated"), P.due("max_negated"))
                P.e.activation(parts(K.a_p[:, n % 3, :]), K.PS[:, 2 * (n % 2):2 * (n % 2) + 2, 0:HALF_T], ACT.Exp,
                               bias=K.a_st[:, n % 3, 1:2], accum_out=K.a_st[:, n % 3, 2:3]).then_inc(P.sem("exp_done"), P.adds("exp_done"))
            P.e.wait_ge(P.sem("att_out_done"), P.due("att_out_done", 2))

        P.loop(2, body, qk_staged=2, vT_ready=1, logits_done=16, max_negated=16, exp_done=16, att_out_done=2)

    def dve(self, K, P):
        e = P.e

        def take_out(i, t):
            P.e.wait_ge(P.sem("att_out_done"), P.due("att_out_done"))
            h = sl(2 * i + t + 4)
            view = lambda ap, par: flat(ap[:, h, :]).rearrange("p (j r c) -> p r j c", r=2, c=128)[:, par]
            o = [K.PS[:, 6 + par, 128:384].rearrange("p (j c) -> p j c", j=2) for par in range(2)]
            for par in range(2):
                last = e.tensor_copy(view(K.HH, par), o[par])
            last.then_inc(P.sem("att_out_hi"), P.adds("att_out_hi"))
            P.e.wait_ge(P.sem("att_out_hi"), P.due("att_out_hi", 0))
            for par in range(2):
                last = e.tensor_tensor(view(K.HL, par), o[par], view(K.HH, par).bitcast(F32), ALU.subtract)
            last.then_inc(P.sem("att_out_lo"), P.adds("att_out_lo"))

        def body(i):
            for n in range(self.N + 2):
                if n < self.N:
                    st = K.a_st[:, n % 3]
                    P.e.wait_ge(P.sem("logits_done"), P.due("logits_done"))
                    e.tensor_reduce(st[:, 0:1], K.PS[:, 2 * (n % 2):2 * (n % 2) + 2, 0:HALF_T], AX.XY, ALU.max).then_inc(P.sem("dve_order"), P.adds("dve_order"))
                    P.e.wait_ge(P.sem("dve_order"), P.due("dve_order", 0))
                    e.tensor_scalar(st[:, 1:2], st[:, 0:1], -1.0, None, ALU.mult).then_inc(P.sem("max_negated"), P.adds("max_negated"))
                if 1 <= n <= self.N:
                    st, p = K.a_st[:, (n - 1) % 3], K.a_p[:, (n - 1) % 3, :]
                    P.e.wait_ge(P.sem("exp_done"), P.due("exp_done"))
                    e.reciprocal(st[:, 3:4], st[:, 2:3]).then_inc(P.sem("dve_order"), P.adds("dve_order"))
                    P.e.wait_ge(P.sem("dve_order"), P.due("dve_order", 0))
                    e.tensor_scalar(p, p, st[:, 3:4], None, ALU.mult).then_inc(P.sem("probs_ready"), P.adds("probs_ready"))
                if n >= 2:
                    s = n % 2
                    P.e.wait_ge(P.sem("probs_transposed"), P.due("probs_transposed"))
                    e.tensor_copy(K.a_pT[:, s, 0:4, :].rearrange("p a n -> p (a n)"), K.PS[:, 4 + s, :])
                    e.tensor_copy(K.a_pT[0:16, s, 4, :], K.PS[0:16, 6 + s, 0:128]).then_inc(P.sem("probsT_ready"), P.adds("probsT_ready"))
                if n == 10:
                    take_out(i, 0)
            take_out(i, 1)

        P.loop(2, body, dve_order=32, logits_done=16, max_negated=16, exp_done=16, probs_ready=16, probs_transposed=16,
               probsT_ready=16, att_out_done=2, att_out_hi=2, att_out_lo=2)

    def pe(self, K, P):
        for j, (k0, kn) in enumerate(self.KEYS):
            out = K.PS[0:kn, 7, k0:k0 + 128] if j < 4 else K.PS[0:kn, 5, 0:128]
            last = P.e.transpose(out, K.a_kv[:, 1, k0:k0 + kn], K.ident[:, :])
        last.then_inc(P.sem("v_transposed"), P.adds("v_transposed"))
        P.e.wait_ge(P.sem("k_staged"), P.due("k_staged", 2))

        def body(i):
            for n in range(self.N + 3):
                if n < self.N:
                    t, u, b = self.UNITS[n]
                    if n % 8 == 0:
                        P.e.wait_ge(P.sem("qk_staged"), P.due("qk_staged"))
                    if n >= 2:
                        P.e.wait_ge(P.sem("exp_done"), P.due("exp_done"))
                    if n % 8 == 0 or n >= 2:
                        P.settle()
                    for part, (t0, tn) in enumerate(T3):
                        last = P.e.matmul(K.PS[:, 2 * (n % 2) + part, 0:tn], K.a_qs[0:64, 2 * t + u, 128 * b:128 * b + 128],
                                          flat(K.a_ks[0:64, sl(i), t0:t0 + tn]), start=True, stop=True)
                    last.then_inc(P.sem("logits_done"), P.adds("logits_done"))
                if n == 11:
                    P.e.wait_ge(P.sem("att_out_lo"), P.due("att_out_lo"))
                if 2 <= n < self.N + 2:
                    m = n - 2
                    P.e.wait_ge(P.sem("probs_ready"), P.due("probs_ready"))
                    for j, (k0, kn) in enumerate(self.KEYS):
                        out = K.PS[0:kn, 4 + m % 2, k0:k0 + 128] if j < 4 else K.PS[0:kn, 6 + m % 2, 0:128]
                        last = P.e.transpose(out, K.a_p[:, m % 3, k0:k0 + kn], K.ident[:, :])
                    last.then_inc(P.sem("probs_transposed"), P.adds("probs_transposed"))
                if n >= 3:
                    m = n - 3
                    t, u, b = self.UNITS[m]
                    if m == 0:
                        P.e.wait_ge(P.sem("vT_ready"), P.due("vT_ready"))
                    P.e.wait_ge(P.sem("probsT_ready"), P.due("probsT_ready"))
                    for j, (k0, kn) in enumerate(self.KEYS):
                        c = 128 + 128 * (b // 2)
                        last = P.e.matmul(K.PS[64 * u:64 * u + 64, 6 + b % 2, c:c + 128], K.a_v64[0:kn, j, :],
                                          K.a_pT[0:kn, m % 2, j, :], start=(j == 0), stop=(j == 4))
                    if m % 8 == 7:
                        last.then_inc(P.sem("att_out_done"), P.adds("att_out_done"))
            P.e.wait_ge(P.sem("exp_done"), P.due("exp_done", 2))
            P.e.wait_ge(P.sem("att_out_lo"), P.due("att_out_lo"))

        P.loop(2, body, qk_staged=2, logits_done=16, exp_done=16, probs_ready=16, probs_transposed=16, probsT_ready=16,
               vT_ready=1, att_out_done=2, att_out_lo=2)


class SplitYa(Stage):

    def act(self, K, P):
        P.e.activation(K.HH[:, 0:4, :], K.ya[:, :, :], ACT.Copy).then_inc(P.sem("ya_hi"), P.adds("ya_hi"))

    def dve(self, K, P):
        P.e.wait_ge(P.sem("ya_hi"), P.due("ya_hi"))
        P.e.tensor_tensor(K.HL[:, 0:4, :], K.ya[:, :, :], K.HH[:, 0:4, :].bitcast(F32), ALU.subtract)


class GatedNarrow(Narrow):

    def __init__(self, nk, xh, xl, gate):
        super().__init__(nk, xh, xl, gate)

    def act(self, K, P):
        narrow_split(K, P, self.nk, split_act)
        split_last(K, P, split_act)

    def dve(self, K, P):
        narrow_split(K, P, self.nk, split_dve)
        for t in range(8):
            sum_wait(P, t)
            P.e.tensor_tensor(self.dst[:, t, :], self.dst[:, t, :], K.PS[:, t, 0:S], ALU.mult).then_inc(P.sem("sum_stored"), P.adds("sum_stored"))
        split_last(K, P, split_dve)


class Merge(Stage):

    def dve(self, K, P):
        for t in range(8):
            P.e.tensor_tensor(K.gates[:, t, :], K.gates[:, t, :], K.gates[:, 8 + t, :], ALU.add).then_inc(P.sem("merged"), P.adds("merged"))
        for t in range(8):
            P.e.wait_ge(P.sem("merged_hi"), P.due("merged_hi"))
            P.e.wait_ge(P.sem("merged"), P.due("merged", 0))
            P.e.tensor_tensor(K.XL[:, t, 0:S], K.gates[:, t, :], K.XH[:, t, 0:S].bitcast(F32), ALU.subtract)

    def act(self, K, P):
        for t in range(8):
            P.e.wait_ge(P.sem("merged"), P.due("merged"))
            P.e.activation(K.XH[:, t, 0:S], K.gates[:, t, :], ACT.Copy).then_inc(P.sem("merged_hi"), P.adds("merged_hi"))


def block3(K):
    real = ((META, S),)
    st = [Load(K.loads3), RmsNorm(K.XM, K.p["mix_norm_g"], T3), GateRows(), Store(7, K.XH, K.XL, K.rp, toks=T3),
          CentredShift(), Load(K.loads3b), RwkvPrepare(), Load(K.loads3c), RwkvScan(), Load(K.loads3d), RwkvOutput(),
          RmsNorm(K.XM, K.p["mix_norm_g"], T3), Load(K.loads3e), Store(2, K.XH, K.XL, K.a_q, toks=real, off=META),
          Store(1, K.XH, K.XL, K.a_kv, toks=T3), QkNormRope(), GroupedAttention(), SplitYa(),
          Store(8, K.XH, K.XL, K.gates, toks=real, off=META, func=ACT.Sigmoid),
          GatedNarrow(4, K.HH, K.HL, K.gates[:, 0:8, :]), GatedNarrow(4, K.HH[:, 4:8, :], K.HL[:, 4:8, :], K.gates[:, 8:16, :]),
          Merge(), Narrow(8, K.XH, K.XL, K.X), RmsNorm(K.X, K.p["ffn3_norm_g"])]
    for c0, n in FF3_CHUNKS:
        st += [SquaredReluUp(n // 2, K.XH, K.XL), Narrow(n, K.HH, K.HL, K.X)]
    return st + [RmsNorm(K.X, K.p["final3_norm_g"], out=K.X)]


def specs3():
    v = [("mix_norm_g", "mix_norm_g_3", 0), ("ffn3_norm_g", "ffn_norm_g_3", 0), ("final3_norm_g", "final_norm_g_3", None),
         ("k_k", "k_k_3", 0), ("k_a", "k_a_3", 0), ("r_k", "r_k_3", 0), ("lnx_g", "lnx_g_3", 0), ("lnx_b", "lnx_b_3", 0)]
    v += [(f"decay_w0{d}", "decay_w0_3", (0, d)) for d in range(2)] + [(f"icl_a0{d}", "icl_a0_3", (0, d)) for d in range(2)]
    v += [("q_norm_g", "q_norm_g_3", 0), ("k_norm_g", "k_norm_g_3", 0)]
    return v


def weights3(a):
    w = a["w_in_3"][0]
    rk = 1952
    out = [wide_panels(w[:, 0:1792]), wide_panels(w[:, rk:rk + 512]), wide_panels(w[:, rk + 512:rk + 768]),
           wide_panels(w[:, rk + 768:]), narrow_panels(a["w_branch_rwkv_3"][0]), narrow_panels(a["w_branch_attn_3"][0]),
           narrow_panels(a["w_out_3"][0])]
    for c0, n in FF3_CHUNKS:
        c = slice(128 * c0, 128 * (c0 + n))
        out += [wide_panels(a["w_ff1_3"][0][:, c]), narrow_panels(a["w_ff2_3"][0][c])]
    return out


def consts3():
    r = np.arange(128)
    tile, tok = (r % 64) // 16, r % 16
    ct, ck = np.arange(64) // 16, np.arange(64) % 16
    same = tile[:, None] == ct[None, :]
    gram = []
    for d in range(2):
        before = (tok[:, None] < ck[None, :]) if d == 0 else (tok[:, None] > ck[None, :])
        after = (tok[:, None] > ck[None, :]) if d == 0 else (tok[:, None] < ck[None, :])
        here = before | (tok[:, None] == ck[None, :])
        gram += [same & before, same & here, same & before, same & here, same & after]
    block = np.repeat(tile[:, None] == np.arange(4)[None, :], 64, axis=1)
    eye = np.tile(np.eye(64), (2, 2))
    head = (r[:, None] // 64) == (r[None, :] // 64)
    rot = np.zeros((128, 128))
    for d in range(128):
        if (d % 32) < 16:
            rot[d + 16, d] = -1.0
        else:
            rot[d - 16, d] = 1.0
    inv = np.float32(10000.0) ** (-np.arange(16, dtype=np.float32) * np.float32(2.0) / np.float32(32))
    t = np.arange(S)
    row, colu = (t // 64).astype(np.float32), (t % 64).astype(np.float32)
    ang = np.zeros((128, TM), np.float32)
    for d in range(128):
        pos = row if (d % 64) < 32 else colu
        ang[d, META:] = pos * inv[d % 16]
    reset = np.broadcast_to((np.arange(TM) % 16 != 0), (128, TM))
    f = lambda x: np.ascontiguousarray(x.astype(np.float32))
    return {"gram_mask": f(np.concatenate(gram, axis=1).reshape(128, 2, 320)), "block_mask": f(block), "eye64": f(eye.reshape(128, 2, 64)),
            "head_ones": f(head), "rot": f(rot), "rope": f(np.stack([np.cos(ang), np.sin(ang)], axis=1)), "reset16": f(reset)}


class Prologue(Stage):

    def act(self, K, P):
        for dst, src in K.loads:
            P.e.dma_start(dst, src).then_inc(P.sem("inputs_loaded"), P.adds("inputs_loaded", 16))
        P.e.wait_ge(P.sem("inputs_loaded"), P.due("inputs_loaded", 0))
        for _ in range(2):
            split_act(K, P)

    def dve(self, K, P):
        for t in range(2):
            P.e.memset(K.zero_credit[:, t:t + 1], 0.0).then_inc(P.sem(f"tile_evacuated{t}"), 2)
        for _ in range(2):
            split_dve(K, P)
        


class Epilogue(Stage):

    def __init__(self, src):
        self.src = src

    def act(self, K, P):
        P.e.dma_start(K.out, self.src).then_inc(P.sem("output_stored"), P.adds("output_stored", 16))
        P.e.wait_ge(P.sem("output_stored"), P.due("output_stored", 0))


def block1(K):
    g1, hh, hl = K.p, K.HH, K.HL
    st = [RmsNorm(K.X, g1["att_norm_g"]), ForgetGates(K.w_fl, 16),
          Store(4, K.XH, K.XL, K.q1), Store(4, K.XH, K.XL, K.k1), Store(4, K.XH, K.XL, K.v1),
          ForgettingAttention(), Narrow(8, K.XH, K.XL, K.X)]
    st += ffn1(K, 0)
    st += [RmsNorm(K.X, g1["hgrn_norm_g"]), LowerBounds(),
           Store(4, K.XH, K.XL, K.q1h, func=ACT.Silu), Store(4, K.XH, K.XL, K.g1, func=ACT.Silu),
           Store(4, K.XH, K.XL, K.f1, func=ACT.Sigmoid), Store(4, K.XH, K.XL, K.i1),
           Hgrn(), Narrow(8, K.XH, K.XL, K.X)]
    st += ffn1(K, 1)
    st += [RmsNorm(K.X, g1["final_norm_g"], out=K.X)]
    return st


def ffn1(K, layer):
    conv = ([K.p[f"ffn_conv_w{layer}{j}"] for j in range(3)], K.p[f"ffn_conv_b{layer}"])
    st = [RmsNorm(K.X, K.p[f"ffn_norm_g{layer}"])]
    for c0, n in FFN_CHUNKS:
        up = GatedUp(n, c0, conv)
        up.xh, up.xl = K.XH, K.XL
        st += [up, Narrow(n, K.HH, K.HL, K.X)]
    return st


def vec_specs():
    v = [("att_norm_g", "att_norm_g", 0), ("hgrn_norm_g", "hgrn_norm_g", 0), ("hgrn_onorm_g", "hgrn_onorm_g", 0),
         ("final_norm_g", "final_norm_g", None)]
    for l in range(2):
        v += [(f"ffn_norm_g{l}", "ffn_norm_g", l), (f"ffn_conv_b{l}", "ffn_conv_b", l)]
        v += [(f"ffn_conv_w{l}{j}", "ffn_conv_w", (l, j)) for j in range(3)]
    return v


CONSTS = [("ident", 128), ("inv_d", 128), ("inv_dv", 128), ("causal", 128), ("ones_row", 512), ("reset64", 512),
          ("causal64", 256), ("one_col", 2), ("flip", 128), ("keep_upper", 128)]


def program(nc, args, out):
    n_panels = args["weights"].shape[0]
    with ExitStack() as ctx:
        K, M = Places(), Mem(nc)
        K.XM, _ = M.new("X", [128, KT, TM])
        K.X = K.XM[:, :, META:TM]
        K.XH, xa = M.new("XH", [128, KT, TM], F32R)
        K.XL, xb = M.new("XL", [128, KT, TM], F32R)
        K.W, _ = M.new("W", [128, 2, PANEL])
        K.WH, _ = M.new("WH", [128, 2, PANEL], F32R)
        K.WL, _ = M.new("WL", [128, 2, PANEL], F32R)
        K.HH, ha = M.new("HH", [128, 12, S], F32R)
        K.HL, _ = M.new("HL", [128, 12, S], F32R)
        consts, _ = M.new("consts", [128, sum(n for _, n in CONSTS)])
        params, _ = M.new("params", [128, args["params"].shape[1]])
        K.R, _ = M.new("R", [128, TM])
        K.zero_credit, _ = M.new("zero_credit", [128, 8])
        K.att_b_f, _ = M.new("att_b_f", [16, 1])
        K.lb_logits, _ = M.new("lb_logits", [128, 16])
        K.lbt, _ = M.new("lbt", [128, 24])
        K.lb, _ = M.new("lb", [128, 16])
        K.PS = ctx.enter_context(nc.psum_tensor("PS", [128, 8, 512], F32))
        at = 0
        cols = {}
        for name, n in CONSTS:
            cols[name] = consts[:, at:at + n]
            at += n
        K.ident, K.inv_d, K.inv_dv, K.causal = cols["ident"], cols["inv_d"], cols["inv_dv"], cols["causal"]
        K.ones_row, K.reset64, K.causal64, K.one_col = cols["ones_row"], cols["reset64"], cols["causal64"], cols["one_col"]
        K.flip, K.keep_upper = cols["flip"], cols["keep_upper"]
        K.p, at = {}, 0
        for name, n in args["param_tiles"]:
            K.p[name] = params[:, at:at + n]
            at += n
        scr = M.at
        room = (M.end - scr) // 32 * 8

        def v(name, shape, words, base=None, dt=F32):
            assert words + int(np.prod(shape[1:])) <= (room if base is None else 24 * S), (name, room)
            return nc.alloc_sbuf_tensor_at(name, shape, dt, offset=(scr if base is None else base) + 4 * words)

        K.Y = v("Y", [128, KT, TM], 0)
        K.w_fl = v("w_fl", [128, KT, 16], 4224)
        K.q1, K.k1 = v("q1", [128, 8, S], 0, ha), v("k1", [128, 8, S], 4096, ha)
        K.qa, K.ka = v("qa", [128, 4, S], 8192, ha), v("ka", [128, 4, S], 10240, ha)
        K.v1 = v("v1", [128, 8, S], 0)
        K.c_rows, K.gate_rows = v("c_rows", [16, S], 4608), v("gate_rows", [16, 2, S], 5120)
        K.pr, K.pT, K.st = v("pr", [128, 3, S], 6144), v("pT", [128, 2, S], 7680), v("st", [128, 3, 4], 10240)
        K.vs, K.vT = v("vs", [128, S], 8704), v("vT", [128, 2, S], 9216)

        K.q1h, K.f1 = v("q1h", [128, 8, S], 0), v("f1", [128, 8, S], 4096)
        K.i1, K.g1 = v("i1", [128, 8, S], 0, ha), v("g1", [128, 8, S], 4096, ha)
        K.h_eb, K.h_ki, K.h_ks, K.h_qd = (v(n, [128, 2, S], 8192 + 1024 * j) for j, n in enumerate(("h_eb", "h_ki", "h_ks", "h_qd")))
        K.aT = v("aT", [128, 256], 12288)
        K.h_b, K.h_k, K.h_i = v("h_b", [128, S], 8192, ha), v("h_k", [128, S], 8704, ha), v("h_i", [128, S], 9216, ha)
        K.diag = v("diag", [128, 2, S], 8192, ha)
        K.iT, K.ksT = v("iT", [128, 4, 128], 9728, ha), v("ksT", [128, 4, 128], 10240, ha)
        K.sp, K.o_sq = v("sp", [128, 8, 128], 10752, ha), v("o_sq", [128, S], 11776, ha)
        K.lf = nc.alloc_sbuf_tensor_at("lf", [128, 8, S], F32, offset=xb)

        K.CV, K.CF = v("CV", [128, 2, 2, S], 4224), v("CF", [128, 2, 2, S], 6272)
        K.SG, K.HF = v("SG", [128, 2, S], 6272), v("HF", [128, 2, S], 7296)

        K.F = v("F", [128, KT, S], 8320)
        K.in2 = v("in2", [128, 24, S], 0, ha)
        K.d_q, K.d_k = (nc.alloc_sbuf_tensor_at(n, [128, 2, 2, S], F32, offset=xa + 4 * 2048 * j) for j, n in enumerate(("d_q", "d_k")))
        K.d_p = nc.alloc_sbuf_tensor_at("d_p", [128, 2, 3, S], F32, offset=xb)
        K.d_vT, K.d_pT, K.d_diag = v("d_vT", [128, 2, S], 0), v("d_pT", [128, 2, S], 1024), v("d_diag", [128, 4, S], 2048)
        K.bias, K.d_st, K.lam = v("bias", [128, 4, 512], 5120), v("d_st", [128, 3, 2, 4], 4096), v("lam", [128, 256], 7184)
        K.lamt, K.bias_t, K.onehot = v("lamt", [128, 8], 7440), v("bias_t", [33, 4], 7448), v("onehot", [33, BIAS_W], 7456)
        K.d_sq = v("d_sq", [128, S], 9128)
        K.bias_rows, K.lam_prod = v("bias_rows", [4, BIAS_W], 9640), v("lam_prod", [128, 128], 10280)
        K.bias_dram = nc.dram_tensor("bias_spread", (4, BIAS_W), F32, kind="Internal").ap()
        K.uv2 = v("uv2", [128, 16, S], 0, ha)
        K.u2, K.v2 = K.uv2[:, 0:8, :], K.uv2[:, 8:16, :]
        K.ws, K.sgu_b, K.one_row2 = v("ws", [128, 8, 128], 4224), v("sgu_b", [1, 8, 128], 5248), K.ones_row
        K.s_vT = v("s_vT", [128, 2, S], 6272)

        if 3 in BLOCKS:
            rest = 4 * 4 * TM
            K.w_gd = v("w_gd", [128, KT, 160], 4224)
            K.mu, K.mu_rest = v("mu", [128, 16, 2], 5504), v("mu_rest", [128, 16], 5536)
            K.rp = v("rp", [128, 16, TM], 0, ha)
            rz = nc.alloc_sbuf_tensor_at("rz", [128, 16 * TM], F32, offset=xa)
            K.rz = rz[:, :].rearrange("p (q t) -> p q t", q=16)
            K.yt = rz[:, 4 * TM:8 * TM].rearrange("p (n c) -> p n c", c=64)
            K.ar = [v("ar0", [128, 4, 4, TM], 0, ha), v("ar1", [128, 4, 4, TM], 0)]
            K.t_s, K.t_a = v("t_s", [128, 2, TM], rest, ha), v("t_a", [128, 2, TM], rest + 2 * TM, ha)
            K.t_k, K.t_n = v("t_k", [128, 2, TM], rest + 4 * TM, ha), v("t_n", [128, TM], rest + 6 * TM, ha)
            K.head_ones = v("head_ones", [128, 128], rest + 7 * TM, ha)
            K.wc = v("wc", [128, 2, 4, N_CHUNK], rest)
            K.reset16, t_kk0, K.t_bi, K.t_bx, K.t_en = (v(f"prepare{j}", [128, TM], rest + 264 + TM * j) for j in range(5))
            K.t_u, K.t_kk = K.t_en, (t_kk0, K.R)
            at = rest + 264 + 5 * TM
            K.w2, K.a2 = v("w2", [128, 512], at), v("a2", [128, 512], at + 512)
            K.t_bc, K.t_c = v("t_bc", [128, N_CHUNK], at + 1024), v("t_c", [128, 2], at + 1064)

            def row(base, at, *named):
                out = []
                for name, shape in named:
                    out.append(v(name, shape, at, base))
                    at += int(np.prod(shape[1:]))
                return out

            (c_st0, c_g0, K.c_n2, K.c_n4, K.c_n8, K.c_p, K.c_bt, c_v0, K.c_r) = row(ha, rest, ("c_st", [128, 2, 5, 64]), ("c_g", [128, 2, 320]), ("c_n2", [128, 2, 128]), ("c_n4", [128, 2, 128]),
                                ("c_n8", [128, 2, 64]), ("c_p", [128, 2, 2, 64]), ("c_bt", [128, 4, 64]), ("c_v", [128, 512]),
                                ("c_r", [128, 512]))
            (K.c_u, c_s0, K.c_y, K.c_yr, K.gram_mask, K.block_mask, K.eye64, c_st1, c_g1) = row(None, rest + 264, ("c_u", [128, 512]), ("c_s", [128, 512]), ("c_y", [128, 512]), ("c_yr", [128, 2, 64]),
                                ("gram_mask", [128, 2, 320]), ("block_mask", [128, 256]), ("eye64", [128, 2, 64]),
                                ("c_st1", [128, 2, 5, 64]), ("c_g1", [128, 2, 320]))
            c_v1 = nc.alloc_sbuf_tensor_at("c_v1", [128, 512], F32, offset=xa + 4 * 12 * TM)
            c_s1 = nc.alloc_sbuf_tensor_at("c_s1", [128, 512], F32, offset=xa + 4 * (12 * TM + 512))
            K.c_s = (c_s0, c_s1)
            K.c_st, K.c_g, K.c_v = (c_st0, c_st1), (c_g0, c_g1), (c_v0, c_v1)
            K.ya = v("ya", [128, 4, S], room - 2048 - 8)
            K.y2, K.yf = v("y2", [128, N_CHUNK, 64], 0, ha), v("yf", [128, 4, S], 2112, ha)
            K.g_c = v("g_c", [128, 2, N_CHUNK], 4160, ha)
            K.g2a, K.g2b = v("g2a", [128, 512], 0), v("g2b", [32, 512], 512)
            (K.a_q, K.a_kv, K.a_t, K.rope, K.rot, K.a_ks, K.a_vT, K.a_p, K.a_st, K.a_pT, K.head_ones2, K.a_v64) = row(None, 0, ("a_q", [128, 4, S]), ("a_kv", [128, 2, TM]), ("a_t", [128, 2, TM]), ("rope", [128, 2, TM]),
                                ("rot", [128, 128]), ("a_ks", [64, 2, TM]), ("a_vT", [128, 5, 128]), 
                                ("a_p", [128, 3, TM]), ("a_st", [128, 4, 4]), ("a_pT", [128, 2, 5, 128]), ("head_ones2", [128, 128]), ("a_v64", [128, 5, 64]))
            K.a_qs = v("a_qs", [64, 4, S], 4 * S + 2 * TM)
            K.gates = v("gates", [128, 16, S], 0)
            A = args
            K.loads3 = [(K.w_gd[:, :, :], A["w_gd"]), (K.mu[:, 0:15, :], A["mu"]), (K.mu[0:32, 15:16, :], A["mu_tail"]),
                        (K.XM[:, :, 0:META], A["meta"])]
            K.loads3b = [(K.w2[:, :], A["w2"]), (K.a2[:, :], A["a2"]), (K.reset16[:, :], A["c3_reset16"]), (K.head_ones[:, :], A["c3_head_ones"])]
            K.loads3c = [(K.gram_mask[:, :, :], A["c3_gram_mask"]), (K.block_mask[:, :], A["c3_block_mask"]), (K.eye64[:, :, :], A["c3_eye64"])]
            K.loads3d = [(K.g2a[:, :], A["g2"][0:128, :]), (K.g2b[:, :], A["g2"][128:160, :])]
            K.loads3e = [(K.rope[:, :, :], A["c3_rope"]), (K.rot[:, :], A["c3_rot"]), (K.head_ones2[:, :], A["c3_head_ones"])]

        K.halves = lambda t, u: t[:, 0:S].rearrange("p (j u c) -> p u j c", u=2, c=64)[:, u]
        K.halves_ps = lambda u: K.PS[:, (7, 3)[u], 0:256].rearrange("p (j c) -> p j c", c=64)
        K.weights = args["weights"]
        K.out = out
        K.loads = [(consts[:, :], args["consts"]), (params[:, :], args["params"]), (K.X[:, :, 0:S], args["x"])]
        if 1 in BLOCKS:
            K.loads += [(K.att_b_f[:, :], args["att_b_f"]), (K.lb_logits[:, :], args["lb_logits"]),
                        (K.w_fl[:, :, :], args["w_fl"])]
        if 2 in BLOCKS:
            K.loads2 = [(K.lam[:, :], args["lam"].partition_broadcast(128)), (K.bias_t[0:32, :], args["rel_bias"]),
                        (K.onehot[:, :], args["onehot"])]
            K.loads2b = [(K.ws[:, :, :], args["ws"]), (K.sgu_b[0:1, :, :], args["sgu_b"])]
        stages = [Prologue()]
        if 1 in BLOCKS:
            stages += block1(K)
        if 2 in BLOCKS:
            stages += block2(K)
        if 3 in BLOCKS:
            stages += block3(K)
        stages += [Epilogue(K.X[:, :, 0:S])]

        sems = {}
        block = ctx.enter_context(nc.Block())

        def engine(e, tag):
            P = Engine(ctx, nc, sems, e, tag)
            P.split_left, P.split_par = n_panels, 0
            return P

        def left_after_prologue(P, stage):
            if isinstance(stage, Prologue):
                P.split_left = n_panels - 2

        @block.sync
        def _(e):
            stream_sync(K, engine(e, "sync"), n_panels)

        pairs = list(zip(stages, stages[1:]))
        for st, after in pairs:
            if isinstance(after, Wide) and after.n >= 3:
                after.after_norm = st.before_panels = st.gives_normed
                after.after_narrow = st.gives_sums
            if isinstance(after, RmsNorm) and st.gives_sums:
                after.after_sums = st.before_norm = True
            if isinstance(after, Narrow) and isinstance(st, (GatedUp, SquaredReluUp)):
                after.after_wide = True

        @block.tensor
        def _(e):
            P = engine(e, "pe")
            for st, after in pairs + [(stages[-1], None)]:
                st.pe(K, P)
                onto_wide = isinstance(after, Wide) and after.n >= 3 and (st.gives_normed or st.gives_sums or st.gives_banks)
                if onto_wide or (isinstance(after, Narrow) and after.after_wide):
                    P.stage_end_open()
                else:
                    P.stage_end()

        @block.scalar
        def _(e):
            P = engine(e, "act")
            for st, after in pairs + [(stages[-1], None)]:
                st.act(K, P)
                left_after_prologue(P, st)
                if isinstance(after, RmsNorm) and after.after_sums:
                    P.stage_end_open()
                else:
                    P.stage_end()
                    P.count("sum_stored", 8 if st.gives_sums else 0)

        @block.vector
        def _(e):
            P = engine(e, "dve")
            for st in stages:
                st.dve(K, P)
                left_after_prologue(P, st)
                P.stage_end()


def wide_panels(w):
    return w.reshape(KT, 128, -1, 256).transpose(2, 1, 0, 3).reshape(-1, 128, PANEL)


def narrow_panels(w):
    return w.reshape(-1, 2, 128, D).transpose(0, 2, 1, 3).reshape(-1, 128, PANEL)


def paired_panels(gate, value):
    g = gate.reshape(KT, 128, -1, 1, 128)
    v = value.reshape(KT, 128, -1, 1, 128)
    return np.concatenate([g, v], axis=3).transpose(2, 1, 0, 3, 4).reshape(-1, 128, PANEL)


def ffn_panels(gate, value, down, chunks):
    out = []
    for c0, n in chunks:
        c = slice(128 * c0, 128 * (c0 + n))
        out += [paired_panels(gate[:, c], value[:, c]), narrow_panels(down[c])]
    return out


def weights1(a):
    w = a["att_w_in"][0]
    out = [wide_panels(w[:, 0:3 * D]), narrow_panels(a["att_w_out"][0])]
    up, down = a["ffn_w_up"], a["ffn_w_down"]
    out += ffn_panels(up[0][:, :FFN], up[0][:, FFN:], down[0], FFN_CHUNKS)
    w = a["hgrn_w_in"][0]
    out += [wide_panels(w[:, c * D:(c + 1) * D]) for c in (0, 3, 1, 2)] + [narrow_panels(a["hgrn_w_out"][0])]
    out += ffn_panels(up[1][:, :FFN], up[1][:, FFN:], down[1], FFN_CHUNKS)
    return out


def make_consts():
    r = np.arange(128)
    c = {
        "ident": np.eye(128),
        "inv_d": np.full((128, 128), 1.0 / D),
        "inv_dv": np.full((128, 128), 1.0 / 128),
        "causal": np.where(r[None, :] <= r[:, None], 0.0, NEG),
        "ones_row": np.ones((128, 512)),
        "reset64": np.broadcast_to((np.arange(512) % 64 != 0).astype(np.float32), (128, 512)),
        "causal64": (np.arange(256)[None, :] % 64 >= (r % 64)[:, None]).astype(np.float32),
        "one_col": np.ones((128, 2)),
        "flip": np.eye(128)[::-1],
        "keep_upper": (r[:, None] <= r[None, :]).astype(np.float32),
    }
    return np.ascontiguousarray(np.concatenate([c[n].astype(np.float32) for n, _ in CONSTS], axis=1))


def kernel(**inputs):
    import concourse.bacc as bacc
    from concourse.bass_utils import run_bass_kernel_spmd

    a = {k: np.asarray(v) for k, v in inputs.items()}
    cols, tiles = [], []
    for name, key, idx in (vec_specs() if 1 in BLOCKS else []) + (specs2() if 2 in BLOCKS else []) + (specs3() if 3 in BLOCKS else []):
        x = a[key] if idx is None else a[key][idx]
        if x.size == 64:
            x = np.concatenate([x, x])
        cols.append(x.reshape(-1, 128).T)
        tiles.append((name, cols[-1].shape[1]))
    weights = []
    if 1 in BLOCKS:
        weights += weights1(a)
    if 2 in BLOCKS:
        weights += weights2(a)
    if 3 in BLOCKS:
        weights += weights3(a)
    arrays = {
        "weights": np.concatenate(weights, axis=0),
        "x": a["x"][0].T.reshape(KT, 128, S).transpose(1, 0, 2),
        "params": np.concatenate(cols, axis=1),
        "consts": make_consts(),
    }
    if 1 in BLOCKS:
        arrays["att_b_f"] = a["att_b_f"].reshape(16, 1)
        arrays["lb_logits"] = a["hgrn_lb_logits"].reshape(2, KT, 128).transpose(2, 0, 1).reshape(128, 16)
        arrays["w_fl"] = a["att_w_in"][0][:, 3 * D:].reshape(KT, 128, 16).transpose(1, 0, 2)
    if 2 in BLOCKS:
        arrays["lam"] = a["diff_lambda_2"].reshape(256)
        arrays["rel_bias"] = a["rel_bias_2"]
        arrays["onehot"] = bucket_onehot()
        arrays["ws"] = a["sgu_w_2"][0].transpose(2, 0, 1)
        arrays["sgu_b"] = a["sgu_b_2"]
    if 3 in BLOCKS:
        w, mu = a["w_in_3"][0], a["rwkv_shift_3"][0]
        arrays["w_gd"] = w[:, 1792:1952].reshape(KT, 128, 160).transpose(1, 0, 2)
        arrays["mu"] = mu[:, 0:1920].reshape(2, 15, 128).transpose(2, 1, 0)
        arrays["mu_tail"] = mu[:, 1920:].T.reshape(32, 1, 2)
        arrays["meta"] = a["meta_tokens_3"].T.reshape(KT, 128, META).transpose(1, 0, 2)
        arrays["w2"] = a["decay_w2_3"].reshape(128, 512)
        arrays["a2"] = a["icl_a2_3"].reshape(128, 512)
        arrays["g2"] = a["gate_w2_3"].reshape(160, 512)
        for name, x in consts3().items():
            arrays["c3_" + name] = x
    nc = bacc.Bacc("TRN2", target_bir_lowering=False, num_devices=1)
    sent, args = {}, {}
    for name, x in arrays.items():
        sent["in_" + name] = np.ascontiguousarray(x)
        args[name] = nc.dram_tensor("in_" + name, x.shape, mybir.dt.from_np(x.dtype), kind="ExternalInput").ap()
    args["param_tiles"] = tiles
    out = nc.dram_tensor("out_0", (128, KT, S), F32, kind="ExternalOutput").ap()
    program(nc, args, out)
    r = run_bass_kernel_spmd(nc, [sent], core_ids=[0])
    y = r.results[0]["out_0"]
    return y.transpose(1, 0, 2).reshape(D, S).T.reshape(1, S, D)
```
